# Optimizing a Trainium2 kernel written in Bass

```python
import functools
import jax, jax.numpy as jnp
from jax import lax
import numpy as np

D_MODEL = 1024
BATCH = 1
SEQ = 1024
DEPTH = 1
DEC_BATCH = 8
DEC_SEQ = 4
PAST_LEN = 2048
PAGE_SIZE = 128

M_HEADS = 4
M_HEAD_DIM = D_MODEL // 8
D_A = M_HEADS * M_HEAD_DIM
CONV_W = 4
M_CHUNK = 128
N_HEADS = 8
HEAD_DIM = D_MODEL // 16
D_B = N_HEADS * HEAD_DIM
KV_GROUPS = 2
HEADS_PER_GROUP = N_HEADS // KV_GROUPS
KV_W = KV_GROUPS * HEAD_DIM
CMP_STRIDE = 16
CMP_BLOCK = 2 * CMP_STRIDE
SLC_BLOCK = 64
N_SELECT = 16
WINDOW = 512
Q_BLOCK = 128
D_FF = -(-8 * D_MODEL // (3 * 256)) * 256
RMS_EPS = 1e-6
NEG = -1e30
BIG = 1e30
SIZES = (2 * D_A, D_A, D_A, M_HEADS, M_HEADS, D_B, KV_W, KV_W, KV_W, KV_W, KV_W, KV_W, 3 * N_HEADS, 2 * D_MODEL)
SPLITS = tuple(int(s) for s in np.cumsum(SIZES)[:-1])
D_IN = sum(SIZES)

kernel_name = "hybrid_mlstm_nsa_decoder_step"

def rmsnorm(x, g):
    xf = x.astype(jnp.float32)
    y = xf * lax.rsqrt(jnp.mean(xf * xf, axis=-1, keepdims=True) + RMS_EPS)
    return (y * g.astype(jnp.float32)).astype(x.dtype)

def alibi_slopes():
    return jnp.asarray(2.0 ** (-8.0 * np.arange(1, N_HEADS + 1) / N_HEADS), jnp.float32)

def masked_softmax(s, mask):
    p = jax.nn.softmax(jnp.where(mask, s, NEG), axis=-1)
    return jnp.where(mask, p, 0.0)

def pad_rows(a, mult):
    pad = (-a.shape[1]) % mult
    return jnp.pad(a, ((0, 0), (0, pad)) + ((0, 0),) * (a.ndim - 2))

def gather_pages(pool, page_table):
    rows = pool[page_table]
    return rows.reshape((page_table.shape[0], -1) + pool.shape[2:])

def causal_conv(u, buf, w, b):
    T = u.shape[1]
    ext = jnp.concatenate([buf.astype(u.dtype), u], axis=1)
    out = b + ext[:, 0:T] * w[0]
    for j in range(1, CONV_W):
        out = out + ext[:, j:j + T] * w[j]
    return out, ext[:, T:]

def mlstm_chunk(carry, inp):
    C, n, m = carry
    q, k, v, ig, lf = inp
    L = q.shape[1]
    Fh = jnp.cumsum(lf, axis=1).transpose(0, 2, 1)
    igh = ig.transpose(0, 2, 1)
    causal = jnp.tril(jnp.ones((L, L), dtype=bool))
    D = jnp.where(causal, Fh[:, :, :, None] - Fh[:, :, None, :] + igh[:, :, None, :], NEG)
    a = Fh + m[:, :, None]
    m_t = jnp.maximum(a, D.max(-1))
    S = jnp.einsum('bthd,bshd->bhts', q, k) * jnp.exp(D - m_t[..., None])
    inter = jnp.exp(a - m_t)
    num = jnp.einsum('bhts,bshd->bthd', S, v) + inter.transpose(0, 2, 1)[..., None] * jnp.einsum('bthk,bhkv->bthv', q, C)
    den = S.sum(-1) + inter * jnp.einsum('bthk,bhk->bht', q, n)
    denom = jnp.maximum(jnp.abs(den), jnp.exp(-m_t)).transpose(0, 2, 1)[..., None]
    h = num / denom
    F_L = Fh[:, :, -1]
    w_s = F_L[:, :, None] - Fh + igh
    m_new = jnp.maximum(F_L + m, w_s.max(-1))
    decay = jnp.exp(F_L + m - m_new)
    ws = jnp.exp(w_s - m_new[..., None])
    C_new = decay[..., None, None] * C + jnp.einsum('bhs,bshk,bshv->bhkv', ws, k, v)
    n_new = decay[..., None] * n + jnp.einsum('bhs,bshk->bhk', ws, k)
    return (C_new, n_new, m_new), h

def mlstm_branch(qk_pre, v_pre, o_pre, i_pre, f_pre, conv_buf, C, n, m, conv_w, conv_b, head_g):
    f32 = jnp.float32
    B, T = qk_pre.shape[:2]
    qk, conv_new = causal_conv(qk_pre, conv_buf, conv_w, conv_b)
    qk = jax.nn.silu(qk.astype(f32))
    q = qk[..., :D_A].reshape(B, T, M_HEADS, M_HEAD_DIM)
    k = qk[..., D_A:].reshape(B, T, M_HEADS, M_HEAD_DIM) * (M_HEAD_DIM ** -0.5)
    v = v_pre.astype(f32).reshape(B, T, M_HEADS, M_HEAD_DIM)
    ig = i_pre.astype(f32)
    lf = jax.nn.log_sigmoid(f_pre.astype(f32))
    L = M_CHUNK if T % M_CHUNK == 0 else T
    nc = T // L

    def chunks(a):
        return jnp.swapaxes(a.reshape((B, nc, L) + a.shape[2:]), 0, 1)

    (C1, n1, m1), h = lax.scan(mlstm_chunk, (C, n, m), (chunks(q), chunks(k), chunks(v), chunks(ig), chunks(lf)))
    h = jnp.swapaxes(h, 0, 1).reshape(B, T, M_HEADS, M_HEAD_DIM)
    mu = jnp.mean(h, axis=-1, keepdims=True)
    var = jnp.mean(jnp.square(h - mu), axis=-1, keepdims=True)
    hn = ((h - mu) * lax.rsqrt(var + RMS_EPS)).reshape(B, T, D_A) * head_g.astype(f32)
    out = jax.nn.sigmoid(o_pre.astype(f32)) * hn
    return out.astype(qk_pre.dtype), conv_new, C1, n1, m1

def compress(rows, w_pos, w_proj):
    B, Lp = rows.shape[:2]
    sub = rows.reshape(B, Lp // CMP_STRIDE, CMP_STRIDE, KV_GROUPS, HEAD_DIM)
    head = jnp.einsum('bnjgd,jd->bngd', sub, w_pos[:CMP_STRIDE])
    tail = jnp.einsum('bnjgd,jd->bngd', sub, w_pos[CMP_STRIDE:])
    pooled = head[:, :-1] + tail[:, 1:]
    return jnp.einsum('bngd,de->bnge', pooled, w_proj)

def to_blocks(a):
    B, Lp = a.shape[:2]
    return a.reshape(B, Lp // SLC_BLOCK, SLC_BLOCK, KV_GROUPS, HEAD_DIM).transpose(0, 3, 1, 2, 4)

def nsa_attend(q, qpos, g, kc, vc, c_end, ksb, vsb, kw, vw, wpos, slopes):
    f32 = jnp.float32
    B, T = q.shape[:2]
    G, I, dh = KV_GROUPS, HEADS_PER_GROUP, HEAD_DIM
    scale = dh ** -0.5
    qg = q.reshape(B, T, G, I, dh)
    gg = g.reshape(B, T, G, I, 3)
    sl = slopes.reshape(G, I)[None, None, :, :, None]
    tq = qpos.astype(f32)
    dist_c = tq[:, None] - c_end[None, :].astype(f32)
    mask_c = (c_end[None, :] <= qpos[:, None])[None, :, None, None, :]
    s_c = jnp.einsum('btgid,bngd->btgin', qg, kc).astype(f32) * scale - sl * dist_c[None, :, None, None, :]
    p_c = masked_softmax(s_c, mask_c)
    o_c = jnp.einsum('btgin,bngd->btgid', p_c.astype(vc.dtype), vc)
    NC = kc.shape[1]
    NS = ksb.shape[2]
    c_start = jnp.arange(NC, dtype=jnp.int32) * CMP_STRIDE
    s_start = jnp.arange(NS, dtype=jnp.int32) * SLC_BLOCK
    overlap = ((c_start[:, None] < s_start[None, :] + SLC_BLOCK) & (c_start[:, None] + CMP_BLOCK > s_start[None, :])).astype(f32)
    imp = jnp.einsum('btgin,nj->btgj', p_c, overlap)
    blk = jnp.arange(NS, dtype=jnp.int32)[None, :]
    cur = (qpos // SLC_BLOCK)[:, None]
    forced = (blk == 0) | (blk == cur) | (blk == cur - 1)
    valid = s_start[None, :] <= qpos[:, None]
    score = jnp.where(forced[None, :, None, :], BIG, jnp.where(valid[None, :, None, :], imp, NEG))
    n_sel = min(N_SELECT, NS)
    _, idx = lax.top_k(score, n_sel)
    idx_g = idx.transpose(0, 2, 1, 3).reshape(B, G, T * n_sel)
    gather = jax.vmap(jax.vmap(lambda a, i: a[i]))
    kg = gather(ksb, idx_g).reshape(B, G, T, n_sel, SLC_BLOCK, dh)
    vg = gather(vsb, idx_g).reshape(B, G, T, n_sel, SLC_BLOCK, dh)
    pos_s = idx[..., None] * SLC_BLOCK + jnp.arange(SLC_BLOCK, dtype=jnp.int32)
    dist_s = tq[None, :, None, None, None] - pos_s.astype(f32)
    mask_s = (pos_s <= qpos[None, :, None, None, None]).reshape(B, T, G, 1, n_sel * SLC_BLOCK)
    s_s = jnp.einsum('btgid,bgtnpd->btginp', qg, kg).astype(f32) * scale - sl[..., None] * dist_s[:, :, :, None]
    p_s = masked_softmax(s_s.reshape(B, T, G, I, n_sel * SLC_BLOCK), mask_s).reshape(B, T, G, I, n_sel, SLC_BLOCK)
    o_s = jnp.einsum('btginp,bgtnpd->btgid', p_s.astype(vg.dtype), vg)
    delta = qpos[:, None] - wpos[None, :]
    mask_w = ((delta >= 0) & (delta <= WINDOW) & (wpos[None, :] >= 0))[None, :, None, None, :]
    s_w = jnp.einsum('btgid,bwgd->btgiw', qg, kw).astype(f32) * scale - sl * delta.astype(f32)[None, :, None, None, :]
    p_w = masked_softmax(s_w, mask_w)
    o_w = jnp.einsum('btgiw,bwgd->btgid', p_w.astype(vw.dtype), vw)
    o = gg[..., 0:1] * o_c + gg[..., 1:2] * o_s + gg[..., 2:3] * o_w
    return o.reshape(B, T, G * I * dh).astype(q.dtype)

def nsa_prompt(q, g, kc, vc, ks, vs, kw, vw, cmp, slopes):
    B, S = q.shape[:2]
    pos_k, pos_v, proj_k, proj_v = cmp
    kc_s = compress(pad_rows(kc, SLC_BLOCK), pos_k, proj_k)
    vc_s = compress(pad_rows(vc, SLC_BLOCK), pos_v, proj_v)
    c_end = jnp.arange(kc_s.shape[1], dtype=jnp.int32) * CMP_STRIDE + (CMP_BLOCK - 1)
    ksb = to_blocks(pad_rows(ks, SLC_BLOCK))
    vsb = to_blocks(pad_rows(vs, SLC_BLOCK))
    kw_pad = jnp.pad(kw, ((0, 0), (WINDOW, 0), (0, 0), (0, 0)))
    vw_pad = jnp.pad(vw, ((0, 0), (WINDOW, 0), (0, 0), (0, 0)))

    def one_block(start):
        qb = lax.dynamic_slice_in_dim(q, start, Q_BLOCK, axis=1)
        gb = lax.dynamic_slice_in_dim(g, start, Q_BLOCK, axis=1)
        kwb = lax.dynamic_slice_in_dim(kw_pad, start, WINDOW + Q_BLOCK, axis=1)
        vwb = lax.dynamic_slice_in_dim(vw_pad, start, WINDOW + Q_BLOCK, axis=1)
        qpos = start + jnp.arange(Q_BLOCK, dtype=jnp.int32)
        wpos = start - WINDOW + jnp.arange(WINDOW + Q_BLOCK, dtype=jnp.int32)
        return nsa_attend(qb, qpos, gb, kc_s, vc_s, c_end, ksb, vsb, kwb, vwb, wpos, slopes)

    starts = jnp.arange(S // Q_BLOCK, dtype=jnp.int32) * Q_BLOCK
    o = lax.map(one_block, starts)
    o = jnp.moveaxis(o, 0, 1).reshape(B, S, D_B)
    keep = min(WINDOW, S)
    return o, kw[:, S - keep:], vw[:, S - keep:]

def nsa_sample(q, g, kc, vc, ks, vs, kw, vw, cmp, slopes, pools, win, page_table):
    T = q.shape[1]
    pos_k, pos_v, proj_k, proj_v = cmp
    pool_kc, pool_vc, pool_ks, pool_vs = pools
    buf_kw, buf_vw = win
    past_len = page_table.shape[1] * PAGE_SIZE

    def full(pool, new):
        past = gather_pages(pool, page_table).astype(new.dtype)
        return pad_rows(jnp.concatenate([past, new], axis=1), SLC_BLOCK)

    kc_s = compress(full(pool_kc, kc), pos_k, proj_k)
    vc_s = compress(full(pool_vc, vc), pos_v, proj_v)
    c_end = jnp.arange(kc_s.shape[1], dtype=jnp.int32) * CMP_STRIDE + (CMP_BLOCK - 1)
    ksb = to_blocks(full(pool_ks, ks))
    vsb = to_blocks(full(pool_vs, vs))
    kw_all = jnp.concatenate([buf_kw.astype(kw.dtype), kw], axis=1)
    vw_all = jnp.concatenate([buf_vw.astype(vw.dtype), vw], axis=1)
    wbuf = buf_kw.shape[1]
    wpos = past_len - wbuf + jnp.arange(wbuf + T, dtype=jnp.int32)
    qpos = past_len + jnp.arange(T, dtype=jnp.int32)
    o = nsa_attend(q, qpos, g, kc_s, vc_s, c_end, ksb, vsb, kw_all, vw_all, wpos, slopes)
    keep = min(WINDOW, wbuf + T)
    return o, kw_all[:, wbuf + T - keep:], vw_all[:, wbuf + T - keep:]

def swiglu(h, w_in, w_out):
    gate, up = jnp.split(h @ w_in, 2, axis=-1)
    return (jax.nn.silu(gate) * up) @ w_out

def trunk_layer(x, lp, conv_buf, C, n, m, attend):
    (g_mix, w_in, b_in, conv_w, conv_b, m_norm, w_a, w_b, w_o, g_ffn, w_ffn_in, w_ffn_out) = lp
    B, T = x.shape[:2]
    h = rmsnorm(x, g_mix)
    proj = h @ w_in + b_in
    (m_qk, m_v, m_o, m_i, m_f, a_q, a_kc, a_vc, a_ks, a_vs, a_kw, a_vw, a_g, g_mrg) = jnp.split(proj, SPLITS, axis=-1)
    h_a, conv_new, C1, n1, m1 = mlstm_branch(m_qk, m_v, m_o, m_i, m_f, conv_buf, C, n, m, conv_w, conv_b, m_norm)

    def kv(a):
        return a.reshape(B, T, KV_GROUPS, HEAD_DIM)

    kc, vc, ks, vs, kw, vw = kv(a_kc), kv(a_vc), kv(a_ks), kv(a_vs), kv(a_kw), kv(a_vw)
    q = a_q.reshape(B, T, N_HEADS, HEAD_DIM)
    gates = jax.nn.sigmoid(a_g.astype(jnp.float32)).reshape(B, T, N_HEADS, 3)
    o_b, kw_state, vw_state = attend(q, gates, kc, vc, ks, vs, kw, vw)
    gm = jax.nn.sigmoid(g_mrg.astype(jnp.float32)).astype(x.dtype)
    y = gm[..., :D_MODEL] * (h_a @ w_a) + gm[..., D_MODEL:] * (o_b @ w_b)
    x = x + y @ w_o
    x = x + swiglu(rmsnorm(x, g_ffn), w_ffn_in, w_ffn_out)
    return x, (kc, vc, ks, vs, kw_state, vw_state, conv_new, C1, n1, m1)

def setup_inputs(seed: int = 0) -> dict:
    key = jax.random.key(seed)
    ks = jax.random.split(key, 40)
    f32 = jnp.float32

    def nrm(k, shape, s=1.0):
        return s * jax.random.normal(k, shape, f32)

    n_pages = PAST_LEN // PAGE_SIZE
    in_use = DEC_BATCH * n_pages
    n_pool = in_use + -(-in_use // 4)
    win_buf = min(WINDOW, PAST_LEN)
    page_table = jax.random.permutation(ks[0], n_pool)[:in_use].reshape(DEC_BATCH, n_pages).astype(jnp.int32)
    pool_shape = (DEPTH, n_pool, PAGE_SIZE, KV_GROUPS, HEAD_DIM)
    win_shape = (DEPTH, DEC_BATCH, win_buf, KV_GROUPS, HEAD_DIM)
    b_in = nrm(ks[1], (DEPTH, D_IN), 0.02)
    b_in = b_in.at[:, SPLITS[3]:SPLITS[4]].add(jnp.linspace(3.0, 6.0, M_HEADS, dtype=f32))
    return {
        "x_prompt": nrm(ks[2], (BATCH, SEQ, D_MODEL)),
        "x_sample": nrm(ks[3], (DEC_BATCH, DEC_SEQ, D_MODEL)),
        "cache_k_cmp": nrm(ks[4], pool_shape),
        "cache_v_cmp": nrm(ks[5], pool_shape),
        "cache_k_slc": nrm(ks[6], pool_shape),
        "cache_v_slc": nrm(ks[7], pool_shape),
        "state_k_win": nrm(ks[8], win_shape),
        "state_v_win": nrm(ks[9], win_shape),
        "state_conv": nrm(ks[10], (DEPTH, DEC_BATCH, CONV_W - 1, 2 * D_A)),
        "state_C": nrm(ks[11], (DEPTH, DEC_BATCH, M_HEADS, M_HEAD_DIM, M_HEAD_DIM), 0.1),
        "state_n": nrm(ks[12], (DEPTH, DEC_BATCH, M_HEADS, M_HEAD_DIM), 0.1),
        "state_m": nrm(ks[13], (DEPTH, DEC_BATCH, M_HEADS)),
        "page_table": page_table,
        "norm_mix": 1.0 + nrm(ks[14], (DEPTH, D_MODEL), 0.02),
        "w_in": nrm(ks[15], (DEPTH, D_MODEL, D_IN), D_MODEL ** -0.5),
        "b_in": b_in,
        "conv_w": nrm(ks[16], (DEPTH, CONV_W, 2 * D_A), CONV_W ** -0.5),
        "conv_b": nrm(ks[17], (DEPTH, 2 * D_A), 0.02),
        "cmp_pos_k": (1.0 + nrm(ks[18], (DEPTH, CMP_BLOCK, HEAD_DIM), 0.5)) * CMP_BLOCK ** -0.5,
        "cmp_pos_v": (1.0 + nrm(ks[19], (DEPTH, CMP_BLOCK, HEAD_DIM), 0.5)) * CMP_BLOCK ** -0.5,
        "cmp_proj_k": nrm(ks[20], (DEPTH, HEAD_DIM, HEAD_DIM), HEAD_DIM ** -0.5),
        "cmp_proj_v": nrm(ks[21], (DEPTH, HEAD_DIM, HEAD_DIM), HEAD_DIM ** -0.5),
        "m_norm": 1.0 + nrm(ks[22], (DEPTH, D_A), 0.02),
        "w_a": nrm(ks[23], (DEPTH, D_A, D_MODEL), D_A ** -0.5),
        "w_b": nrm(ks[24], (DEPTH, D_B, D_MODEL), D_B ** -0.5),
        "w_o": nrm(ks[25], (DEPTH, D_MODEL, D_MODEL), D_MODEL ** -0.5),
        "norm_ffn": 1.0 + nrm(ks[26], (DEPTH, D_MODEL), 0.02),
        "w_ffn_in": nrm(ks[27], (DEPTH, D_MODEL, 2 * D_FF), D_MODEL ** -0.5),
        "w_ffn_out": nrm(ks[28], (DEPTH, D_FF, D_MODEL), D_FF ** -0.5),
        "norm_final": 1.0 + nrm(ks[29], (D_MODEL,), 0.02),
    }

def reference(x_prompt, x_sample, cache_k_cmp, cache_v_cmp, cache_k_slc, cache_v_slc, state_k_win, state_v_win,
              state_conv, state_C, state_n, state_m, page_table, norm_mix, w_in, b_in, conv_w, conv_b,
              cmp_pos_k, cmp_pos_v, cmp_proj_k, cmp_proj_v, m_norm, w_a, w_b, w_o, norm_ffn, w_ffn_in,
              w_ffn_out, norm_final):
    f32 = jnp.float32
    slopes = alibi_slopes()
    yp, ys = x_prompt, x_sample
    p_states, s_states = [], []
    for l in range(DEPTH):
        lp = (norm_mix[l], w_in[l], b_in[l], conv_w[l], conv_b[l], m_norm[l], w_a[l], w_b[l], w_o[l],
              norm_ffn[l], w_ffn_in[l], w_ffn_out[l])
        cmp = (cmp_pos_k[l], cmp_pos_v[l], cmp_proj_k[l], cmp_proj_v[l])
        attend_p = functools.partial(nsa_prompt, cmp=cmp, slopes=slopes)
        conv0 = jnp.zeros((BATCH, CONV_W - 1, 2 * D_A), yp.dtype)
        C0 = jnp.zeros((BATCH, M_HEADS, M_HEAD_DIM, M_HEAD_DIM), f32)
        n0 = jnp.zeros((BATCH, M_HEADS, M_HEAD_DIM), f32)
        m0 = jnp.full((BATCH, M_HEADS), NEG, f32)
        yp, st_p = trunk_layer(yp, lp, conv0, C0, n0, m0, attend_p)
        p_states.append(st_p)
        attend_s = functools.partial(nsa_sample, cmp=cmp, slopes=slopes,
                                     pools=(cache_k_cmp[l], cache_v_cmp[l], cache_k_slc[l], cache_v_slc[l]),
                                     win=(state_k_win[l], state_v_win[l]), page_table=page_table)
        ys, st_s = trunk_layer(ys, lp, state_conv[l], state_C[l].astype(f32), state_n[l].astype(f32),
                               state_m[l].astype(f32), attend_s)
        s_states.append(st_s)
    y_prompt = rmsnorm(yp, norm_final)
    y_sample = rmsnorm(ys, norm_final)
    P = [jnp.stack(a) for a in zip(*p_states)]
    S = [jnp.stack(a) for a in zip(*s_states)]
    return (y_prompt, y_sample, P[0], S[0], P[1], S[1], P[2], S[2], P[3], S[3], P[4], S[4],
            P[5], S[5], P[6], S[6], P[7], S[7], P[8], S[8], P[9], S[9])


_drawn_inputs = setup_inputs


def setup_inputs(seed=0):
    import zlib

    import numpy as np

    out = dict(_drawn_inputs(seed))
    spreads = {}
    factors = {'m_norm': 8.0, 'norm_ffn': 4.023, 'norm_final': 2.931}
    for name, (base, spread) in spreads.items():
        noise = np.random.default_rng([zlib.crc32(name.encode()), seed]).standard_normal(out[name].shape)
        drawn = base * np.exp(spread * noise) if base else spread * noise
        out[name] = __import__('jax').numpy.asarray(drawn.astype(out[name].dtype))
    for name, factor in factors.items():
        out[name] = (out[name] * factor).astype(out[name].dtype)
    return out
```

```python
from contextlib import ExitStack

import numpy as np

import concourse.bass as bass
from concourse import mybir

F32 = mybir.dt.float32
I32 = mybir.dt.int32
U32 = mybir.dt.uint32
ALU = mybir.AluOpType
ACT = mybir.ActivationFunctionType
AX = mybir.AxisListType

P = 128
DM = 1024
KD = DM // P
SEQ = 1024
NB, NT = 8, 4
NS_TOK = NB * NT
TOK = SEQ + NS_TOK
QT = SEQ // P
TT = QT + 1
PAST, PAGE = 2048, 128
MH, MD = 4, 128
DA = MH * MD
CW = 4
NH, HD, NG = 8, 64, 2
HG = NH // NG
GD = NG * HD
STRIDE, CBLK = 16, 32
NSUB = PAST // STRIDE
SBLK, NSEL = 64, 16
NBLK = PAST // SBLK + 1
WIN = 512
DFF = 2816
FT = DFF // P
EPS = 1e-6
NEG = -1e30
BIG = 1e30
SLOPES = [2.0 ** -(h + 1) for h in range(NH)]
KSCALE = float(MD) ** -0.5
QSCALE = float(HD) ** -0.5

C_QK, C_V, C_O, C_I, C_F = 0, 1024, 1536, 2048, 2052
C_AQ, C_KV, C_G, C_MRG = 2056, 2568, 3336, 3360
R_KC, R_VC, R_KS, R_IG, R_FG, R_VS, R_KW, R_VW, R_G, R_END = 0, 128, 256, 384, 388, 392, 520, 648, 776, 800
RW = DA + R_END

CH = TOK // 3
NCH = TOK // CH
XT = CH // 4
TOKEN_CHUNKS = [(0, 512), (512, 512), (1024, NS_TOK)]


class Chain:

    def __init__(self, eng, sem, start=0):
        self.eng, self.sem, self.n = eng, sem, start

    def __call__(self, ins):
        self.n += 1
        ins.then_inc(self.sem, 1)
        self.eng.wait_ge(self.sem, self.n)


def place_constants(k):
    nc = k.nc
    k.ident = k.sb("ident", [P, P])
    k.ones = k.sb("ones", [P, P])
    k.vector_rows = k.sb("vector_rows", [92, P])
    k.cols = k.sb("vector_cols", [P, 92])
    k.rstd_x = k.sb("rstd_x", [P, TT])
    k.ss_x = k.sb("sum_squares_x", [P, TT])
    k.c_norm_mix, k.c_conv_w, k.c_conv_b, k.c_m_norm, k.c_norm_ffn = 0, 8, 40, 48, 52
    k.c_b_qk, k.c_b_o, k.c_b_mrg, k.c_b_q = 60, 68, 72, 88


def stage_norm_in(k):
    nc, ps = k.nc, k.ps
    x_all = k.at("x_all", k.X_OFF, [P, TT, DM])
    square = k.at("x_square", k.X_OFF + TT * DM * 4, [P, DM])
    s_x = [k.sem(f"x_loaded{i}") for i in range(3)]
    s_rows, s_rows_t = k.sem("rows_loaded"), k.sem("rows_turned")
    s_const, s_ss, s_rstd, s_h = k.sem("constants"), k.sem("sum_squares"), k.sem("rstd_ready"), k.sem("h_ready")
    s_turn, s_evac_a, s_evac_v = k.sem("h_turned"), k.sem("hT_evac_act"), k.sem("hT_evac_dve")
    lots = [(0, 2), (2, 5), (5, 8)]

    def token_rows(tt):
        return P if tt < QT else NS_TOK

    with nc.Block() as block:

        @block.sync
        def _(sp):
            xp = k.x_prompt[0].rearrange("(t p) d -> p t d", p=P)
            for n, (a, b) in enumerate(lots):
                sp.dma_start(x_all[:, a:b, :], xp[:, a:b, :]).then_inc(s_x[n], 16)
            sp.dma_start(x_all[0:NS_TOK, QT, :], k.x_sample.rearrange("b t d -> (b t) d")).then_inc(s_x[2], 16)

        @block.gpsimd
        def _(pool):
            pool.memset(k.ones[:], 1.0).then_inc(s_const, 1)
            pool.memset(k.ident[:], 0.0).then_inc(s_const, 1)
            pool.wait_ge(s_const, 2)
            pool.affine_select(out=k.ident[:], in_=k.ident[:], compare_op=ALU.not_equal, fill=1.0, base=0,
                               pattern=[[-1, P]], channel_multiplier=1).then_inc(s_const, 1)
            pool.memset(k.ss_x[:], 1.0).then_inc(s_const, 1)

        @block.scalar
        def _(act):
            rows = k.vector_rows
            for first, n, src in (
                (k.c_norm_mix, 8, k.norm_mix[0].rearrange("(k p) -> k p", p=P)),
                (k.c_conv_w, 32, k.conv_w.rearrange("o w (k p) -> (o w k) p", p=P)),
                (k.c_conv_b, 8, k.conv_b[0].rearrange("(k p) -> k p", p=P)),
                (k.c_m_norm, 4, k.m_norm[0].rearrange("(k p) -> k p", p=P)),
                (k.c_norm_ffn, 8, k.norm_ffn[0].rearrange("(k p) -> k p", p=P)),
                (k.c_b_qk, 8, k.b_in[0, C_QK:C_V].rearrange("(k p) -> k p", p=P)),
                (k.c_b_o, 4, k.b_in[0, C_O:C_I].rearrange("(k p) -> k p", p=P)),
                (k.c_b_mrg, 16, k.b_in[0, C_MRG:].rearrange("(k p) -> k p", p=P)),
            ):
                act.dma_start(rows[first:first + n, :], src).then_inc(s_rows, 16)
            q_bias = k.b_in[0, C_AQ:C_KV].rearrange("(g i d) -> i g d", g=NG, i=HG)
            act.dma_start(rows[k.c_b_q:k.c_b_q + HG, :].rearrange("i (g d) -> i g d", g=NG), q_bias)\
               .then_inc(s_rows, 16)
            act.wait_ge(s_const, 4)
            for tt in range(TT):
                if tt in (0, 2, 5):
                    n = (0, 2, 5).index(tt)
                    act.wait_ge(s_x[n], 32 if n == 2 else 16)
                r = token_rows(tt)
                if tt:
                    act.wait_ge(s_ss, tt)
                act.activation(square[0:r, :], x_all[0:r, tt, :], ACT.Square,
                               accum_out=k.ss_x[0:r, tt:tt + 1]).then_inc(s_ss, 1)
            act.wait_ge(s_rstd, 1)
            act.activation(k.rstd_x[:], k.rstd_x[:], ACT.Sqrt).then_inc(s_rstd, 1)
            for kd in range(KD):
                act.wait_ge(s_turn, kd + 1)
                if kd == 0:
                    act.wait_ge(s_rows_t, 2)
                g = k.cols[:, k.c_norm_mix + kd:k.c_norm_mix + kd + 1]
                act.activation(k.hT[:, kd, 512:1024], ps[:, 3 * (kd % 2) + 1, :], ACT.Copy, scale=g)\
                   .then_inc(s_evac_a, 1)

        @block.vector
        def _(dve):
            dve.wait_ge(s_rows_t, 1)
            dve.tensor_copy(k.cols[:], ps[:, 6, 0:92]).then_inc(s_rows_t, 1)
            dve.wait_ge(s_ss, TT)
            dve.tensor_scalar(k.rstd_x[:], k.ss_x[:], 1.0 / DM, EPS, ALU.mult, ALU.add).then_inc(s_rstd, 1)
            dve.wait_ge(s_rstd, 2)
            dve.reciprocal(k.rstd_x[:], k.rstd_x[:]).then_inc(s_rstd, 1)
            dve.wait_ge(s_rstd, 3)
            for tt in range(TT):
                r = token_rows(tt)
                dve.tensor_scalar(x_all[0:r, tt, :], x_all[0:r, tt, :], k.rstd_x[0:r, tt:tt + 1], None,
                                  ALU.mult).then_inc(s_h, 1)
            for kd in range(KD):
                dve.wait_ge(s_turn, kd + 1)
                dve.wait_ge(s_rows_t, 2)
                g = k.cols[:, k.c_norm_mix + kd:k.c_norm_mix + kd + 1]
                dve.tensor_scalar(k.hT[:, kd, 0:512], ps[:, 3 * (kd % 2), :], g, None, ALU.mult)
                dve.tensor_scalar(k.hT[:, kd, SEQ:TOK], ps[:, 3 * (kd % 2) + 2, 0:NS_TOK], g, None, ALU.mult)\
                   .then_inc(s_evac_v, 1)

        @block.tensor
        def _(pe):
            pe.wait_ge(s_const, 3)
            pe.wait_ge(s_rows, 16 * 9)
            pe.transpose(ps[:, 6, 0:92], k.vector_rows[:], k.ident[0:92, 0:92]).then_inc(s_rows_t, 1)
            for kd in range(KD):
                if kd >= 2:
                    pe.wait_ge(s_evac_v, kd - 1)
                    pe.wait_ge(s_evac_a, kd - 1)
                for tt in range(TT):
                    if kd == 0:
                        pe.wait_ge(s_h, tt + 1)
                    r = token_rows(tt)
                    mm = pe.transpose(ps[:, 3 * (kd % 2) + tt // 4, (tt % 4) * P:(tt % 4) * P + r],
                                      x_all[0:r, tt, kd * P:(kd + 1) * P], k.ident[0:r, 0:r])
                mm.then_inc(s_turn, 1)


def stage_token_major(k):
    nc, ps = k.nc, k.ps
    w = k.at("w_rows", k.X_OFF, [P, KD, RW])
    bias = k.at("b_rows", k.X_OFF + KD * RW * 4, [P, RW])
    s_w = [k.sem(f"w_rows_loaded{i}") for i in range(4)]
    s_bias = k.sem("b_rows_loaded")
    s_mm, s_evac = k.sem("rows_product"), k.sem("rows_evac")
    s_zero, s_kt, s_kt_evac = k.sem("kT_zeroed"), k.sem("k_turned"), k.sem("kT_evac")
    s_store, s_ring = k.rows_stored, k.windows_stored
    segments = [(0, 512, C_V), (512, 896, C_KV), (896, 904, C_I), (904, RW, C_KV + 384)]
    groups = [(0, 512), (512, 904), (904, RW)]

    def token_rows(tt):
        return P if tt < QT else NS_TOK

    with nc.Block() as block:

        @block.sync
        def _(sp):
            w_in = k.w_in[0].rearrange("(k p) n -> p k n", p=P)
            for n, (a, b, c) in enumerate(segments):
                sp.dma_start(w[:, :, a:b], w_in[:, :, c:c + b - a]).then_inc(s_w[n], 16)
            for a, b, c in segments:
                sp.dma_start(bias[:, a:b], k.b_in[0, c:c + b - a].partition_broadcast(P)).then_inc(s_bias, 16)
            outs = [(R_KC, k.o_k_cmp), (R_VC, k.o_v_cmp), (R_KS, k.o_k_slc), (R_VS, k.o_v_slc)]
            for tt in range(TT):
                sp.wait_ge(s_evac, 3 * (tt + 1))
                for col, (o_p, o_s) in outs:
                    if tt < QT:
                        dst = o_p[0, 0, tt * P:(tt + 1) * P].rearrange("t g d -> t (g d)")
                        sp.dma_start(dst, k.rows[:, tt, col:col + GD]).then_inc(s_store, 16)
                    else:
                        dst = o_s[0].rearrange("b t g d -> (b t) (g d)")
                        sp.dma_start(dst, k.rows[0:NS_TOK, tt, col:col + GD]).then_inc(s_store, 16)
                for col, (o_p, o_s), past in ((R_KW, k.o_k_win, k.state_k_win), (R_VW, k.o_v_win, k.state_v_win)):
                    if QT // 2 <= tt < QT:
                        dst = o_p[0, 0, (tt - 4) * P:(tt - 3) * P].rearrange("t g d -> t (g d)")
                        sp.dma_start(dst, k.rows[:, tt, col:col + GD]).then_inc(s_store, 16)
                    elif tt == QT:
                        for b in range(NB):
                            dst = o_s[0, b, WIN - NT:].rearrange("t g d -> t (g d)")
                            sp.dma_start(dst, k.rows[NT * b:NT * (b + 1), tt, col:col + GD]).then_inc(s_store, 16)
            sp.wait_ge(s_store, 16 * (4 * TT + 2 * 4 + 2 * NB))

        @block.scalar
        def _(act):
            for past, o in ((k.state_k_win, k.o_k_win[1]), (k.state_v_win, k.o_v_win[1])):
                act.dma_start(o[0, :, 0:WIN - NT].rearrange("b t g d -> b (t g d)"),
                              past[0, :, NT:].rearrange("b t g d -> b (t g d)")).then_inc(s_ring, 16)
            for tt in range(TT):
                r = token_rows(tt)
                act.wait_ge(s_kt, tt + 1)
                act.wait_ge(s_zero, 1)
                bank = 6 + tt % 2
                for which in range(2):
                    for g in range(NG):
                        rows = slice(g * HD, (g + 1) * HD)
                        ins = act.copy(k.kT_pad[rows, 2 * which + g, tt * P:tt * P + r],
                                       ps[rows, bank, which * P:which * P + r])
                ins.then_inc(s_kt_evac, 1)
            act.wait_ge(s_ring, 32)

        @block.gpsimd
        def _(pool):
            pool.memset(k.kT_pad[:], 0.0).then_inc(s_zero, 1)

        @block.vector
        def _(dve):
            dve.memset(k.v_aug[:, :, :, MD:MD + 1], 1.0)
            dve.wait_ge(s_bias, 64)
            for tt in range(TT):
                r = token_rows(tt)
                for n, (a, b) in enumerate(groups):
                    dve.wait_ge(s_mm, 3 * tt + n + 1)
                    src = ps[0:r, n + 3 * (tt % 2), 0:b - a]
                    if n == 0:
                        dve.tensor_tensor(k.v_aug[0:r, tt, :, 0:MD], src.rearrange("p (h d) -> p h d", h=MH),
                                          bias[0:r, a:b].rearrange("p (h d) -> p h d", h=MH), ALU.add)\
                           .then_inc(s_evac, 1)
                    else:
                        dve.tensor_tensor(k.rows[0:r, tt, a - DA:b - DA], src, bias[0:r, a:b], ALU.add)\
                           .then_inc(s_evac, 1)

        @block.tensor
        def _(pe):
            def turn(tt):
                r = token_rows(tt)
                pe.wait_ge(s_evac, 3 * (tt + 1))
                if tt >= 2:
                    pe.wait_ge(s_kt_evac, tt - 1)
                for which, col in enumerate((R_KS, R_KW)):
                    mm = pe.transpose(ps[:, 6 + tt % 2, which * P:which * P + r],
                                      k.rows[0:r, tt, col:col + GD], k.ident[0:r, 0:r])
                mm.then_inc(s_kt, 1)

            for tt in range(TT):
                r = token_rows(tt)
                for n, (a, b) in enumerate(groups):
                    if tt == 0:
                        for i in ((0,), (1, 2), (3,))[n]:
                            pe.wait_ge(s_w[i], 16)
                    if tt >= 2:
                        pe.wait_ge(s_evac, 3 * (tt - 2) + n + 1)
                    for kd in range(KD):
                        mm = pe.matmul(ps[0:r, n + 3 * (tt % 2), 0:b - a], k.hT[:, kd, tt * P:tt * P + r],
                                       w[:, kd, a:b], start=(kd == 0), stop=(kd == KD - 1))
                    mm.then_inc(s_mm, 1)
                if tt:
                    turn(tt - 1)
            turn(TT - 1)


def stage_feature_major(k):
    nc, ps = k.nc, k.ps
    RING = 3
    NJ = 16
    off = k.RING_OFF
    ring = [k.at(f"w_ring{i}", off + i * 4096, [P, KD, P]) for i in range(RING)]
    off += RING * 4096
    pre = [k.at(f"qk_pre{i}", off + i * TOK * 4, [P, TOK]) for i in range(2)]
    off += 2 * TOK * 4
    conv = [k.at(f"qk_conv{i}", off + i * TOK * 4, [P, TOK]) for i in range(2)]
    off += 2 * TOK * 4
    ext = k.at("sample_ext", off, [P, NB, CW - 1 + NT])
    past_rows = k.at("conv_past", k.AQ_OFF + 3 * TOK * 4, [NB * (CW - 1), 2 * DA])
    CO = NS_TOK + CW - 1
    tail = k.at("conv_tail", k.AT_OFF, [CO, 2 * DA])
    s_full = [k.sem(f"w_ring_full{i}") for i in range(RING)]
    s_used, s_past = k.sem("w_ring_used"), k.sem("conv_past_loaded")
    s_mm, s_evac, s_o_evac = k.sem("feat_product"), k.sem("feat_evac"), k.sem("o_gate_evac")
    s_conv, s_silu = k.sem("conv_ready"), k.sem("silu_ready")
    s_tail, s_tail_evac, s_tail_out, s_chain = k.sem("tail_turned"), k.sem("tail_evac"), k.tail_stored, k.sem("conv_chain")

    def w_cols(j):
        w_in = k.w_in[0].rearrange("(k p) n -> p k n", p=P)
        if j < 8:
            return [(slice(0, P), w_in[:, :, C_QK + j * P:C_QK + (j + 1) * P])]
        if j < 12:
            i = j - 8
            return [(slice(g * HD, (g + 1) * HD), w_in[:, :, C_AQ + (g * HG + i) * HD:C_AQ + (g * HG + i + 1) * HD])
                    for g in range(NG)]
        return [(slice(0, P), w_in[:, :, C_O + (j - 12) * P:C_O + (j - 11) * P])]

    n_dmas = [0] * RING
    full_at = []
    for j in range(NJ):
        n_dmas[j % RING] += len(w_cols(j))
        full_at.append(16 * n_dmas[j % RING])

    def banks(j):
        return [3 * (j % 2) + c for c in range(3)]

    with nc.Block() as block:

        @block.sync
        def _(sp):
            sp.dma_start(past_rows[:], k.state_conv[0].rearrange("b r c -> (b r) c")).then_inc(s_past, 16)
            for j in range(NJ):
                if j >= RING:
                    sp.wait_ge(s_used, j - RING + 1)
                for cols, src in w_cols(j):
                    sp.dma_start(ring[j % RING][:, :, cols], src).then_inc(s_full[j % RING], 16)
            sp.wait_ge(s_tail_evac, 8)
            n = 1
            sp.dma_start(k.o_conv[0][0, 0], tail[0:CW - 1, :]).then_inc(s_tail_out, 16)
            for b in range(NB):
                first = CW - 1 + NT * b + 1
                sp.dma_start(k.o_conv[1][0, b], tail[first:first + CW - 1, :]).then_inc(s_tail_out, 16)
                n += 1
            sp.wait_ge(s_tail_out, 16 * n)

        @block.tensor
        def _(pe):
            def turn_tail(j):
                pe.wait_ge(s_evac, 3 * (j + 1))
                if j >= 1:
                    pe.wait_ge(s_tail_evac, j)
                pe.transpose(ps[0:CO, 6, 0:P], pre[j % 2][:, SEQ - CW + 1:TOK], k.ident[:])
                if j == 0:
                    pe.wait_ge(s_past, 16)
                pe.transpose(ps[:, 7, 0:NB * (CW - 1)], past_rows[:, j * P:(j + 1) * P],
                             k.ident[0:NB * (CW - 1), 0:NB * (CW - 1)]).then_inc(s_tail, 1)

            for j in range(NJ):
                pe.wait_ge(s_full[j % RING], full_at[j])
                if j >= 14:
                    pe.wait_ge(s_o_evac, 3 * (j - 13))
                elif j >= 2:
                    pe.wait_ge(s_evac, 3 * (j - 1))
                for c, (t0, tn) in enumerate(TOKEN_CHUNKS):
                    for kd in range(KD):
                        mm = pe.matmul(ps[:, banks(j)[c], 0:tn], ring[j % RING][:, kd, :],
                                       k.hT[:, kd, t0:t0 + tn], start=(kd == 0), stop=(kd == KD - 1))
                    if c == 2:
                        mm.then_inc(s_used, 1)
                    else:
                        mm.then_inc(s_mm, 1)
                if 1 <= j <= 8:
                    turn_tail(j - 1)

        @block.scalar
        def _(act):
            for j in range(NJ):
                if j < 8:
                    act.wait_ge(s_conv, j + 1)
                    act.activation(k.qk[:, j, :], conv[j % 2][:], ACT.Silu).then_inc(s_silu, 1)
                elif j >= 12:
                    for c, (t0, tn) in enumerate(TOKEN_CHUNKS):
                        if c < 2:
                            act.wait_ge(s_mm, 2 * j + c + 1)
                        else:
                            act.wait_ge(s_used, j + 1)
                        if j == 12 and c == 0:
                            act.wait_ge(s_tail_out, 16 * (1 + NB))
                        bcol = k.cols[:, k.c_b_o + j - 12:k.c_b_o + j - 11]
                        act.activation(k.aT[:, j - 12, t0:t0 + tn], ps[:, banks(j)[c], 0:tn], ACT.Sigmoid,
                                       bias=bcol).then_inc(s_o_evac, 1)

        @block.vector
        def _(dve):
            link = Chain(dve, s_chain)

            def convolve(j):
                buf, out = pre[j % 2], conv[j % 2]
                tap = [k.cols[:, k.c_conv_w + 8 * t + j:k.c_conv_w + 8 * t + j + 1] for t in range(CW)]
                b = k.cols[:, k.c_conv_b + j:k.c_conv_b + j + 1]
                dve.wait_ge(s_tail, j + 1)
                dve.tensor_copy(tail[:, j * P:(j + 1) * P], ps[0:CO, 6, 0:P])
                dve.tensor_copy(ext[:, :, 0:CW - 1], ps[:, 7, 0:NB * (CW - 1)].rearrange("p (b r) -> p b r", b=NB))\
                   .then_inc(s_tail_evac, 1)
                link(dve.tensor_copy(ext[:, :, CW - 1:], buf[:, SEQ:TOK].rearrange("p (b t) -> p b t", b=NB)))
                if j >= 2:
                    dve.wait_ge(s_silu, j - 1)
                link(dve.tensor_scalar(out[:, 0:SEQ], buf[:, 0:SEQ], tap[CW - 1], b, ALU.mult, ALU.add))
                for t in range(1, CW):
                    link(dve.scalar_tensor_tensor(out[:, t:SEQ], buf[:, 0:SEQ - t], tap[CW - 1 - t],
                                                  out[:, t:SEQ], ALU.mult, ALU.add))
                cs = out[:, SEQ:TOK].rearrange("p (b t) -> p b t", b=NB)
                link(dve.tensor_scalar(cs, ext[:, :, 0:NT], tap[0], b, ALU.mult, ALU.add))
                for t in range(1, CW):
                    ins = dve.scalar_tensor_tensor(cs, ext[:, :, t:t + NT], tap[t], cs, ALU.mult, ALU.add)
                    if t < CW - 1:
                        link(ins)
                ins.then_inc(s_conv, 1)

            def scale_keys(j):
                dve.wait_ge(s_silu, j + 1)
                dve.tensor_scalar(k.qk[:, j, :], k.qk[:, j, :], KSCALE, None, ALU.mult)

            for j in range(12):
                for c, (t0, tn) in enumerate(TOKEN_CHUNKS):
                    if c < 2:
                        dve.wait_ge(s_mm, 2 * j + c + 1)
                    else:
                        dve.wait_ge(s_used, j + 1)
                    src = ps[:, banks(j)[c], 0:tn]
                    if j < 8:
                        dve.tensor_scalar(pre[j % 2][:, t0:t0 + tn], src, k.cols[:, k.c_b_qk + j:k.c_b_qk + j + 1],
                                          None, ALU.add).then_inc(s_evac, 1)
                    else:
                        bcol = k.cols[:, k.c_b_q + j - 8:k.c_b_q + j - 7]
                        dve.tensor_scalar(k.aq[:, j - 8, t0:t0 + tn], src, bcol, QSCALE, ALU.add, ALU.mult)\
                           .then_inc(s_evac, 1)
                if j < 8:
                    dve.wait_ge(s_evac, 3 * (j + 1))
                    convolve(j)
                if 5 <= j <= 8:
                    scale_keys(j - 1)


def stage_gates(k):
    nc, ps = k.nc, k.ps
    off = k.RING_OFF

    def row(name, n=TOK):
        nonlocal off
        t = k.at(name, off, [MH, n])
        off += n * 4
        return t

    u, f_m = row("gate_u"), row("gate_F")
    lf = k.at("gate_lf", k.SPARE_OFF, [MH, TOK])
    reset = k.at("gate_reset", k.SPARE_OFF + TOK * 4, [MH, TOK])
    neg_m = k.neg_m
    s_zero, s_turn, s_copy, s_chain = k.sem("gate_zeroed"), k.sem("gate_turned"), k.sem("gate_copied"), k.sem("gate_chain")
    s_abs, s_soft, s_args, s_exp, s_m0 = (k.sem("gate_abs"), k.sem("gate_softplus"), k.sem("gate_args"),
                                          k.sem("gate_exps"), k.sem("m0_loaded"))
    s_cols, s_cols_evac, s_m_out = k.sem("gate_cols"), k.sem("gate_cols_evac"), k.m_stored
    s_const = k.sem("gate_constants")

    def per_sample(t):
        return t[:, SEQ:TOK].rearrange("h (b t) -> h b t", b=NB)

    def per_chunk(t):
        return t[:, 0:SEQ].rearrange("h (c t) -> h c t", c=QT)

    with nc.Block() as block:

        @block.sync
        def _(sp):
            sp.dma_start(k.m_s0[:], k.state_m[0].rearrange("b h -> h b")).then_inc(s_m0, 16)
            sp.wait_ge(s_args, 1)
            sp.dma_start(k.o_m[0][0].rearrange("b h -> h b"), k.m_c[:, QT:QT + 1]).then_inc(s_m_out, 16)
            sp.dma_start(k.o_m[1][0].rearrange("b h -> h b"), k.m_s1[:]).then_inc(s_m_out, 16)
            sp.wait_ge(s_m_out, 32)

        @block.gpsimd
        def _(pool):
            pool.memset(reset[:], 1.0).then_inc(s_const, 1)
            pool.memset(k.select[:], 0.0).then_inc(s_const, 1)
            pool.memset(k.packed[:], 0.0).then_inc(s_const, 1)
            pool.wait_ge(s_const, 3)
            pool.memset(per_chunk(reset)[:, :, 0:1], 0.0)
            pool.memset(per_sample(reset)[:, :, 0:1], 0.0)
            for q in range(2):
                rows = k.select[32 * q:32 * q + MH]
                ins = pool.affine_select(out=rows, in_=rows, compare_op=ALU.not_equal, fill=1.0, base=0,
                                         pattern=[[-1, MH], [0, P]], channel_multiplier=1)
            ins.then_inc(s_const, 1)

        @block.tensor
        def _(pe):
            for which, col in enumerate((R_IG, R_FG)):
                for tt in range(TT):
                    r = P if tt < QT else NS_TOK
                    mm = pe.transpose(ps[0:MH, 3 * which + tt // 4, (tt % 4) * P:(tt % 4) * P + r],
                                      k.rows[0:r, tt, col:col + MH], k.ident[0:r, 0:r])
                mm.then_inc(s_turn, 1)
            pe.wait_ge(s_exp, 5)
            pe.wait_ge(s_args, 3)
            pe.wait_ge(s_const, 4)
            for tt in range(TT):
                r = P if tt < QT else NS_TOK
                pe.transpose(ps[0:r, tt // 4, (tt % 4) * P:(tt % 4 + 1) * P],
                             k.packed[:, tt * P:tt * P + r], k.ident[:])
            for h in range(MH):
                mm = pe.matmul(ps[:, 6, 16 * h:16 * h + 16], k.select[0:MH, h, :], k.decay_row[:],
                               start=True, stop=True)
            mm.then_inc(s_cols, 1)

        @block.scalar
        def _(act):
            act.wait_ge(s_abs, 1)
            act.activation(u[:], u[:], ACT.Exp, scale=-1.0).then_inc(s_soft, 1)
            act.wait_ge(s_soft, 1)
            act.activation(u[:], u[:], ACT.Ln, bias=1.0).then_inc(s_soft, 1)
            act.wait_ge(s_args, 3)
            act.wait_ge(s_const, 4)
            act.activation(k.packed[32:32 + MH, :], lf[:], ACT.Exp).then_inc(s_exp, 1)
            act.activation(k.packed[64:64 + MH, :], f_m[:], ACT.Exp, scale=-1.0).then_inc(s_exp, 1)
            act.activation(k.packed[96:96 + MH, :], reset[:], ACT.Exp).then_inc(s_exp, 1)
            act.activation(k.decay_row[:, 0:QT], k.decay_row[:, 0:QT], ACT.Exp).then_inc(s_exp, 1)
            act.activation(k.decay_row[:, QT:], k.decay_row[:, QT:], ACT.Exp).then_inc(s_exp, 1)

        @block.vector
        def _(dve):
            link = Chain(dve, s_chain)
            dve.wait_ge(s_turn, 2)
            ig, fg = f_m, lf
            for which, dst in enumerate((ig, fg)):
                dve.tensor_copy(dst[:, 0:512], ps[0:MH, 3 * which, :])
                dve.tensor_copy(dst[:, 512:SEQ], ps[0:MH, 3 * which + 1, :])
                ins = dve.tensor_copy(dst[:, SEQ:], ps[0:MH, 3 * which + 2, 0:NS_TOK])
            link(ins)
            dve.scalar_tensor_tensor(u[:], fg[:], -1.0, fg[:], ALU.mult, ALU.max).then_inc(s_abs, 1)
            dve.wait_ge(s_soft, 2)
            link(dve.scalar_tensor_tensor(lf[:], fg[:], 0.0, u[:], ALU.min, ALU.subtract))
            dve.wait_ge(s_const, 4)
            link(dve.tensor_tensor_scan(u[:], reset[:], lf[:], 0.0, ALU.mult, ALU.add))
            link(dve.tensor_tensor(lf[:], ig[:], u[:], ALU.subtract))
            link(dve.tensor_copy(f_m[:], u[:]))
            link(dve.tensor_copy(u[:], lf[:]))
            m_run = neg_m
            link(dve.memset(k.m_c[:, 0:1], NEG))
            for c in range(QT):
                t = slice(c * P, (c + 1) * P)
                link(dve.tensor_tensor_scan(m_run[:, t], u[:, t], u[:, t], k.m_c[:, c:c + 1], ALU.max, ALU.max))
                link(dve.tensor_tensor(k.m_c[:, c + 1:c + 2], f_m[:, t][:, P - 1:P], m_run[:, t][:, P - 1:P], ALU.add))
            dve.wait_ge(s_m0, 16)
            su, sm = per_sample(u), per_sample(m_run)
            for t in range(NT):
                before = k.m_s0[:].unsqueeze(2) if t == 0 else sm[:, :, t - 1:t]
                link(dve.tensor_tensor(sm[:, :, t:t + 1], before, su[:, :, t:t + 1], ALU.max))
            dve.tensor_tensor(k.m_s1[:].unsqueeze(2), per_sample(f_m)[:, :, NT - 1:], sm[:, :, NT - 1:], ALU.add)\
               .then_inc(s_args, 1)
            dve.wait_ge(s_args, 1)
            def both(out, in0, in1, op):
                dve.tensor_tensor(per_chunk(out), in0[0].to_broadcast([MH, QT, P]), in1[0].to_broadcast([MH, QT, P]), op)
                return dve.tensor_tensor(per_sample(out), in0[1].to_broadcast([MH, NB, NT]),
                                         in1[1].to_broadcast([MH, NB, NT]), op)

            m_start = (k.m_c[:, 0:QT].unsqueeze(2), k.m_s0[:].unsqueeze(2))
            m_all = (per_chunk(m_run), sm)
            m_last = (per_chunk(m_run)[:, :, P - 1:P], sm[:, :, NT - 1:])
            both(lf, m_start, m_all, ALU.subtract)
            both(reset, (per_chunk(u), su), m_last, ALU.subtract)
            dve.tensor_tensor(k.decay_row[:, 0:QT].unsqueeze(2), m_start[0], m_last[0], ALU.subtract)
            dve.tensor_tensor(k.decay_row[:, QT:].unsqueeze(2), m_start[1], m_last[1], ALU.subtract)
            dve.tensor_copy(k.packed[0:MH, :], u[:])
            dve.tensor_tensor(f_m[:], f_m[:], m_run[:], ALU.add).then_inc(s_args, 1)
            dve.wait_ge(s_args, 2)
            dve.tensor_scalar(neg_m[:], m_run[:], -1.0, None, ALU.mult).then_inc(s_args, 1)
            dve.wait_ge(s_cols, 1)
            for tt in range(TT):
                r = P if tt < QT else NS_TOK
                src = ps[0:r, tt // 4, (tt % 4) * P:(tt % 4 + 1) * P].rearrange("p (q x) -> p q x", q=4)[:, :, 0:MH]
                dve.tensor_copy(k.gate_cols[0:r, tt, :, :], src)
            dve.tensor_copy(k.decay[:], ps[:, 6, 0:64].rearrange("p (h c) -> p h c", h=MH)).then_inc(s_cols_evac, 1)


def stage_mlstm(k):
    nc, ps = k.nc, k.ps
    V1 = MD + 1
    off = k.SPARE_OFF

    def work(name, shape):
        nonlocal off
        t = k.at(name, off, shape)
        size = 4
        for n in shape[1:]:
            size *= n
        off += (size + 31) // 32 * 32
        return t

    weight = work("mlstm_E", [P, MH, P])
    wt = work("mlstm_W", [P, MH, P])
    kws = work("mlstm_Kw", [P, MH, P])
    qi = work("mlstm_Qi", [P, MH, P])
    assert off <= k.HT_OFF
    C_s = k.at("C_samples", k.RING_OFF, [P, NB * MH, V1])
    off = k.WORK_OFF
    hn = work("mlstm_hn", [P, MH, P])
    C_p = work("C_prompt", [P, MH, V1])
    q_b = k.qk[:, 0:MH, 0:NB * (NS_TOK + NT)]
    stats, mv = work("ln_stats", [P, MH, 6]), work("ln_mean_var", [P, MH, 2])
    den, r, tmp = work("ln_den", [P, MH]), work("ln_r", [P, MH]), work("ln_tmp", [P, MH])
    n_cols, n_rows = work("n_cols", [P, NB * MH + MH]), work("n_rows", [NB * MH + MH, P])
    n_in = work("n_in", [NB * MH, P])
    block_of, ws_b = work("in_sample", [NS_TOK, NB]), work("ws_by_sample", [NS_TOK, NB, MH])
    assert off <= k.TOP
    n_c, n_n, s_zero = k.sem("C_loaded"), k.sem("n_loaded"), k.sem("mlstm_zeroed")
    s_bc, s_st, s_kt = k.sem("gates_broadcast"), k.sem("qk_product"), k.sem("keys_turned")
    s_exp, s_mask, s_wt, s_kws, s_qi = (k.sem("E_exps"), k.sem("E_masked"), k.sem("W_ready"), k.sem("Kw_ready"),
                                        k.sem("Qi_ready"))
    s_num, s_dc, s_c, s_var, s_root = (k.sem("num_product"), k.sem("dC_product"), k.sem("C_updated"),
                                       k.sem("var_ready"), k.sem("root_ready"))
    s_hn, s_hnt, s_at, s_out, s_chain = (k.sem("hn_ready"), k.sem("hn_turned"), k.sem("aT_ready"),
                                         k.states_stored, k.sem("mlstm_chain"))
    s_nt, s_nr = k.sem("n_turned"), k.sem("n_rows_ready")
    BCM, BCI, ST, KT, NUM, DC = 0, 1, 2, 3, 4, 6
    S = QT

    def tokens(c):
        return (P if c < S else NS_TOK), slice(c * P, min((c + 1) * P, TOK))

    def heads(bank, n):
        return ps[:, bank, 0:MH * n].rearrange("p (h t) -> p h t", h=MH)

    def pair(bank, h):
        return ps[:, bank + h // 2, (h % 2) * V1:(h % 2 + 1) * V1]

    with nc.Block() as block:

        @block.sync
        def _(sp):
            sp.dma_start(C_s[:, :, 0:MD], k.state_C[0].rearrange("b h k v -> k (b h) v")).then_inc(n_c, 16)
            sp.dma_start(n_in[:], k.state_n[0].rearrange("b h k -> (b h) k")).then_inc(n_n, 16)
            sp.wait_ge(s_c, MH * QT)
            sp.dma_start(k.o_C[0][0, 0].rearrange("h k v -> k h v"), C_p[:, :, 0:MD]).then_inc(s_out, 16)
            sp.wait_ge(s_c, MH * (QT + NB))
            sp.dma_start(k.o_C[1][0].rearrange("b h k v -> k (b h) v"), C_s[:, :, 0:MD]).then_inc(s_out, 16)
            sp.wait_ge(s_nr, 1)
            sp.dma_start(k.o_n[1][0].rearrange("b h k -> (b h) k"), n_rows[0:NB * MH, :]).then_inc(s_out, 16)
            sp.dma_start(k.o_n[0][0, 0], n_rows[NB * MH:, :]).then_inc(s_out, 16)
            sp.wait_ge(s_out, 64)

        @block.gpsimd
        def _(pool):
            pool.memset(C_p[:], 0.0).then_inc(s_zero, 1)
            pool.memset(block_of[:], 1.0).then_inc(s_zero, 1)
            pool.wait_ge(s_zero, 2)
            pool.affine_select(out=block_of[:], in_=block_of[:], compare_op=ALU.is_ge, fill=0.0, base=0,
                               pattern=[[-NT, NB]], channel_multiplier=1).then_inc(s_zero, 1)
            pool.wait_ge(s_zero, 3)
            pool.affine_select(out=block_of[:], in_=block_of[:], compare_op=ALU.is_ge, fill=0.0, base=NT - 1,
                               pattern=[[NT, NB]], channel_multiplier=-1).then_inc(s_zero, 1)
            for c in range(S):
                pool.wait_ge(s_exp, MH * (c + 1))
                if c == 4:
                    pool.wait_ge(s_num, 3)
                    pool.wait_ge(s_qi, 3)
                    pool.memset(q_b, 0.0).then_inc(s_zero, 1)
                pool.affine_select(out=weight[:], in_=weight[:], compare_op=ALU.is_ge, fill=0.0, base=0,
                                   pattern=[[0, MH], [1, P]], channel_multiplier=-1).then_inc(s_mask, 1)
            pool.wait_ge(s_exp, MH * (S + 1))
            e = weight[0:NS_TOK, :, 0:NS_TOK]
            pool.affine_select(out=e, in_=e, compare_op=ALU.is_ge, fill=0.0, base=0,
                               pattern=[[0, MH], [1, NS_TOK]], channel_multiplier=-1).then_inc(s_mask, 1)
            pool.wait_ge(s_mask, S + 1)
            for h in range(MH):
                eh = weight[0:NS_TOK, h, 0:NS_TOK].rearrange("p (b t) -> p b t", b=NB)
                ins = pool.affine_select(out=eh, in_=eh, compare_op=ALU.is_ge, fill=0.0, base=0,
                                         pattern=[[-NT, NB], [0, NT]], channel_multiplier=1)
            ins.then_inc(s_mask, 1)

        @block.tensor
        def _(pe):
            pe.wait_ge(n_n, 16)
            pe.transpose(ps[:, DC, 0:NB * MH], n_in[:], k.ident[0:NB * MH, 0:NB * MH]).then_inc(s_nt, 1)
            for c in range(S + 1):
                n, t = tokens(c)
                if c:
                    pe.wait_ge(s_exp, MH * c)
                    pe.wait_ge(s_qi, c)
                    pe.wait_ge(s_wt, c)
                    pe.wait_ge(s_at, c)
                for h in range(MH):
                    pe.matmul(heads(BCM, n)[:, h], k.select[0:MH, h, :], k.neg_m[:, t], start=True, stop=True)
                for h in range(MH):
                    mm = pe.matmul(heads(BCI, n)[:, h], k.select[32:32 + MH, h, :], k.packed[32:32 + MH, t],
                                   start=True, stop=True)
                mm.then_inc(s_bc, 1)
                for h in range(MH):
                    mm = pe.matmul(heads(ST, n)[0:n, h], k.qk[:, MH + h, t], k.qk[:, h, t], start=True, stop=True)
                mm.then_inc(s_st, 1)
                for h in range(MH):
                    mm = pe.transpose(ps[0:n, KT, h * P:(h + 1) * P], k.qk[:, MH + h, t], k.ident[:])
                mm.then_inc(s_kt, 1)
                pe.wait_ge(s_wt, c + 1)
                pe.wait_ge(s_qi, c + 1)
                if c == 0:
                    pe.wait_ge(s_zero, 1)
                if c < S:
                    if c:
                        pe.wait_ge(s_c, MH * c)
                else:
                    pe.wait_ge(n_c, 16)
                    pe.wait_ge(s_nt, 2)
                for h in range(MH):
                    pe.matmul(pair(NUM, h)[0:n], wt[0:n, h, 0:n], k.v_aug[0:n, c, h, :], start=True, stop=False)
                    if c < S:
                        mm = pe.matmul(pair(NUM, h), qi[:, h, :], C_p[:, h, :], start=False, stop=True)
                    else:
                        for b in range(NB):
                            mm = pe.matmul(pair(NUM, h)[0:n], q_b[:, h, b * NS_TOK:(b + 1) * NS_TOK],
                                           C_s[:, b * MH + h, :], start=False, stop=(b == NB - 1))
                mm.then_inc(s_num, 1)
                if c < S:
                    pe.wait_ge(s_kws, c + 1)
                    if c == 0:
                        pe.wait_ge(s_nt, 2)
                    for h in range(MH):
                        mm = pe.matmul(pair(DC, h), kws[:, h, :], k.v_aug[:, c, h, :], start=True, stop=True)
                    mm.then_inc(s_dc, 1)
                else:
                    for b in range(NB):
                        pe.wait_ge(s_kws, c + b + 1)
                        pe.wait_ge(s_c, MH * (S + b))
                        for h in range(MH):
                            mm = pe.matmul(pair(DC, h), kws[0:n, h, :], k.v_aug[0:n, c, h, :], start=True, stop=True)
                        mm.then_inc(s_dc, 1)
                pe.wait_ge(s_hn, c + 1)
                for h in range(MH):
                    mm = pe.transpose(heads(KT, n)[:, h], hn[0:n, h, :], k.ident[0:n, 0:n])
                mm.then_inc(s_hnt, 1)
            pe.wait_ge(s_c, MH * (S + NB))
            pe.wait_ge(s_at, S + 1)
            pe.wait_ge(s_nt, 3)
            pe.transpose(ps[0:NB * MH + MH, KT, 0:P], n_cols[:], k.ident[:]).then_inc(s_nt, 1)

        @block.scalar
        def _(act):
            for c in range(S + 1):
                n, t = tokens(c)
                act.wait_ge(s_bc, c + 1)
                if c:
                    act.wait_ge(s_wt, c)
                for h in range(MH):
                    act.activation(weight[0:n, h, 0:n], heads(BCM, n)[0:n, h], ACT.Exp,
                                   bias=k.gate_cols[0:n, c, 0, h:h + 1]).then_inc(s_exp, 1)
                act.wait_ge(s_var, c + 1)
                act.activation(tmp[0:n], tmp[0:n], ACT.Sqrt).then_inc(s_root, 1)

        @block.vector
        def _(dve):
            link = Chain(dve, s_chain)
            dve.wait_ge(s_nt, 1)
            dve.tensor_copy(C_s[:, :, MD], ps[:, DC, 0:NB * MH]).then_inc(s_nt, 1)
            for c in range(S + 1):
                n, t = tokens(c)
                sample = c == S
                dve.wait_ge(s_bc, c + 1)
                if c:
                    dve.wait_ge(s_num, c)
                if not sample:
                    dve.tensor_tensor(qi[:], k.qk[:, 0:MH, t], heads(BCI, n), ALU.mult).then_inc(s_qi, 1)
                else:
                    dve.wait_ge(s_zero, 5)
                    for h in range(MH):
                        dst = q_b[:, h, :].rearrange("p (b x) -> p b x", b=NB)[:, :, 0:NT]
                        ins = dve.tensor_tensor(dst, k.qk[:, h, t].rearrange("p (b t) -> p b t", b=NB),
                                                heads(BCI, n)[:, h].rearrange("p (b t) -> p b t", b=NB), ALU.mult)
                    ins.then_inc(s_qi, 1)
                dve.wait_ge(s_st, c + 1)
                dve.wait_ge(s_mask, c + 1 if not sample else S + 2)
                dve.tensor_tensor(wt[0:n, :, 0:n], heads(ST, n)[0:n], weight[0:n, :, 0:n], ALU.mult).then_inc(s_wt, 1)
                dve.wait_ge(s_kt, c + 1)
                if not sample:
                    if c:
                        dve.wait_ge(s_dc, c)
                    w_s = k.gate_cols[:, c, 3, :].unsqueeze(2).to_broadcast([P, MH, P])
                    dve.tensor_tensor(kws[:], heads(KT, P), w_s, ALU.mult).then_inc(s_kws, 1)
                else:
                    for b in range(NB):
                        ins = dve.tensor_scalar(ws_b[:, b, :], k.gate_cols[0:n, c, 3, :], block_of[:, b:b + 1], None,
                                                ALU.mult)
                    link(ins)
                    for b in range(NB):
                        dve.wait_ge(s_dc, S + b)
                        dve.tensor_tensor(kws[0:n], heads(KT, P)[0:n],
                                          ws_b[:, b, :].unsqueeze(2).to_broadcast([n, MH, P]), ALU.mult)\
                           .then_inc(s_kws, 1)
                        if b == 0:
                            dve.wait_ge(s_num, S + 1)
                        dve.wait_ge(s_dc, S + b + 1)
                        for h in range(MH):
                            i = b * MH + h
                            dve.scalar_tensor_tensor(C_s[:, i, :], C_s[:, i, :], k.decay[:, h, QT + b:QT + b + 1],
                                                     pair(DC, h), ALU.mult, ALU.add).then_inc(s_c, 1)
                dve.wait_ge(s_num, c + 1)
                for h in range(MH):
                    dve.bn_stats(stats[0:n, h, :], pair(NUM, h)[0:n, 0:MD])
                    ins = dve.tensor_copy(den[0:n, h:h + 1], pair(NUM, h)[0:n, MD:V1])
                link(ins)
                for h in range(MH):
                    dve.bn_aggr(mv[0:n, h, :], stats[0:n, h, :])
                link(dve.scalar_tensor_tensor(r[0:n], den[0:n], -1.0, den[0:n], ALU.mult, ALU.max))
                link(dve.tensor_tensor(den[0:n], r[0:n], k.gate_cols[0:n, c, 2, :], ALU.max))
                link(dve.reciprocal(r[0:n], den[0:n]))
                link(dve.tensor_tensor(tmp[0:n], mv[0:n, :, 1], r[0:n], ALU.mult))
                link(dve.tensor_tensor(tmp[0:n], tmp[0:n], r[0:n], ALU.mult))
                dve.tensor_scalar(tmp[0:n], tmp[0:n], EPS, None, ALU.add).then_inc(s_var, 1)
                dve.wait_ge(s_root, c + 1)
                link(dve.reciprocal(den[0:n], tmp[0:n]))
                link(dve.tensor_tensor(r[0:n], r[0:n], den[0:n], ALU.mult))
                if c:
                    dve.wait_ge(s_hnt, c)
                for h in range(MH):
                    ins = dve.tensor_scalar(hn[0:n, h, :], pair(NUM, h)[0:n, 0:MD], mv[0:n, h, 0:1], r[0:n, h:h + 1],
                                            ALU.subtract, ALU.mult)
                ins.then_inc(s_hn, 1)
                if not sample:
                    dve.wait_ge(s_dc, c + 1)
                    for h in range(MH):
                        dve.scalar_tensor_tensor(C_p[:, h, :], C_p[:, h, :], k.decay[:, h, c:c + 1], pair(DC, h),
                                                 ALU.mult, ALU.add).then_inc(s_c, 1)
                dve.wait_ge(s_hnt, c + 1)
                for h in range(MH):
                    ins = dve.scalar_tensor_tensor(k.aT[:, h, t], heads(KT, n)[:, h],
                                                   k.cols[:, k.c_m_norm + h:k.c_m_norm + h + 1], k.aT[:, h, t],
                                                   ALU.mult, ALU.mult)
                ins.then_inc(s_at, 1)
            dve.wait_ge(s_c, MH * (S + NB))
            dve.tensor_copy(n_cols[:, 0:NB * MH], C_s[:, :, MD])
            dve.tensor_copy(n_cols[:, NB * MH:], C_p[:, :, MD]).then_inc(s_nt, 1)
            dve.wait_ge(s_nt, 4)
            dve.tensor_copy(n_rows[:], ps[0:NB * MH + MH, KT, 0:P]).then_inc(s_nr, 1)


def stage_compress(k):
    nc, ps = k.nc, k.ps
    ROW = STRIDE * GD
    off = k.CMP_END
    x = [k.at(f"strides{i}", off + i * ROW * 4, [P, ROW]) for i in range(2)]
    off += 2 * ROW * 4
    w_pos = [k.at(f"pos_weights{i}", off + i * STRIDE * HD * 4, [P, STRIDE, HD]) for i in range(4)]
    off += 4 * STRIDE * HD * 4
    prod = [k.at(f"pos_product{i}", off + i * ROW * 4, [P, ROW]) for i in range(2)]
    off = k.SPARE_OFF
    half_sums = [k.at(f"half_sums{i}", off + i * 1024, [P, 2, GD]) for i in range(2)]
    off += 2048
    second_t = [k.at(f"second_halfT{i}", off + i * 512, [P, P]) for i in range(2)]
    pooled_t = [k.at(f"pooledT{i}", off + 1024 + i * 512, [P, P]) for i in range(2)]
    off += 2048
    proj = [k.at(f"cmp_proj{i}", off + i * 512, [P, P]) for i in range(2)]
    off += 1024
    table = k.at("page_rows", off, [P, NB], I32)
    lane = k.at("stride_in_page", off + 32, [P, NB], I32)
    scratch = k.at("page_scratch", off + 64, [P, NB])
    assert off + 128 <= k.HT_OFF
    units = [(s, kv) for s in range(NB) for kv in range(2)] + [(NB, kv) for kv in range(2)]
    s_x = [k.sem(f"strides_loaded{i}") for i in range(2)]
    s_xp = [k.sem(f"prompt_strides_loaded{i}") for i in range(2)]
    s_w, s_pt, s_idx, s_zero, s_proj = (k.sem("pos_loaded"), k.sem("table_loaded"), k.sem("indices_ready"),
                                        k.sem("cmp_zeroed"), k.sem("proj_loaded"))
    s_first, s_second, s_sums, s_turn = (k.sem("first_product"), k.sem("second_product"), k.sem("half_sums_ready"),
                                         k.sem("halves_turned"))
    s_sec_t, s_pool, s_map, s_evac, s_chain = (k.sem("second_copied"), k.sem("pooled"), k.sem("mapped"),
                                               k.sem("cmp_evac"), k.sem("cmp_chain"))

    def loaded(eng, u):
        if u < 2 * NB:
            eng.wait_ge(s_x[u % 2], 16 * (u // 2 + 1))
        else:
            eng.wait_ge(s_xp[u % 2], 16)

    def strides(u):
        return NSUB if units[u][0] < NB else SEQ // STRIDE

    with nc.Block() as block:

        @block.sync
        def _(sp):
            for q in range(PAST // PAGE):
                entry = k.page_table[:, q:q + 1].rearrange("b q -> q b").to_broadcast([PAGE // STRIDE, NB])
                sp.dma_start(table[q * 8:(q + 1) * 8, :], entry).then_inc(s_pt, 16)
            for half in range(2):
                for kv, src in enumerate((k.cmp_pos_k, k.cmp_pos_v)):
                    rows = src[0, half * STRIDE:(half + 1) * STRIDE].rearrange("j d -> (j d)").partition_broadcast(P)
                    sp.dma_start(w_pos[2 * kv + half][:].rearrange("p j d -> p (j d)"), rows).then_inc(s_w, 16)
            sp.wait_ge(s_zero, 1)
            for kv, src in enumerate((k.cmp_proj_k, k.cmp_proj_v)):
                for g in range(NG):
                    rows = slice(g * HD, (g + 1) * HD)
                    sp.dma_start(proj[kv][rows, rows], src[0]).then_inc(s_proj, 16)
            for u in range(2 * NB, len(units)):
                sp.wait_ge(s_second, u - 1)
                sp.wait_ge(s_first, u - 1)
                src = (k.o_k_cmp, k.o_v_cmp)[units[u][1]][0][0, 0]
                sp.dma_start(x[u % 2][0:strides(u), :], src.rearrange("(n j) g d -> n (j g d)", j=STRIDE))\
                  .then_inc(s_xp[u % 2], 16)

        @block.gpsimd
        def _(pool):
            pool.memset(proj[0][:], 0.0)
            pool.memset(proj[1][:], 0.0)
            pool.memset(k.kc_pad[:], 0.0).then_inc(s_zero, 1)
            pool.iota(lane[:], pattern=[[0, NB]], base=0, channel_multiplier=1).then_inc(s_zero, 1)
            pool.wait_ge(s_idx, 1)

            def gather(u):
                s, kv = units[u]
                cache = (k.cache_k_cmp, k.cache_v_cmp)[kv]
                pool.indirect_dma_start(
                    out=x[u % 2][:], out_offset=None,
                    in_=cache[0].rearrange("q (s j) g d -> (q s) (j g d)", j=STRIDE),
                    in_offset=bass.IndirectOffsetOnAxis(ap=k.page_idx[:, s:s + 1], axis=0)).then_inc(s_x[u % 2], 16)

            gather(0)
            for u in range(len(units)):
                n = strides(u)
                if 1 <= u + 1 < 2 * NB:
                    if u >= 1:
                        pool.wait_ge(s_second, u)
                        pool.wait_ge(s_first, u)
                    gather(u + 1)
                loaded(pool, u)
                if u == 0:
                    pool.wait_ge(s_w, 64)
                if u:
                    pool.wait_ge(s_sums, u)
                w = w_pos[2 * units[u][1]][0:n].unsqueeze(2).to_broadcast([n, STRIDE, NG, HD])
                pool.tensor_tensor(prod[0][0:n].rearrange("p (j g d) -> p j g d", j=STRIDE, g=NG),
                                   x[u % 2][0:n].rearrange("p (j g d) -> p j g d", j=STRIDE, g=NG), w,
                                   ALU.mult).then_inc(s_first, 1)

        @block.vector
        def _(dve):
            link = Chain(dve, s_chain)
            dve.wait_ge(s_zero, 2)
            dve.wait_ge(s_pt, 16 * 16)
            link(dve.tensor_single_scalar(lane[:], lane[:], 7, ALU.bitwise_and))
            link(dve.tensor_copy(scratch[:], lane[:]))
            dve.scalar_tensor_tensor(k.page_idx[:], table[:], 8.0, scratch[:], ALU.mult, ALU.add).then_inc(s_idx, 1)

            def pool_pair(u):
                n = strides(u)
                dve.wait_ge(s_sec_t, u + 1)
                if u >= 2:
                    dve.wait_ge(s_map, u - 1)
                dve.tensor_tensor(pooled_t[u % 2][:, 0:n - 1], ps[:, u % 2, 0:n - 1], second_t[u % 2][:, 1:n], ALU.add)\
                   .then_inc(s_pool, 1)

            for u in range(len(units)):
                n = strides(u)
                loaded(dve, u)
                if u == 0:
                    dve.wait_ge(s_w, 64)
                w = w_pos[2 * units[u][1] + 1][0:n].unsqueeze(2).to_broadcast([n, STRIDE, NG, HD])
                dve.tensor_tensor(prod[1][0:n].rearrange("p (j g d) -> p j g d", j=STRIDE, g=NG),
                                  x[u % 2][0:n].rearrange("p (j g d) -> p j g d", j=STRIDE, g=NG), w,
                                  ALU.mult).then_inc(s_second, 1)
                dve.wait_ge(s_second, u + 1)
                if u >= 2:
                    dve.wait_ge(s_turn, u - 1)
                dve.tensor_reduce(half_sums[u % 2][0:n, 1, :], prod[1][0:n].rearrange("p (j x) -> p x j", j=STRIDE),
                                  AX.X, ALU.add)
                dve.wait_ge(s_first, u + 1)
                dve.tensor_reduce(half_sums[u % 2][0:n, 0, :], prod[0][0:n].rearrange("p (j x) -> p x j", j=STRIDE),
                                  AX.X, ALU.add).then_inc(s_sums, 1)
                dve.wait_ge(s_sums, u + 1)
                if u:
                    pool_pair(u - 1)
            pool_pair(len(units) - 1)

        @block.scalar
        def _(act):
            def copy_second(u):
                n = strides(u)
                act.wait_ge(s_turn, u + 1)
                if u >= 2:
                    act.wait_ge(s_pool, u - 1)
                act.copy(second_t[u % 2][:, 0:n], ps[:, 2 + u % 2, 0:n]).then_inc(s_sec_t, 1)

            def keep(u):
                s, kv = units[u]
                n = strides(u) - 1
                bank = 4 + u % 2
                act.wait_ge(s_map, u + 1)
                if kv:
                    act.copy(k.vc[0:n, s, :], ps[0:n, bank, 0:GD]).then_inc(s_evac, 1)
                elif s < NB:
                    act.copy(k.kc_t[:, s, 0:n], ps[:, bank, 0:n]).then_inc(s_evac, 1)
                else:
                    act.wait_ge(s_zero, 1)
                    for g in range(NG):
                        rows = slice(g * HD, (g + 1) * HD)
                        ins = act.copy(k.kc_pad[rows, g, 0:n], ps[rows, bank, 0:n])
                    ins.then_inc(s_evac, 1)

            for u in range(len(units)):
                copy_second(u)
                if u:
                    keep(u - 1)
            keep(len(units) - 1)

        @block.tensor
        def _(pe):
            def map_unit(u):
                n = strides(u) - 1
                bank = 4 + u % 2
                pe.wait_ge(s_pool, u + 1)
                if u >= 2:
                    pe.wait_ge(s_evac, u - 1)
                if units[u][1]:
                    mm = pe.matmul(ps[0:n, bank, 0:GD], pooled_t[u % 2][:, 0:n], proj[1][:], start=True, stop=True)
                else:
                    mm = pe.matmul(ps[:, bank, 0:n], proj[0][:], pooled_t[u % 2][:, 0:n], start=True, stop=True)
                mm.then_inc(s_map, 1)

            pe.wait_ge(s_proj, 64)
            for u in range(len(units)):
                n = strides(u)
                pe.wait_ge(s_sums, u + 1)
                if u >= 2:
                    pe.wait_ge(s_pool, u - 1)
                pe.transpose(ps[:, u % 2, 0:n], half_sums[u % 2][0:n, 0, :], k.ident[0:n, 0:n])
                pe.transpose(ps[:, 2 + u % 2, 0:n], half_sums[u % 2][0:n, 1, :], k.ident[0:n, 0:n]).then_inc(s_turn, 1)
                if u:
                    map_unit(u - 1)
            map_unit(len(units) - 1)


def stage_nsa_prompt(k):
    nc, ps = k.nc, k.ps
    NCB = SEQ // STRIDE - 1
    WT = WIN // P + 1
    LW = WT * P
    LC = 120
    off = k.CMP_END
    tables = k.at("bias_tables", off, [P, HG, SEQ + LW + LC])
    off += HG * (SEQ + LW + LC) * 4
    SLEN = SEQ + LW + 64
    s_buf = [k.at(f"scores{i}", off + i * SLEN * 4, [P, SLEN]) for i in range(2)]
    off += 2 * SLEN * 4
    NPT = 4
    pt_buf = [k.at(f"probsT{i}", off + i * 2048, [P, 4, P]) for i in range(NPT)]
    off += NPT * 2048
    assert off <= k.TOP
    off = k.SPARE_OFF
    dist = k.at("distance", off, [P, SEQ])
    off += SEQ * 4
    dist_c = k.at("distance_cmp", off, [P, LC])
    off += 512
    top = [k.at(f"row_max{i}", off + 64 * i, [P, 3]) for i in range(2)]
    neg_top = [k.at(f"row_neg_max{i}", off + 64 * i + 32, [P, 3]) for i in range(2)]
    off += 128
    sums = [k.at(f"row_sum{i}", off + 64 * i, [P, 3]) for i in range(2)]
    factor = [k.at(f"row_factor{i}", off + 64 * i + 32, [P, 3]) for i in range(2)]
    off += 128
    valid = k.at("has_block", off, [P, 1])
    off += 32
    assert off <= k.HT_OFF
    units = [(g, qt, i) for g in range(NG) for qt in range(QT) for i in range(HG)]
    NU = len(units)

    def key_tiles(qt):
        first = max(0, qt - WT + 1)
        return ([("slc", kt, kt * P, P) for kt in range(qt + 1)]
                + [("win", kt, SEQ + (kt - first) * P, P) for kt in range(first, qt + 1)]
                + [("cmp", 0, SEQ + LW, NCB)])

    groups = []
    for n, (g, qt, i) in enumerate(units):
        tiles = key_tiles(qt)
        for a in range(0, len(tiles), 4):
            groups.append((n, tiles[a:a + 4], a + 4 >= len(tiles)))
    first_group = [min(x for x, gr in enumerate(groups) if gr[0] == n) for n in range(NU)] + [len(groups)]
    def evacs_before(which, x):
        return (x + 1 - which) // 2

    s_tab, s_gate = k.sem("tables_ready"), k.sem("branch_gates_ready")
    s_a, s_b = k.sem("slc_scores"), k.sem("win_cmp_scores")
    s_ta, s_tb, s_neg = k.sem("slc_biased"), k.sem("win_cmp_biased"), k.sem("neg_max_ready")
    s_exp, s_fac, s_p, s_chain = k.sem("probs_exp"), k.sem("factor_ready"), k.sem("probs_ready"), k.sem("nsa_chain")
    s_turn, s_pv, s_out, s_scaled = k.sem("probs_turned"), k.sem("pv_product"), k.sem("nsa_out_evac"), k.sem("tables_scaled")
    s_ev = [k.sem("probsT_evac_act"), k.sem("probsT_evac_dve")]
    s_iota = k.sem("distances")

    with nc.Block() as block:

        @block.gpsimd
        def _(pool):
            pool.iota(dist[:], pattern=[[1, SEQ]], base=-(SEQ - P), channel_multiplier=-1,
                      allow_small_or_imprecise_dtypes=True).then_inc(s_iota, 1)
            pool.iota(dist_c[:], pattern=[[STRIDE, LC]], base=CBLK - 1 - 56 * STRIDE, channel_multiplier=-1,
                      allow_small_or_imprecise_dtypes=True).then_inc(s_iota, 1)
            pool.memset(valid[:], 1.0).then_inc(s_iota, 1)
            pool.tensor_copy(k.kT_last[:], k.kT_pad[:, :, SEQ:TOK])
            pool.wait_ge(s_iota, 3)
            pool.affine_select(out=valid[:], in_=valid[:], compare_op=ALU.is_ge, fill=0.0, base=-(CBLK - 1),
                               pattern=[[0, 1]], channel_multiplier=1).then_inc(s_iota, 1)
            pool.wait_ge(s_tab, 3 * HG)
            slc, win, cmp = tables[:, :, 0:SEQ], tables[:, :, SEQ:SEQ + LW], tables[:, :, SEQ + LW:]
            pool.affine_select(out=slc, in_=slc, compare_op=ALU.is_ge, fill=NEG, base=SEQ - P,
                               pattern=[[0, HG], [-1, SEQ]], channel_multiplier=1)
            pool.affine_select(out=cmp, in_=cmp, compare_op=ALU.is_ge, fill=NEG, base=56 * STRIDE - CBLK + 1,
                               pattern=[[0, HG], [-STRIDE, LC]], channel_multiplier=1)
            pool.affine_select(out=win, in_=win, compare_op=ALU.is_ge, fill=NEG, base=WIN,
                               pattern=[[0, HG], [-1, LW]], channel_multiplier=1).then_inc(s_tab, 1)
            pool.wait_ge(s_tab, 3 * HG + 1)
            pool.affine_select(out=win, in_=win, compare_op=ALU.is_ge, fill=NEG, base=0,
                               pattern=[[0, HG], [1, LW]], channel_multiplier=-1).then_inc(s_tab, 1)

        @block.tensor
        def _(pe):
            def scores(n):
                g, qt, i = units[n]
                q = k.aq[:, i, qt * P:(qt + 1) * P]
                if n:
                    pe.wait_ge(s_ta, n)
                keys = (qt + 1) * P
                for a in range(0, keys, 512):
                    m = min(512, keys - a)
                    mm = pe.matmul(ps[:, a // 512, 0:m], q, k.kT_pad[:, g, a:a + m], start=True, stop=True)
                mm.then_inc(s_a, 1)
                if n:
                    pe.wait_ge(s_tb, n)
                first = max(0, qt - WT + 1) * P
                for a in range(0, keys - first, 512):
                    m = min(512, keys - first - a)
                    pe.matmul(ps[:, 2 + a // 512, 0:m], q, k.kT_pad[:, 2 + g, first + a:first + a + m],
                              start=True, stop=True)
                pe.matmul(ps[:, 3, P:P + NCB], q, k.kc_pad[:, g, 0:NCB], start=True, stop=True).then_inc(s_b, 1)

            def turn(x):
                n, tiles, _ = groups[x]
                pe.wait_ge(s_p, n + 1)
                if x >= 2:
                    pe.wait_ge(s_ev[x % 2], evacs_before(x % 2, x))
                for c, (_, _, col, m) in enumerate(tiles):
                    mm = pe.transpose(ps[0:m, 4 + x % 2, c * P:(c + 1) * P], s_buf[n % 2][:, col:col + m], k.ident[:])
                mm.then_inc(s_turn, 1)

            def pv(x):
                n, tiles, last = groups[x]
                g, qt, i = units[n]
                pe.wait_ge(s_ev[x % 2], evacs_before(x % 2, x) + 1)
                if x == first_group[n] and n >= 2:
                    pe.wait_ge(s_out, n - 1)
                for c, (branch, kt, _, m) in enumerate(tiles):
                    cols = slice(g * HD, (g + 1) * HD)
                    if branch == "cmp":
                        v = k.vc[0:m, NB, cols]
                    else:
                        r = R_VS if branch == "slc" else R_VW
                        v = k.rows[:, kt, r + g * HD:r + (g + 1) * HD]
                    mm = pe.matmul(ps[cols, 6 + n % 2, 0:P], v, pt_buf[x % NPT][0:m, c, :],
                                   start=(x == first_group[n] and c == 0), stop=(last and c == len(tiles) - 1))
                mm.then_inc(s_pv, 1)

            scores(0)
            for n in range(NU):
                if n + 1 < NU:
                    scores(n + 1)
                for x in range(first_group[n], first_group[n + 1]):
                    turn(x)
                    if x > first_group[n]:
                        pv(x - 1)
                pv(first_group[n + 1] - 1)

        def evacuate(eng, copy, which, x):
            n, tiles, last = groups[x]
            eng.wait_ge(s_turn, x + 1)
            if x >= NPT:
                eng.wait_ge(s_pv, x - NPT + 1)
            full = sum(1 for t in tiles if t[3] == P)
            ins = None
            if full:
                ins = copy(pt_buf[x % NPT][:, 0:full, :].rearrange("p c q -> p (c q)"), ps[:, 4 + x % 2, 0:full * P])
            if full < len(tiles):
                m = tiles[full][3]
                ins = copy(pt_buf[x % NPT][0:m, full, :], ps[0:m, 4 + x % 2, full * P:(full + 1) * P])
            ins.then_inc(s_ev[which], 1)

        @block.scalar
        def _(act):
            def finish(n):
                g, qt, i = units[n]
                rows = slice(g * HD, (g + 1) * HD)
                act.wait_ge(s_pv, first_group[n + 1])
                act.copy(k.bT[rows, i, qt * P:(qt + 1) * P], ps[rows, 6 + n % 2, 0:P]).then_inc(s_out, 1)

            for r, tiles in ((P, slice(0, QT)), (NS_TOK, slice(QT, TT))):
                g_pre = k.rows[0:r, tiles, R_G:R_END].rearrange("p t (h b) -> p t h b", h=NH)
                act.activation(k.gates[0:r, tiles, :, 0:2], g_pre[:, :, :, 1:3], ACT.Sigmoid)
                ins = act.activation(k.gates[0:r, tiles, :, 2:3], g_pre[:, :, :, 0:1], ACT.Sigmoid)
            ins.then_inc(s_gate, 1)
            for n in range(NU):
                g, qt, i = units[n]
                s = s_buf[n % 2]
                act.wait_ge(s_neg, n + 1)
                for br, (a, m) in enumerate(((0, (qt + 1) * P), (SEQ, min(qt + 1, WT) * P), (SEQ + LW, NCB))):
                    ins = act.activation(s[:, a:a + m], s[:, a:a + m], ACT.Exp, bias=neg_top[n % 2][:, br:br + 1],
                                         accum_out=sums[n % 2][:, br:br + 1])
                ins.then_inc(s_exp, 1)
                if n:
                    for x in range(first_group[n - 1], first_group[n]):
                        if x % 2 == 0:
                            evacuate(act, act.copy, 0, x)
                    finish(n - 1)
            for x in range(first_group[NU - 1], first_group[NU]):
                if x % 2 == 0:
                    evacuate(act, act.copy, 0, x)
            finish(NU - 1)

        @block.vector
        def _(dve):
            link = Chain(dve, s_chain)
            dve.wait_ge(s_iota, 2)
            for i in range(HG):
                dve.tensor_scalar(tables[:, i, 0:SEQ], dist[:], SLOPES[i], None, ALU.mult).then_inc(s_tab, 1)
                dve.tensor_scalar(tables[:, i, SEQ:SEQ + LW], dist[:, SEQ - LW:], SLOPES[i], None, ALU.mult)\
                   .then_inc(s_tab, 1)
                dve.tensor_scalar(tables[:, i, SEQ + LW:], dist_c[:], SLOPES[i], None, ALU.mult).then_inc(s_tab, 1)
            dve.wait_ge(s_tab, 3 * HG + 2)
            dve.wait_ge(s_gate, 1)
            dve.wait_ge(s_iota, 4)
            for n in range(NU):
                g, qt, i = units[n]
                s, b = s_buf[n % 2], n % 2
                if n == NU // 2:
                    link(dve.tensor_scalar(tables[:], tables[:], 2.0 ** -HG, None, ALU.mult))
                tab = tables[:, i, :]
                keys = (qt + 1) * P
                win = min(qt + 1, WT) * P
                if n >= 2:
                    dve.wait_ge(s_turn, first_group[n - 1])
                dve.wait_ge(s_a, n + 1)
                two = ps[:, 0:2, :].rearrange("p a n -> p (a n)")
                dve.tensor_tensor_reduce(s[:, 0:keys], two[:, 0:keys], tab[:, SEQ - keys:SEQ], 1.0, 3 * NEG,
                                         ALU.add, ALU.max, top[b][:, 0:1]).then_inc(s_ta, 1)
                dve.wait_ge(s_b, n + 1)
                two = ps[:, 2:4, :].rearrange("p a n -> p (a n)")
                dve.tensor_tensor_reduce(s[:, SEQ:SEQ + win], two[:, 0:win], tab[:, SEQ + LW - win:SEQ + LW], 1.0,
                                         3 * NEG, ALU.add, ALU.max, top[b][:, 1:2])
                dve.tensor_tensor_reduce(s[:, SEQ + LW:SEQ + LW + NCB], ps[:, 3, P:P + NCB],
                                         tab[:, SEQ + LW + 56 - 8 * qt:][:, 0:NCB], 1.0, 3 * NEG, ALU.add, ALU.max,
                                         top[b][:, 2:3]).then_inc(s_tb, 1)
                dve.wait_ge(s_tb, n + 1)
                dve.tensor_scalar(neg_top[b][:], top[b][:], -1.0, None, ALU.mult).then_inc(s_neg, 1)
                if n:
                    for x in range(first_group[n - 1], first_group[n]):
                        if x % 2 == 1:
                            evacuate(dve, dve.tensor_copy, 1, x)
                dve.wait_ge(s_exp, n + 1)
                link(dve.reciprocal(factor[b][:], sums[b][:]))
                h = g * HG + i
                link(dve.tensor_tensor(factor[b][:], factor[b][:], k.gates[:, qt, h, :], ALU.mult))
                if qt == 0:
                    link(dve.tensor_tensor(factor[b][:, 2:3], factor[b][:, 2:3], valid[:], ALU.mult))
                dve.tensor_scalar(s[:, 0:keys], s[:, 0:keys], factor[b][:, 0:1], None, ALU.mult)
                dve.tensor_scalar(s[:, SEQ:SEQ + win], s[:, SEQ:SEQ + win], factor[b][:, 1:2], None, ALU.mult)
                dve.tensor_scalar(s[:, SEQ + LW:SEQ + LW + NCB], s[:, SEQ + LW:SEQ + LW + NCB], factor[b][:, 2:3],
                                  None, ALU.mult).then_inc(s_p, 1)
            for x in range(first_group[NU - 1], first_group[NU]):
                if x % 2 == 1:
                    evacuate(dve, dve.tensor_copy, 1, x)


def stage_nsa_samples(k):
    nc, ps = k.nc, k.ps
    HALF = NB // 2
    R = NH * NT
    ROW = STRIDE * GD
    NC = NSUB - 1
    SLC, SNEW, WINC, WNEW, CMP = 0, PAST, PAST + NS_TOK, PAST + NS_TOK + WIN, PAST + 2 * NS_TOK + WIN
    WA = WIN // P
    low = k.SPARE_OFF
    rel = k.at("slc_distance", low, [P, PAST])
    assert low + PAST * 4 <= k.HT_OFF
    off = k.KT_OFF
    score = k.at("sample_scores", off, [P, CMP + P])
    off += (CMP + P) * 4
    q_pad = k.at("sample_q_pad", off, [P, NB, R])
    off += NB * R * 4
    k_new = k.at("sample_k_newT", off, [P, 2, NS_TOK])
    off += 2 * NS_TOK * 4
    new_bias = k.at("new_bias", off, [P, 2, NS_TOK])
    off += 256
    same = k.at("same_token", off, [P, P])
    off += 512
    token_of = k.at("token_of_row", off, [NS_TOK, 2, P])
    off += 1024
    rel_c = k.at("cmp_distance", off, [P, P])
    off += 512
    assert off <= k.VA_OFF
    off = k.CMP_END
    NX = 4
    x = [k.at(f"sample_rows{i}", (k.AQ_OFF if i < 2 else off) + i % 2 * ROW * 4, [P, STRIDE, GD]) for i in range(NX)]
    off += 2 * ROW * 4
    kt = k.at("sample_kT", off, [P, PAST])
    off += PAST * 4
    ktw = k.at("sample_kwT", off, [P, WIN])
    off += WIN * 4
    xw = [k.at(f"window_rows{i}", off + i * 2048, [P, WA, GD]) for i in range(2)]
    off += 4096
    NTILE = STRIDE + WA + 3
    pt_off = off
    pt = k.at("sample_probsT", off, [P, NTILE, P])
    off += NTILE * P * 4
    rel_w = k.at("win_distance", off, [P, WIN])
    off += WIN * 4
    win_mask = k.at("win_mask", off, [P, WA])
    row_gates = k.at("row_gates", off + 32, [P, 2, 3])
    off += 64

    def col(name, n=1, dtype=F32):
        nonlocal off
        t = k.at(name, off, [P, n], dtype)
        off += (n * 4 + 31) // 32 * 32
        return t

    ids = col("row_id", 1, I32)
    ints = [col(f"row_int{i}", 1, I32) for i in range(3)]
    slope, t_of, b4_of, h_of = col("row_slope"), col("row_t"), col("row_b4"), col("row_h")
    head_hot = col("row_head", NH)
    a_iota, tmp = col("a_iota", WA), col("row_tmp", 32)
    tmp2 = col("row_tmp2", 32)
    picked = col("gates_picked", 3 * NH)
    tops, neg_tops, sums, factor = col("s_top", 3), col("s_neg_top", 3), col("s_sum", 3), col("s_factor", 3)
    padded = col("cmp_probs_padded", 4 * (NBLK + 1))
    part, imp, rank = col("block_part", NBLK), col("importance", NBLK), col("block_rank", NBLK)
    drop = col("block_drop", NBLK)
    before = k.at("block_before", off, [P, NBLK, NBLK])
    off += NBLK * NBLK * 4
    assert off <= k.TOP, (off, k.TOP)
    gt = k.at("block_gt", pt_off, [P, NBLK, NBLK])
    eq = k.at("block_eq", pt_off + (NBLK * NBLK * 4 + 31) // 32 * 32, [P, NBLK, NBLK])
    assert 2 * NBLK * NBLK * 4 + 64 <= NTILE * P * 4

    s_iota, s_setup, s_chain, s_chain_p = k.sem("s_iotas"), k.sem("s_setup"), k.sem("s_chain"), k.sem("s_chain_pool")
    s_x = [k.sem(f"sample_rows_loaded{i}") for i in range(NX)]
    s_xw = [k.sem(f"window_rows_loaded{i}") for i in range(2)]
    s_turn, s_scores, s_cmp_scores = k.sem("s_k_turned"), k.sem("s_scores_done"), k.sem("s_cmp_scores")
    s_ev = [k.sem("s_turn_evac_act"), k.sem("s_turn_evac_dve")]
    s_tables, s_q = k.sem("s_tables_ready"), k.sem("s_queries_ready")
    s_neg, s_exp, s_pb, s_imp = k.sem("s_neg_ready"), k.sem("s_exps"), k.sem("s_blocks_ready"), k.sem("s_importance")
    s_p, s_pv, s_out, s_slc_used = k.sem("s_probs_ready"), k.sem("s_pv_product"), k.sem("s_out_evac"), k.sem("s_x_used")
    s_xw_used = k.sem("s_xw_used")

    loads = [(h, kv, b) for h in range(2) for kv in range(2) for b in range(HALF)]
    KLOTS = (STRIDE + WA) // 4
    ptiles = ([(SLC + j * P, P) for j in range(STRIDE)] + [(WINC + a * P, P) for a in range(WA)]
              + [(SNEW, NS_TOK), (WNEW, NS_TOK), (CMP, NC)])
    PLOTS = (len(ptiles) + 3) // 4
    LOTS = HALF * KLOTS + PLOTS

    def evacs(which, x):
        return (x + 1 - which) // 2

    with nc.Block() as block:

        @block.sync
        def _(sp):
            for n, (h, kv, b) in enumerate(loads):
                if n >= 2:
                    h_, kv_, b_ = loads[n - 2]
                    sp.wait_ge(s_xw_used if kv_ else s_scores, HALF * h_ + b_ + 1)
                src = (k.state_k_win, k.state_v_win)[kv][0, HALF * h + b]
                sp.dma_start(xw[n % 2][:].rearrange("p a x -> p (a x)"),
                             src.rearrange("(p a) g d -> p (a g d)", a=WA)).then_inc(s_xw[n % 2], 16)

        @block.gpsimd
        def _(pool):
            link = Chain(pool, s_chain_p)

            def gather(n):
                h, kv, b = loads[n]
                if n >= NX:
                    pool.wait_ge(s_slc_used, n - NX + 1)
                cache = (k.cache_k_slc, k.cache_v_slc)[kv]
                pool.indirect_dma_start(
                    out=x[n % NX][:].rearrange("p j x -> p (j x)"), out_offset=None,
                    in_=cache[0].rearrange("q (s j) g d -> (q s) (j g d)", j=STRIDE),
                    in_offset=bass.IndirectOffsetOnAxis(ap=k.page_idx[:, HALF * h + b:HALF * h + b + 1], axis=0))\
                    .then_inc(s_x[n % NX], 16)

            io = dict(allow_small_or_imprecise_dtypes=True)
            pool.iota(ids[:], pattern=[[0, 1]], base=0, channel_multiplier=1).then_inc(s_iota, 1)
            pool.iota(a_iota[:], pattern=[[1, WA]], base=0, channel_multiplier=0, **io).then_inc(s_iota, 1)
            pool.iota(head_hot[:], pattern=[[1, NH]], base=0, channel_multiplier=0, **io).then_inc(s_iota, 1)
            pool.iota(new_bias[:], pattern=[[-4 * HALF, 2], [1, NS_TOK]], base=0, channel_multiplier=0, **io)\
                .then_inc(s_iota, 1)
            pool.memset(q_pad[:], 0.0).then_inc(s_iota, 1)
            pool.memset(padded[:], 0.0).then_inc(s_iota, 1)
            pool.iota(rel_c[:], pattern=[[STRIDE, P]], base=CBLK - 1 - PAST, channel_multiplier=0, **io)
            pool.iota(rel_w[:], pattern=[[1, WA], [WA, P]], base=-WIN, channel_multiplier=0, **io)
            pool.iota(rel[:], pattern=[[1, STRIDE], [STRIDE, NSUB]], base=-PAST, channel_multiplier=0, **io)
            pool.memset(same[:], 0.0)
            pool.memset(token_of[:], 0.0)
            link(pool.memset(before[:], 0.0))
            pool.wait_ge(s_q, 1)
            gather(0)
            gather(1)
            for i in range(HG):
                v = same[:].rearrange("p (b i t) -> p b i t", i=HG, t=NT)
                link(pool.affine_select(out=v, in_=v, compare_op=ALU.not_equal, fill=1.0, base=-NT * i,
                                        pattern=[[-NT * HG, P // (NT * HG)], [0, HG], [-1, NT]], channel_multiplier=1))
            for h in range(2):
                v = token_of[:, h, :].rearrange("p (b h t) -> p b h t", b=HALF, t=NT)
                link(pool.affine_select(out=v, in_=v, compare_op=ALU.not_equal, fill=1.0, base=-NT * HALF * h,
                                        pattern=[[-NT, HALF], [0, NH], [-1, NT]], channel_multiplier=1))
            pool.affine_select(out=before[:], in_=before[:], compare_op=ALU.is_ge, fill=1.0, base=0,
                               pattern=[[-1, NBLK], [1, NBLK]], channel_multiplier=0).then_inc(s_tables, 1)
            for n in range(2, len(loads)):
                gather(n)

        @block.tensor
        def _(pe):
            lot = [0]

            def turn(tiles):
                x_ = lot[0]
                if x_ >= 2:
                    pe.wait_ge(s_ev[x_ % 2], evacs(x_ % 2, x_))
                for c, (src, rows, m) in enumerate(tiles):
                    mm = pe.transpose(ps[0:m, 6 + x_ % 2, c * P:c * P + rows], src, k.ident[0:rows, 0:rows])
                mm.then_inc(s_turn, 1)
                lot[0] += 1

            def evacuated(x_):
                pe.wait_ge(s_ev[x_ % 2], evacs(x_ % 2, x_) + 1)

            pe.wait_ge(s_setup, 1)
            pe.wait_ge(s_tables, 1)
            for h in range(2):
                for b in range(HALF):
                    bb = HALF * h + b
                    rows = slice(R * b, R * (b + 1))
                    n = 2 * HALF * h + b
                    if b == 0 and h:
                        pe.wait_ge(s_out, h)
                    if b == 0:
                        for q in range(HALF):
                            mm = pe.matmul(ps[R * q:R * (q + 1), 5, 2 * NS_TOK:2 * NS_TOK + NC], q_pad[:, bb + q, :],
                                           k.kc_t[:, bb + q, 0:NC], start=True, stop=True)
                        mm.then_inc(s_cmp_scores, 1)
                        mm = pe.matmul(ps[:, 5, 256:256 + 3 * NH], token_of[:, h, :],
                                       k.gates[0:NS_TOK, QT].rearrange("p h b -> p (h b)"), start=True, stop=True)
                        mm.then_inc(s_cmp_scores, 1)
                    pe.wait_ge(s_x[n % NX], 16 * (n // NX + 1))
                    x0 = lot[0]
                    for j in range(0, STRIDE, 4):
                        turn([(x[n % NX][:, j + c, :], P, P) for c in range(4)])
                    pe.wait_ge(s_xw[n % 2], 16 * (n // 2 + 1))
                    turn([(xw[n % 2][:, a, :], P, P) for a in range(WA)])
                    for c in range(PAST // 512):
                        evacuated(x0 + c)
                        mm = pe.matmul(ps[rows, c, :], q_pad[:, bb, :], kt[:, c * 512:(c + 1) * 512],
                                       start=True, stop=True)
                    mm.then_inc(s_slc_used, 1)
                    evacuated(x0 + KLOTS - 1)
                    pe.matmul(ps[rows, 4, :], q_pad[:, bb, :], ktw[:], start=True, stop=True)
                    for which in range(2):
                        mm = pe.matmul(ps[rows, 5, which * NS_TOK:(which + 1) * NS_TOK], q_pad[:, bb, :],
                                       k_new[:, which, :], start=True, stop=True)
                    mm.then_inc(s_scores, 1)
                pe.wait_ge(s_pb, h + 1)
                pe.matmul(ps[:, 5, 320:320 + NBLK], same[:], part[:], start=True, stop=True).then_inc(s_imp, 1)
                pe.wait_ge(s_p, h + 1)
                for a in range(0, len(ptiles), 4):
                    turn([(score[:, c:c + m], P, m) for c, m in ptiles[a:a + 4]])
                evacuated(lot[0] - 2)
                evacuated(lot[0] - 1)
                for b in range(HALF):
                    n = 2 * HALF * h + HALF + b
                    out = ps[:, 4, R * b:R * (b + 1)]
                    cols = slice(R * b, R * (b + 1))
                    pe.wait_ge(s_x[n % NX], 16 * (n // NX + 1))
                    for j in range(STRIDE):
                        mm = pe.matmul(out, x[n % NX][:, j, :], pt[:, j, cols], start=(j == 0), stop=False)
                    mm.then_inc(s_slc_used, 1)
                    pe.wait_ge(s_xw[n % 2], 16 * (n // 2 + 1))
                    for a in range(WA):
                        mm = pe.matmul(out, xw[n % 2][:, a, :], pt[:, STRIDE + a, cols], start=False, stop=False)
                    mm.then_inc(s_xw_used, 1)
                    t0 = STRIDE + WA
                    pe.matmul(out, k.rows[0:NS_TOK, QT, R_VS:R_VS + GD], pt[0:NS_TOK, t0, cols], start=False, stop=False)
                    pe.matmul(out, k.rows[0:NS_TOK, QT, R_VW:R_VW + GD], pt[0:NS_TOK, t0 + 1, cols], start=False,
                              stop=False)
                    mm = pe.matmul(out, k.vc[0:NC, HALF * h + b, :], pt[0:NC, t0 + 2, cols], start=False, stop=True)
                mm.then_inc(s_pv, 1)

        def evacuate(eng, copy, which, h, n):
            x_ = LOTS * h + n
            if x_ % 2 != which:
                return
            eng.wait_ge(s_turn, x_ + 1)
            src = ps[:, 6 + x_ % 2, :]
            if n < HALF * KLOTS:
                b, c = n // KLOTS, n % KLOTS
                done = HALF * h + b
                if done:
                    eng.wait_ge(s_scores, done)
                dst = kt[:, c * 512:(c + 1) * 512] if c < KLOTS - 1 else ktw[:]
                copy(dst, src).then_inc(s_ev[which], 1)
                return
            a = 4 * (n - HALF * KLOTS)
            if h:
                eng.wait_ge(s_pv, h)
            if a + 4 <= STRIDE + WA:
                copy(pt[:, a:a + 4, :].rearrange("p c q -> p (c q)"), src).then_inc(s_ev[which], 1)
                return
            for c, (_, m) in enumerate(ptiles[a:a + 4]):
                ins = copy(pt[0:m, a + c, :], ps[0:m, 6 + x_ % 2, c * P:(c + 1) * P])
            ins.then_inc(s_ev[which], 1)

        @block.scalar
        def _(act):
            for h in range(2):
                act.wait_ge(s_neg, 2 * h + 1)
                act.activation(score[:, CMP:CMP + NC], score[:, CMP:CMP + NC], ACT.Exp, bias=neg_tops[:, 2:3],
                               accum_out=sums[:, 2:3]).then_inc(s_exp, 1)
                for n in range(HALF * KLOTS):
                    evacuate(act, act.copy, 0, h, n)
                act.wait_ge(s_neg, 2 * h + 2)
                act.activation(score[:, SLC:SNEW + NS_TOK], score[:, SLC:SNEW + NS_TOK], ACT.Exp,
                               bias=neg_tops[:, 0:1], accum_out=sums[:, 0:1])
                act.activation(score[:, WINC:WNEW + NS_TOK], score[:, WINC:WNEW + NS_TOK], ACT.Exp,
                               bias=neg_tops[:, 1:2], accum_out=sums[:, 1:2]).then_inc(s_exp, 1)
                for n in range(HALF * KLOTS, LOTS):
                    evacuate(act, act.copy, 0, h, n)

        @block.vector
        def _(dve):
            link = Chain(dve, s_chain)
            dve.wait_ge(s_iota, 6)
            for g in range(NG):
                rows = slice(g * HD, (g + 1) * HD)
                for i in range(HG):
                    dve.tensor_copy(q_pad[rows, :, (HG * g + i) * NT:(HG * g + i + 1) * NT],
                                    k.aq[rows, i, SEQ:TOK].rearrange("p (b t) -> p b t", b=NB))
                for which in range(2):
                    ins = dve.tensor_copy(k_new[rows, which, :], k.kT_last[rows, 2 * which + g, :])
            ins.then_inc(s_q, 1)
            link(dve.tensor_single_scalar(ints[0][:], ids[:], 3, ALU.bitwise_and))
            link(dve.tensor_copy(t_of[:], ints[0][:]))
            link(dve.tensor_single_scalar(ints[0][:], ids[:], 5, ALU.arith_shift_right))
            link(dve.tensor_scalar(b4_of[:], ints[0][:], 4.0, None, ALU.mult))
            link(dve.tensor_single_scalar(ints[1][:], ids[:], 2, ALU.arith_shift_right))
            link(dve.tensor_single_scalar(ints[1][:], ints[1][:], 7, ALU.bitwise_and))
            link(dve.tensor_copy(h_of[:], ints[1][:]))
            link(dve.tensor_scalar(ints[2][:], ints[1][:], -1.0, 126.0, ALU.mult, ALU.add))
            link(dve.tensor_single_scalar(slope[:].bitcast(I32), ints[2][:], 23, ALU.logical_shift_left))
            link(dve.tensor_scalar(head_hot[:], head_hot[:], h_of[:], None, ALU.is_equal))
            link(dve.tensor_scalar(win_mask[:], a_iota[:], t_of[:], NEG, ALU.is_lt, ALU.mult))
            for h in range(2):
                v = new_bias[:, h, :]
                link(dve.tensor_scalar(v, v, b4_of[:], None, ALU.subtract))
                link(dve.tensor_scalar(tmp[:], v, 0.0, None, ALU.is_ge))
                link(dve.tensor_scalar(tmp2[:], v, t_of[:], None, ALU.is_le))
                link(dve.tensor_tensor(tmp[:], tmp[:], tmp2[:], ALU.mult))
                link(dve.tensor_scalar(tmp2[:], v, slope[:], None, ALU.mult))
                link(dve.tensor_tensor(tmp2[:], tmp2[:], tmp[:], ALU.mult))
                link(dve.tensor_scalar(tmp[:], tmp[:], -1.0, BIG, ALU.add, ALU.mult))
                ins = dve.tensor_tensor(v, tmp[:], tmp2[:], ALU.add)
                if h == 0:
                    link(ins)
            ins.then_inc(s_setup, 1)
            dve.wait_ge(s_tables, 1)
            for h in range(2):
                dve.wait_ge(s_cmp_scores, 2 * h + 2)
                s_c = score[:, CMP:CMP + NC]
                link(dve.scalar_tensor_tensor(s_c, rel_c[:, 0:NC], slope[:], ps[:, 5, 64:64 + NC], ALU.mult, ALU.add))
                link(dve.tensor_reduce(tops[:, 2:3], s_c, AX.X, ALU.max))
                dve.tensor_scalar(neg_tops[:, 2:3], tops[:, 2:3], -1.0, None, ALU.mult).then_inc(s_neg, 1)
                picked_v = picked[:].rearrange("p (h b) -> p h b", h=NH)
                link(dve.tensor_tensor(picked_v, ps[:, 5, 256:256 + 3 * NH].rearrange("p (h b) -> p h b", h=NH),
                                       head_hot[:].unsqueeze(2).to_broadcast([P, NH, 3]), ALU.mult))
                link(dve.tensor_reduce(row_gates[:, h, :], picked[:].rearrange("p (h b) -> p b h", h=NH), AX.X, ALU.add))
                dve.wait_ge(s_exp, 2 * h + 1)
                link(dve.reciprocal(factor[:, 2:3], sums[:, 2:3]))
                link(dve.tensor_scalar(padded[:, 1:1 + NC], s_c, factor[:, 2:3], None, ALU.mult))
                link(dve.tensor_scalar(s_c, padded[:, 1:1 + NC], row_gates[:, h, 2:3], None, ALU.mult))
                link(dve.tensor_reduce(part[:], padded[:, 0:4 * NBLK].rearrange("p (j x) -> p j x", x=4), AX.X, ALU.add))
                dve.tensor_tensor(part[:].unsqueeze(2), part[:].unsqueeze(2),
                                  padded[:, 4:4 * NBLK + 4].rearrange("p (j x) -> p j x", x=4)[:, :, 0:1], ALU.add)\
                   .then_inc(s_pb, 1)
                for n in range(HALF * KLOTS):
                    evacuate(dve, dve.tensor_copy, 1, h, n)
                dve.wait_ge(s_imp, h + 1)
                link(dve.tensor_copy(imp[:], ps[:, 5, 320:320 + NBLK]))
                link(dve.memset(imp[:, 0:1], BIG))
                link(dve.memset(imp[:, NBLK - 2:NBLK], BIG))
                other = imp[:].unsqueeze(1).to_broadcast([P, NBLK, NBLK])
                own = imp[:].unsqueeze(2).to_broadcast([P, NBLK, NBLK])
                dve.tensor_tensor(gt[:], other, own, ALU.is_gt)
                link(dve.tensor_tensor(eq[:], other, own, ALU.is_equal))
                link(dve.tensor_tensor(eq[:], eq[:], before[:], ALU.mult))
                link(dve.tensor_tensor(gt[:], gt[:], eq[:], ALU.add))
                link(dve.tensor_reduce(rank[:], gt[:], AX.X, ALU.add))
                link(dve.tensor_scalar(drop[:], rank[:], float(NSEL) - 0.5, NEG, ALU.is_ge, ALU.mult))
                dve.wait_ge(s_scores, HALF * (h + 1))
                for c in range(PAST // 512):
                    cs = slice(c * 512, (c + 1) * 512)
                    ins = dve.scalar_tensor_tensor(score[:, cs], rel[:, cs], slope[:], ps[:, c, :], ALU.mult, ALU.add)
                dve.tensor_tensor(score[:, SNEW:SNEW + NS_TOK], ps[:, 5, 0:NS_TOK], new_bias[:, h, :], ALU.add)
                dve.scalar_tensor_tensor(score[:, WINC:WNEW], rel_w[:], slope[:], ps[:, 4, :], ALU.mult, ALU.add)
                link(dve.tensor_tensor(score[:, WNEW:WNEW + NS_TOK], ps[:, 5, NS_TOK:2 * NS_TOK], new_bias[:, h, :],
                                       ALU.add))
                by_block = score[:, SLC:SNEW].rearrange("p (j b r) -> p j b r", j=STRIDE, r=SBLK // STRIDE)
                dropped = drop[:, 0:NBLK - 1].unsqueeze(1).unsqueeze(3).to_broadcast(
                    [P, STRIDE, NBLK - 1, SBLK // STRIDE])
                dve.tensor_tensor(by_block, by_block, dropped, ALU.add)
                first = score[:, WINC:WNEW].rearrange("p (a n) -> p a n", a=WA)[:, :, 0]
                link(dve.tensor_tensor(first, first, win_mask[:], ALU.add))
                dve.tensor_reduce(tops[:, 0:1], score[:, SLC:SNEW + NS_TOK], AX.X, ALU.max)
                link(dve.tensor_reduce(tops[:, 1:2], score[:, WINC:WNEW + NS_TOK], AX.X, ALU.max))
                dve.tensor_scalar(neg_tops[:, 0:2], tops[:, 0:2], -1.0, None, ALU.mult).then_inc(s_neg, 1)
                dve.wait_ge(s_exp, 2 * h + 2)
                link(dve.reciprocal(factor[:, 0:2], sums[:, 0:2]))
                link(dve.tensor_tensor(factor[:, 0:2], factor[:, 0:2], row_gates[:, h, 0:2], ALU.mult))
                dve.tensor_scalar(score[:, SLC:SNEW + NS_TOK], score[:, SLC:SNEW + NS_TOK], factor[:, 0:1], None, ALU.mult)
                dve.tensor_scalar(score[:, WINC:WNEW + NS_TOK], score[:, WINC:WNEW + NS_TOK], factor[:, 1:2], None,
                                  ALU.mult).then_inc(s_p, 1)
                for n in range(HALF * KLOTS, LOTS):
                    evacuate(dve, dve.tensor_copy, 1, h, n)
                dve.wait_ge(s_pv, h + 1)
                for g in range(NG):
                    rows = slice(g * HD, (g + 1) * HD)
                    src = ps[rows, 4, 0:R * HALF].rearrange("p (b g i t) -> p b g i t", b=HALF, g=NG, i=HG)[:, :, g]
                    t0 = SEQ + h * HALF * NT
                    dst = k.bT[rows, :, t0:t0 + HALF * NT].rearrange("p i (b t) -> p b i t", b=HALF)
                    ins = dve.tensor_copy(dst, src)
                ins.then_inc(s_out, 1)


def stage_merge(k):
    nc, ps = k.nc, k.ps
    RING, RING_O = 3, 4
    KG = 2 * KD + MH + HG
    y = k.at("merged_yT", k.ROWS_OFF, [P, KD, TOK])
    off = k.QK_OFF
    ring = [k.at(f"merge_ring{i}", off + i * KG * 512, [P, KG, P]) for i in range(RING)]
    ss = k.at("x1_square_sums", off, [P, TOK])
    rs = k.at("x1_rstd", off + TOK * 4, [P, TOK])
    square = [k.at(f"x1_square{i}", off + 2 * TOK * 4 + i * CH * 4, [P, CH]) for i in range(2)]
    off += RING * KG * 512
    ring_o = [k.at(f"w_o_ring{i}", off + i * KD * 512, [P, KD, P]) for i in range(RING_O)]
    off += RING_O * KD * 512
    sig = [k.at(f"merge_sigmoid{i}", off + i * 2 * CH * 4, [P, 2, CH]) for i in range(2)]
    off += 4 * CH * 4
    prod = [k.at(f"merge_product{i}", off + i * 2 * CH * 4, [P, 2, CH]) for i in range(2)]
    off += 4 * CH * 4
    assert off <= k.TOP
    x_rows = k.at("x_rows", k.VA_OFF, [XT, TOK // XT, DM])
    s_w = [k.sem(f"merge_ring_full{i}") for i in range(RING)]
    s_wo = [k.sem(f"w_o_ring_full{i}") for i in range(RING_O)]
    s_g, s_ab, s_sig, s_prod, s_y = (k.sem("gate_product"), k.sem("branch_product"), k.sem("merge_sigmoids"),
                                     k.sem("merge_products"), k.sem("y_ready"))
    s_x, s_o, s_x1, s_sq, s_ss = (k.sem("x_rows_loaded"), k.sem("w_o_product"), k.sem("x1_ready"),
                                  k.sem("x1_squared"), k.sem("x1_summed"))
    s_tot, s_rs = k.sem("x1_totals"), k.sem("x1_rstd_ready")
    NU = KD * NCH

    def chunk(c):
        return slice(c * CH, (c + 1) * CH)

    with nc.Block() as block:

        @block.sync
        def _(sp):
            w_in = k.w_in[0].rearrange("(k p) n -> p k n", p=P)
            w_a = k.w_a[0].rearrange("(k p) n -> p k n", p=P)
            w_b = k.w_b[0].rearrange("(g i d) n -> g d i n", g=NG, i=HG)
            for f in range(KD):
                if f >= RING:
                    sp.wait_ge(s_ab, NCH * (f - RING + 1))
                slot, full, cols = ring[f % RING], s_w[f % RING], slice(f * P, (f + 1) * P)
                for part in range(2):
                    src = w_in[:, :, C_MRG + part * DM + f * P:C_MRG + part * DM + (f + 1) * P]
                    sp.dma_start(slot[:, part * KD:(part + 1) * KD, :], src).then_inc(full, 16)
                sp.dma_start(slot[:, 2 * KD:2 * KD + MH, :], w_a[:, :, cols]).then_inc(full, 16)
                for g in range(NG):
                    sp.dma_start(slot[g * HD:(g + 1) * HD, 2 * KD + MH:, :], w_b[g, :, :, cols]).then_inc(full, 16)
            sp.wait_ge(s_ab, NU)
            whole = SEQ // XT
            sp.dma_start(x_rows[:, 0:whole, :], k.x_prompt[0, 0:whole * XT].rearrange("(t p) d -> p t d", p=XT))\
              .then_inc(s_x, 16)
            sp.dma_start(x_rows[0:SEQ - whole * XT, whole, :], k.x_prompt[0, whole * XT:]).then_inc(s_x, 16)
            sp.dma_start(x_rows[SEQ - whole * XT:, whole, :], k.x_sample.rearrange("b t d -> (b t) d"))\
              .then_inc(s_x, 16)

        @block.gpsimd
        def _(pool):
            w_o = k.w_o[0].rearrange("(k p) n -> p k n", p=P)
            for f in range(RING_O):
                pool.dma_start(ring_o[f][:], w_o[:, :, f * P:(f + 1) * P]).then_inc(s_wo[f], 16)
            for u in range(NU):
                pool.wait_ge(s_prod, u + 1)
                f, c = u // NCH, u % NCH
                pool.tensor_tensor(y[:, f, chunk(c)], prod[u % 2][:, 0, :], prod[u % 2][:, 1, :], ALU.add)\
                    .then_inc(s_y, 1)
            for u in range(NU):
                f, c = u // NCH, u % NCH
                if f + RING_O < KD and c == 0:
                    pool.wait_ge(s_o, NCH * (f + 1))
                    pool.dma_start(ring_o[f % RING_O][:], w_o[:, :, (f + RING_O) * P:(f + RING_O + 1) * P])\
                        .then_inc(s_wo[f % RING_O], 16)
                if f:
                    pool.wait_ge(s_sq, u + 1)
                    if f > 1:
                        pool.wait_ge(s_ss, u - 2 * NCH + 1)
                    pool.tensor_tensor(ss[:, chunk(c)], ss[:, chunk(c)], square[u % 2][:], ALU.add).then_inc(s_ss, 1)

        @block.scalar
        def _(act):
            for u in range(NU):
                f, c = u // NCH, u % NCH
                act.wait_ge(s_g, u + 1)
                if u >= 2:
                    act.wait_ge(s_prod, u - 1)
                for part in range(2):
                    col = k.c_b_mrg + part * KD + f
                    ins = act.activation(sig[u % 2][:, part, :], ps[:, 4 * (u % 2) + part, 0:CH], ACT.Sigmoid,
                                         bias=k.cols[:, col:col + 1])
                ins.then_inc(s_sig, 1)
            for u in range(NU):
                f, c = u // NCH, u % NCH
                act.wait_ge(s_x1, u + 1)
                if u >= NCH + 2:
                    act.wait_ge(s_ss, u - NCH - 1)
                dst = ss[:, chunk(c)] if f == 0 else square[u % 2][:]
                act.activation(dst, k.x1[:, f, chunk(c)], ACT.Square).then_inc(s_sq, 1)
            for c in range(NCH):
                act.wait_ge(s_rs, 3 * c + 1)
                act.activation(rs[:, chunk(c)], rs[:, chunk(c)], ACT.Sqrt).then_inc(s_rs, 1)

        @block.vector
        def _(dve):
            for u in range(NU):
                dve.wait_ge(s_sig, u + 1)
                dve.wait_ge(s_ab, u + 1)
                if u >= 2:
                    dve.wait_ge(s_y, u - 1)
                dve.tensor_tensor(prod[u % 2][:], sig[u % 2][:], ps[:, 4 * (u % 2) + 2:4 * (u % 2) + 4, 0:CH], ALU.mult)\
                   .then_inc(s_prod, 1)
            for u in range(NU):
                f, c = u // NCH, u % NCH
                dve.wait_ge(s_o, u + 1)
                dve.tensor_copy(k.x1[:, f, chunk(c)], ps[:, u % 4, 0:CH]).then_inc(s_x1, 1)
            for c in range(NCH):
                dve.wait_ge(s_tot, c + 1)
                if c:
                    dve.wait_ge(s_rs, 3 * c)
                dve.tensor_scalar(rs[:, chunk(c)], ps[:, 4 + c, 0:CH], 1.0 / DM, EPS, ALU.mult, ALU.add).then_inc(s_rs, 1)
                dve.wait_ge(s_rs, 3 * c + 2)
                dve.reciprocal(rs[:, chunk(c)], rs[:, chunk(c)]).then_inc(s_rs, 1)
                dve.wait_ge(s_rs, 3 * c + 3)
                for f in range(KD):
                    g = k.cols[:, k.c_norm_ffn + f:k.c_norm_ffn + f + 1]
                    dve.scalar_tensor_tensor(k.h2[:, f, chunk(c)], k.x1[:, f, chunk(c)], g, rs[:, chunk(c)],
                                             ALU.mult, ALU.mult)

        @block.tensor
        def _(pe):
            for u in range(NU):
                f, c = u // NCH, u % NCH
                w = ring[f % RING]
                if c == 0:
                    pe.wait_ge(s_w[f % RING], 80 * (f // RING + 1))
                if u >= 2:
                    pe.wait_ge(s_sig, u - 1)
                    pe.wait_ge(s_prod, u - 1)
                for part in range(2):
                    for kd in range(KD):
                        mm = pe.matmul(ps[:, 4 * (u % 2) + part, 0:CH], w[:, part * KD + kd, :], k.hT[:, kd, chunk(c)],
                                       start=(kd == 0), stop=(kd == KD - 1))
                mm.then_inc(s_g, 1)
                for part, src in enumerate((k.aT, k.bT)):
                    for h in range(MH):
                        mm = pe.matmul(ps[:, 4 * (u % 2) + 2 + part, 0:CH], w[:, 2 * KD + part * MH + h, :],
                                       src[:, h, chunk(c)], start=(h == 0), stop=(h == MH - 1))
                mm.then_inc(s_ab, 1)
            pe.wait_ge(s_y, NU)
            for u in range(NU):
                f, c = u // NCH, u % NCH
                if c == 0:
                    pe.wait_ge(s_wo[f % RING_O], 16 * (f // RING_O + 1))
                if u >= 4:
                    pe.wait_ge(s_x1, u - 3)
                for kd in range(KD):
                    pe.matmul(ps[:, u % 4, 0:CH], ring_o[f % RING_O][:, kd, :], y[:, kd, chunk(c)],
                              start=(kd == 0), stop=False)
                if u == 0:
                    pe.wait_ge(s_x, 48)
                for t in range(CH // XT):
                    mm = pe.matmul(ps[:, u % 4, t * XT:(t + 1) * XT],
                                   x_rows[:, c * (CH // XT) + t, f * P:(f + 1) * P], k.ident[0:XT, 0:XT],
                                   start=False, stop=(t == CH // XT - 1))
                mm.then_inc(s_o, 1)
            for c in range(NCH):
                pe.wait_ge(s_ss, NU - NCH - NCH + c + 1)
                pe.matmul(ps[:, 4 + c, 0:CH], k.ones[:], ss[:, chunk(c)], start=True, stop=True).then_inc(s_tot, 1)


def stage_ffn(k):
    nc, ps = k.nc, k.ps
    RING, WF, RING_D = 2, 2, 3
    off = k.ROWS_OFF + KD * TOK * 4
    act_t = k.at("ffn_actT", off, [P, FT, TOK])
    off += FT * TOK * 4
    ring = [k.at(f"ffn_ring{i}", off + i * KD * 2 * WF * 512, [P, KD, 2, WF * P]) for i in range(RING)]
    off += RING * KD * 2 * WF * 512
    silu = [k.at(f"ffn_silu{i}", off + i * CH * 4, [P, CH]) for i in range(2)]
    off += 2 * CH * 4
    assert off <= k.TOP
    ring_d = [k.at(f"down_ring{i}", k.ROWS_OFF + i * FT * 512, [P, FT, P]) for i in range(RING_D)]
    s_w = [k.sem(f"ffn_ring_full{i}") for i in range(RING)]
    s_wd = [k.sem(f"down_ring_full{i}") for i in range(RING_D)]
    s_gu, s_silu, s_act, s_d, s_x2 = (k.sem("gate_up_product"), k.sem("silu_done"), k.sem("act_ready"),
                                      k.sem("down_product"), k.sem("x2_ready"))
    NU, ND = FT * NCH, KD * NCH

    def chunk(c):
        return slice(c * CH, (c + 1) * CH)

    with nc.Block() as block:

        @block.sync
        def _(sp):
            w = k.w_ffn_in[0].rearrange("(k p) n -> p k n", p=P)
            for n in range(FT // WF):
                if n >= RING:
                    sp.wait_ge(s_gu, NCH * WF * (n - RING + 1))
                for part in range(2):
                    src = w[:, :, part * DFF + n * WF * P:part * DFF + (n + 1) * WF * P]
                    sp.dma_start(ring[n % RING][:, :, part, :], src).then_inc(s_w[n % RING], 16)
            w = k.w_ffn_out[0].rearrange("(k p) n -> p k n", p=P)
            sp.wait_ge(s_gu, NU)
            for f in range(KD):
                if f >= RING_D:
                    sp.wait_ge(s_d, NCH * (f - RING_D + 1))
                sp.dma_start(ring_d[f % RING_D][:], w[:, :, f * P:(f + 1) * P]).then_inc(s_wd[f % RING_D], 16)

        @block.scalar
        def _(act):
            for u in range(NU):
                act.wait_ge(s_gu, u + 1)
                if u >= 2:
                    act.wait_ge(s_act, u - 1)
                act.activation(silu[u % 2][:], ps[:, 2 * (u % 4), 0:CH], ACT.Silu).then_inc(s_silu, 1)

        @block.vector
        def _(dve):
            for u in range(NU):
                f, c = u // NCH, u % NCH
                dve.wait_ge(s_silu, u + 1)
                dve.tensor_tensor(act_t[:, f, chunk(c)], silu[u % 2][:], ps[:, 2 * (u % 4) + 1, 0:CH], ALU.mult)\
                   .then_inc(s_act, 1)
            for u in range(ND):
                f, c = u // NCH, u % NCH
                dve.wait_ge(s_d, u + 1)
                dve.tensor_tensor(k.x1[:, f, chunk(c)], k.x1[:, f, chunk(c)], ps[:, u % 4, 0:CH], ALU.add)\
                   .then_inc(s_x2, 1)

        @block.tensor
        def _(pe):
            for u in range(NU):
                f, c = u // NCH, u % NCH
                n = f // WF
                if c == 0 and f % WF == 0:
                    pe.wait_ge(s_w[n % RING], 32 * (n // RING + 1))
                if u >= 4:
                    pe.wait_ge(s_act, u - 3)
                for part in range(2):
                    for kd in range(KD):
                        mm = pe.matmul(ps[:, 2 * (u % 4) + part, 0:CH],
                                       ring[n % RING][:, kd, part, (f % WF) * P:(f % WF + 1) * P],
                                       k.h2[:, kd, chunk(c)], start=(kd == 0), stop=(kd == KD - 1))
                mm.then_inc(s_gu, 1)
            pe.wait_ge(s_act, NU)
            for u in range(ND):
                f, c = u // NCH, u % NCH
                if c == 0:
                    pe.wait_ge(s_wd[f % RING_D], 16 * (f // RING_D + 1))
                if u >= 4:
                    pe.wait_ge(s_x2, u - 3)
                for kf in range(FT):
                    mm = pe.matmul(ps[:, u % 4, 0:CH], ring_d[f % RING_D][:, kf, :], act_t[:, kf, chunk(c)],
                                   start=(kf == 0), stop=(kf == FT - 1))
                mm.then_inc(s_d, 1)


def stage_final(k):
    nc, ps = k.nc, k.ps
    NX = TOK // XT
    off = k.ROWS_OFF
    weight = k.at("final_weight", off, [P, DM])
    off += DM * 4
    square = k.at("final_square", off, [P, DM])
    off += DM * 4
    y = [k.at(f"final_rows{i}", off + i * DM * 4, [P, DM]) for i in range(3)]
    off += 3 * DM * 4
    ss = k.at("final_square_sums", off, [P, NX])
    rs = k.at("final_rstd", off + 64, [P, NX])
    s_w, s_turn, s_ss, s_rs, s_y = (k.sem("final_weight_loaded"), k.sem("final_turned"), k.sem("final_ss"),
                                    k.sem("final_rstd_ready"), k.sem("final_ready"))
    s_out = k.y_stored

    with nc.Block() as block:

        @block.sync
        def _(sp):
            sp.dma_start(weight[:], k.norm_final.partition_broadcast(P)).then_inc(s_w, 16)
            n_out = [0] * 3
            for t in range(NX):
                sp.wait_ge(s_y, t + 1)
                a, b = t * XT, (t + 1) * XT
                m = max(0, min(b, SEQ) - a)
                sp.dma_start(k.y_prompt[0, a:a + m], y[t % 3][0:m, :]).then_inc(s_out[t % 3], 16)
                n_out[t % 3] += 16
                if m < XT:
                    sp.dma_start(k.y_sample.rearrange("b t d -> (b t) d"), y[t % 3][m:XT, :]).then_inc(s_out[t % 3], 16)
                    n_out[t % 3] += 16
            for i in range(3):
                sp.wait_ge(s_out[i], n_out[i])

        @block.tensor
        def _(pe):
            for t in range(NX):
                if t >= 3:
                    pe.wait_ge(s_y, t - 2)
                for f in range(KD):
                    mm = pe.transpose(ps[0:XT, 2 * (t % 3) + f // 4, (f % 4) * P:(f % 4 + 1) * P],
                                      k.x1[:, f, t * XT:(t + 1) * XT], k.ident[:])
                mm.then_inc(s_turn, 1)

        @block.scalar
        def _(act):
            def root(t):
                act.wait_ge(s_rs, 3 * t + 1)
                act.activation(rs[0:XT, t:t + 1], rs[0:XT, t:t + 1], ACT.Sqrt).then_inc(s_rs, 1)

            for t in range(NX):
                act.wait_ge(s_turn, t + 1)
                if t:
                    act.wait_ge(s_ss, t)
                rows = ps[0:XT, 2 * (t % 3):2 * (t % 3) + 2, :].rearrange("p a n -> p (a n)")
                act.activation(square[0:XT], rows, ACT.Square, accum_out=ss[0:XT, t:t + 1]).then_inc(s_ss, 1)
                if t:
                    root(t - 1)
            root(NX - 1)

        @block.vector
        def _(dve):
            dve.wait_ge(s_w, 16)
            n_out = 0
            for t in range(NX):
                r = rs[0:XT, t:t + 1]
                dve.wait_ge(s_ss, t + 1)
                dve.tensor_scalar(r, ss[0:XT, t:t + 1], 1.0 / DM, EPS, ALU.mult, ALU.add).then_inc(s_rs, 1)
                dve.wait_ge(s_rs, 3 * t + 2)
                dve.reciprocal(r, r).then_inc(s_rs, 1)
                dve.wait_ge(s_rs, 3 * t + 3)
                if t >= 3:
                    dve.wait_ge(s_out[t % 3], 16 * (t // 3))
                rows = ps[0:XT, 2 * (t % 3):2 * (t % 3) + 2, :].rearrange("p a n -> p (a n)")
                dve.scalar_tensor_tensor(y[t % 3][0:XT], rows, r, weight[0:XT], ALU.mult, ALU.mult).then_inc(s_y, 1)


class Kit:

    BASE = 16512

    def __init__(self, nc, ctx):
        self.nc, self.ctx, self.low, self.stage_sems = nc, ctx, 0, []

    def at(self, name, offset, shape, dtype=F32):
        return self.nc.alloc_sbuf_tensor_at(name, shape, dtype, offset=self.BASE + offset)

    def sb(self, name, shape, dtype=F32):
        t = self.at(name, self.low, shape, dtype)
        size = 4
        for n in shape[1:]:
            size *= n
        self.low += (size + 31) // 32 * 32
        assert self.low <= self.HT_OFF
        return t

    def sem(self, name):
        s = self.nc.alloc_semaphore(name)
        self.stage_sems.append(s)
        return s

    def end_sems(self):
        self.nc.clear_and_free_semaphores(self.stage_sems)
        self.nc.all_engine_barrier()
        self.stage_sems = []

    HT_OFF = 14592
    ROWS_OFF = HT_OFF + KD * TOK * 4
    KT_OFF = ROWS_OFF + TT * R_END * 4
    VA_OFF = KT_OFF + 4 * TOK * 4
    AQ_OFF = VA_OFF + (TT * MH * (MD + 1) * 4 + 31) // 32 * 32
    X_OFF = AQ_OFF
    AT_OFF = AQ_OFF + HG * TOK * 4
    QK_OFF = AT_OFF + MH * TOK * 4
    RING_OFF = QK_OFF + 8 * TOK * 4
    PACK_OFF = RING_OFF + NB * MH * (MD + 1) * 4
    WORK_OFF = PACK_OFF + 2 * TOK * 4
    CMP_END = QK_OFF + (NB * P + NG * HD + (NB + 1) * GD) * 4
    TOP = 229376 - 16512


STAGES = [stage_norm_in, stage_token_major, stage_feature_major, stage_gates, stage_mlstm, stage_compress,
          stage_nsa_prompt, stage_nsa_samples, stage_merge, stage_ffn, stage_final]


def build(nc, ins, outs):
    with ExitStack() as ctx:
        k = Kit(nc, ctx)
        (k.x_prompt, k.x_sample, k.cache_k_cmp, k.cache_v_cmp, k.cache_k_slc, k.cache_v_slc, k.state_k_win,
         k.state_v_win, k.state_conv, k.state_C, k.state_n, k.state_m, k.page_table, k.norm_mix, k.w_in, k.b_in,
         k.conv_w, k.conv_b, k.cmp_pos_k, k.cmp_pos_v, k.cmp_proj_k, k.cmp_proj_v, k.m_norm, k.w_a, k.w_b, k.w_o,
         k.norm_ffn, k.w_ffn_in, k.w_ffn_out, k.norm_final) = ins
        k.y_prompt, k.y_sample = outs[0:2]
        (k.o_k_cmp, k.o_v_cmp, k.o_k_slc, k.o_v_slc, k.o_k_win, k.o_v_win, k.o_conv, k.o_C, k.o_n, k.o_m) = [
            tuple(outs[2 + 2 * n:4 + 2 * n]) for n in range(10)]
        k.ps = ctx.enter_context(nc.psum_tensor("banks", [P, 8, 512], F32))
        k.rows_stored, k.windows_stored, k.tail_stored, k.m_stored, k.states_stored = [
            ctx.enter_context(nc.semaphore(f"{name}_stored")) for name in ("rows", "windows", "tail", "m", "states")]
        k.y_stored = [ctx.enter_context(nc.semaphore(f"y_stored{i}")) for i in range(3)]
        place_constants(k)
        k.select = k.sb("select_head", [P, MH, P])
        k.gate_cols = k.sb("gate_cols", [P, TT, 4, MH])
        k.decay, k.decay_row = k.sb("decay", [P, MH, QT + NB]), k.sb("decay_row", [MH, QT + NB])
        k.m_c, k.m_s0, k.m_s1 = k.sb("m_chunks", [MH, QT + 1]), k.sb("m_samples", [MH, NB]), k.sb("m_samples_new", [MH, NB])
        k.gates, k.page_idx = k.sb("branch_gates", [P, TT, NH, 3]), k.sb("page_idx", [P, NB], I32)
        k.SPARE_OFF = k.low
        k.hT = k.at("hT", k.HT_OFF, [P, KD, TOK])
        k.rows = k.at("token_rows", k.ROWS_OFF, [P, TT, R_END])
        k.kT_pad = k.at("kT_pad", k.KT_OFF, [P, 4, TOK])
        k.v_aug = k.at("v_and_ones", k.VA_OFF, [P, TT, MH, MD + 1])
        k.aq = k.at("nsa_qT", k.AQ_OFF, [P, HG, TOK])
        k.aT = k.at("mlstm_outT", k.AT_OFF, [P, MH, TOK])
        k.qk = k.at("mlstm_qkT", k.QK_OFF, [P, 8, TOK])
        k.packed = k.at("gates_packed", k.PACK_OFF, [P, TOK])
        k.neg_m = k.at("neg_m", k.PACK_OFF + TOK * 4, [MH, TOK])
        k.kT_last = k.at("kT_new_rows", k.VA_OFF + HG * TOK * 4, [P, 4, NS_TOK])
        k.bT = k.at("nsa_outT", k.VA_OFF, [P, HG, TOK])
        k.kc_t = k.at("kcT_samples", k.QK_OFF, [P, NB, P])
        k.kc_pad = k.at("kcT_prompt_pad", k.QK_OFF + NB * P * 4, [P, NG, HD])
        k.vc = k.at("vc", k.QK_OFF + (NB * P + NG * HD) * 4, [P, NB + 1, GD])
        k.x1 = k.at("x1T", k.HT_OFF, [P, KD, TOK])
        k.h2 = k.at("h2T", k.ROWS_OFF, [P, KD, TOK])
        with nc.allow_non_contiguous_dma(reason="small vectors and states"):
            for stage in STAGES:
                stage(k)
                if stage in (stage_mlstm, stage_nsa_samples):
                    k.end_sems()


_INS = ["x_prompt", "x_sample", "cache_k_cmp", "cache_v_cmp", "cache_k_slc", "cache_v_slc", "state_k_win",
        "state_v_win", "state_conv", "state_C", "state_n", "state_m", "page_table", "norm_mix", "w_in", "b_in",
        "conv_w", "conv_b", "cmp_pos_k", "cmp_pos_v", "cmp_proj_k", "cmp_proj_v", "m_norm", "w_a", "w_b", "w_o",
        "norm_ffn", "w_ffn_in", "w_ffn_out", "norm_final"]
_OUTS = [(1, SEQ, DM), (NB, NT, DM)]
for _ in range(4):
    _OUTS += [(1, 1, SEQ, NG, HD), (1, NB, NT, NG, HD)]
for _ in range(2):
    _OUTS += [(1, 1, WIN, NG, HD), (1, NB, WIN, NG, HD)]
_OUTS += [(1, 1, CW - 1, 2 * DA), (1, NB, CW - 1, 2 * DA), (1, 1, MH, MD, MD), (1, NB, MH, MD, MD),
          (1, 1, MH, MD), (1, NB, MH, MD), (1, 1, MH), (1, NB, MH)]


def kernel(**inputs):
    import numpy as _np
    import concourse.bacc as _bacc
    from concourse import mybir as _mybir
    from concourse.bass_utils import run_bass_kernel_spmd as _run

    nc = _bacc.Bacc("TRN2", target_bir_lowering=False, num_devices=1)
    arrays, ins, outs = {}, [], []
    for name in _INS:
        a = _np.ascontiguousarray(inputs[name])
        arrays[f"in_{name}_dram"] = a
        ins.append(nc.dram_tensor(f"in_{name}_dram", a.shape, _mybir.dt.from_np(a.dtype), kind="ExternalInput").ap())
    for i, shape in enumerate(_OUTS):
        outs.append(nc.dram_tensor(f"out_{i}_dram", shape, _mybir.dt.float32, kind="ExternalOutput").ap())
    build(nc, ins, outs)
    r = _run(nc, [arrays], core_ids=[0])
    return tuple(r.results[0][f"out_{i}_dram"] for i in range(len(_OUTS)))
```

```python
from contextlib import ExitStack

import numpy as np

import concourse.bass as bass
from concourse import mybir

F32 = mybir.dt.float32
I32 = mybir.dt.int32
F32R = mybir.dt.float32r
U32 = mybir.dt.uint32
ALU = mybir.AluOpType
ACT = mybir.ActivationFunctionType
AX = mybir.AxisListType

P = 128
DM = 1024
KD = DM // P
SEQ = 1024
NB, NT = 8, 4
NS_TOK = NB * NT
TOK = SEQ + NS_TOK
QT = SEQ // P
TT = QT + 1
PAST, PAGE = 2048, 128
MH, MD = 4, 128
DA = MH * MD
CW = 4
NH, HD, NG = 8, 64, 2
HG = NH // NG
GD = NG * HD
STRIDE, CBLK = 16, 32
NSUB = PAST // STRIDE
SBLK, NSEL = 64, 16
NBLK = PAST // SBLK + 1
WIN = 512
DFF = 2816
FT = DFF // P
EPS = 1e-6
NEG = -1e30
BIG = 1e30
SLOPES = [2.0 ** -(h + 1) for h in range(NH)]
KSCALE = float(MD) ** -0.5
QSCALE = float(HD) ** -0.5

C_QK, C_V, C_O, C_I, C_F = 0, 1024, 1536, 2048, 2052
C_AQ, C_KV, C_G, C_MRG = 2056, 2568, 3336, 3360
R_KC, R_VC, R_KS, R_IG, R_FG, R_VS, R_KW, R_VW, R_G, R_END = 0, 128, 256, 384, 388, 392, 520, 648, 776, 800
RW = DA + R_END

CH = TOK // 3
NCH = TOK // CH
XT = CH // 4
TOKEN_CHUNKS = [(0, 512), (512, 512), (1024, NS_TOK)]


class Chain:

    def __init__(self, eng, sem, start=0):
        self.eng, self.sem, self.n = eng, sem, start

    def __call__(self, ins):
        self.n += 1
        ins.then_inc(self.sem, 1)
        self.eng.wait_ge(self.sem, self.n)


def place_constants(k):
    nc = k.nc
    k.ident = k.sb("ident", [P, P])
    k.ones = k.sb("ones", [P, P])
    k.cols = k.sb("vector_cols", [P, 92])
    k.SPARE2_OFF = k.low
    k.vector_rows = k.sb("vector_rows", [92, P])
    k.rstd_x = k.sb("rstd_x", [P, TT])
    k.ss_x = k.sb("sum_squares_x", [P, TT])
    k.c_norm_mix, k.c_conv_w, k.c_conv_b, k.c_m_norm, k.c_norm_ffn = 0, 8, 40, 48, 52
    k.c_b_qk, k.c_b_o, k.c_b_mrg, k.c_b_q = 60, 68, 72, 88


def stage_norm_in(k):
    nc, ps = k.nc, k.ps
    x_all = k.at("x_all", k.X_OFF, [P, TT, DM])
    square = k.at("x_square", k.X_OFF + TT * DM * 4, [P, DM])
    s_x = [k.sem(f"x_loaded{i}") for i in range(3)]
    s_rows, s_rows_t = k.sem("rows_loaded"), k.sem("rows_turned")
    s_const, s_ss, s_rstd, s_h = k.sem("constants"), k.sem("sum_squares"), k.sem("rstd_ready"), k.sem("h_ready")
    s_turn, s_evac_a, s_evac_v = k.sem("h_turned"), k.sem("hT_evac_act"), k.sem("hT_evac_dve")
    lots = [(0, 2), (2, 5), (5, 8)]

    def token_rows(tt):
        return P if tt < QT else NS_TOK

    with nc.Block() as block:

        @block.sync
        def _(sp):
            xp = k.x_prompt[0].rearrange("(t p) d -> p t d", p=P)
            for n, (a, b) in enumerate(lots):
                sp.dma_start(x_all[:, a:b, :], xp[:, a:b, :]).then_inc(s_x[n], 16)
            sp.dma_start(x_all[0:NS_TOK, QT, :], k.x_sample.rearrange("b t d -> (b t) d")).then_inc(s_x[2], 16)

        @block.gpsimd
        def _(pool):
            pool.memset(k.ones[:], 1.0).then_inc(s_const, 1)
            pool.memset(k.ident[:], 0.0).then_inc(s_const, 1)
            pool.wait_ge(s_const, 2)
            pool.affine_select(out=k.ident[:], in_=k.ident[:], compare_op=ALU.not_equal, fill=1.0, base=0,
                               pattern=[[-1, P]], channel_multiplier=1).then_inc(s_const, 1)
            pool.memset(k.ss_x[:], 1.0).then_inc(s_const, 1)

        @block.scalar
        def _(act):
            rows = k.vector_rows
            for first, n, src in (
                (k.c_norm_mix, 8, k.norm_mix[0].rearrange("(k p) -> k p", p=P)),
                (k.c_conv_w, 32, k.conv_w.rearrange("o w (k p) -> (o w k) p", p=P)),
                (k.c_conv_b, 8, k.conv_b[0].rearrange("(k p) -> k p", p=P)),
                (k.c_m_norm, 4, k.m_norm[0].rearrange("(k p) -> k p", p=P)),
                (k.c_norm_ffn, 8, k.norm_ffn[0].rearrange("(k p) -> k p", p=P)),
                (k.c_b_qk, 8, k.b_in[0, C_QK:C_V].rearrange("(k p) -> k p", p=P)),
                (k.c_b_o, 4, k.b_in[0, C_O:C_I].rearrange("(k p) -> k p", p=P)),
                (k.c_b_mrg, 16, k.b_in[0, C_MRG:].rearrange("(k p) -> k p", p=P)),
            ):
                act.dma_start(rows[first:first + n, :], src).then_inc(s_rows, 16)
            q_bias = k.b_in[0, C_AQ:C_KV].rearrange("(g i d) -> i g d", g=NG, i=HG)
            act.dma_start(rows[k.c_b_q:k.c_b_q + HG, :].rearrange("i (g d) -> i g d", g=NG), q_bias)\
               .then_inc(s_rows, 16)
            act.wait_ge(s_const, 4)
            for tt in range(TT):
                if tt in (0, 2, 5):
                    n = (0, 2, 5).index(tt)
                    act.wait_ge(s_x[n], 32 if n == 2 else 16)
                r = token_rows(tt)
                if tt:
                    act.wait_ge(s_ss, tt)
                act.activation(square[0:r, :], x_all[0:r, tt, :], ACT.Square,
                               accum_out=k.ss_x[0:r, tt:tt + 1]).then_inc(s_ss, 1)
            act.wait_ge(s_rstd, 1)
            act.activation(k.rstd_x[:], k.rstd_x[:], ACT.Sqrt).then_inc(s_rstd, 1)
            for kd in range(KD):
                act.wait_ge(s_turn, kd + 1)
                if kd == 0:
                    act.wait_ge(s_rows_t, 2)
                g = k.cols[:, k.c_norm_mix + kd:k.c_norm_mix + kd + 1]
                act.activation(k.hT[:, kd, 512:1024], ps[:, 3 * (kd % 2) + 1, :], ACT.Copy, scale=g)\
                   .then_inc(s_evac_a, 1)

        @block.vector
        def _(dve):
            dve.wait_ge(s_rows_t, 1)
            dve.tensor_copy(k.cols[:], ps[:, 6, 0:92]).then_inc(s_rows_t, 1)
            dve.wait_ge(s_ss, TT)
            dve.tensor_scalar(k.rstd_x[:], k.ss_x[:], 1.0 / DM, EPS, ALU.mult, ALU.add).then_inc(s_rstd, 1)
            dve.wait_ge(s_rstd, 2)
            dve.reciprocal(k.rstd_x[:], k.rstd_x[:]).then_inc(s_rstd, 1)
            dve.wait_ge(s_rstd, 3)
            for tt in range(TT):
                r = token_rows(tt)
                dve.tensor_scalar(x_all[0:r, tt, :], x_all[0:r, tt, :], k.rstd_x[0:r, tt:tt + 1], None,
                                  ALU.mult).then_inc(s_h, 1)
            for kd in range(KD):
                dve.wait_ge(s_turn, kd + 1)
                dve.wait_ge(s_rows_t, 2)
                g = k.cols[:, k.c_norm_mix + kd:k.c_norm_mix + kd + 1]
                dve.tensor_scalar(k.hT[:, kd, 0:512], ps[:, 3 * (kd % 2), :], g, None, ALU.mult)
                dve.tensor_scalar(k.hT[:, kd, SEQ:TOK], ps[:, 3 * (kd % 2) + 2, 0:NS_TOK], g, None, ALU.mult)\
                   .then_inc(s_evac_v, 1)

        @block.tensor
        def _(pe):
            pe.wait_ge(s_const, 3)
            pe.wait_ge(s_rows, 16 * 9)
            pe.transpose(ps[:, 6, 0:92], k.vector_rows[:], k.ident[0:92, 0:92]).then_inc(s_rows_t, 1)
            for kd in range(KD):
                if kd >= 2:
                    pe.wait_ge(s_evac_v, kd - 1)
                    pe.wait_ge(s_evac_a, kd - 1)
                for tt in range(TT):
                    if kd == 0:
                        pe.wait_ge(s_h, tt + 1)
                    r = token_rows(tt)
                    mm = pe.transpose(ps[:, 3 * (kd % 2) + tt // 4, (tt % 4) * P:(tt % 4) * P + r],
                                      x_all[0:r, tt, kd * P:(kd + 1) * P], k.ident[0:r, 0:r])
                mm.then_inc(s_turn, 1)


def stage_token_major(k):
    nc, ps = k.nc, k.ps
    w = k.at("w_rows", k.X_OFF, [P, KD, RW])
    bias = k.at("b_rows", k.X_OFF + KD * RW * 4, [P, RW])
    s_w = [k.sem(f"w_rows_loaded{i}") for i in range(4)]
    s_bias = k.sem("b_rows_loaded")
    s_mm, s_evac = k.sem("rows_product"), k.sem("rows_evac")
    s_zero, s_kt, s_kt_evac = k.sem("kT_zeroed"), k.sem("k_turned"), k.sem("kT_evac")
    s_store, s_ring = k.rows_stored, k.windows_stored
    segments = [(0, 512, C_V), (512, 896, C_KV), (896, 904, C_I), (904, RW, C_KV + 384)]
    groups = [(0, 512), (512, 904), (904, RW)]

    def token_rows(tt):
        return P if tt < QT else NS_TOK

    with nc.Block() as block:

        @block.sync
        def _(sp):
            w_in = k.w_in[0].rearrange("(k p) n -> p k n", p=P)
            for n, (a, b, c) in enumerate(segments):
                sp.dma_start(w[:, :, a:b], w_in[:, :, c:c + b - a]).then_inc(s_w[n], 16)
            for a, b, c in segments:
                sp.dma_start(bias[:, a:b], k.b_in[0, c:c + b - a].partition_broadcast(P)).then_inc(s_bias, 16)
            outs = [(R_KC, k.o_k_cmp), (R_VC, k.o_v_cmp), (R_KS, k.o_k_slc), (R_VS, k.o_v_slc)]
            for tt in range(TT):
                sp.wait_ge(s_evac, 3 * (tt + 1))
                for col, (o_p, o_s) in outs:
                    if tt < QT:
                        dst = o_p[0, 0, tt * P:(tt + 1) * P].rearrange("t g d -> t (g d)")
                        sp.dma_start(dst, k.rows[:, tt, col:col + GD]).then_inc(s_store, 16)
                    else:
                        dst = o_s[0].rearrange("b t g d -> (b t) (g d)")
                        sp.dma_start(dst, k.rows[0:NS_TOK, tt, col:col + GD]).then_inc(s_store, 16)
                for col, (o_p, o_s), past in ((R_KW, k.o_k_win, k.state_k_win), (R_VW, k.o_v_win, k.state_v_win)):
                    if QT // 2 <= tt < QT:
                        dst = o_p[0, 0, (tt - 4) * P:(tt - 3) * P].rearrange("t g d -> t (g d)")
                        sp.dma_start(dst, k.rows[:, tt, col:col + GD]).then_inc(s_store, 16)
                    elif tt == QT:
                        for b in range(NB):
                            dst = o_s[0, b, WIN - NT:].rearrange("t g d -> t (g d)")
                            sp.dma_start(dst, k.rows[NT * b:NT * (b + 1), tt, col:col + GD]).then_inc(s_store, 16)
            sp.wait_ge(s_store, 16 * (4 * TT + 2 * 4 + 2 * NB))

        @block.scalar
        def _(act):
            for past, o in ((k.state_k_win, k.o_k_win[1]), (k.state_v_win, k.o_v_win[1])):
                act.dma_start(o[0, :, 0:WIN - NT].rearrange("b t g d -> b (t g d)"),
                              past[0, :, NT:].rearrange("b t g d -> b (t g d)")).then_inc(s_ring, 16)
            for tt in range(TT):
                r = token_rows(tt)
                act.wait_ge(s_kt, tt + 1)
                act.wait_ge(s_zero, 1)
                bank = 6 + tt % 2
                for which in range(2):
                    for g in range(NG):
                        rows = slice(g * HD, (g + 1) * HD)
                        ins = act.copy(k.kT_pad[rows, 2 * which + g, tt * P:tt * P + r],
                                       ps[rows, bank, which * P:which * P + r])
                ins.then_inc(s_kt_evac, 1)
            act.wait_ge(s_ring, 32)

        @block.gpsimd
        def _(pool):
            pool.memset(k.kT_pad[:], 0.0).then_inc(s_zero, 1)

        @block.vector
        def _(dve):
            dve.memset(k.v_aug[:, :, :, MD:MD + 1], 1.0)
            dve.wait_ge(s_bias, 64)
            for tt in range(TT):
                r = token_rows(tt)
                for n, (a, b) in enumerate(groups):
                    dve.wait_ge(s_mm, 3 * tt + n + 1)
                    src = ps[0:r, n + 3 * (tt % 2), 0:b - a]
                    if n == 0:
                        dve.tensor_tensor(k.v_aug[0:r, tt, :, 0:MD], src.rearrange("p (h d) -> p h d", h=MH),
                                          bias[0:r, a:b].rearrange("p (h d) -> p h d", h=MH), ALU.add)\
                           .then_inc(s_evac, 1)
                    else:
                        dve.tensor_tensor(k.rows[0:r, tt, a - DA:b - DA], src, bias[0:r, a:b], ALU.add)\
                           .then_inc(s_evac, 1)

        @block.tensor
        def _(pe):
            def turn(tt):
                r = token_rows(tt)
                pe.wait_ge(s_evac, 3 * (tt + 1))
                if tt >= 2:
                    pe.wait_ge(s_kt_evac, tt - 1)
                for which, col in enumerate((R_KS, R_KW)):
                    mm = pe.transpose(ps[:, 6 + tt % 2, which * P:which * P + r],
                                      k.rows[0:r, tt, col:col + GD], k.ident[0:r, 0:r])
                mm.then_inc(s_kt, 1)

            for tt in range(TT):
                r = token_rows(tt)
                for n, (a, b) in enumerate(groups):
                    if tt == 0:
                        for i in ((0,), (1, 2), (3,))[n]:
                            pe.wait_ge(s_w[i], 16)
                    if tt >= 2:
                        pe.wait_ge(s_evac, 3 * (tt - 2) + n + 1)
                    for kd in range(KD):
                        mm = pe.matmul(ps[0:r, n + 3 * (tt % 2), 0:b - a], k.hT[:, kd, tt * P:tt * P + r],
                                       w[:, kd, a:b], start=(kd == 0), stop=(kd == KD - 1))
                    mm.then_inc(s_mm, 1)
                if tt:
                    turn(tt - 1)
            turn(TT - 1)


def stage_feature_major(k):
    nc, ps = k.nc, k.ps
    RING = 3
    NJ = 16
    off = k.RING_OFF
    ring = [k.at(f"w_ring{i}", off + i * 4096, [P, KD, P]) for i in range(RING)]
    off += RING * 4096
    pre = [k.at(f"qk_pre{i}", off + i * TOK * 4, [P, TOK]) for i in range(2)]
    off += 2 * TOK * 4
    conv = [k.at(f"qk_conv{i}", off + i * TOK * 4, [P, TOK]) for i in range(2)]
    off += 2 * TOK * 4
    ext = k.at("sample_ext", off, [P, NB, CW - 1 + NT])
    past_rows = k.at("conv_past", k.AQ_OFF + 3 * TOK * 4, [NB * (CW - 1), 2 * DA])
    CO = NS_TOK + CW - 1
    tail = k.at("conv_tail", k.AT_OFF, [CO, 2 * DA])
    s_full = [k.sem(f"w_ring_full{i}") for i in range(RING)]
    s_used, s_past = k.sem("w_ring_used"), k.sem("conv_past_loaded")
    s_mm, s_evac, s_o_evac = k.sem("feat_product"), k.sem("feat_evac"), k.sem("o_gate_evac")
    s_conv, s_silu = k.sem("conv_ready"), k.sem("silu_ready")
    s_tail, s_tail_evac, s_tail_out, s_chain = k.sem("tail_turned"), k.sem("tail_evac"), k.tail_stored, k.sem("conv_chain")

    def w_cols(j):
        w_in = k.w_in[0].rearrange("(k p) n -> p k n", p=P)
        if j < 8:
            return [(slice(0, P), w_in[:, :, C_QK + j * P:C_QK + (j + 1) * P])]
        if j < 12:
            i = j - 8
            return [(slice(g * HD, (g + 1) * HD), w_in[:, :, C_AQ + (g * HG + i) * HD:C_AQ + (g * HG + i + 1) * HD])
                    for g in range(NG)]
        return [(slice(0, P), w_in[:, :, C_O + (j - 12) * P:C_O + (j - 11) * P])]

    n_dmas = [0] * RING
    full_at = []
    for j in range(NJ):
        n_dmas[j % RING] += len(w_cols(j))
        full_at.append(16 * n_dmas[j % RING])

    def banks(j):
        return [3 * (j % 2) + c for c in range(3)]

    with nc.Block() as block:

        @block.sync
        def _(sp):
            sp.dma_start(past_rows[:], k.state_conv[0].rearrange("b r c -> (b r) c")).then_inc(s_past, 16)
            for j in range(NJ):
                if j >= RING:
                    sp.wait_ge(s_used, j - RING + 1)
                for cols, src in w_cols(j):
                    sp.dma_start(ring[j % RING][:, :, cols], src).then_inc(s_full[j % RING], 16)
            sp.wait_ge(s_tail_evac, 8)
            n = 1
            sp.dma_start(k.o_conv[0][0, 0], tail[0:CW - 1, :]).then_inc(s_tail_out, 16)
            for b in range(NB):
                first = CW - 1 + NT * b + 1
                sp.dma_start(k.o_conv[1][0, b], tail[first:first + CW - 1, :]).then_inc(s_tail_out, 16)
                n += 1
            sp.wait_ge(s_tail_out, 16 * n)

        @block.tensor
        def _(pe):
            def turn_tail(j):
                pe.wait_ge(s_evac, 3 * (j + 1))
                if j >= 1:
                    pe.wait_ge(s_tail_evac, j)
                pe.transpose(ps[0:CO, 6, 0:P], pre[j % 2][:, SEQ - CW + 1:TOK], k.ident[:])
                if j == 0:
                    pe.wait_ge(s_past, 16)
                pe.transpose(ps[:, 7, 0:NB * (CW - 1)], past_rows[:, j * P:(j + 1) * P],
                             k.ident[0:NB * (CW - 1), 0:NB * (CW - 1)]).then_inc(s_tail, 1)

            for j in range(NJ):
                pe.wait_ge(s_full[j % RING], full_at[j])
                if j >= 14:
                    pe.wait_ge(s_o_evac, 3 * (j - 13))
                elif j >= 2:
                    pe.wait_ge(s_evac, 3 * (j - 1))
                for c, (t0, tn) in enumerate(TOKEN_CHUNKS):
                    for kd in range(KD):
                        mm = pe.matmul(ps[:, banks(j)[c], 0:tn], ring[j % RING][:, kd, :],
                                       k.hT[:, kd, t0:t0 + tn], start=(kd == 0), stop=(kd == KD - 1))
                    if c == 2:
                        mm.then_inc(s_used, 1)
                    else:
                        mm.then_inc(s_mm, 1)
                if 1 <= j <= 8:
                    turn_tail(j - 1)

        @block.scalar
        def _(act):
            for j in range(NJ):
                if j < 8:
                    act.wait_ge(s_conv, j + 1)
                    act.activation(k.qk[:, j, :], conv[j % 2][:], ACT.Silu).then_inc(s_silu, 1)
                elif j >= 12:
                    for c, (t0, tn) in enumerate(TOKEN_CHUNKS):
                        if c < 2:
                            act.wait_ge(s_mm, 2 * j + c + 1)
                        else:
                            act.wait_ge(s_used, j + 1)
                        if j == 12 and c == 0:
                            act.wait_ge(s_tail_out, 16 * (1 + NB))
                        bcol = k.cols[:, k.c_b_o + j - 12:k.c_b_o + j - 11]
                        act.activation(k.aT[:, j - 12, t0:t0 + tn], ps[:, banks(j)[c], 0:tn], ACT.Sigmoid,
                                       bias=bcol).then_inc(s_o_evac, 1)

        @block.vector
        def _(dve):
            link = Chain(dve, s_chain)

            def convolve(j):
                buf, out = pre[j % 2], conv[j % 2]
                tap = [k.cols[:, k.c_conv_w + 8 * t + j:k.c_conv_w + 8 * t + j + 1] for t in range(CW)]
                b = k.cols[:, k.c_conv_b + j:k.c_conv_b + j + 1]
                dve.wait_ge(s_tail, j + 1)
                dve.tensor_copy(tail[:, j * P:(j + 1) * P], ps[0:CO, 6, 0:P])
                dve.tensor_copy(ext[:, :, 0:CW - 1], ps[:, 7, 0:NB * (CW - 1)].rearrange("p (b r) -> p b r", b=NB))\
                   .then_inc(s_tail_evac, 1)
                link(dve.tensor_copy(ext[:, :, CW - 1:], buf[:, SEQ:TOK].rearrange("p (b t) -> p b t", b=NB)))
                if j >= 2:
                    dve.wait_ge(s_silu, j - 1)
                link(dve.tensor_scalar(out[:, 0:SEQ], buf[:, 0:SEQ], tap[CW - 1], b, ALU.mult, ALU.add))
                for t in range(1, CW):
                    link(dve.scalar_tensor_tensor(out[:, t:SEQ], buf[:, 0:SEQ - t], tap[CW - 1 - t],
                                                  out[:, t:SEQ], ALU.mult, ALU.add))
                cs = out[:, SEQ:TOK].rearrange("p (b t) -> p b t", b=NB)
                link(dve.tensor_scalar(cs, ext[:, :, 0:NT], tap[0], b, ALU.mult, ALU.add))
                for t in range(1, CW):
                    ins = dve.scalar_tensor_tensor(cs, ext[:, :, t:t + NT], tap[t], cs, ALU.mult, ALU.add)
                    if t < CW - 1:
                        link(ins)
                ins.then_inc(s_conv, 1)

            def scale_keys(j):
                dve.wait_ge(s_silu, j + 1)
                dve.tensor_scalar(k.qk[:, j, :], k.qk[:, j, :], KSCALE, None, ALU.mult)

            for j in range(12):
                for c, (t0, tn) in enumerate(TOKEN_CHUNKS):
                    if c < 2:
                        dve.wait_ge(s_mm, 2 * j + c + 1)
                    else:
                        dve.wait_ge(s_used, j + 1)
                    src = ps[:, banks(j)[c], 0:tn]
                    if j < 8:
                        dve.tensor_scalar(pre[j % 2][:, t0:t0 + tn], src, k.cols[:, k.c_b_qk + j:k.c_b_qk + j + 1],
                                          None, ALU.add).then_inc(s_evac, 1)
                    else:
                        bcol = k.cols[:, k.c_b_q + j - 8:k.c_b_q + j - 7]
                        dve.tensor_scalar(k.aq[:, j - 8, t0:t0 + tn], src, bcol, QSCALE, ALU.add, ALU.mult)\
                           .then_inc(s_evac, 1)
                if j < 8:
                    dve.wait_ge(s_evac, 3 * (j + 1))
                    convolve(j)
                if 5 <= j <= 8:
                    scale_keys(j - 1)


def stage_gates(k):
    nc, ps = k.nc, k.ps
    off = k.RING_OFF

    def row(name, n=TOK):
        nonlocal off
        t = k.at(name, off, [MH, n])
        off += n * 4
        return t

    u, f_m = row("gate_u"), row("gate_F")
    lf = k.at("gate_lf", k.SPARE_OFF, [MH, TOK])
    reset = k.at("gate_reset", k.SPARE_OFF + TOK * 4, [MH, TOK])
    neg_m = k.neg_m
    s_zero, s_turn, s_copy, s_chain = k.sem("gate_zeroed"), k.sem("gate_turned"), k.sem("gate_copied"), k.sem("gate_chain")
    s_abs, s_soft, s_args, s_exp, s_m0 = (k.sem("gate_abs"), k.sem("gate_softplus"), k.sem("gate_args"),
                                          k.sem("gate_exps"), k.sem("m0_loaded"))
    s_cols, s_cols_evac, s_m_out = k.sem("gate_cols"), k.sem("gate_cols_evac"), k.m_stored
    s_const = k.sem("gate_constants")

    def per_sample(t):
        return t[:, SEQ:TOK].rearrange("h (b t) -> h b t", b=NB)

    def per_chunk(t):
        return t[:, 0:SEQ].rearrange("h (c t) -> h c t", c=QT)

    with nc.Block() as block:

        @block.sync
        def _(sp):
            sp.dma_start(k.m_s0[:], k.state_m[0].rearrange("b h -> h b")).then_inc(s_m0, 16)
            sp.wait_ge(s_args, 1)
            sp.dma_start(k.o_m[0][0].rearrange("b h -> h b"), k.m_c[:, QT:QT + 1]).then_inc(s_m_out, 16)
            sp.dma_start(k.o_m[1][0].rearrange("b h -> h b"), k.m_s1[:]).then_inc(s_m_out, 16)
            sp.wait_ge(s_m_out, 32)

        @block.gpsimd
        def _(pool):
            pool.memset(reset[:], 1.0).then_inc(s_const, 1)
            pool.memset(k.select[:], 0.0).then_inc(s_const, 1)
            pool.memset(k.packed[:], 0.0).then_inc(s_const, 1)
            pool.wait_ge(s_const, 3)
            pool.memset(per_chunk(reset)[:, :, 0:1], 0.0)
            pool.memset(per_sample(reset)[:, :, 0:1], 0.0)
            for q in range(2):
                rows = k.select[32 * q:32 * q + MH]
                ins = pool.affine_select(out=rows, in_=rows, compare_op=ALU.not_equal, fill=1.0, base=0,
                                         pattern=[[-1, MH], [0, P]], channel_multiplier=1)
            ins.then_inc(s_const, 1)

        @block.tensor
        def _(pe):
            for which, col in enumerate((R_IG, R_FG)):
                for tt in range(TT):
                    r = P if tt < QT else NS_TOK
                    mm = pe.transpose(ps[0:MH, 3 * which + tt // 4, (tt % 4) * P:(tt % 4) * P + r],
                                      k.rows[0:r, tt, col:col + MH], k.ident[0:r, 0:r])
                mm.then_inc(s_turn, 1)
            pe.wait_ge(s_exp, 5)
            pe.wait_ge(s_args, 3)
            pe.wait_ge(s_const, 4)
            for tt in range(TT):
                r = P if tt < QT else NS_TOK
                pe.transpose(ps[0:r, tt // 4, (tt % 4) * P:(tt % 4 + 1) * P],
                             k.packed[:, tt * P:tt * P + r], k.ident[:])
            for h in range(MH):
                mm = pe.matmul(ps[:, 6, 16 * h:16 * h + 16], k.select[0:MH, h, :], k.decay_row[:],
                               start=True, stop=True)
            mm.then_inc(s_cols, 1)

        @block.scalar
        def _(act):
            act.wait_ge(s_abs, 1)
            act.activation(u[:], u[:], ACT.Exp, scale=-1.0).then_inc(s_soft, 1)
            act.wait_ge(s_soft, 1)
            act.activation(u[:], u[:], ACT.Ln, bias=1.0).then_inc(s_soft, 1)
            act.wait_ge(s_args, 3)
            act.wait_ge(s_const, 4)
            act.activation(k.packed[32:32 + MH, :], lf[:], ACT.Exp).then_inc(s_exp, 1)
            act.activation(k.packed[64:64 + MH, :], f_m[:], ACT.Exp, scale=-1.0).then_inc(s_exp, 1)
            act.activation(k.packed[96:96 + MH, :], reset[:], ACT.Exp).then_inc(s_exp, 1)
            act.activation(k.decay_row[:, 0:QT], k.decay_row[:, 0:QT], ACT.Exp).then_inc(s_exp, 1)
            act.activation(k.decay_row[:, QT:], k.decay_row[:, QT:], ACT.Exp).then_inc(s_exp, 1)

        @block.vector
        def _(dve):
            link = Chain(dve, s_chain)
            dve.wait_ge(s_turn, 2)
            ig, fg = f_m, lf
            for which, dst in enumerate((ig, fg)):
                dve.tensor_copy(dst[:, 0:512], ps[0:MH, 3 * which, :])
                dve.tensor_copy(dst[:, 512:SEQ], ps[0:MH, 3 * which + 1, :])
                ins = dve.tensor_copy(dst[:, SEQ:], ps[0:MH, 3 * which + 2, 0:NS_TOK])
            link(ins)
            dve.scalar_tensor_tensor(u[:], fg[:], -1.0, fg[:], ALU.mult, ALU.max).then_inc(s_abs, 1)
            dve.wait_ge(s_soft, 2)
            link(dve.scalar_tensor_tensor(lf[:], fg[:], 0.0, u[:], ALU.min, ALU.subtract))
            dve.wait_ge(s_const, 4)
            link(dve.tensor_tensor_scan(u[:], reset[:], lf[:], 0.0, ALU.mult, ALU.add))
            link(dve.tensor_tensor(lf[:], ig[:], u[:], ALU.subtract))
            link(dve.tensor_copy(f_m[:], u[:]))
            link(dve.tensor_copy(u[:], lf[:]))
            m_run = neg_m
            link(dve.memset(k.m_c[:, 0:1], NEG))
            for c in range(QT):
                t = slice(c * P, (c + 1) * P)
                link(dve.tensor_tensor_scan(m_run[:, t], u[:, t], u[:, t], k.m_c[:, c:c + 1], ALU.max, ALU.max))
                link(dve.tensor_tensor(k.m_c[:, c + 1:c + 2], f_m[:, t][:, P - 1:P], m_run[:, t][:, P - 1:P], ALU.add))
            dve.wait_ge(s_m0, 16)
            su, sm = per_sample(u), per_sample(m_run)
            for t in range(NT):
                before = k.m_s0[:].unsqueeze(2) if t == 0 else sm[:, :, t - 1:t]
                link(dve.tensor_tensor(sm[:, :, t:t + 1], before, su[:, :, t:t + 1], ALU.max))
            dve.tensor_tensor(k.m_s1[:].unsqueeze(2), per_sample(f_m)[:, :, NT - 1:], sm[:, :, NT - 1:], ALU.add)\
               .then_inc(s_args, 1)
            dve.wait_ge(s_args, 1)
            def both(out, in0, in1, op):
                dve.tensor_tensor(per_chunk(out), in0[0].to_broadcast([MH, QT, P]), in1[0].to_broadcast([MH, QT, P]), op)
                return dve.tensor_tensor(per_sample(out), in0[1].to_broadcast([MH, NB, NT]),
                                         in1[1].to_broadcast([MH, NB, NT]), op)

            m_start = (k.m_c[:, 0:QT].unsqueeze(2), k.m_s0[:].unsqueeze(2))
            m_all = (per_chunk(m_run), sm)
            m_last = (per_chunk(m_run)[:, :, P - 1:P], sm[:, :, NT - 1:])
            both(lf, m_start, m_all, ALU.subtract)
            both(reset, (per_chunk(u), su), m_last, ALU.subtract)
            dve.tensor_tensor(k.decay_row[:, 0:QT].unsqueeze(2), m_start[0], m_last[0], ALU.subtract)
            dve.tensor_tensor(k.decay_row[:, QT:].unsqueeze(2), m_start[1], m_last[1], ALU.subtract)
            dve.tensor_copy(k.packed[0:MH, :], u[:])
            dve.tensor_tensor(f_m[:], f_m[:], m_run[:], ALU.add).then_inc(s_args, 1)
            dve.wait_ge(s_args, 2)
            dve.tensor_scalar(neg_m[:], m_run[:], -1.0, None, ALU.mult).then_inc(s_args, 1)
            dve.wait_ge(s_cols, 1)
            for tt in range(TT):
                r = P if tt < QT else NS_TOK
                src = ps[0:r, tt // 4, (tt % 4) * P:(tt % 4 + 1) * P].rearrange("p (q x) -> p q x", q=4)[:, :, 0:MH]
                dve.tensor_copy(k.gate_cols[0:r, tt, :, :], src)
            dve.tensor_copy(k.decay[:], ps[:, 6, 0:64].rearrange("p (h c) -> p h c", h=MH)).then_inc(s_cols_evac, 1)


def stage_mlstm(k):
    nc, ps = k.nc, k.ps
    V1 = MD + 1
    off = k.SPARE_OFF

    def work(name, shape):
        nonlocal off
        t = k.at(name, off, shape)
        size = 4
        for n in shape[1:]:
            size *= n
        off += (size + 31) // 32 * 32
        return t

    weight = work("mlstm_E", [P, MH, P])
    wt = work("mlstm_W", [P, MH, P])
    kws = work("mlstm_Kw", [P, MH, P])
    qi = work("mlstm_Qi", [P, MH, P])
    assert off <= k.HT_OFF
    C_s = k.at("C_samples", k.RING_OFF, [P, NB * MH, V1])
    off = k.WORK_OFF
    hn = work("mlstm_hn", [P, MH, P])
    C_p = work("C_prompt", [P, MH, V1])
    q_b = k.qk[:, 0:MH, 0:NB * (NS_TOK + NT)]
    stats, mv = work("ln_stats", [P, MH, 6]), work("ln_mean_var", [P, MH, 2])
    den, r, tmp = work("ln_den", [P, MH]), work("ln_r", [P, MH]), work("ln_tmp", [P, MH])
    n_cols, n_rows = work("n_cols", [P, NB * MH + MH]), work("n_rows", [NB * MH + MH, P])
    n_in = work("n_in", [NB * MH, P])
    block_of, ws_b = work("in_sample", [NS_TOK, NB]), work("ws_by_sample", [NS_TOK, NB, MH])
    assert off <= k.TOP
    n_c, n_n, s_zero = k.sem("C_loaded"), k.sem("n_loaded"), k.sem("mlstm_zeroed")
    s_bc, s_st, s_kt = k.sem("gates_broadcast"), k.sem("qk_product"), k.sem("keys_turned")
    s_exp, s_mask, s_wt, s_kws, s_qi = (k.sem("E_exps"), k.sem("E_masked"), k.sem("W_ready"), k.sem("Kw_ready"),
                                        k.sem("Qi_ready"))
    s_num, s_dc, s_c, s_var, s_root = (k.sem("num_product"), k.sem("dC_product"), k.sem("C_updated"),
                                       k.sem("var_ready"), k.sem("root_ready"))
    s_hn, s_hnt, s_at, s_out, s_chain = (k.sem("hn_ready"), k.sem("hn_turned"), k.sem("aT_ready"),
                                         k.states_stored, k.sem("mlstm_chain"))
    s_nt, s_nr = k.sem("n_turned"), k.sem("n_rows_ready")
    BCM, BCI, ST, KT, NUM, DC = 0, 1, 2, 3, 4, 6
    S = QT

    def tokens(c):
        return (P if c < S else NS_TOK), slice(c * P, min((c + 1) * P, TOK))

    def heads(bank, n):
        return ps[:, bank, 0:MH * n].rearrange("p (h t) -> p h t", h=MH)

    def pair(bank, h):
        return ps[:, bank + h // 2, (h % 2) * V1:(h % 2 + 1) * V1]

    with nc.Block() as block:

        @block.sync
        def _(sp):
            sp.dma_start(C_s[:, :, 0:MD], k.state_C[0].rearrange("b h k v -> k (b h) v")).then_inc(n_c, 16)
            sp.dma_start(n_in[:], k.state_n[0].rearrange("b h k -> (b h) k")).then_inc(n_n, 16)
            sp.wait_ge(s_c, MH * QT)
            sp.dma_start(k.o_C[0][0, 0].rearrange("h k v -> k h v"), C_p[:, :, 0:MD]).then_inc(s_out, 16)
            sp.wait_ge(s_c, MH * (QT + NB))
            sp.dma_start(k.o_C[1][0].rearrange("b h k v -> k (b h) v"), C_s[:, :, 0:MD]).then_inc(s_out, 16)
            sp.wait_ge(s_nr, 1)
            sp.dma_start(k.o_n[1][0].rearrange("b h k -> (b h) k"), n_rows[0:NB * MH, :]).then_inc(s_out, 16)
            sp.dma_start(k.o_n[0][0, 0], n_rows[NB * MH:, :]).then_inc(s_out, 16)
            sp.wait_ge(s_out, 64)

        @block.gpsimd
        def _(pool):
            pool.memset(C_p[:], 0.0).then_inc(s_zero, 1)
            pool.memset(block_of[:], 1.0).then_inc(s_zero, 1)
            pool.wait_ge(s_zero, 2)
            pool.affine_select(out=block_of[:], in_=block_of[:], compare_op=ALU.is_ge, fill=0.0, base=0,
                               pattern=[[-NT, NB]], channel_multiplier=1).then_inc(s_zero, 1)
            pool.wait_ge(s_zero, 3)
            pool.affine_select(out=block_of[:], in_=block_of[:], compare_op=ALU.is_ge, fill=0.0, base=NT - 1,
                               pattern=[[NT, NB]], channel_multiplier=-1).then_inc(s_zero, 1)
            for c in range(S):
                pool.wait_ge(s_exp, MH * (c + 1))
                if c == 4:
                    pool.wait_ge(s_num, 3)
                    pool.wait_ge(s_qi, 3)
                    pool.memset(q_b, 0.0).then_inc(s_zero, 1)
                pool.affine_select(out=weight[:], in_=weight[:], compare_op=ALU.is_ge, fill=0.0, base=0,
                                   pattern=[[0, MH], [1, P]], channel_multiplier=-1).then_inc(s_mask, 1)
            pool.wait_ge(s_exp, MH * (S + 1))
            e = weight[0:NS_TOK, :, 0:NS_TOK]
            pool.affine_select(out=e, in_=e, compare_op=ALU.is_ge, fill=0.0, base=0,
                               pattern=[[0, MH], [1, NS_TOK]], channel_multiplier=-1).then_inc(s_mask, 1)
            pool.wait_ge(s_mask, S + 1)
            for h in range(MH):
                eh = weight[0:NS_TOK, h, 0:NS_TOK].rearrange("p (b t) -> p b t", b=NB)
                ins = pool.affine_select(out=eh, in_=eh, compare_op=ALU.is_ge, fill=0.0, base=0,
                                         pattern=[[-NT, NB], [0, NT]], channel_multiplier=1)
            ins.then_inc(s_mask, 1)

        @block.tensor
        def _(pe):
            pe.wait_ge(n_n, 16)
            pe.transpose(ps[:, DC, 0:NB * MH], n_in[:], k.ident[0:NB * MH, 0:NB * MH]).then_inc(s_nt, 1)
            for c in range(S + 1):
                n, t = tokens(c)
                if c:
                    pe.wait_ge(s_exp, MH * c)
                    pe.wait_ge(s_qi, c)
                    pe.wait_ge(s_wt, c)
                    pe.wait_ge(s_at, c)
                for h in range(MH):
                    pe.matmul(heads(BCM, n)[:, h], k.select[0:MH, h, :], k.neg_m[:, t], start=True, stop=True)
                for h in range(MH):
                    mm = pe.matmul(heads(BCI, n)[:, h], k.select[32:32 + MH, h, :], k.packed[32:32 + MH, t],
                                   start=True, stop=True)
                mm.then_inc(s_bc, 1)
                for h in range(MH):
                    mm = pe.matmul(heads(ST, n)[0:n, h], k.qk[:, MH + h, t], k.qk[:, h, t], start=True, stop=True)
                mm.then_inc(s_st, 1)
                for h in range(MH):
                    mm = pe.transpose(ps[0:n, KT, h * P:(h + 1) * P], k.qk[:, MH + h, t], k.ident[:])
                mm.then_inc(s_kt, 1)
                pe.wait_ge(s_wt, c + 1)
                pe.wait_ge(s_qi, c + 1)
                if c == 0:
                    pe.wait_ge(s_zero, 1)
                if c < S:
                    if c:
                        pe.wait_ge(s_c, MH * c)
                else:
                    pe.wait_ge(n_c, 16)
                    pe.wait_ge(s_nt, 2)
                for h in range(MH):
                    pe.matmul(pair(NUM, h)[0:n], wt[0:n, h, 0:n], k.v_aug[0:n, c, h, :], start=True, stop=False)
                    if c < S:
                        mm = pe.matmul(pair(NUM, h), qi[:, h, :], C_p[:, h, :], start=False, stop=True)
                    else:
                        for b in range(NB):
                            mm = pe.matmul(pair(NUM, h)[0:n], q_b[:, h, b * NS_TOK:(b + 1) * NS_TOK],
                                           C_s[:, b * MH + h, :], start=False, stop=(b == NB - 1))
                mm.then_inc(s_num, 1)
                if c < S:
                    pe.wait_ge(s_kws, c + 1)
                    if c == 0:
                        pe.wait_ge(s_nt, 2)
                    for h in range(MH):
                        mm = pe.matmul(pair(DC, h), kws[:, h, :], k.v_aug[:, c, h, :], start=True, stop=True)
                    mm.then_inc(s_dc, 1)
                else:
                    for b in range(NB):
                        pe.wait_ge(s_kws, c + b + 1)
                        pe.wait_ge(s_c, MH * (S + b))
                        for h in range(MH):
                            mm = pe.matmul(pair(DC, h), kws[0:n, h, :], k.v_aug[0:n, c, h, :], start=True, stop=True)
                        mm.then_inc(s_dc, 1)
                pe.wait_ge(s_hn, c + 1)
                for h in range(MH):
                    mm = pe.transpose(heads(KT, n)[:, h], hn[0:n, h, :], k.ident[0:n, 0:n])
                mm.then_inc(s_hnt, 1)
            pe.wait_ge(s_c, MH * (S + NB))
            pe.wait_ge(s_at, S + 1)
            pe.wait_ge(s_nt, 3)
            pe.transpose(ps[0:NB * MH + MH, KT, 0:P], n_cols[:], k.ident[:]).then_inc(s_nt, 1)

        @block.scalar
        def _(act):
            for c in range(S + 1):
                n, t = tokens(c)
                act.wait_ge(s_bc, c + 1)
                if c:
                    act.wait_ge(s_wt, c)
                for h in range(MH):
                    act.activation(weight[0:n, h, 0:n], heads(BCM, n)[0:n, h], ACT.Exp,
                                   bias=k.gate_cols[0:n, c, 0, h:h + 1]).then_inc(s_exp, 1)
                act.wait_ge(s_var, c + 1)
                act.activation(tmp[0:n], tmp[0:n], ACT.Sqrt).then_inc(s_root, 1)

        @block.vector
        def _(dve):
            link = Chain(dve, s_chain)
            dve.wait_ge(s_nt, 1)
            dve.tensor_copy(C_s[:, :, MD], ps[:, DC, 0:NB * MH]).then_inc(s_nt, 1)
            for c in range(S + 1):
                n, t = tokens(c)
                sample = c == S
                dve.wait_ge(s_bc, c + 1)
                if c:
                    dve.wait_ge(s_num, c)
                if not sample:
                    dve.tensor_tensor(qi[:], k.qk[:, 0:MH, t], heads(BCI, n), ALU.mult).then_inc(s_qi, 1)
                else:
                    dve.wait_ge(s_zero, 5)
                    for h in range(MH):
                        dst = q_b[:, h, :].rearrange("p (b x) -> p b x", b=NB)[:, :, 0:NT]
                        ins = dve.tensor_tensor(dst, k.qk[:, h, t].rearrange("p (b t) -> p b t", b=NB),
                                                heads(BCI, n)[:, h].rearrange("p (b t) -> p b t", b=NB), ALU.mult)
                    ins.then_inc(s_qi, 1)
                dve.wait_ge(s_st, c + 1)
                dve.wait_ge(s_mask, c + 1 if not sample else S + 2)
                dve.tensor_tensor(wt[0:n, :, 0:n], heads(ST, n)[0:n], weight[0:n, :, 0:n], ALU.mult).then_inc(s_wt, 1)
                dve.wait_ge(s_kt, c + 1)
                if not sample:
                    if c:
                        dve.wait_ge(s_dc, c)
                    w_s = k.gate_cols[:, c, 3, :].unsqueeze(2).to_broadcast([P, MH, P])
                    dve.tensor_tensor(kws[:], heads(KT, P), w_s, ALU.mult).then_inc(s_kws, 1)
                else:
                    for b in range(NB):
                        ins = dve.tensor_scalar(ws_b[:, b, :], k.gate_cols[0:n, c, 3, :], block_of[:, b:b + 1], None,
                                                ALU.mult)
                    link(ins)
                    for b in range(NB):
                        dve.wait_ge(s_dc, S + b)
                        dve.tensor_tensor(kws[0:n], heads(KT, P)[0:n],
                                          ws_b[:, b, :].unsqueeze(2).to_broadcast([n, MH, P]), ALU.mult)\
                           .then_inc(s_kws, 1)
                        if b == 0:
                            dve.wait_ge(s_num, S + 1)
                        dve.wait_ge(s_dc, S + b + 1)
                        for h in range(MH):
                            i = b * MH + h
                            dve.scalar_tensor_tensor(C_s[:, i, :], C_s[:, i, :], k.decay[:, h, QT + b:QT + b + 1],
                                                     pair(DC, h), ALU.mult, ALU.add).then_inc(s_c, 1)
                dve.wait_ge(s_num, c + 1)
                for h in range(MH):
                    dve.bn_stats(stats[0:n, h, :], pair(NUM, h)[0:n, 0:MD])
                    ins = dve.tensor_copy(den[0:n, h:h + 1], pair(NUM, h)[0:n, MD:V1])
                link(ins)
                for h in range(MH):
                    dve.bn_aggr(mv[0:n, h, :], stats[0:n, h, :])
                link(dve.scalar_tensor_tensor(r[0:n], den[0:n], -1.0, den[0:n], ALU.mult, ALU.max))
                link(dve.tensor_tensor(den[0:n], r[0:n], k.gate_cols[0:n, c, 2, :], ALU.max))
                link(dve.reciprocal(r[0:n], den[0:n]))
                link(dve.tensor_tensor(tmp[0:n], mv[0:n, :, 1], r[0:n], ALU.mult))
                link(dve.tensor_tensor(tmp[0:n], tmp[0:n], r[0:n], ALU.mult))
                dve.tensor_scalar(tmp[0:n], tmp[0:n], EPS, None, ALU.add).then_inc(s_var, 1)
                dve.wait_ge(s_root, c + 1)
                link(dve.reciprocal(den[0:n], tmp[0:n]))
                link(dve.tensor_tensor(r[0:n], r[0:n], den[0:n], ALU.mult))
                if c:
                    dve.wait_ge(s_hnt, c)
                for h in range(MH):
                    ins = dve.tensor_scalar(hn[0:n, h, :], pair(NUM, h)[0:n, 0:MD], mv[0:n, h, 0:1], r[0:n, h:h + 1],
                                            ALU.subtract, ALU.mult)
                ins.then_inc(s_hn, 1)
                if not sample:
                    dve.wait_ge(s_dc, c + 1)
                    for h in range(MH):
                        dve.scalar_tensor_tensor(C_p[:, h, :], C_p[:, h, :], k.decay[:, h, c:c + 1], pair(DC, h),
                                                 ALU.mult, ALU.add).then_inc(s_c, 1)
                dve.wait_ge(s_hnt, c + 1)
                for h in range(MH):
                    ins = dve.scalar_tensor_tensor(k.aT[:, h, t], heads(KT, n)[:, h],
                                                   k.cols[:, k.c_m_norm + h:k.c_m_norm + h + 1], k.aT[:, h, t],
                                                   ALU.mult, ALU.mult)
                ins.then_inc(s_at, 1)
            dve.wait_ge(s_c, MH * (S + NB))
            dve.tensor_copy(n_cols[:, 0:NB * MH], C_s[:, :, MD])
            dve.tensor_copy(n_cols[:, NB * MH:], C_p[:, :, MD]).then_inc(s_nt, 1)
            dve.wait_ge(s_nt, 4)
            dve.tensor_copy(n_rows[:], ps[0:NB * MH + MH, KT, 0:P]).then_inc(s_nr, 1)


def stage_compress(k):
    nc, ps = k.nc, k.ps
    ROW = STRIDE * GD
    off = k.CMP_END
    x = [k.at(f"strides{i}", off + i * ROW * 4, [P, ROW]) for i in range(2)]
    off += 2 * ROW * 4
    w_pos = [k.at(f"pos_weights{i}", off + i * STRIDE * HD * 4, [P, STRIDE, HD]) for i in range(4)]
    off += 4 * STRIDE * HD * 4
    prod = [k.at(f"pos_product{i}", off + i * ROW * 4, [P, ROW]) for i in range(2)]
    off = k.SPARE_OFF
    half_sums = [k.at(f"half_sums{i}", off + i * 1024, [P, 2, GD]) for i in range(2)]
    off += 2048
    second_t = [k.at(f"second_halfT{i}", off + i * 512, [P, P]) for i in range(2)]
    pooled_t = [k.at(f"pooledT{i}", off + 1024 + i * 512, [P, P]) for i in range(2)]
    off += 2048
    proj = [k.at(f"cmp_proj{i}", off + i * 512, [P, P]) for i in range(2)]
    off += 1024
    table = k.at("page_rows", off, [P, NB], I32)
    lane = k.at("stride_in_page", off + 32, [P, NB], I32)
    scratch = k.at("page_scratch", off + 64, [P, NB])
    assert off + 128 <= k.HT_OFF
    units = [(s, kv) for s in range(NB) for kv in range(2)] + [(NB, kv) for kv in range(2)]
    s_x = [k.sem(f"strides_loaded{i}") for i in range(2)]
    s_xp = [k.sem(f"prompt_strides_loaded{i}") for i in range(2)]
    s_w, s_pt, s_idx, s_zero, s_proj = (k.sem("pos_loaded"), k.sem("table_loaded"), k.sem("indices_ready"),
                                        k.sem("cmp_zeroed"), k.sem("proj_loaded"))
    s_first, s_second, s_sums, s_turn = (k.sem("first_product"), k.sem("second_product"), k.sem("half_sums_ready"),
                                         k.sem("halves_turned"))
    s_sec_t, s_pool, s_map, s_evac, s_chain = (k.sem("second_copied"), k.sem("pooled"), k.sem("mapped"),
                                               k.sem("cmp_evac"), k.sem("cmp_chain"))

    def loaded(eng, u):
        if u < 2 * NB:
            eng.wait_ge(s_x[u % 2], 16 * (u // 2 + 1))
        else:
            eng.wait_ge(s_xp[u % 2], 16)

    def strides(u):
        return NSUB if units[u][0] < NB else SEQ // STRIDE

    with nc.Block() as block:

        @block.sync
        def _(sp):
            for q in range(PAST // PAGE):
                entry = k.page_table[:, q:q + 1].rearrange("b q -> q b").to_broadcast([PAGE // STRIDE, NB])
                sp.dma_start(table[q * 8:(q + 1) * 8, :], entry).then_inc(s_pt, 16)
            for half in range(2):
                for kv, src in enumerate((k.cmp_pos_k, k.cmp_pos_v)):
                    rows = src[0, half * STRIDE:(half + 1) * STRIDE].rearrange("j d -> (j d)").partition_broadcast(P)
                    sp.dma_start(w_pos[2 * kv + half][:].rearrange("p j d -> p (j d)"), rows).then_inc(s_w, 16)
            sp.wait_ge(s_zero, 1)
            for kv, src in enumerate((k.cmp_proj_k, k.cmp_proj_v)):
                for g in range(NG):
                    rows = slice(g * HD, (g + 1) * HD)
                    sp.dma_start(proj[kv][rows, rows], src[0]).then_inc(s_proj, 16)
            for u in range(2 * NB, len(units)):
                sp.wait_ge(s_second, u - 1)
                sp.wait_ge(s_first, u - 1)
                src = (k.o_k_cmp, k.o_v_cmp)[units[u][1]][0][0, 0]
                sp.dma_start(x[u % 2][0:strides(u), :], src.rearrange("(n j) g d -> n (j g d)", j=STRIDE))\
                  .then_inc(s_xp[u % 2], 16)

        @block.gpsimd
        def _(pool):
            pool.memset(proj[0][:], 0.0)
            pool.memset(proj[1][:], 0.0)
            pool.memset(k.kc_pad[:], 0.0).then_inc(s_zero, 1)
            pool.iota(lane[:], pattern=[[0, NB]], base=0, channel_multiplier=1).then_inc(s_zero, 1)
            pool.wait_ge(s_idx, 1)

            def gather(u):
                s, kv = units[u]
                cache = (k.cache_k_cmp, k.cache_v_cmp)[kv]
                pool.indirect_dma_start(
                    out=x[u % 2][:], out_offset=None,
                    in_=cache[0].rearrange("q (s j) g d -> (q s) (j g d)", j=STRIDE),
                    in_offset=bass.IndirectOffsetOnAxis(ap=k.page_idx[:, s:s + 1], axis=0)).then_inc(s_x[u % 2], 16)

            gather(0)
            for u in range(len(units)):
                n = strides(u)
                if 1 <= u + 1 < 2 * NB:
                    if u >= 1:
                        pool.wait_ge(s_second, u)
                        pool.wait_ge(s_first, u)
                    gather(u + 1)
                loaded(pool, u)
                if u == 0:
                    pool.wait_ge(s_w, 64)
                if u:
                    pool.wait_ge(s_sums, u)
                w = w_pos[2 * units[u][1]][0:n].unsqueeze(2).to_broadcast([n, STRIDE, NG, HD])
                pool.tensor_tensor(prod[0][0:n].rearrange("p (j g d) -> p j g d", j=STRIDE, g=NG),
                                   x[u % 2][0:n].rearrange("p (j g d) -> p j g d", j=STRIDE, g=NG), w,
                                   ALU.mult).then_inc(s_first, 1)

        @block.vector
        def _(dve):
            link = Chain(dve, s_chain)
            dve.wait_ge(s_zero, 2)
            dve.wait_ge(s_pt, 16 * 16)
            link(dve.tensor_single_scalar(lane[:], lane[:], 7, ALU.bitwise_and))
            link(dve.tensor_copy(scratch[:], lane[:]))
            dve.scalar_tensor_tensor(k.page_idx[:], table[:], 8.0, scratch[:], ALU.mult, ALU.add).then_inc(s_idx, 1)

            def pool_pair(u):
                n = strides(u)
                dve.wait_ge(s_sec_t, u + 1)
                if u >= 2:
                    dve.wait_ge(s_map, u - 1)
                dve.tensor_tensor(pooled_t[u % 2][:, 0:n - 1], ps[:, u % 2, 0:n - 1], second_t[u % 2][:, 1:n], ALU.add)\
                   .then_inc(s_pool, 1)

            for u in range(len(units)):
                n = strides(u)
                loaded(dve, u)
                if u == 0:
                    dve.wait_ge(s_w, 64)
                w = w_pos[2 * units[u][1] + 1][0:n].unsqueeze(2).to_broadcast([n, STRIDE, NG, HD])
                dve.tensor_tensor(prod[1][0:n].rearrange("p (j g d) -> p j g d", j=STRIDE, g=NG),
                                  x[u % 2][0:n].rearrange("p (j g d) -> p j g d", j=STRIDE, g=NG), w,
                                  ALU.mult).then_inc(s_second, 1)
                dve.wait_ge(s_second, u + 1)
                if u >= 2:
                    dve.wait_ge(s_turn, u - 1)
                dve.tensor_reduce(half_sums[u % 2][0:n, 1, :], prod[1][0:n].rearrange("p (j x) -> p x j", j=STRIDE),
                                  AX.X, ALU.add)
                dve.wait_ge(s_first, u + 1)
                dve.tensor_reduce(half_sums[u % 2][0:n, 0, :], prod[0][0:n].rearrange("p (j x) -> p x j", j=STRIDE),
                                  AX.X, ALU.add).then_inc(s_sums, 1)
                dve.wait_ge(s_sums, u + 1)
                if u:
                    pool_pair(u - 1)
            pool_pair(len(units) - 1)

        @block.scalar
        def _(act):
            def copy_second(u):
                n = strides(u)
                act.wait_ge(s_turn, u + 1)
                if u >= 2:
                    act.wait_ge(s_pool, u - 1)
                act.copy(second_t[u % 2][:, 0:n], ps[:, 2 + u % 2, 0:n]).then_inc(s_sec_t, 1)

            def keep(u):
                s, kv = units[u]
                n = strides(u) - 1
                bank = 4 + u % 2
                act.wait_ge(s_map, u + 1)
                if kv:
                    act.copy(k.vc[0:n, s, :], ps[0:n, bank, 0:GD]).then_inc(s_evac, 1)
                elif s < NB:
                    act.copy(k.kc_t[:, s, 0:n], ps[:, bank, 0:n]).then_inc(s_evac, 1)
                else:
                    act.wait_ge(s_zero, 1)
                    for g in range(NG):
                        rows = slice(g * HD, (g + 1) * HD)
                        ins = act.copy(k.kc_pad[rows, g, 0:n], ps[rows, bank, 0:n])
                    ins.then_inc(s_evac, 1)

            for u in range(len(units)):
                copy_second(u)
                if u:
                    keep(u - 1)
            keep(len(units) - 1)

        @block.tensor
        def _(pe):
            def map_unit(u):
                n = strides(u) - 1
                bank = 4 + u % 2
                pe.wait_ge(s_pool, u + 1)
                if u >= 2:
                    pe.wait_ge(s_evac, u - 1)
                if units[u][1]:
                    mm = pe.matmul(ps[0:n, bank, 0:GD], pooled_t[u % 2][:, 0:n], proj[1][:], start=True, stop=True)
                else:
                    mm = pe.matmul(ps[:, bank, 0:n], proj[0][:], pooled_t[u % 2][:, 0:n], start=True, stop=True)
                mm.then_inc(s_map, 1)

            pe.wait_ge(s_proj, 64)
            for u in range(len(units)):
                n = strides(u)
                pe.wait_ge(s_sums, u + 1)
                if u >= 2:
                    pe.wait_ge(s_pool, u - 1)
                pe.transpose(ps[:, u % 2, 0:n], half_sums[u % 2][0:n, 0, :], k.ident[0:n, 0:n])
                pe.transpose(ps[:, 2 + u % 2, 0:n], half_sums[u % 2][0:n, 1, :], k.ident[0:n, 0:n]).then_inc(s_turn, 1)
                if u:
                    map_unit(u - 1)
            map_unit(len(units) - 1)


def stage_nsa_prompt(k):
    nc, ps = k.nc, k.ps
    NCB = SEQ // STRIDE - 1
    WT = WIN // P + 1
    LW = WT * P
    LC = 120
    off = k.CMP_END
    tables = k.at("bias_tables", off, [P, HG, SEQ + LW + LC])
    off += HG * (SEQ + LW + LC) * 4
    SLEN = SEQ + LW + 64
    NS = 3
    s_buf = [k.at(f"scores{i}", off + i * SLEN * 4, [P, SLEN]) for i in range(NS)]
    off += NS * SLEN * 4
    NPT = 4
    pt_buf = [k.at(f"probsT{i}", off + i * 2048, [P, 4, P]) for i in range(NPT - 1)]
    off += (NPT - 1) * 2048
    assert off <= k.TOP
    off = k.SPARE_OFF
    dist = k.at("distance", off, [P, SEQ])
    off += SEQ * 4
    dist_c = k.at("distance_cmp", off, [P, LC])
    off += 512
    top = [k.at(f"row_max{i}", off + 64 * i, [P, 3]) for i in range(2)]
    neg_top = [k.at(f"row_neg_max{i}", off + 64 * i + 32, [P, 3]) for i in range(2)]
    off += 128
    sums = [k.at(f"row_sum{i}", off + 64 * i, [P, 3]) for i in range(2)]
    factor = [k.at(f"row_factor{i}", off + 64 * i + 32, [P, 3]) for i in range(2)]
    off += 128
    valid = k.at("has_block", off, [P, 1])
    off += 32
    pt_buf.append(k.at(f"probsT{NPT - 1}", off, [P, 4, P]))
    off += 2048
    assert off <= k.HT_OFF
    units = [(g, qt, i) for g in range(NG) for qt in range(QT) for i in range(HG)]
    NU = len(units)

    def key_tiles(qt):
        first = max(0, qt - WT + 1)
        return ([("slc", kt, kt * P, P) for kt in range(qt + 1)]
                + [("win", kt, SEQ + (kt - first) * P, P) for kt in range(first, qt + 1)]
                + [("cmp", 0, SEQ + LW, NCB)])

    groups = []
    for n, (g, qt, i) in enumerate(units):
        tiles = key_tiles(qt)
        for a in range(0, len(tiles), 4):
            groups.append((n, tiles[a:a + 4], a + 4 >= len(tiles)))
    first_group = [min(x for x, gr in enumerate(groups) if gr[0] == n) for n in range(NU)] + [len(groups)]
    def evacs_before(which, x):
        return (x + 1 - which) // 2

    s_tab, s_gate = k.sem("tables_ready"), k.sem("branch_gates_ready")
    s_a, s_b = k.sem("slc_scores"), k.sem("win_cmp_scores")
    s_ta, s_tb, s_neg = k.sem("slc_biased"), k.sem("win_cmp_biased"), k.sem("neg_max_ready")
    s_exp, s_fac, s_p, s_chain = k.sem("probs_exp"), k.sem("factor_ready"), k.sem("probs_ready"), k.sem("nsa_chain")
    s_turn, s_pv, s_out = k.sem("probs_turned"), k.sem("pv_product"), k.sem("nsa_out_evac")
    s_ev = [k.sem("probsT_evac_act"), k.sem("probsT_evac_dve")]
    s_iota = k.sem("distances")

    with nc.Block() as block:

        @block.gpsimd
        def _(pool):
            pool.iota(dist[:], pattern=[[1, SEQ]], base=-(SEQ - P), channel_multiplier=-1,
                      allow_small_or_imprecise_dtypes=True).then_inc(s_iota, 1)
            pool.iota(dist_c[:], pattern=[[STRIDE, LC]], base=CBLK - 1 - 56 * STRIDE, channel_multiplier=-1,
                      allow_small_or_imprecise_dtypes=True).then_inc(s_iota, 1)
            pool.memset(valid[:], 1.0).then_inc(s_iota, 1)
            pool.tensor_copy(k.kT_last[:], k.kT_pad[:, :, SEQ:TOK])
            pool.wait_ge(s_iota, 3)
            pool.affine_select(out=valid[:], in_=valid[:], compare_op=ALU.is_ge, fill=0.0, base=-(CBLK - 1),
                               pattern=[[0, 1]], channel_multiplier=1).then_inc(s_iota, 1)
            pool.wait_ge(s_tab, 3 * HG)
            slc, win, cmp = tables[:, :, 0:SEQ], tables[:, :, SEQ:SEQ + LW], tables[:, :, SEQ + LW:]
            pool.affine_select(out=slc, in_=slc, compare_op=ALU.is_ge, fill=NEG, base=SEQ - P,
                               pattern=[[0, HG], [-1, SEQ]], channel_multiplier=1)
            pool.affine_select(out=cmp, in_=cmp, compare_op=ALU.is_ge, fill=NEG, base=56 * STRIDE - CBLK + 1,
                               pattern=[[0, HG], [-STRIDE, LC]], channel_multiplier=1)
            pool.affine_select(out=win, in_=win, compare_op=ALU.is_ge, fill=NEG, base=WIN,
                               pattern=[[0, HG], [-1, LW]], channel_multiplier=1).then_inc(s_tab, 1)
            pool.wait_ge(s_tab, 3 * HG + 1)
            pool.affine_select(out=win, in_=win, compare_op=ALU.is_ge, fill=NEG, base=0,
                               pattern=[[0, HG], [1, LW]], channel_multiplier=-1).then_inc(s_tab, 1)

        @block.tensor
        def _(pe):
            def scores(n):
                g, qt, i = units[n]
                q = k.aq[:, i, qt * P:(qt + 1) * P]
                if n:
                    pe.wait_ge(s_ta, n)
                keys = (qt + 1) * P
                for a in range(0, keys, 512):
                    m = min(512, keys - a)
                    mm = pe.matmul(ps[:, a // 512, 0:m], q, k.kT_pad[:, g, a:a + m], start=True, stop=True)
                mm.then_inc(s_a, 1)
                if n:
                    pe.wait_ge(s_tb, n)
                first = max(0, qt - WT + 1) * P
                for a in range(0, keys - first, 512):
                    m = min(512, keys - first - a)
                    pe.matmul(ps[:, 2 + a // 512, 0:m], q, k.kT_pad[:, 2 + g, first + a:first + a + m],
                              start=True, stop=True)
                pe.matmul(ps[:, 3, P:P + NCB], q, k.kc_pad[:, g, 0:NCB], start=True, stop=True).then_inc(s_b, 1)

            def turn(x):
                n, tiles, _ = groups[x]
                pe.wait_ge(s_p, n + 1)
                if x >= 2:
                    pe.wait_ge(s_ev[x % 2], evacs_before(x % 2, x))
                for c, (_, _, col, m) in enumerate(tiles):
                    mm = pe.transpose(ps[0:m, 4 + x % 2, c * P:(c + 1) * P], s_buf[n % NS][:, col:col + m], k.ident[:])
                mm.then_inc(s_turn, 1)

            def pv(x):
                n, tiles, last = groups[x]
                g, qt, i = units[n]
                pe.wait_ge(s_ev[x % 2], evacs_before(x % 2, x) + 1)
                if x == first_group[n] and n >= 2:
                    pe.wait_ge(s_out, n - 1)
                for c, (branch, kt, _, m) in enumerate(tiles):
                    cols = slice(g * HD, (g + 1) * HD)
                    if branch == "cmp":
                        v = k.vc[0:m, NB, cols]
                    else:
                        r = R_VS if branch == "slc" else R_VW
                        v = k.rows[:, kt, r + g * HD:r + (g + 1) * HD]
                    mm = pe.matmul(ps[cols, 6 + n % 2, 0:P], v, pt_buf[x % NPT][0:m, c, :],
                                   start=(x == first_group[n] and c == 0), stop=(last and c == len(tiles) - 1))
                mm.then_inc(s_pv, 1)

            scores(0)
            scores(1)
            for n in range(NU):
                for x in range(first_group[n], first_group[n + 1]):
                    turn(x)
                    if x > first_group[n]:
                        pv(x - 1)
                if n + 2 < NU:
                    scores(n + 2)
                pv(first_group[n + 1] - 1)

        def evacuate(eng, copy, which, x):
            n, tiles, last = groups[x]
            eng.wait_ge(s_turn, x + 1)
            if x >= NPT:
                eng.wait_ge(s_pv, x - NPT + 1)
            full = sum(1 for t in tiles if t[3] == P)
            ins = None
            if full:
                ins = copy(pt_buf[x % NPT][:, 0:full, :].rearrange("p c q -> p (c q)"), ps[:, 4 + x % 2, 0:full * P])
            if full < len(tiles):
                m = tiles[full][3]
                ins = copy(pt_buf[x % NPT][0:m, full, :], ps[0:m, 4 + x % 2, full * P:(full + 1) * P])
            ins.then_inc(s_ev[which], 1)

        @block.scalar
        def _(act):
            def finish(n):
                g, qt, i = units[n]
                rows = slice(g * HD, (g + 1) * HD)
                act.wait_ge(s_pv, first_group[n + 1])
                act.copy(k.bT[rows, i, qt * P:(qt + 1) * P], ps[rows, 6 + n % 2, 0:P]).then_inc(s_out, 1)

            for r, tiles in ((P, slice(0, QT)), (NS_TOK, slice(QT, TT))):
                g_pre = k.rows[0:r, tiles, R_G:R_END].rearrange("p t (h b) -> p t h b", h=NH)
                act.activation(k.gates[0:r, tiles, :, 0:2], g_pre[:, :, :, 1:3], ACT.Sigmoid)
                ins = act.activation(k.gates[0:r, tiles, :, 2:3], g_pre[:, :, :, 0:1], ACT.Sigmoid)
            ins.then_inc(s_gate, 1)

            def exponentials(n):
                g, qt, i = units[n]
                s = s_buf[n % NS]
                act.wait_ge(s_neg, n + 1)
                for br, (a, m) in enumerate(((0, (qt + 1) * P), (SEQ, min(qt + 1, WT) * P), (SEQ + LW, NCB))):
                    ins = act.activation(s[:, a:a + m], s[:, a:a + m], ACT.Exp, bias=neg_top[n % 2][:, br:br + 1],
                                         accum_out=sums[n % 2][:, br:br + 1])
                ins.then_inc(s_exp, 1)

            exponentials(0)
            for n in range(NU):
                own = [x for x in range(first_group[n], first_group[n + 1]) if x % 2 == 0]
                for x in own[:1]:
                    evacuate(act, act.copy, 0, x)
                if n + 1 < NU:
                    exponentials(n + 1)
                for x in own[1:]:
                    evacuate(act, act.copy, 0, x)
                finish(n)

        @block.vector
        def _(dve):
            link = Chain(dve, s_chain)
            dve.wait_ge(s_iota, 2)
            for i in range(HG):
                dve.tensor_scalar(tables[:, i, 0:SEQ], dist[:], SLOPES[i], None, ALU.mult).then_inc(s_tab, 1)
                dve.tensor_scalar(tables[:, i, SEQ:SEQ + LW], dist[:, SEQ - LW:], SLOPES[i], None, ALU.mult)\
                   .then_inc(s_tab, 1)
                dve.tensor_scalar(tables[:, i, SEQ + LW:], dist_c[:], SLOPES[i], None, ALU.mult).then_inc(s_tab, 1)
            dve.wait_ge(s_tab, 3 * HG + 2)
            dve.wait_ge(s_gate, 1)
            dve.wait_ge(s_iota, 4)

            def biased(n):
                g, qt, i = units[n]
                s, b = s_buf[n % NS], n % 2
                if n == NU // 2:
                    link(dve.tensor_scalar(tables[:], tables[:], 2.0 ** -HG, None, ALU.mult))
                tab = tables[:, i, :]
                keys = (qt + 1) * P
                win = min(qt + 1, WT) * P
                if n >= NS:
                    dve.wait_ge(s_turn, first_group[n - NS + 1])
                dve.wait_ge(s_a, n + 1)
                two = ps[:, 0:2, :].rearrange("p a n -> p (a n)")
                dve.tensor_tensor_reduce(s[:, 0:keys], two[:, 0:keys], tab[:, SEQ - keys:SEQ], 1.0, 3 * NEG,
                                         ALU.add, ALU.max, top[b][:, 0:1]).then_inc(s_ta, 1)
                dve.wait_ge(s_b, n + 1)
                two = ps[:, 2:4, :].rearrange("p a n -> p (a n)")
                dve.tensor_tensor_reduce(s[:, SEQ:SEQ + win], two[:, 0:win], tab[:, SEQ + LW - win:SEQ + LW], 1.0,
                                         3 * NEG, ALU.add, ALU.max, top[b][:, 1:2])
                dve.tensor_tensor_reduce(s[:, SEQ + LW:SEQ + LW + NCB], ps[:, 3, P:P + NCB],
                                         tab[:, SEQ + LW + 56 - 8 * qt:][:, 0:NCB], 1.0, 3 * NEG, ALU.add, ALU.max,
                                         top[b][:, 2:3]).then_inc(s_tb, 1)
                dve.wait_ge(s_tb, n + 1)
                dve.tensor_scalar(neg_top[b][:], top[b][:], -1.0, None, ALU.mult).then_inc(s_neg, 1)

            def scaled(n):
                g, qt, i = units[n]
                s, b, h = s_buf[n % NS], n % 2, g * HG + i
                keys = (qt + 1) * P
                dve.wait_ge(s_exp, n + 1)
                link(dve.reciprocal(factor[b][:], sums[b][:]))
                ins = dve.tensor_tensor(factor[b][:], factor[b][:], k.gates[:, qt, h, :], ALU.mult)
                if qt == 0:
                    link(ins)
                    ins = dve.tensor_tensor(factor[b][:, 2:3], factor[b][:, 2:3], valid[:], ALU.mult)
                ins.then_inc(s_fac, 1)
                dve.wait_ge(s_fac, n + 1)
                win = min(qt + 1, WT) * P
                dve.tensor_scalar(s[:, 0:keys], s[:, 0:keys], factor[b][:, 0:1], None, ALU.mult)
                dve.tensor_scalar(s[:, SEQ:SEQ + win], s[:, SEQ:SEQ + win], factor[b][:, 1:2], None, ALU.mult)
                dve.tensor_scalar(s[:, SEQ + LW:SEQ + LW + NCB], s[:, SEQ + LW:SEQ + LW + NCB], factor[b][:, 2:3],
                                  None, ALU.mult).then_inc(s_p, 1)

            biased(0)
            scaled(0)
            for n in range(NU):
                if n + 1 < NU:
                    biased(n + 1)
                for x in range(first_group[n], first_group[n + 1]):
                    if x % 2 == 1:
                        evacuate(dve, dve.tensor_copy, 1, x)
                if n + 1 < NU:
                    scaled(n + 1)


def stage_nsa_samples(k):
    nc, ps = k.nc, k.ps
    HALF = NB // 2
    R = NH * NT
    ROW = STRIDE * GD
    NC = NSUB - 1
    SLC, SNEW, WINC, WNEW, CMP = 0, PAST, PAST + NS_TOK, PAST + NS_TOK + WIN, PAST + 2 * NS_TOK + WIN
    WA = WIN // P
    low = k.SPARE_OFF
    rel = k.at("slc_distance", low, [P, PAST])
    assert low + PAST * 4 <= k.HT_OFF
    off = k.KT_OFF
    score = k.at("sample_scores", off, [P, CMP + P])
    off += (CMP + P) * 4
    q_pad = k.at("sample_q_pad", off, [P, NB, R])
    off += NB * R * 4
    k_new = k.at("sample_k_newT", off, [P, 2, NS_TOK])
    off += 2 * NS_TOK * 4
    new_bias = k.at("new_bias", off, [P, 2, NS_TOK])
    off += 256
    same = k.at("same_token", off, [P, P])
    off += 512
    token_of = k.at("token_of_row", off, [NS_TOK, 2, P])
    off += 1024
    rel_c = k.at("cmp_distance", off, [P, P])
    off += 512
    assert off <= k.VA_OFF
    off = k.CMP_END
    NX = 4
    x = [k.at(f"sample_rows{i}", (k.AQ_OFF if i < 2 else off) + i % 2 * ROW * 4, [P, STRIDE, GD]) for i in range(NX)]
    off += 2 * ROW * 4
    kt = k.at("sample_kT", off, [P, PAST])
    off += PAST * 4
    ktw = k.at("sample_kwT", off, [P, WIN])
    off += WIN * 4
    xw = [k.at(f"window_rows{i}", off + i * 2048, [P, WA, GD]) for i in range(2)]
    off += 4096
    NTILE = STRIDE + WA + 3
    pt_off = off
    pt = k.at("sample_probsT", off, [P, NTILE, P])
    off += NTILE * P * 4
    rel_w = k.at("win_distance", off, [P, WIN])
    off += WIN * 4
    win_mask = k.at("win_mask", off, [P, WA])
    row_gates = k.at("row_gates", off + 32, [P, 2, 3])
    off += 64

    def col(name, n=1, dtype=F32):
        nonlocal off
        t = k.at(name, off, [P, n], dtype)
        off += (n * 4 + 31) // 32 * 32
        return t

    ids = col("row_id", 1, I32)
    ints = [col(f"row_int{i}", 1, I32) for i in range(3)]
    slope, t_of, b4_of, h_of = col("row_slope"), col("row_t"), col("row_b4"), col("row_h")
    head_hot = col("row_head", NH)
    a_iota, tmp = col("a_iota", WA), col("row_tmp", 32)
    tmp2 = col("row_tmp2", 32)
    picked = col("gates_picked", 3 * NH)
    tops, neg_tops, sums, factor = col("s_top", 3), col("s_neg_top", 3), col("s_sum", 3), col("s_factor", 3)
    padded = col("cmp_probs_padded", 4 * (NBLK + 1))
    part, imp, rank = col("block_part", NBLK), col("importance", NBLK), col("block_rank", NBLK)
    drop = col("block_drop", NBLK)
    before = k.at("block_before", off, [P, NBLK, NBLK])
    off += NBLK * NBLK * 4
    assert off <= k.TOP, (off, k.TOP)
    gt = k.at("block_gt", pt_off, [P, NBLK, NBLK])
    eq = k.at("block_eq", pt_off + (NBLK * NBLK * 4 + 31) // 32 * 32, [P, NBLK, NBLK])
    assert 2 * NBLK * NBLK * 4 + 64 <= NTILE * P * 4

    s_iota, s_setup, s_chain, s_chain_p = k.sem("s_iotas"), k.sem("s_setup"), k.sem("s_chain"), k.sem("s_chain_pool")
    s_x = [k.sem(f"sample_rows_loaded{i}") for i in range(NX)]
    s_xw = [k.sem(f"window_rows_loaded{i}") for i in range(2)]
    s_turn, s_scores, s_cmp_scores = k.sem("s_k_turned"), k.sem("s_scores_done"), k.sem("s_cmp_scores")
    s_ev = [k.sem("s_turn_evac_act"), k.sem("s_turn_evac_dve")]
    s_tables, s_q = k.sem("s_tables_ready"), k.sem("s_queries_ready")
    s_neg, s_exp, s_pb, s_imp = k.sem("s_neg_ready"), k.sem("s_exps"), k.sem("s_blocks_ready"), k.sem("s_importance")
    s_p, s_pv, s_out, s_slc_used = k.sem("s_probs_ready"), k.sem("s_pv_product"), k.sem("s_out_evac"), k.sem("s_x_used")
    s_xw_used = k.sem("s_xw_used")

    loads = [(h, kv, b) for h in range(2) for kv in range(2) for b in range(HALF)]
    KLOTS = (STRIDE + WA) // 4
    ptiles = ([(SLC + j * P, P) for j in range(STRIDE)] + [(WINC + a * P, P) for a in range(WA)]
              + [(SNEW, NS_TOK), (WNEW, NS_TOK), (CMP, NC)])
    PLOTS = (len(ptiles) + 3) // 4
    LOTS = HALF * KLOTS + PLOTS

    def evacs(which, x):
        return (x + 1 - which) // 2

    with nc.Block() as block:

        @block.sync
        def _(sp):
            for n, (h, kv, b) in enumerate(loads):
                if n >= 2:
                    h_, kv_, b_ = loads[n - 2]
                    sp.wait_ge(s_xw_used if kv_ else s_scores, HALF * h_ + b_ + 1)
                src = (k.state_k_win, k.state_v_win)[kv][0, HALF * h + b]
                sp.dma_start(xw[n % 2][:].rearrange("p a x -> p (a x)"),
                             src.rearrange("(p a) g d -> p (a g d)", a=WA)).then_inc(s_xw[n % 2], 16)

        @block.gpsimd
        def _(pool):
            link = Chain(pool, s_chain_p)

            def gather(n):
                h, kv, b = loads[n]
                if n >= NX:
                    pool.wait_ge(s_slc_used, n - NX + 1)
                cache = (k.cache_k_slc, k.cache_v_slc)[kv]
                pool.indirect_dma_start(
                    out=x[n % NX][:].rearrange("p j x -> p (j x)"), out_offset=None,
                    in_=cache[0].rearrange("q (s j) g d -> (q s) (j g d)", j=STRIDE),
                    in_offset=bass.IndirectOffsetOnAxis(ap=k.page_idx[:, HALF * h + b:HALF * h + b + 1], axis=0))\
                    .then_inc(s_x[n % NX], 16)

            io = dict(allow_small_or_imprecise_dtypes=True)
            pool.iota(ids[:], pattern=[[0, 1]], base=0, channel_multiplier=1).then_inc(s_iota, 1)
            pool.iota(a_iota[:], pattern=[[1, WA]], base=0, channel_multiplier=0, **io).then_inc(s_iota, 1)
            pool.iota(head_hot[:], pattern=[[1, NH]], base=0, channel_multiplier=0, **io).then_inc(s_iota, 1)
            pool.iota(new_bias[:], pattern=[[-4 * HALF, 2], [1, NS_TOK]], base=0, channel_multiplier=0, **io)\
                .then_inc(s_iota, 1)
            pool.memset(q_pad[:], 0.0).then_inc(s_iota, 1)
            pool.memset(padded[:], 0.0).then_inc(s_iota, 1)
            pool.iota(rel_c[:], pattern=[[STRIDE, P]], base=CBLK - 1 - PAST, channel_multiplier=0, **io)
            pool.iota(rel_w[:], pattern=[[1, WA], [WA, P]], base=-WIN, channel_multiplier=0, **io)
            pool.iota(rel[:], pattern=[[1, STRIDE], [STRIDE, NSUB]], base=-PAST, channel_multiplier=0, **io)
            pool.memset(same[:], 0.0)
            pool.memset(token_of[:], 0.0)
            link(pool.memset(before[:], 0.0))
            pool.wait_ge(s_q, 1)
            gather(0)
            gather(1)
            for i in range(HG):
                v = same[:].rearrange("p (b i t) -> p b i t", i=HG, t=NT)
                link(pool.affine_select(out=v, in_=v, compare_op=ALU.not_equal, fill=1.0, base=-NT * i,
                                        pattern=[[-NT * HG, P // (NT * HG)], [0, HG], [-1, NT]], channel_multiplier=1))
            for h in range(2):
                v = token_of[:, h, :].rearrange("p (b h t) -> p b h t", b=HALF, t=NT)
                link(pool.affine_select(out=v, in_=v, compare_op=ALU.not_equal, fill=1.0, base=-NT * HALF * h,
                                        pattern=[[-NT, HALF], [0, NH], [-1, NT]], channel_multiplier=1))
            pool.affine_select(out=before[:], in_=before[:], compare_op=ALU.is_ge, fill=1.0, base=0,
                               pattern=[[-1, NBLK], [1, NBLK]], channel_multiplier=0).then_inc(s_tables, 1)
            for n in range(2, len(loads)):
                gather(n)

        @block.tensor
        def _(pe):
            lot = [0]

            def turn(tiles):
                x_ = lot[0]
                if x_ >= 2:
                    pe.wait_ge(s_ev[x_ % 2], evacs(x_ % 2, x_))
                for c, (src, rows, m) in enumerate(tiles):
                    mm = pe.transpose(ps[0:m, 6 + x_ % 2, c * P:c * P + rows], src, k.ident[0:rows, 0:rows])
                mm.then_inc(s_turn, 1)
                lot[0] += 1

            def evacuated(x_):
                pe.wait_ge(s_ev[x_ % 2], evacs(x_ % 2, x_) + 1)

            pe.wait_ge(s_setup, 1)
            pe.wait_ge(s_tables, 1)
            for h in range(2):
                for b in range(HALF):
                    bb = HALF * h + b
                    rows = slice(R * b, R * (b + 1))
                    n = 2 * HALF * h + b
                    if b == 0 and h:
                        pe.wait_ge(s_out, h)
                    if b == 0:
                        for q in range(HALF):
                            mm = pe.matmul(ps[R * q:R * (q + 1), 5, 2 * NS_TOK:2 * NS_TOK + NC], q_pad[:, bb + q, :],
                                           k.kc_t[:, bb + q, 0:NC], start=True, stop=True)
                        mm.then_inc(s_cmp_scores, 1)
                        mm = pe.matmul(ps[:, 5, 256:256 + 3 * NH], token_of[:, h, :],
                                       k.gates[0:NS_TOK, QT].rearrange("p h b -> p (h b)"), start=True, stop=True)
                        mm.then_inc(s_cmp_scores, 1)
                    pe.wait_ge(s_x[n % NX], 16 * (n // NX + 1))
                    x0 = lot[0]
                    for j in range(0, STRIDE, 4):
                        turn([(x[n % NX][:, j + c, :], P, P) for c in range(4)])
                    pe.wait_ge(s_xw[n % 2], 16 * (n // 2 + 1))
                    turn([(xw[n % 2][:, a, :], P, P) for a in range(WA)])
                    for c in range(PAST // 512):
                        evacuated(x0 + c)
                        mm = pe.matmul(ps[rows, c, :], q_pad[:, bb, :], kt[:, c * 512:(c + 1) * 512],
                                       start=True, stop=True)
                    mm.then_inc(s_slc_used, 1)
                    evacuated(x0 + KLOTS - 1)
                    pe.matmul(ps[rows, 4, :], q_pad[:, bb, :], ktw[:], start=True, stop=True)
                    for which in range(2):
                        mm = pe.matmul(ps[rows, 5, which * NS_TOK:(which + 1) * NS_TOK], q_pad[:, bb, :],
                                       k_new[:, which, :], start=True, stop=True)
                    mm.then_inc(s_scores, 1)
                pe.wait_ge(s_pb, h + 1)
                pe.matmul(ps[:, 5, 320:320 + NBLK], same[:], part[:], start=True, stop=True).then_inc(s_imp, 1)
                pe.wait_ge(s_p, h + 1)
                for a in range(0, len(ptiles), 4):
                    turn([(score[:, c:c + m], P, m) for c, m in ptiles[a:a + 4]])
                evacuated(lot[0] - 2)
                evacuated(lot[0] - 1)
                for b in range(HALF):
                    n = 2 * HALF * h + HALF + b
                    out = ps[:, 4, R * b:R * (b + 1)]
                    cols = slice(R * b, R * (b + 1))
                    pe.wait_ge(s_x[n % NX], 16 * (n // NX + 1))
                    for j in range(STRIDE):
                        mm = pe.matmul(out, x[n % NX][:, j, :], pt[:, j, cols], start=(j == 0), stop=False)
                    mm.then_inc(s_slc_used, 1)
                    pe.wait_ge(s_xw[n % 2], 16 * (n // 2 + 1))
                    for a in range(WA):
                        mm = pe.matmul(out, xw[n % 2][:, a, :], pt[:, STRIDE + a, cols], start=False, stop=False)
                    mm.then_inc(s_xw_used, 1)
                    t0 = STRIDE + WA
                    pe.matmul(out, k.rows[0:NS_TOK, QT, R_VS:R_VS + GD], pt[0:NS_TOK, t0, cols], start=False, stop=False)
                    pe.matmul(out, k.rows[0:NS_TOK, QT, R_VW:R_VW + GD], pt[0:NS_TOK, t0 + 1, cols], start=False,
                              stop=False)
                    mm = pe.matmul(out, k.vc[0:NC, HALF * h + b, :], pt[0:NC, t0 + 2, cols], start=False, stop=True)
                mm.then_inc(s_pv, 1)

        def evacuate(eng, copy, which, h, n):
            x_ = LOTS * h + n
            if x_ % 2 != which:
                return
            eng.wait_ge(s_turn, x_ + 1)
            src = ps[:, 6 + x_ % 2, :]
            if n < HALF * KLOTS:
                b, c = n // KLOTS, n % KLOTS
                done = HALF * h + b
                if done:
                    eng.wait_ge(s_scores, done)
                dst = kt[:, c * 512:(c + 1) * 512] if c < KLOTS - 1 else ktw[:]
                copy(dst, src).then_inc(s_ev[which], 1)
                return
            a = 4 * (n - HALF * KLOTS)
            if h:
                eng.wait_ge(s_pv, h)
            if a + 4 <= STRIDE + WA:
                copy(pt[:, a:a + 4, :].rearrange("p c q -> p (c q)"), src).then_inc(s_ev[which], 1)
                return
            for c, (_, m) in enumerate(ptiles[a:a + 4]):
                ins = copy(pt[0:m, a + c, :], ps[0:m, 6 + x_ % 2, c * P:(c + 1) * P])
            ins.then_inc(s_ev[which], 1)

        @block.scalar
        def _(act):
            for h in range(2):
                act.wait_ge(s_neg, 2 * h + 1)
                act.activation(score[:, CMP:CMP + NC], score[:, CMP:CMP + NC], ACT.Exp, bias=neg_tops[:, 2:3],
                               accum_out=sums[:, 2:3]).then_inc(s_exp, 1)
                for n in range(HALF * KLOTS):
                    evacuate(act, act.copy, 0, h, n)
                act.wait_ge(s_neg, 2 * h + 2)
                act.activation(score[:, SLC:SNEW + NS_TOK], score[:, SLC:SNEW + NS_TOK], ACT.Exp,
                               bias=neg_tops[:, 0:1], accum_out=sums[:, 0:1])
                act.activation(score[:, WINC:WNEW + NS_TOK], score[:, WINC:WNEW + NS_TOK], ACT.Exp,
                               bias=neg_tops[:, 1:2], accum_out=sums[:, 1:2]).then_inc(s_exp, 1)
                for n in range(HALF * KLOTS, LOTS):
                    evacuate(act, act.copy, 0, h, n)

        @block.vector
        def _(dve):
            link = Chain(dve, s_chain)
            dve.wait_ge(s_iota, 6)
            for g in range(NG):
                rows = slice(g * HD, (g + 1) * HD)
                for i in range(HG):
                    dve.tensor_copy(q_pad[rows, :, (HG * g + i) * NT:(HG * g + i + 1) * NT],
                                    k.aq[rows, i, SEQ:TOK].rearrange("p (b t) -> p b t", b=NB))
                for which in range(2):
                    ins = dve.tensor_copy(k_new[rows, which, :], k.kT_last[rows, 2 * which + g, :])
            ins.then_inc(s_q, 1)
            link(dve.tensor_single_scalar(ints[0][:], ids[:], 3, ALU.bitwise_and))
            link(dve.tensor_copy(t_of[:], ints[0][:]))
            link(dve.tensor_single_scalar(ints[0][:], ids[:], 5, ALU.arith_shift_right))
            link(dve.tensor_scalar(b4_of[:], ints[0][:], 4.0, None, ALU.mult))
            link(dve.tensor_single_scalar(ints[1][:], ids[:], 2, ALU.arith_shift_right))
            link(dve.tensor_single_scalar(ints[1][:], ints[1][:], 7, ALU.bitwise_and))
            link(dve.tensor_copy(h_of[:], ints[1][:]))
            link(dve.tensor_scalar(ints[2][:], ints[1][:], -1.0, 126.0, ALU.mult, ALU.add))
            link(dve.tensor_single_scalar(slope[:].bitcast(I32), ints[2][:], 23, ALU.logical_shift_left))
            link(dve.tensor_scalar(head_hot[:], head_hot[:], h_of[:], None, ALU.is_equal))
            link(dve.tensor_scalar(win_mask[:], a_iota[:], t_of[:], NEG, ALU.is_lt, ALU.mult))
            for h in range(2):
                v = new_bias[:, h, :]
                link(dve.tensor_scalar(v, v, b4_of[:], None, ALU.subtract))
                link(dve.tensor_scalar(tmp[:], v, 0.0, None, ALU.is_ge))
                link(dve.tensor_scalar(tmp2[:], v, t_of[:], None, ALU.is_le))
                link(dve.tensor_tensor(tmp[:], tmp[:], tmp2[:], ALU.mult))
                link(dve.tensor_scalar(tmp2[:], v, slope[:], None, ALU.mult))
                link(dve.tensor_tensor(tmp2[:], tmp2[:], tmp[:], ALU.mult))
                link(dve.tensor_scalar(tmp[:], tmp[:], -1.0, BIG, ALU.add, ALU.mult))
                ins = dve.tensor_tensor(v, tmp[:], tmp2[:], ALU.add)
                if h == 0:
                    link(ins)
            ins.then_inc(s_setup, 1)
            dve.wait_ge(s_tables, 1)
            for h in range(2):
                dve.wait_ge(s_cmp_scores, 2 * h + 2)
                s_c = score[:, CMP:CMP + NC]
                link(dve.scalar_tensor_tensor(s_c, rel_c[:, 0:NC], slope[:], ps[:, 5, 64:64 + NC], ALU.mult, ALU.add))
                link(dve.tensor_reduce(tops[:, 2:3], s_c, AX.X, ALU.max))
                dve.tensor_scalar(neg_tops[:, 2:3], tops[:, 2:3], -1.0, None, ALU.mult).then_inc(s_neg, 1)
                picked_v = picked[:].rearrange("p (h b) -> p h b", h=NH)
                link(dve.tensor_tensor(picked_v, ps[:, 5, 256:256 + 3 * NH].rearrange("p (h b) -> p h b", h=NH),
                                       head_hot[:].unsqueeze(2).to_broadcast([P, NH, 3]), ALU.mult))
                link(dve.tensor_reduce(row_gates[:, h, :], picked[:].rearrange("p (h b) -> p b h", h=NH), AX.X, ALU.add))
                dve.wait_ge(s_exp, 2 * h + 1)
                link(dve.reciprocal(factor[:, 2:3], sums[:, 2:3]))
                link(dve.tensor_scalar(padded[:, 1:1 + NC], s_c, factor[:, 2:3], None, ALU.mult))
                link(dve.tensor_scalar(s_c, padded[:, 1:1 + NC], row_gates[:, h, 2:3], None, ALU.mult))
                link(dve.tensor_reduce(part[:], padded[:, 0:4 * NBLK].rearrange("p (j x) -> p j x", x=4), AX.X, ALU.add))
                dve.tensor_tensor(part[:].unsqueeze(2), part[:].unsqueeze(2),
                                  padded[:, 4:4 * NBLK + 4].rearrange("p (j x) -> p j x", x=4)[:, :, 0:1], ALU.add)\
                   .then_inc(s_pb, 1)
                for n in range(HALF * KLOTS):
                    evacuate(dve, dve.tensor_copy, 1, h, n)
                dve.wait_ge(s_imp, h + 1)
                link(dve.tensor_copy(imp[:], ps[:, 5, 320:320 + NBLK]))
                link(dve.memset(imp[:, 0:1], BIG))
                link(dve.memset(imp[:, NBLK - 2:NBLK], BIG))
                other = imp[:].unsqueeze(1).to_broadcast([P, NBLK, NBLK])
                own = imp[:].unsqueeze(2).to_broadcast([P, NBLK, NBLK])
                dve.tensor_tensor(gt[:], other, own, ALU.is_gt)
                link(dve.tensor_tensor(eq[:], other, own, ALU.is_equal))
                link(dve.tensor_tensor(eq[:], eq[:], before[:], ALU.mult))
                link(dve.tensor_tensor(gt[:], gt[:], eq[:], ALU.add))
                link(dve.tensor_reduce(rank[:], gt[:], AX.X, ALU.add))
                link(dve.tensor_scalar(drop[:], rank[:], float(NSEL) - 0.5, NEG, ALU.is_ge, ALU.mult))
                dve.wait_ge(s_scores, HALF * (h + 1))
                for c in range(PAST // 512):
                    cs = slice(c * 512, (c + 1) * 512)
                    ins = dve.scalar_tensor_tensor(score[:, cs], rel[:, cs], slope[:], ps[:, c, :], ALU.mult, ALU.add)
                dve.tensor_tensor(score[:, SNEW:SNEW + NS_TOK], ps[:, 5, 0:NS_TOK], new_bias[:, h, :], ALU.add)
                dve.scalar_tensor_tensor(score[:, WINC:WNEW], rel_w[:], slope[:], ps[:, 4, :], ALU.mult, ALU.add)
                link(dve.tensor_tensor(score[:, WNEW:WNEW + NS_TOK], ps[:, 5, NS_TOK:2 * NS_TOK], new_bias[:, h, :],
                                       ALU.add))
                by_block = score[:, SLC:SNEW].rearrange("p (j b r) -> p j b r", j=STRIDE, r=SBLK // STRIDE)
                dropped = drop[:, 0:NBLK - 1].unsqueeze(1).unsqueeze(3).to_broadcast(
                    [P, STRIDE, NBLK - 1, SBLK // STRIDE])
                dve.tensor_tensor(by_block, by_block, dropped, ALU.add)
                first = score[:, WINC:WNEW].rearrange("p (a n) -> p a n", a=WA)[:, :, 0]
                link(dve.tensor_tensor(first, first, win_mask[:], ALU.add))
                dve.tensor_reduce(tops[:, 0:1], score[:, SLC:SNEW + NS_TOK], AX.X, ALU.max)
                link(dve.tensor_reduce(tops[:, 1:2], score[:, WINC:WNEW + NS_TOK], AX.X, ALU.max))
                dve.tensor_scalar(neg_tops[:, 0:2], tops[:, 0:2], -1.0, None, ALU.mult).then_inc(s_neg, 1)
                dve.wait_ge(s_exp, 2 * h + 2)
                link(dve.reciprocal(factor[:, 0:2], sums[:, 0:2]))
                link(dve.tensor_tensor(factor[:, 0:2], factor[:, 0:2], row_gates[:, h, 0:2], ALU.mult))
                dve.tensor_scalar(score[:, SLC:SNEW + NS_TOK], score[:, SLC:SNEW + NS_TOK], factor[:, 0:1], None, ALU.mult)
                dve.tensor_scalar(score[:, WINC:WNEW + NS_TOK], score[:, WINC:WNEW + NS_TOK], factor[:, 1:2], None,
                                  ALU.mult).then_inc(s_p, 1)
                for n in range(HALF * KLOTS, LOTS):
                    evacuate(dve, dve.tensor_copy, 1, h, n)
                dve.wait_ge(s_pv, h + 1)
                for g in range(NG):
                    rows = slice(g * HD, (g + 1) * HD)
                    src = ps[rows, 4, 0:R * HALF].rearrange("p (b g i t) -> p b g i t", b=HALF, g=NG, i=HG)[:, :, g]
                    t0 = SEQ + h * HALF * NT
                    dst = k.bT[rows, :, t0:t0 + HALF * NT].rearrange("p i (b t) -> p b i t", b=HALF)
                    ins = dve.tensor_copy(dst, src)
                ins.then_inc(s_out, 1)



def split_product(pe, out, w_h, w_l, kt, x_h, x_l, kd, pieces, first, last):
    for n, (w, x) in enumerate(((w_l, x_h), (w_h, x_l), (w_h, x_h))):
        for bank, cols in pieces:
            mm = pe.matmul(out[:, bank, 0:cols.stop - cols.start], w[:, kt, :], x[:, kd, cols],
                           start=(first and n == 0), stop=(last and n == 2))
    return mm


def stage_merge(k):
    nc, ps = k.nc, k.ps
    KB = 4
    NRAW, NSPLIT, LEAD = 5, 3, 2
    act_bytes = HG * TOK * 4
    hT_l, hT_h = k.at("hT_l", k.HT_OFF, [P, KD, TOK], F32R), k.at("hT_h", k.ROWS_OFF, [P, KD, TOK], F32R)
    b_l, b_h = k.at("bT_l", k.VA_OFF, [P, HG, TOK], F32R), k.at("bT_h", k.AQ_OFF, [P, HG, TOK], F32R)
    a_l, a_h = k.at("aT_l", k.AT_OFF, [P, MH, TOK], F32R), k.at("aT_h", k.QK_OFF, [P, MH, TOK], F32R)
    off = k.QK_OFF + act_bytes
    y, y_l = k.at("merged_yT", off, [P, KD, TOK]), k.at("y_l", off, [P, KD, TOK], F32R)
    y_h = k.at("y_h", k.ROWS_OFF, [P, KD, TOK], F32R)
    off += KD * TOK * 4
    w_h = [k.at(f"merge_w_h{i}", off + 2 * i * KB * 512, [P, KB, P], F32R) for i in range(NSPLIT)]
    w_l = [k.at(f"merge_w_l{i}", off + (2 * i + 1) * KB * 512, [P, KB, P], F32R) for i in range(NSPLIT)]
    off += 2 * NSPLIT * KB * 512
    assert off <= k.TOP
    off = k.ROWS_OFF + KD * TOK * 4
    raw = [k.at(f"merge_raw{i}", off + i * KB * 512, [P, KB, P]) for i in range(NRAW)]
    assert off + NRAW * KB * 512 <= k.VA_OFF
    off = k.SPARE2_OFF
    sig = [k.at(f"merge_sigmoid{i}", off + i * TOK * 4, [P, NCH, CH]) for i in range(2)]
    tmp = k.at("merge_product", off + 2 * TOK * 4, [P, NCH, CH])
    assert off + 3 * TOK * 4 <= k.HT_OFF
    off = k.VA_OFF
    x_rows = k.at("x_rows", off, [P, TT, DM])
    off += TT * DM * 4
    ss = k.at("x1_square_sums", off, [P, TOK])
    square = [k.at(f"x1_square{i}", off + (1 + i) * TOK * 4, [P, TOK]) for i in range(2)]
    assert off + 3 * TOK * 4 <= k.QK_OFF + act_bytes
    XG = 4

    blocks = []
    for f in range(KD):
        blocks += [("gate_a", 0, f), ("gate_a", KB, f), ("a", 0, f), ("gate_b", 0, f), ("gate_b", KB, f), ("b", 0, f)]
    NM = len(blocks)
    for f in range(KD):
        blocks += [("o", 0, f), ("o", KB, f)]
    NBK = len(blocks)
    ends = [src in "ab" or kt0 == KB for src, kt0, _ in blocks]
    product = [sum(ends[:n]) for n in range(NBK)]
    n_dma, full_at = [0] * NRAW, []
    for n, (src, _, _) in enumerate(blocks):
        n_dma[n % NRAW] += NG if src == "b" else 1
        full_at.append(16 * n_dma[n % NRAW])

    s_raw = [k.sem(f"merge_raw_full{i}") for i in range(NRAW)]
    s_h, s_l, s_used = k.sem("w_h_ready"), k.sem("w_l_ready"), k.sem("w_block_used")
    s_xh, s_xl = k.sem("operand_h_ready"), k.sem("operand_l_ready")
    s_sig, s_mul, s_y = k.sem("merge_sigmoids"), k.sem("merge_products"), k.sem("y_ready")
    s_x = [k.sem(f"x_cols_loaded{i}") for i in range(XG)]
    s_xt, s_xt_copied, s_x1 = k.sem("x_turned"), k.sem("xT_copied"), k.sem("x1_ready")
    s_sq, s_ss, s_tot, s_rs = k.sem("x1_squared"), k.sem("x1_summed"), k.sem("x1_totals"), k.sem("x1_rstd_ready")
    LAST_GATE = NM - 1

    def chunk(c):
        return slice(c * CH, (c + 1) * CH)

    def banks(p):
        return ps[:, 3 * (p % 2):3 * (p % 2) + NCH, 0:CH]

    def flat(t):
        return t[:].rearrange("p c n -> p (c n)")

    with nc.Block() as block:

        @block.sync
        def _(sp):
            w_in = k.w_in[0].rearrange("(k p) n -> p k n", p=P)
            w_a, w_o = (w[0].rearrange("(k p) n -> p k n", p=P) for w in (k.w_a, k.w_o))
            w_b = k.w_b[0].rearrange("(g i d) n -> g d i n", g=NG, i=HG)
            for n, (src, kt, f) in enumerate(blocks):
                if n >= NRAW:
                    sp.wait_ge(s_l, n - NRAW + 1)
                slot, full = raw[n % NRAW], s_raw[n % NRAW]
                cols = slice(f * P, (f + 1) * P)
                if src == "b":
                    for g in range(NG):
                        sp.dma_start(slot[g * HD:(g + 1) * HD], w_b[g, :, :, cols]).then_inc(full, 16)
                elif src == "a":
                    sp.dma_start(slot[:], w_a[:, :, cols]).then_inc(full, 16)
                elif src == "o":
                    sp.dma_start(slot[:], w_o[:, kt:kt + KB, cols]).then_inc(full, 16)
                else:
                    c = C_MRG + (src == "gate_b") * DM + f * P
                    sp.dma_start(slot[:], w_in[:, kt:kt + KB, c:c + P]).then_inc(full, 16)

        @block.gpsimd
        def _(pool):
            for f in range(KD):
                pool.wait_ge(s_mul, 2 * (f + 1))
                pool.tensor_tensor(y[:, f, :], y[:, f, :], flat(tmp), ALU.add).then_inc(s_y, 1)
            pool.wait_ge(s_used, NM)
            xp = k.x_prompt[0].rearrange("(t p) d -> p t d", p=P)
            for i in range(XG):
                cols = slice(i * DM // XG, (i + 1) * DM // XG)
                pool.dma_start(x_rows[:, 0:QT, cols], xp[:, :, cols]).then_inc(s_x[i], 16)
                pool.dma_start(x_rows[0:NS_TOK, QT, cols], k.x_sample.rearrange("b t d -> (b t) d")[:, cols])\
                    .then_inc(s_x[i], 16)
            for f in range(1, KD):
                pool.wait_ge(s_sq, f + 1)
                if f > 1:
                    pool.wait_ge(s_ss, f - 1)
                pool.tensor_tensor(ss[:], ss[:], square[f % 2][:], ALU.add).then_inc(s_ss, 1)

        @block.scalar
        def _(act):
            def split(n):
                if n >= NBK:
                    return
                act.wait_ge(s_raw[n % NRAW], full_at[n])
                if n >= NSPLIT:
                    act.wait_ge(s_used, n - NSPLIT + 1)
                act.copy(w_h[n % NSPLIT][:], raw[n % NRAW][:]).then_inc(s_h, 1)

            for n in range(LEAD):
                split(n)
            for src, dst, count in ((k.hT, hT_h, KD), (k.aT, a_h, MH)):
                for kd in range(count):
                    act.copy(dst[:, kd, :], src[:, kd, :]).then_inc(s_xh, 1)
            for n, (src, _, f) in enumerate(blocks[:NM]):
                split(n + LEAD)
                if n == 0:
                    for kd in range(HG):
                        act.copy(b_h[:, kd, :], k.bT[:, kd, :]).then_inc(s_xh, 1)
                if src.startswith("gate") and ends[n]:
                    part = int(src == "gate_b")
                    act.wait_ge(s_used, n + 1)
                    if f:
                        act.wait_ge(s_mul, 2 * f - 1 + part)
                    col = k.c_b_mrg + part * KD + f
                    act.activation(sig[part][:], banks(product[n]), ACT.Sigmoid,
                                   bias=k.cols[:, col:col + 1]).then_inc(s_sig, 1)
            act.wait_ge(s_used, LAST_GATE)
            for kd in range(KD):
                act.wait_ge(s_y, kd + 1)
                act.copy(y_h[:, kd, :], y[:, kd, :]).then_inc(s_xh, 1)

            def square_tile(f):
                act.wait_ge(s_x1, f + 1)
                if f >= 3:
                    act.wait_ge(s_ss, f - 2)
                act.activation(square[f % 2][:] if f else ss[:], k.x1[:, f, :], ACT.Square).then_inc(s_sq, 1)

            for f in range(KD):
                for j, (a, m) in enumerate(TOKEN_CHUNKS):
                    act.wait_ge(s_xt, 3 * f + j + 1)
                    act.copy(k.x1[:, f, a:a + m], ps[:, 6 + (3 * f + j) % 2, 0:m]).then_inc(s_xt_copied, 1)
                split(NM + 2 * f + LEAD)
                if f:
                    square_tile(f - 1)
                split(NM + 2 * f + 1 + LEAD)
            square_tile(KD - 1)
            act.wait_ge(s_rs, 1)
            act.activation(k.rs[:], k.rs[:], ACT.Sqrt).then_inc(s_rs, 1)

        @block.vector
        def _(dve):
            def split(n):
                if n >= NBK:
                    return
                dve.wait_ge(s_h, n + 1)
                dve.tensor_tensor(w_l[n % NSPLIT][:], raw[n % NRAW][:], w_h[n % NSPLIT][:].bitcast(F32), ALU.subtract)\
                   .then_inc(s_l, 1)

            def split_operand(src, h, l, kd, n):
                dve.wait_ge(s_xh, n + 1)
                dve.tensor_tensor(l[:, kd, :], src[:, kd, :], h[:, kd, :].bitcast(F32), ALU.subtract).then_inc(s_xl, 1)

            for n in range(LEAD):
                split(n)
            for kd in range(KD):
                split_operand(k.hT, hT_h, hT_l, kd, kd)
            for kd in range(MH):
                split_operand(k.aT, a_h, a_l, kd, KD + kd)
            for n, (src, _, f) in enumerate(blocks[:NM]):
                split(n + LEAD)
                if n == 0:
                    for kd in range(HG):
                        split_operand(k.bT, b_h, b_l, kd, KD + MH + kd)
                if src in "ab":
                    part = int(src == "b")
                    dve.wait_ge(s_sig, 2 * f + part + 1)
                    dve.wait_ge(s_used, n + 1)
                    if part == 0:
                        dst = y[:, f, :].rearrange("p (c n) -> p c n", c=NCH)
                    else:
                        if f:
                            dve.wait_ge(s_y, f)
                        dst = tmp[:]
                    dve.tensor_tensor(dst, sig[part][:], banks(product[n]), ALU.mult).then_inc(s_mul, 1)
            for kd in range(KD):
                split_operand(y, y_h, y_l, kd, KD + MH + HG + kd)
            for f in range(KD):
                n = NM + 2 * f
                split(n + LEAD)
                split(n + 1 + LEAD)
                dve.wait_ge(s_used, n + 2)
                dve.wait_ge(s_xt_copied, 3 * (f + 1))
                x1 = k.x1[:, f, :].rearrange("p (c n) -> p c n", c=NCH)
                dve.tensor_tensor(x1, x1, banks(product[n]), ALU.add).then_inc(s_x1, 1)
            for c in range(NCH):
                dve.wait_ge(s_tot, c + 1)
                ins = dve.tensor_scalar(k.rs[:, chunk(c)], ps[:, c, 0:CH], 1.0 / DM, EPS, ALU.mult, ALU.add)
            ins.then_inc(s_rs, 1)
            dve.wait_ge(s_rs, 2)
            dve.reciprocal(k.rs[:], k.rs[:])

        @block.tensor
        def _(pe):
            pieces = [(c, chunk(c)) for c in range(NCH)]
            operand = {"gate_a": (hT_h, hT_l, 0), "gate_b": (hT_h, hT_l, 0), "a": (a_h, a_l, KD),
                       "b": (b_h, b_l, KD + MH), "o": (y_h, y_l, KD + MH + HG)}
            for n, (src, kt0, f) in enumerate(blocks):
                p = product[n]
                if kt0 == 0:
                    if src.startswith("gate") and p:
                        pe.wait_ge(s_sig, 2 * f + int(src == "gate_b"))
                    elif src in "ab" and p > 1:
                        pe.wait_ge(s_mul, 2 * f + int(src == "b"))
                    elif src == "o" and f < 2:
                        pe.wait_ge(s_sig, 2 * KD)
                        pe.wait_ge(s_mul, 2 * KD)
                    elif src == "o":
                        pe.wait_ge(s_x1, f - 1)
                h, l, base = operand[src]
                pe.wait_ge(s_l, n + 1)
                for kt in range(KB):
                    if f == 0:
                        pe.wait_ge(s_xl, base + kt0 + kt + 1)
                    mm = split_product(pe, banks(p), w_h[n % NSPLIT], w_l[n % NSPLIT], kt, h, l, kt0 + kt, pieces,
                                       kt0 + kt == 0, ends[n] and kt == KB - 1)
                mm.then_inc(s_used, 1)
                if src == "o" and kt0 == 0:
                    if f % (KD // XG) == 0:
                        pe.wait_ge(s_x[f // (KD // XG)], 32)
                    for j, (a, m) in enumerate(TOKEN_CHUNKS):
                        if 3 * f + j >= 2:
                            pe.wait_ge(s_xt_copied, 3 * f + j - 1)
                        for t in range(0, m, P):
                            r = min(P, m - t)
                            mm = pe.transpose(ps[:, 6 + (3 * f + j) % 2, t:t + r],
                                              x_rows[0:r, (a + t) // P, f * P:(f + 1) * P], k.ident[0:r, 0:r])
                        mm.then_inc(s_xt, 1)
            pe.wait_ge(s_x1, KD)
            pe.wait_ge(s_ss, KD - 1)
            for c in range(NCH):
                pe.matmul(ps[:, c, 0:CH], k.ones[:], ss[:, chunk(c)], start=True, stop=True).then_inc(s_tot, 1)


def stage_ffn(k):
    nc, ps = k.nc, k.ps
    HT = TOK // 2
    HC = HT // 2
    KB = KD
    NRAW, NSPLIT, LEAD = 3, 3, 2
    off = k.ROWS_OFF
    h2_h, h2_l = (k.at(f"h2_{s}", off + i * KD * HT * 4, [P, KD, HT], F32R) for i, s in enumerate("hl"))
    off += 2 * KD * HT * 4
    act_h, act_l = (k.at(f"act_{s}", off + i * FT * HT * 4, [P, FT, HT], F32R) for i, s in enumerate("hl"))
    off += 2 * FT * HT * 4
    raw = [k.at(f"ffn_raw{i}", off + i * KB * 512, [P, KB, P]) for i in range(NRAW)]
    off += NRAW * KB * 512
    w_h = [k.at(f"ffn_w_h{i}", off + 2 * i * KB * 512, [P, KB, P], F32R) for i in range(NSPLIT)]
    w_l = [k.at(f"ffn_w_l{i}", off + (2 * i + 1) * KB * 512, [P, KB, P], F32R) for i in range(NSPLIT)]
    off += 2 * NSPLIT * KB * 512
    assert off <= k.TOP
    off = k.SPARE2_OFF + TOK * 4
    gu = [k.at(f"ffn_act{i}", off + i * HT * 4, [P, HT]) for i in range(2)]
    off += 2 * HT * 4
    h2 = [k.at(f"h2_tile{i}", off + i * HT * 4, [P, HT]) for i in range(2)]
    off += 2 * HT * 4
    assert off <= k.HT_OFF

    half = []
    for f in range(FT):
        half += [("gate", 0, KD, f), ("up", 0, KD, f)]
    NGU = len(half)
    for f in range(KD):
        half += [("down", kt, min(KB, FT - kt), f) for kt in range(0, FT, KB)]
    NH_ = len(half)
    blocks = [(hf,) + b for hf in range(2) for b in half]
    NBK = len(blocks)
    s_raw = [k.sem(f"ffn_raw_full{i}") for i in range(NRAW)]
    s_h, s_l, s_used = k.sem("ffn_w_h_ready"), k.sem("ffn_w_l_ready"), k.sem("ffn_block_used")
    s_t2, s_h2h, s_h2 = k.sem("h2_tile_ready"), k.sem("h2_h_ready"), k.sem("h2_ready")
    s_silu, s_mul, s_ah, s_al, s_x2 = (k.sem("silu_done"), k.sem("act_multiplied"), k.sem("act_h_ready"),
                                       k.sem("act_l_ready"), k.sem("x2_ready"))

    def pair(bank):
        return ps[:, bank:bank + 2, 0:HC]

    def two(t):
        return t.rearrange("p (c n) -> p c n", c=2)

    def down_bank(f):
        return 2 * (f % 4)

    with nc.Block() as block:

        @block.sync
        def _(sp):
            w_gu = k.w_ffn_in[0].rearrange("(k p) n -> p k n", p=P)
            w_down = k.w_ffn_out[0].rearrange("(k p) n -> p k n", p=P)
            for n, (hf, src, kt, m, f) in enumerate(blocks):
                if n >= NRAW:
                    sp.wait_ge(s_l, n - NRAW + 1)
                if src == "down":
                    w = w_down[:, kt:kt + m, f * P:(f + 1) * P]
                else:
                    c = (src == "up") * DFF + f * P
                    w = w_gu[:, :, c:c + P]
                sp.dma_start(raw[n % NRAW][:, 0:m, :], w).then_inc(s_raw[n % NRAW], 16)

        @block.gpsimd
        def _(pool):
            for hf in range(2):
                for kd in range(KD):
                    u = KD * hf + kd
                    pool.wait_ge(s_h2h, u + 1)
                    pool.tensor_tensor(h2_l[:, kd, :], h2[u % 2][:], h2_h[:, kd, :].bitcast(F32), ALU.subtract)\
                        .then_inc(s_h2, 1)
                for f in range(FT):
                    u = FT * hf + f
                    pool.wait_ge(s_ah, u + 1)
                    pool.tensor_tensor(act_l[:, f, :], gu[u % 2][:], act_h[:, f, :].bitcast(F32), ALU.subtract)\
                        .then_inc(s_al, 1)

        @block.scalar
        def _(act):
            def split(n):
                if n >= NBK:
                    return
                m = blocks[n][3]
                act.wait_ge(s_raw[n % NRAW], 16 * (n // NRAW + 1))
                if n >= NSPLIT:
                    act.wait_ge(s_used, n - NSPLIT + 1)
                act.copy(w_h[n % NSPLIT][:, 0:m, :], raw[n % NRAW][:, 0:m, :]).then_inc(s_h, 1)

            def h2_tile(u):
                act.wait_ge(s_t2, u + 1)
                act.copy(h2_h[:, u % KD, :], h2[u % 2][:]).then_inc(s_h2h, 1)

            def act_high(u):
                act.wait_ge(s_mul, u + 1)
                act.copy(act_h[:, u % FT, :], gu[u % 2][:]).then_inc(s_ah, 1)

            for n in range(LEAD):
                split(n)
            for kd in range(KD):
                h2_tile(kd)
            for n, (hf, src, kt, m, f) in enumerate(blocks):
                split(n + LEAD)
                u = FT * hf + f
                if src == "gate":
                    if f:
                        act_high(u - 1)
                    act.wait_ge(s_used, n + 1)
                    if u >= 2:
                        act.wait_ge(s_al, u - 1)
                    act.activation(two(gu[u % 2][:]), pair(4 * (f % 2)), ACT.Silu).then_inc(s_silu, 1)
                elif src == "down" and kt == 0:
                    if f == 0:
                        act_high(FT * hf + FT - 1)
                    if hf == 0:
                        h2_tile(KD + f)

        @block.vector
        def _(dve):
            def split(n):
                if n >= NBK:
                    return
                m = blocks[n][3]
                dve.wait_ge(s_h, n + 1)
                dve.tensor_tensor(w_l[n % NSPLIT][:, 0:m, :], raw[n % NRAW][:, 0:m, :],
                                  w_h[n % NSPLIT][:, 0:m, :].bitcast(F32), ALU.subtract).then_inc(s_l, 1)

            def h2_tile(hf, kd):
                u = KD * hf + kd
                if u >= 2:
                    dve.wait_ge(s_h2, u - 1)
                tokens = slice(hf * HT, (hf + 1) * HT)
                dve.scalar_tensor_tensor(h2[u % 2][:], k.x1[:, kd, tokens],
                                         k.cols[:, k.c_norm_ffn + kd:k.c_norm_ffn + kd + 1], k.rs[:, tokens],
                                         ALU.mult, ALU.mult).then_inc(s_t2, 1)

            for n in range(LEAD):
                split(n)
            for kd in range(KD):
                h2_tile(0, kd)
            for n, (hf, src, kt, m, f) in enumerate(blocks):
                split(n + LEAD)
                u = FT * hf + f
                if src == "up":
                    dve.wait_ge(s_silu, u + 1)
                    dve.wait_ge(s_used, n + 1)
                    dve.tensor_tensor(two(gu[u % 2][:]), two(gu[u % 2][:]), pair(4 * (f % 2) + 2), ALU.mult)\
                       .then_inc(s_mul, 1)
                elif src == "down":
                    if kt == 0 and hf == 0:
                        dve.wait_ge(s_used, NGU)
                        h2_tile(1, f)
                    if kt + m == FT:
                        dve.wait_ge(s_used, n + 1)
                        x1 = two(k.x1[:, f, hf * HT:(hf + 1) * HT])
                        dve.tensor_tensor(x1, x1, pair(down_bank(f)), ALU.add).then_inc(s_x2, 1)

        @block.tensor
        def _(pe):
            for n, (hf, src, kt0, m, f) in enumerate(blocks):
                u = FT * hf + f
                pe.wait_ge(s_l, n + 1)
                if src == "down":
                    if kt0 == 0:
                        if f < 4:
                            pe.wait_ge(s_mul, FT * (hf + 1) - (1 if f < 2 else 0))
                        else:
                            pe.wait_ge(s_x2, KD * hf + f - 3)
                    if f == 0:
                        pe.wait_ge(s_al, FT * hf + kt0 + m)
                    first_bank = down_bank(f)
                    x_h, x_l = act_h, act_l
                else:
                    if src == "gate" and f >= 2:
                        pe.wait_ge(s_mul, u - 1)
                    elif src == "gate" and hf:
                        pe.wait_ge(s_x2, KD - 2 + 2 * f)
                    first_bank = 4 * (f % 2) + 2 * int(src == "up")
                    x_h, x_l = h2_h, h2_l
                pieces = [(first_bank + c, slice(c * HC, (c + 1) * HC)) for c in range(2)]
                for kt in range(m):
                    if src == "gate" and f == 0:
                        pe.wait_ge(s_h2, KD * hf + kt + 1)
                    last = kt0 + kt == (FT if src == "down" else KD) - 1
                    mm = split_product(pe, ps, w_h[n % NSPLIT], w_l[n % NSPLIT], kt, x_h, x_l, kt0 + kt, pieces,
                                       kt0 + kt == 0, last)
                mm.then_inc(s_used, 1)


def stage_final(k):
    nc, ps = k.nc, k.ps
    NX = TOK // XT
    off = k.ROWS_OFF
    weight = k.at("final_weight", off, [P, DM])
    off += DM * 4
    square = k.at("final_square", off, [P, DM])
    off += DM * 4
    y = [k.at(f"final_rows{i}", off + i * DM * 4, [P, DM]) for i in range(3)]
    off += 3 * DM * 4
    ss = k.at("final_square_sums", off, [P, NX])
    rs = k.at("final_rstd", off + 64, [P, NX])
    s_w, s_turn, s_ss, s_rs, s_y = (k.sem("final_weight_loaded"), k.sem("final_turned"), k.sem("final_ss"),
                                    k.sem("final_rstd_ready"), k.sem("final_ready"))
    s_out = k.y_stored

    with nc.Block() as block:

        @block.sync
        def _(sp):
            sp.dma_start(weight[:], k.norm_final.partition_broadcast(P)).then_inc(s_w, 16)
            n_out = [0] * 3
            for t in range(NX):
                sp.wait_ge(s_y, t + 1)
                a, b = t * XT, (t + 1) * XT
                m = max(0, min(b, SEQ) - a)
                sp.dma_start(k.y_prompt[0, a:a + m], y[t % 3][0:m, :]).then_inc(s_out[t % 3], 16)
                n_out[t % 3] += 16
                if m < XT:
                    sp.dma_start(k.y_sample.rearrange("b t d -> (b t) d"), y[t % 3][m:XT, :]).then_inc(s_out[t % 3], 16)
                    n_out[t % 3] += 16
            for i in range(3):
                sp.wait_ge(s_out[i], n_out[i])

        @block.tensor
        def _(pe):
            for t in range(NX):
                if t >= 3:
                    pe.wait_ge(s_y, t - 2)
                for f in range(KD):
                    mm = pe.transpose(ps[0:XT, 2 * (t % 3) + f // 4, (f % 4) * P:(f % 4 + 1) * P],
                                      k.x1[:, f, t * XT:(t + 1) * XT], k.ident[:])
                mm.then_inc(s_turn, 1)

        @block.scalar
        def _(act):
            def root(t):
                act.wait_ge(s_rs, 3 * t + 1)
                act.activation(rs[0:XT, t:t + 1], rs[0:XT, t:t + 1], ACT.Sqrt).then_inc(s_rs, 1)

            for t in range(NX):
                act.wait_ge(s_turn, t + 1)
                if t:
                    act.wait_ge(s_ss, t)
                rows = ps[0:XT, 2 * (t % 3):2 * (t % 3) + 2, :].rearrange("p a n -> p (a n)")
                act.activation(square[0:XT], rows, ACT.Square, accum_out=ss[0:XT, t:t + 1]).then_inc(s_ss, 1)
                if t:
                    root(t - 1)
            root(NX - 1)

        @block.vector
        def _(dve):
            dve.wait_ge(s_w, 16)
            n_out = 0
            for t in range(NX):
                r = rs[0:XT, t:t + 1]
                dve.wait_ge(s_ss, t + 1)
                dve.tensor_scalar(r, ss[0:XT, t:t + 1], 1.0 / DM, EPS, ALU.mult, ALU.add).then_inc(s_rs, 1)
                dve.wait_ge(s_rs, 3 * t + 2)
                dve.reciprocal(r, r).then_inc(s_rs, 1)
                dve.wait_ge(s_rs, 3 * t + 3)
                if t >= 3:
                    dve.wait_ge(s_out[t % 3], 16 * (t // 3))
                rows = ps[0:XT, 2 * (t % 3):2 * (t % 3) + 2, :].rearrange("p a n -> p (a n)")
                dve.scalar_tensor_tensor(y[t % 3][0:XT], rows, r, weight[0:XT], ALU.mult, ALU.mult).then_inc(s_y, 1)


class Kit:

    BASE = 16512

    def __init__(self, nc, ctx):
        self.nc, self.ctx, self.low, self.stage_sems = nc, ctx, 0, []

    def at(self, name, offset, shape, dtype=F32):
        return self.nc.alloc_sbuf_tensor_at(name, shape, dtype, offset=self.BASE + offset)

    def sb(self, name, shape, dtype=F32):
        t = self.at(name, self.low, shape, dtype)
        size = 4
        for n in shape[1:]:
            size *= n
        self.low += (size + 31) // 32 * 32
        assert self.low <= self.HT_OFF
        return t

    def sem(self, name):
        s = self.nc.alloc_semaphore(name)
        self.stage_sems.append(s)
        return s

    def end_sems(self):
        self.nc.clear_and_free_semaphores(self.stage_sems)
        self.nc.all_engine_barrier()
        self.stage_sems = []

    HT_OFF = 14592
    ROWS_OFF = HT_OFF + KD * TOK * 4
    KT_OFF = ROWS_OFF + TT * R_END * 4
    VA_OFF = KT_OFF + 4 * TOK * 4
    AQ_OFF = VA_OFF + (TT * MH * (MD + 1) * 4 + 31) // 32 * 32
    X_OFF = AQ_OFF
    AT_OFF = AQ_OFF + HG * TOK * 4
    QK_OFF = AT_OFF + MH * TOK * 4
    RING_OFF = QK_OFF + 8 * TOK * 4
    PACK_OFF = RING_OFF + NB * MH * (MD + 1) * 4
    WORK_OFF = PACK_OFF + 2 * TOK * 4
    CMP_END = QK_OFF + (NB * P + NG * HD + (NB + 1) * GD) * 4
    TOP = 229376 - 16512


STAGES = [stage_norm_in, stage_token_major, stage_feature_major, stage_gates, stage_mlstm, stage_compress,
          stage_nsa_prompt, stage_nsa_samples, stage_merge, stage_ffn, stage_final]


def build(nc, ins, outs):
    with ExitStack() as ctx:
        k = Kit(nc, ctx)
        (k.x_prompt, k.x_sample, k.cache_k_cmp, k.cache_v_cmp, k.cache_k_slc, k.cache_v_slc, k.state_k_win,
         k.state_v_win, k.state_conv, k.state_C, k.state_n, k.state_m, k.page_table, k.norm_mix, k.w_in, k.b_in,
         k.conv_w, k.conv_b, k.cmp_pos_k, k.cmp_pos_v, k.cmp_proj_k, k.cmp_proj_v, k.m_norm, k.w_a, k.w_b, k.w_o,
         k.norm_ffn, k.w_ffn_in, k.w_ffn_out, k.norm_final) = ins
        k.y_prompt, k.y_sample = outs[0:2]
        (k.o_k_cmp, k.o_v_cmp, k.o_k_slc, k.o_v_slc, k.o_k_win, k.o_v_win, k.o_conv, k.o_C, k.o_n, k.o_m) = [
            tuple(outs[2 + 2 * n:4 + 2 * n]) for n in range(10)]
        k.ps = ctx.enter_context(nc.psum_tensor("banks", [P, 8, 512], F32))
        k.rows_stored, k.windows_stored, k.tail_stored, k.m_stored, k.states_stored = [
            ctx.enter_context(nc.semaphore(f"{name}_stored")) for name in ("rows", "windows", "tail", "m", "states")]
        k.y_stored = [ctx.enter_context(nc.semaphore(f"y_stored{i}")) for i in range(3)]
        place_constants(k)
        k.select = k.sb("select_head", [P, MH, P])
        k.gate_cols = k.sb("gate_cols", [P, TT, 4, MH])
        k.decay, k.decay_row = k.sb("decay", [P, MH, QT + NB]), k.sb("decay_row", [MH, QT + NB])
        k.m_c, k.m_s0, k.m_s1 = k.sb("m_chunks", [MH, QT + 1]), k.sb("m_samples", [MH, NB]), k.sb("m_samples_new", [MH, NB])
        k.gates, k.page_idx = k.sb("branch_gates", [P, TT, NH, 3]), k.sb("page_idx", [P, NB], I32)
        k.SPARE_OFF = k.low
        k.hT = k.at("hT", k.HT_OFF, [P, KD, TOK])
        k.rows = k.at("token_rows", k.ROWS_OFF, [P, TT, R_END])
        k.kT_pad = k.at("kT_pad", k.KT_OFF, [P, 4, TOK])
        k.v_aug = k.at("v_and_ones", k.VA_OFF, [P, TT, MH, MD + 1])
        k.aq = k.at("nsa_qT", k.AQ_OFF, [P, HG, TOK])
        k.aT = k.at("mlstm_outT", k.AT_OFF, [P, MH, TOK])
        k.qk = k.at("mlstm_qkT", k.QK_OFF, [P, 8, TOK])
        k.packed = k.at("gates_packed", k.PACK_OFF, [P, TOK])
        k.neg_m = k.at("neg_m", k.PACK_OFF + TOK * 4, [MH, TOK])
        k.kT_last = k.at("kT_new_rows", k.VA_OFF + HG * TOK * 4, [P, 4, NS_TOK])
        k.bT = k.at("nsa_outT", k.VA_OFF, [P, HG, TOK])
        k.kc_t = k.at("kcT_samples", k.QK_OFF, [P, NB, P])
        k.kc_pad = k.at("kcT_prompt_pad", k.QK_OFF + NB * P * 4, [P, NG, HD])
        k.vc = k.at("vc", k.QK_OFF + (NB * P + NG * HD) * 4, [P, NB + 1, GD])
        k.x1 = k.at("x1T", k.HT_OFF, [P, KD, TOK])
        k.rs = k.at("x1_rstd", k.SPARE2_OFF, [P, TOK])
        with nc.allow_non_contiguous_dma(reason="small vectors and states"):
            for stage in STAGES:
                stage(k)
                if stage in (stage_mlstm, stage_nsa_samples):
                    k.end_sems()


_INS = ["x_prompt", "x_sample", "cache_k_cmp", "cache_v_cmp", "cache_k_slc", "cache_v_slc", "state_k_win",
        "state_v_win", "state_conv", "state_C", "state_n", "state_m", "page_table", "norm_mix", "w_in", "b_in",
        "conv_w", "conv_b", "cmp_pos_k", "cmp_pos_v", "cmp_proj_k", "cmp_proj_v", "m_norm", "w_a", "w_b", "w_o",
        "norm_ffn", "w_ffn_in", "w_ffn_out", "norm_final"]
_OUTS = [(1, SEQ, DM), (NB, NT, DM)]
for _ in range(4):
    _OUTS += [(1, 1, SEQ, NG, HD), (1, NB, NT, NG, HD)]
for _ in range(2):
    _OUTS += [(1, 1, WIN, NG, HD), (1, NB, WIN, NG, HD)]
_OUTS += [(1, 1, CW - 1, 2 * DA), (1, NB, CW - 1, 2 * DA), (1, 1, MH, MD, MD), (1, NB, MH, MD, MD),
          (1, 1, MH, MD), (1, NB, MH, MD), (1, 1, MH), (1, NB, MH)]


def kernel(**inputs):
    import numpy as _np
    import concourse.bacc as _bacc
    from concourse import mybir as _mybir
    from concourse.bass_utils import run_bass_kernel_spmd as _run

    nc = _bacc.Bacc("TRN2", target_bir_lowering=False, num_devices=1)
    arrays, ins, outs = {}, [], []
    for name in _INS:
        a = _np.ascontiguousarray(inputs[name])
        arrays[f"in_{name}_dram"] = a
        ins.append(nc.dram_tensor(f"in_{name}_dram", a.shape, _mybir.dt.from_np(a.dtype), kind="ExternalInput").ap())
    for i, shape in enumerate(_OUTS):
        outs.append(nc.dram_tensor(f"out_{i}_dram", shape, _mybir.dt.float32, kind="ExternalOutput").ap())
    build(nc, ins, outs)
    r = _run(nc, [arrays], core_ids=[0])
    return tuple(r.results[0][f"out_{i}_dram"] for i in range(len(_OUTS)))
```

```python
from contextlib import ExitStack

import concourse.bass as bass
from concourse import mybir

F32 = mybir.dt.float32
I32 = mybir.dt.int32
F32R = mybir.dt.float32r
U32 = mybir.dt.uint32
ALU = mybir.AluOpType
ACT = mybir.ActivationFunctionType
AX = mybir.AxisListType

P = 128
DM = 1024
KD = DM // P
SEQ = 1024
NB, NT = 8, 4
NS_TOK = NB * NT
TOK = SEQ + NS_TOK
QT = SEQ // P
TT = QT + 1
PAST, PAGE = 2048, 128
MH, MD = 4, 128
DA = MH * MD
CW = 4
NH, HD, NG = 8, 64, 2
HG = NH // NG
GD = NG * HD
STRIDE, CBLK = 16, 32
NSUB = PAST // STRIDE
SBLK, NSEL = 64, 16
NBLK = PAST // SBLK + 1
WIN = 512
DFF = 2816
FT = DFF // P
EPS = 1e-6
NEG = -1e30
BIG = 1e30
SLOPES = [2.0 ** -(h + 1) for h in range(NH)]
KSCALE = float(MD) ** -0.5
QSCALE = float(HD) ** -0.5

C_QK, C_V, C_O, C_I, C_F = 0, 1024, 1536, 2048, 2052
C_AQ, C_KV, C_G, C_MRG = 2056, 2568, 3336, 3360
O_KC, O_VC, O_KS, O_KW, O_END = 0, 128, 256, 384, 512
R_IG, R_FG, R_VS, R_VW, R_G, R_END = 0, 4, 8, 136, 264, 288
RW = DA + O_END + R_END

CH = TOK // 3
NCH = TOK // CH
FFN_RAW = 3
XT = CH // 4
TOKEN_CHUNKS = [(0, 512), (512, 512), (1024, NS_TOK)]


class Chain:

    def __init__(self, eng, sem, start=0):
        self.eng, self.sem, self.n = eng, sem, start

    def __call__(self, ins):
        self.n += 1
        ins.then_inc(self.sem, 1)
        self.eng.wait_ge(self.sem, self.n)



def split_product(pe, out, w_h, w_l, kt, x_h, x_l, kd, pieces, first, last):
    for n, (w, x) in enumerate(((w_l, x_h), (w_h, x_l), (w_h, x_h))):
        for bank, cols in pieces:
            mm = pe.matmul(out[:, bank, 0:cols.stop - cols.start], w[:, kt, :], x[:, kd, cols],
                           start=(first and n == 0), stop=(last and n == 2))
    return mm


def place_constants(k):
    nc = k.nc
    k.ident = k.sb("ident", [P, P])
    k.ones = k.sb("ones", [P, P])
    k.cols = k.sb("vector_cols", [P, 92])
    k.SPARE2_OFF = k.low
    k.vector_rows = k.sb("vector_rows", [92, P])
    k.rstd_x = k.sb("rstd_x", [P, TT])
    k.ss_x = k.sb("sum_squares_x", [P, TT])
    k.c_norm_mix, k.c_conv_w, k.c_conv_b, k.c_m_norm, k.c_norm_ffn = 0, 8, 40, 48, 52
    k.c_b_qk, k.c_b_o, k.c_b_mrg, k.c_b_q = 60, 68, 72, 88


def stage_norm_in(k):
    nc, ps = k.nc, k.ps
    x_all = k.at("x_all", k.ROWS_OFF, [P, TT, DM])
    square = k.at("x_square", k.ROWS_OFF + TT * DM * 4, [P, DM])
    s_x = [k.sem(f"x_loaded{i}") for i in range(3)]
    s_rows, s_rows_t = k.sem("rows_loaded"), k.sem("rows_turned")
    s_const, s_ss, s_rstd, s_h = k.sem("constants"), k.sem("sum_squares"), k.sem("rstd_ready"), k.sem("h_ready")
    s_turn, s_evac_a, s_evac_v = k.sem("h_turned"), k.sem("hT_evac_act"), k.sem("hT_evac_dve")
    lots = [(0, 2), (2, 5), (5, 8)]
    k.w_rows = k.at("w_rows", k.X_OFF, [P, KD, RW])
    k.b_rows = k.at("b_rows", k.X_OFF + KD * RW * 4, [P, RW])
    k.page_rows = k.at("page_rows", k.SPARE_OFF, [P, NB], I32)
    k.s_w_rows, k.s_b_rows = [k.sem(f"w_rows_loaded{i}") for i in range(6)], k.sem("b_rows_loaded")
    k.s_table = k.sem("table_loaded")
    k.row_segments = [(0, 512, C_V), (512, 896, C_KV), (896, 1024, C_KV + 512), (1024, 1032, C_I),
                      (1032, 1160, C_KV + 384), (1160, RW, C_KV + 640)]

    def token_rows(tt):
        return P if tt < QT else NS_TOK

    with nc.Block() as block:

        @block.sync
        def _(sp):
            xp = k.x_prompt[0].rearrange("(t p) d -> p t d", p=P)
            for n, (a, b) in enumerate(lots):
                sp.dma_start(x_all[:, a:b, :], xp[:, a:b, :]).then_inc(s_x[n], 16)
            sp.dma_start(x_all[0:NS_TOK, QT, :], k.x_sample.rearrange("b t d -> (b t) d")).then_inc(s_x[2], 16)
            for q in range(PAST // PAGE):
                entry = k.page_table[:, q:q + 1].rearrange("b q -> q b").to_broadcast([PAGE // STRIDE, NB])
                sp.dma_start(k.page_rows[q * 8:(q + 1) * 8, :], entry).then_inc(k.s_table, 16)
            w_in = k.w_in[0].rearrange("(k p) n -> p k n", p=P)
            for n, (a, b, c) in enumerate(k.row_segments):
                sp.dma_start(k.w_rows[:, :, a:b], w_in[:, :, c:c + b - a]).then_inc(k.s_w_rows[n], 16)
            for a, b, c in k.row_segments:
                sp.dma_start(k.b_rows[:, a:b], k.b_in[0, c:c + b - a].partition_broadcast(P)).then_inc(k.s_b_rows, 16)

        @block.gpsimd
        def _(pool):
            pool.memset(k.ones[:], 1.0).then_inc(s_const, 1)
            pool.memset(k.ident[:], 0.0).then_inc(s_const, 1)
            pool.wait_ge(s_const, 2)
            pool.affine_select(out=k.ident[:], in_=k.ident[:], compare_op=ALU.not_equal, fill=1.0, base=0,
                               pattern=[[-1, P]], channel_multiplier=1).then_inc(s_const, 1)
            pool.memset(k.ss_x[:], 1.0).then_inc(s_const, 1)

        @block.scalar
        def _(act):
            rows = k.vector_rows
            for first, n, src in (
                (k.c_norm_mix, 8, k.norm_mix[0].rearrange("(k p) -> k p", p=P)),
                (k.c_conv_w, 32, k.conv_w.rearrange("o w (k p) -> (o w k) p", p=P)),
                (k.c_conv_b, 8, k.conv_b[0].rearrange("(k p) -> k p", p=P)),
                (k.c_m_norm, 4, k.m_norm[0].rearrange("(k p) -> k p", p=P)),
                (k.c_norm_ffn, 8, k.norm_ffn[0].rearrange("(k p) -> k p", p=P)),
                (k.c_b_qk, 8, k.b_in[0, C_QK:C_V].rearrange("(k p) -> k p", p=P)),
                (k.c_b_o, 4, k.b_in[0, C_O:C_I].rearrange("(k p) -> k p", p=P)),
                (k.c_b_mrg, 16, k.b_in[0, C_MRG:].rearrange("(k p) -> k p", p=P)),
            ):
                act.dma_start(rows[first:first + n, :], src).then_inc(s_rows, 16)
            q_bias = k.b_in[0, C_AQ:C_KV].rearrange("(g i d) -> i g d", g=NG, i=HG)
            act.dma_start(rows[k.c_b_q:k.c_b_q + HG, :].rearrange("i (g d) -> i g d", g=NG), q_bias)\
               .then_inc(s_rows, 16)
            act.wait_ge(s_const, 4)
            for tt in range(TT):
                if tt in (0, 2, 5):
                    n = (0, 2, 5).index(tt)
                    act.wait_ge(s_x[n], 32 if n == 2 else 16)
                r = token_rows(tt)
                if tt:
                    act.wait_ge(s_ss, tt)
                act.activation(square[0:r, :], x_all[0:r, tt, :], ACT.Square,
                               accum_out=k.ss_x[0:r, tt:tt + 1]).then_inc(s_ss, 1)
            act.wait_ge(s_rstd, 1)
            act.activation(k.rstd_x[:], k.rstd_x[:], ACT.Sqrt).then_inc(s_rstd, 1)
            for kd in range(KD):
                act.wait_ge(s_turn, kd + 1)
                if kd == 0:
                    act.wait_ge(s_rows_t, 2)
                g = k.cols[:, k.c_norm_mix + kd:k.c_norm_mix + kd + 1]
                act.activation(k.hT[:, kd, 512:1024], ps[:, 3 * (kd % 2) + 1, :], ACT.Copy, scale=g)\
                   .then_inc(s_evac_a, 1)

        @block.vector
        def _(dve):
            dve.wait_ge(s_rows_t, 1)
            dve.tensor_copy(k.cols[:], ps[:, 6, 0:92]).then_inc(s_rows_t, 1)
            dve.wait_ge(s_ss, TT)
            dve.tensor_scalar(k.rstd_x[:], k.ss_x[:], 1.0 / DM, EPS, ALU.mult, ALU.add).then_inc(s_rstd, 1)
            dve.wait_ge(s_rstd, 2)
            dve.reciprocal(k.rstd_x[:], k.rstd_x[:]).then_inc(s_rstd, 1)
            dve.wait_ge(s_rstd, 3)
            for tt in range(TT):
                r = token_rows(tt)
                dve.tensor_scalar(x_all[0:r, tt, :], x_all[0:r, tt, :], k.rstd_x[0:r, tt:tt + 1], None,
                                  ALU.mult).then_inc(s_h, 1)
            for kd in range(KD):
                dve.wait_ge(s_turn, kd + 1)
                dve.wait_ge(s_rows_t, 2)
                g = k.cols[:, k.c_norm_mix + kd:k.c_norm_mix + kd + 1]
                dve.tensor_scalar(k.hT[:, kd, 0:512], ps[:, 3 * (kd % 2), :], g, None, ALU.mult)
                dve.tensor_scalar(k.hT[:, kd, SEQ:TOK], ps[:, 3 * (kd % 2) + 2, 0:NS_TOK], g, None, ALU.mult)\
                   .then_inc(s_evac_v, 1)

        @block.tensor
        def _(pe):
            pe.wait_ge(s_const, 3)
            pe.wait_ge(s_rows, 16 * 9)
            pe.transpose(ps[:, 6, 0:92], k.vector_rows[:], k.ident[0:92, 0:92]).then_inc(s_rows_t, 1)
            for kd in range(KD):
                if kd >= 2:
                    pe.wait_ge(s_evac_v, kd - 1)
                    pe.wait_ge(s_evac_a, kd - 1)
                for tt in range(TT):
                    if kd == 0:
                        pe.wait_ge(s_h, tt + 1)
                    r = token_rows(tt)
                    mm = pe.transpose(ps[:, 3 * (kd % 2) + tt // 4, (tt % 4) * P:(tt % 4) * P + r],
                                      x_all[0:r, tt, kd * P:(kd + 1) * P], k.ident[0:r, 0:r])
                mm.then_inc(s_turn, 1)


class Compress:

    def __init__(self, k, tag, sequences, off, top, spare, banks):
        self.k, self.tag, self.banks = k, tag, banks
        row = STRIDE * GD
        self.units = [(s, kv) for s in sequences for kv in range(2)]
        self.x = [k.at(f"{tag}_strides{i}", off + i * row * 4, [P, row]) for i in range(2)]
        off += 2 * row * 4
        self.w_pos = [k.at(f"{tag}_pos_weights{i}", off + i * STRIDE * HD * 4, [P, STRIDE, HD]) for i in range(4)]
        off += 4 * STRIDE * HD * 4
        self.prod = [k.at(f"{tag}_pos_product{i}", off + i * row * 4, [P, row]) for i in range(2)]
        assert off + 2 * row * 4 <= top
        off = spare
        self.half_sums = [k.at(f"{tag}_half_sums{i}", off + i * 1024, [P, 2, GD]) for i in range(2)]
        off += 2048
        self.second_t = [k.at(f"{tag}_second_halfT{i}", off + i * 512, [P, P]) for i in range(2)]
        self.pooled_t = [k.at(f"{tag}_pooledT{i}", off + 1024 + i * 512, [P, P]) for i in range(2)]
        off += 2048
        self.proj = [k.at(f"{tag}_proj{i}", off + i * 512, [P, P]) for i in range(2)]
        off += 1024
        assert off <= k.HT_OFF
        self.s_x = [k.sem(f"{tag}_strides_loaded{i}") for i in range(2)]
        (self.s_w, self.s_zero, self.s_proj, self.s_first, self.s_second, self.s_sums, self.s_turn, self.s_sec_t,
         self.s_pool, self.s_map, self.s_evac) = [
            k.sem(f"{tag}_{name}") for name in
            ("pos_loaded", "proj_zeroed", "proj_loaded", "first_product", "second_product", "half_sums_ready",
             "halves_turned", "second_copied", "pooled", "mapped", "evac")]

    def strides(self, u):
        return NSUB if self.units[u][0] < NB else SEQ // STRIDE

    def load_weights(self, sp):
        k = self.k
        for half in range(2):
            for kv, src in enumerate((k.cmp_pos_k, k.cmp_pos_v)):
                rows = src[0, half * STRIDE:(half + 1) * STRIDE].rearrange("j d -> (j d)").partition_broadcast(P)
                sp.dma_start(self.w_pos[2 * kv + half][:].rearrange("p j d -> p (j d)"), rows).then_inc(self.s_w, 16)
        sp.wait_ge(self.s_zero, 1)
        for kv, src in enumerate((k.cmp_proj_k, k.cmp_proj_v)):
            for g in range(NG):
                rows = slice(g * HD, (g + 1) * HD)
                sp.dma_start(self.proj[kv][rows, rows], src[0]).then_inc(self.s_proj, 16)

    def zero(self, pool):
        pool.memset(self.proj[0][:], 0.0)
        pool.memset(self.proj[1][:], 0.0).then_inc(self.s_zero, 1)

    def buffer_free(self, eng, u):
        if u >= 2:
            eng.wait_ge(self.s_second, u - 1)
            eng.wait_ge(self.s_first, u - 1)

    def product(self, eng, u, half, done):
        n, kv = self.strides(u), self.units[u][1]
        eng.wait_ge(self.s_x[u % 2], 16 * (u // 2 + 1))
        if u == 0:
            eng.wait_ge(self.s_w, 64)
        w = self.w_pos[2 * kv + half][0:n].unsqueeze(2).to_broadcast([n, STRIDE, NG, HD])
        eng.tensor_tensor(self.prod[half][0:n].rearrange("p (j g d) -> p j g d", j=STRIDE, g=NG),
                          self.x[u % 2][0:n].rearrange("p (j g d) -> p j g d", j=STRIDE, g=NG), w,
                          ALU.mult).then_inc(done, 1)

    def first_half(self, pool, u):
        if u:
            pool.wait_ge(self.s_sums, u)
        self.product(pool, u, 0, self.s_first)

    def second_half_and_sums(self, dve, u):
        n = self.strides(u)
        self.product(dve, u, 1, self.s_second)
        dve.wait_ge(self.s_second, u + 1)
        if u >= 2:
            dve.wait_ge(self.s_turn, u - 1)
        sums = self.half_sums[u % 2]
        dve.tensor_reduce(sums[0:n, 1, :], self.prod[1][0:n].rearrange("p (j x) -> p x j", j=STRIDE), AX.X, ALU.add)
        dve.wait_ge(self.s_first, u + 1)
        dve.tensor_reduce(sums[0:n, 0, :], self.prod[0][0:n].rearrange("p (j x) -> p x j", j=STRIDE), AX.X,
                          ALU.add).then_inc(self.s_sums, 1)
        dve.wait_ge(self.s_sums, u + 1)

    def pool_pair(self, dve, u):
        n = self.strides(u)
        dve.wait_ge(self.s_sec_t, u + 1)
        if u >= 2:
            dve.wait_ge(self.s_map, u - 1)
        bank = self.banks[0]
        dve.tensor_tensor(self.pooled_t[u % 2][:, 0:n - 1], self.k.ps[:, bank, 0:n - 1],
                          self.second_t[u % 2][:, 1:n], ALU.add).then_inc(self.s_pool, 1)

    def turn(self, pe, u):
        n = self.strides(u)
        pe.wait_ge(self.s_sums, u + 1)
        if u:
            pe.wait_ge(self.s_pool, u)
        for half in range(2):
            bank = self.banks[half]
            mm = pe.transpose(self.k.ps[:, bank, 0:n], self.half_sums[u % 2][0:n, half, :],
                              self.k.ident[0:n, 0:n])
        mm.then_inc(self.s_turn, 1)

    def map(self, pe, u):
        n = self.strides(u) - 1
        bank = self.banks[2]
        if u == 0:
            pe.wait_ge(self.s_proj, 64)
        pe.wait_ge(self.s_pool, u + 1)
        if u:
            pe.wait_ge(self.s_evac, u)
        if self.units[u][1]:
            mm = pe.matmul(self.k.ps[0:n, bank, 0:GD], self.pooled_t[u % 2][:, 0:n], self.proj[1][:],
                           start=True, stop=True)
        else:
            mm = pe.matmul(self.k.ps[:, bank, 0:n], self.proj[0][:], self.pooled_t[u % 2][:, 0:n],
                           start=True, stop=True)
        mm.then_inc(self.s_map, 1)

    def copy_second(self, act, u):
        n = self.strides(u)
        bank = self.banks[1]
        act.wait_ge(self.s_turn, u + 1)
        if u >= 2:
            act.wait_ge(self.s_pool, u - 1)
        act.copy(self.second_t[u % 2][:, 0:n], self.k.ps[:, bank, 0:n]).then_inc(self.s_sec_t, 1)

    def keep(self, act, u):
        k = self.k
        s, kv = self.units[u]
        n = self.strides(u) - 1
        bank = self.banks[2]
        act.wait_ge(self.s_map, u + 1)
        if kv:
            act.copy(k.vc_s[0:n, s, :] if s < NB else k.vc_p[0:n], k.ps[0:n, bank, 0:GD])\
               .then_inc(self.s_evac, 1)
        else:
            act.copy(k.kc_s[:, s, 0:n] if s < NB else k.kc_p[:, 0:n], k.ps[:, bank, 0:n])\
               .then_inc(self.s_evac, 1)


def stage_token_major(k):
    nc, ps = k.nc, k.ps
    w, bias, table, segments = k.w_rows, k.b_rows, k.page_rows, k.row_segments
    s_w, s_bias, s_pt = k.s_w_rows, k.s_b_rows, k.s_table
    lane = k.at("stride_in_page", k.SPARE_OFF + 32, [P, NB], I32)
    scratch = k.at("page_scratch", k.SPARE_OFF + 64, [P, NB])
    job = Compress(k, "cmp", range(NB), k.X_OFF + (KD + 1) * RW * 4, k.OUT_OFF, k.SPARE_OFF + 96, (5, 6, 7))
    NUNIT = len(job.units)
    s_idx, s_iota, s_chain = k.sem("indices_ready"), k.sem("lanes"), k.sem("cmp_chain")
    slots, NBANK = 3 * TT, 4
    order = [QT] + list(range(QT))
    slot_of = [u * (slots - 3) // NUNIT for u in range(NUNIT)]
    s_mm, s_evac = k.sem("rows_product"), k.sem("rows_evac")
    s_kt, s_kt_evac = k.sem("k_turned"), k.sem("kT_evac")
    s_store, s_ring = k.rows_stored, k.windows_stored
    groups = [(0, DA), (DA, DA + O_END), (DA + O_END, RW)]

    def token_rows(tt):
        return P if tt < QT else NS_TOK

    with nc.Block() as block:

        @block.sync
        def _(sp):
            job.load_weights(sp)
            for past, o in ((k.state_k_win, k.o_k_win[1]), (k.state_v_win, k.o_v_win[1])):
                sp.dma_start(o[0, :, 0:WIN - NT].rearrange("b t g d -> b (t g d)"),
                             past[0, :, NT:].rearrange("b t g d -> b (t g d)")).then_inc(s_ring, 16)
            outs = [(k.rows_out, O_KC, k.o_k_cmp), (k.rows_out, O_VC, k.o_v_cmp), (k.rows_out, O_KS, k.o_k_slc),
                    (k.rows, R_VS, k.o_v_slc)]
            for pos, tt in enumerate(order):
                sp.wait_ge(s_evac, 3 * (pos + 1))
                for rows, col, (o_p, o_s) in outs:
                    if tt < QT:
                        dst = o_p[0, 0, tt * P:(tt + 1) * P].rearrange("t g d -> t (g d)")
                        sp.dma_start(dst, rows[:, tt, col:col + GD]).then_inc(s_store, 16)
                    else:
                        dst = o_s[0].rearrange("b t g d -> (b t) (g d)")
                        sp.dma_start(dst, rows[0:NS_TOK, tt, col:col + GD]).then_inc(s_store, 16)
                for rows, col, (o_p, o_s) in ((k.rows_out, O_KW, k.o_k_win), (k.rows, R_VW, k.o_v_win)):
                    if QT // 2 <= tt < QT:
                        dst = o_p[0, 0, (tt - 4) * P:(tt - 3) * P].rearrange("t g d -> t (g d)")
                        sp.dma_start(dst, rows[:, tt, col:col + GD]).then_inc(s_store, 16)
                    elif tt == QT:
                        for b in range(NB):
                            dst = o_s[0, b, WIN - NT:].rearrange("t g d -> t (g d)")
                            sp.dma_start(dst, rows[NT * b:NT * (b + 1), tt, col:col + GD]).then_inc(s_store, 16)
            sp.wait_ge(s_store, 16 * (4 * TT + 2 * 4 + 2 * NB))
            sp.wait_ge(s_ring, 32)

        @block.gpsimd
        def _(pool):
            pool.iota(lane[:], pattern=[[0, NB]], base=0, channel_multiplier=1).then_inc(s_iota, 1)
            job.zero(pool)
            pool.wait_ge(s_idx, 1)

            def gather(u):
                s, kv = job.units[u]
                cache = (k.cache_k_cmp, k.cache_v_cmp)[kv]
                job.buffer_free(pool, u)
                pool.indirect_dma_start(
                    out=job.x[u % 2][:], out_offset=None,
                    in_=cache[0].rearrange("q (s j) g d -> (q s) (j g d)", j=STRIDE),
                    in_offset=bass.IndirectOffsetOnAxis(ap=k.page_idx[:, s:s + 1], axis=0)).then_inc(job.s_x[u % 2], 16)

            gather(0)
            gather(1)
            for u in range(NUNIT):
                job.first_half(pool, u)
                if u + 2 < NUNIT:
                    gather(u + 2)

        @block.scalar
        def _(act):
            def copy_keys(pos):
                tt = order[pos]
                r = token_rows(tt)
                act.wait_ge(s_kt, pos + 1)
                act.copy(k.kT[:, :, tt * P:tt * P + r],
                         ps[:, 4, 0:2 * P].rearrange("p (w t) -> p w t", w=2)[:, :, 0:r]).then_inc(s_kt_evac, 1)

            for slot in range(slots):
                if slot % 3 == 2 and slot > 2:
                    copy_keys(slot // 3 - 1)
                for u in range(NUNIT):
                    if slot_of[u] + 2 == slot:
                        job.copy_second(act, u)
                        if u:
                            job.keep(act, u - 1)
            copy_keys(TT - 1)
            job.keep(act, NUNIT - 1)

        @block.vector
        def _(dve):
            link = Chain(dve, s_chain)
            dve.memset(k.v_aug[:, :, :, MD:MD + 1], 1.0)
            dve.wait_ge(s_iota, 1)
            dve.wait_ge(s_pt, 16 * 16)
            link(dve.tensor_single_scalar(lane[:], lane[:], 7, ALU.bitwise_and))
            link(dve.tensor_copy(scratch[:], lane[:]))
            dve.scalar_tensor_tensor(k.page_idx[:], table[:], 8.0, scratch[:], ALU.mult, ALU.add).then_inc(s_idx, 1)
            dve.wait_ge(s_bias, 96)
            for slot in range(slots):
                tt, n = order[slot // 3], slot % 3
                r = token_rows(tt)
                a, b = groups[n]
                dve.wait_ge(s_mm, slot + 1)
                src = ps[0:r, slot % NBANK, 0:b - a]
                if n == 0:
                    dve.tensor_tensor(k.v_aug[0:r, tt, :, 0:MD], src.rearrange("p (h d) -> p h d", h=MH),
                                      bias[0:r, a:b].rearrange("p (h d) -> p h d", h=MH), ALU.add)\
                       .then_inc(s_evac, 1)
                else:
                    dst = k.rows_out if n == 1 else k.rows
                    dve.tensor_tensor(dst[0:r, tt, :], src, bias[0:r, a:b], ALU.add)\
                       .then_inc(s_evac, 1)
                for u in range(NUNIT):
                    if slot_of[u] == slot:
                        job.second_half_and_sums(dve, u)
                        if u:
                            job.pool_pair(dve, u - 1)
            job.pool_pair(dve, NUNIT - 1)

        @block.tensor
        def _(pe):
            def turn(pos):
                tt = order[pos]
                r = token_rows(tt)
                pe.wait_ge(s_evac, 3 * (pos + 1))
                if pos:
                    pe.wait_ge(s_kt_evac, pos)
                for which, col in enumerate((O_KS, O_KW)):
                    mm = pe.transpose(ps[:, 4, which * P:which * P + r],
                                      k.rows_out[0:r, tt, col:col + GD], k.ident[0:r, 0:r])
                mm.then_inc(s_kt, 1)

            for slot in range(slots):
                tt, n = order[slot // 3], slot % 3
                r = token_rows(tt)
                a, b = groups[n]
                if slot < 3:
                    for i in ((0,), (1, 2), (3, 4, 5))[n]:
                        pe.wait_ge(s_w[i], 16)
                if slot >= NBANK:
                    pe.wait_ge(s_evac, slot - NBANK + 1)
                for kd in range(KD):
                    mm = pe.matmul(ps[0:r, slot % NBANK, 0:b - a], k.hT[:, kd, tt * P:tt * P + r],
                                   w[:, kd, a:b], start=(kd == 0), stop=(kd == KD - 1))
                mm.then_inc(s_mm, 1)
                if n == 2 and slot > 2:
                    turn(slot // 3 - 1)
                for u in range(NUNIT):
                    if slot_of[u] + 2 == slot:
                        job.turn(pe, u)
                        if u:
                            job.map(pe, u - 1)
            turn(TT - 1)
            job.map(pe, NUNIT - 1)


def stage_feature_major(k):
    nc, ps = k.nc, k.ps
    NRAW, NSPLIT, LEAD, KB = 2, 3, 2, 4
    NJ = 16
    NBK = NJ * KD // KB
    off = k.RING_OFF
    hT_h, hT_l = k.at("fm_hT_h", off, [P, KD, TOK], F32R), k.at("fm_hT_l", k.HT_OFF, [P, KD, TOK], F32R)
    off += KD * TOK * 4
    raw = [k.at(f"fm_raw{i}", off + i * KB * 512, [P, KB, P]) for i in range(NRAW)]
    off += NRAW * KB * 512
    w_h = [k.at(f"fm_w_h{i}", off + 2 * i * KB * 512, [P, KB, P], F32R) for i in range(NSPLIT)]
    w_l = [k.at(f"fm_w_l{i}", off + (2 * i + 1) * KB * 512, [P, KB, P], F32R) for i in range(NSPLIT)]
    assert off + 2 * NSPLIT * KB * 512 <= k.TOP
    pre = [k.at(f"qk_pre{i}", k.AQ_OFF + i * TOK * 4, [P, TOK]) for i in range(2)]
    conv = [k.at(f"qk_conv{i}", k.AQ_OFF + (2 + i) * TOK * 4, [P, TOK]) for i in range(2)]
    CO = NS_TOK + CW - 1
    tail = k.at("conv_tail", k.AT_OFF, [CO, 2 * DA])
    past_rows = k.at("conv_past", k.AT_OFF + 8 * DA, [NB * (CW - 1), 2 * DA])
    ext = k.at("sample_ext", k.AT_OFF + 16 * DA, [P, NB, CW - 1 + NT])
    s_raw = [k.sem(f"fm_raw_full{i}") for i in range(NRAW)]
    s_h, s_l, s_used, s_past = k.sem("fm_w_h"), k.sem("fm_w_l"), k.sem("fm_block_used"), k.sem("conv_past_loaded")
    s_xh, s_xl = k.sem("hT_h_ready"), k.sem("hT_l_ready")
    s_evac, s_o_evac = k.sem("feat_evac"), k.sem("o_gate_evac")
    s_conv, s_silu = k.sem("conv_ready"), k.sem("silu_ready")
    s_tail, s_tail_evac, s_tail_out, s_chain = k.sem("tail_turned"), k.sem("tail_evac"), k.tail_stored, k.sem("conv_chain")
    PER = KD // KB

    def w_cols(j, kt):
        w_in = k.w_in[0].rearrange("(k p) n -> p k n", p=P)[:, kt:kt + KB]
        if j < 8:
            return [(slice(0, P), w_in[:, :, C_QK + j * P:C_QK + (j + 1) * P])]
        if j < 12:
            i = j - 8
            return [(slice(g * HD, (g + 1) * HD), w_in[:, :, C_AQ + (g * HG + i) * HD:C_AQ + (g * HG + i + 1) * HD])
                    for g in range(NG)]
        return [(slice(0, P), w_in[:, :, C_O + (j - 12) * P:C_O + (j - 11) * P])]

    n_dmas = [0] * NRAW
    full_at = []
    for n in range(NBK):
        n_dmas[n % NRAW] += len(w_cols(n // PER, 0))
        full_at.append(16 * n_dmas[n % NRAW])

    def banks(j):
        return ps[:, 3 * (j % 2):3 * (j % 2) + NCH, 0:CH]

    def chunks(t):
        return t.rearrange("p (c n) -> p c n", c=NCH)

    with nc.Block() as block:

        @block.sync
        def _(sp):
            for n in range(NBK):
                if n >= NRAW:
                    sp.wait_ge(s_l, n - NRAW + 1)
                for cols, src in w_cols(n // PER, n % PER * KB):
                    sp.dma_start(raw[n % NRAW][:, :, cols], src).then_inc(s_raw[n % NRAW], 16)
                if n == 1:
                    sp.dma_start(past_rows[:], k.state_conv[0].rearrange("b r c -> (b r) c")).then_inc(s_past, 16)
                if n == 12 * PER - 1:
                    sp.wait_ge(s_tail_evac, 8)
                    sp.dma_start(k.o_conv[0][0, 0], tail[0:CW - 1, :]).then_inc(s_tail_out, 16)
                    for b in range(NB):
                        first = CW - 1 + NT * b + 1
                        sp.dma_start(k.o_conv[1][0, b], tail[first:first + CW - 1, :]).then_inc(s_tail_out, 16)
            sp.wait_ge(s_tail_out, 16 * (1 + NB))

        @block.tensor
        def _(pe):
            pieces = [(c, slice(c * CH, (c + 1) * CH)) for c in range(NCH)]

            def turn_tail(j):
                pe.wait_ge(s_evac, j + 1)
                if j >= 1:
                    pe.wait_ge(s_tail_evac, j)
                pe.transpose(ps[0:CO, 6, 0:P], pre[j % 2][:, SEQ - CW + 1:TOK], k.ident[:])
                if j == 0:
                    pe.wait_ge(s_past, 16)
                pe.transpose(ps[:, 7, 0:NB * (CW - 1)], past_rows[:, j * P:(j + 1) * P],
                             k.ident[0:NB * (CW - 1), 0:NB * (CW - 1)]).then_inc(s_tail, 1)

            for n in range(NBK):
                j, kt0 = n // PER, n % PER * KB
                if kt0 == 0:
                    if j >= 14:
                        pe.wait_ge(s_o_evac, j - 13)
                    elif j >= 2:
                        pe.wait_ge(s_evac, j - 1)
                pe.wait_ge(s_l, n + 1)
                for kt in range(KB):
                    if j == 0:
                        pe.wait_ge(s_xl, kt0 + kt + 1)
                    mm = split_product(pe, banks(j), w_h[n % NSPLIT], w_l[n % NSPLIT], kt, hT_h, hT_l, kt0 + kt,
                                       pieces, kt0 + kt == 0, kt0 + kt == KD - 1)
                mm.then_inc(s_used, 1)
                if kt0 + KB == KD and 1 <= j <= 8:
                    turn_tail(j - 1)

        @block.gpsimd
        def _(pool):
            for n in range(NBK):
                pool.wait_ge(s_h, n + 1)
                pool.tensor_tensor(w_l[n % NSPLIT][:], raw[n % NRAW][:], w_h[n % NSPLIT][:].bitcast(F32), ALU.subtract)\
                    .then_inc(s_l, 1)
                if n % PER == PER - 1 and n // PER - 2 in range(4, 8):
                    j = n // PER - 2
                    pool.wait_ge(s_silu, j + 1)
                    pool.tensor_scalar(k.qk[:, j, :], k.qk[:, j, :], KSCALE, None, ALU.mult)

            pool.wait_ge(s_used, NBK)
            for kd in range(KD - 3, KD):
                pool.tensor_tensor(k.hT[:, kd, :], hT_h[:, kd, :].bitcast(F32), hT_l[:, kd, :].bitcast(F32), ALU.add)

        @block.scalar
        def _(act):
            def split(n):
                if n >= NBK:
                    return
                act.wait_ge(s_raw[n % NRAW], full_at[n])
                if n >= NSPLIT:
                    act.wait_ge(s_used, n - NSPLIT + 1)
                act.copy(w_h[n % NSPLIT][:], raw[n % NRAW][:]).then_inc(s_h, 1)

            for n in range(LEAD):
                split(n)
            for kd in range(KD):
                act.copy(hT_h[:, kd, :], k.hT[:, kd, :]).then_inc(s_xh, 1)
            for n in range(NBK):
                split(n + LEAD)
                j = n // PER
                if n % PER == 0 and 1 <= j <= 8:
                    act.wait_ge(s_conv, j)
                    act.activation(k.qk[:, j - 1, :], conv[(j - 1) % 2][:], ACT.Silu).then_inc(s_silu, 1)
                if n % PER == PER - 1 and j >= 12:
                    act.wait_ge(s_used, n + 1)
                    if j == 12:
                        act.wait_ge(s_tail_out, 16 * (1 + NB))
                    bcol = k.cols[:, k.c_b_o + j - 12:k.c_b_o + j - 11]
                    act.activation(chunks(k.aT[:, j - 12, :]), banks(j), ACT.Sigmoid, bias=bcol).then_inc(s_o_evac, 1)

        @block.vector
        def _(dve):
            link = Chain(dve, s_chain)

            def convolve(j):
                buf, out = pre[j % 2], conv[j % 2]
                tap = [k.cols[:, k.c_conv_w + 8 * t + j:k.c_conv_w + 8 * t + j + 1] for t in range(CW)]
                b = k.cols[:, k.c_conv_b + j:k.c_conv_b + j + 1]
                if j >= 2:
                    dve.wait_ge(s_silu, j - 1)
                link(dve.tensor_scalar(out[:, 0:SEQ], buf[:, 0:SEQ], tap[CW - 1], b, ALU.mult, ALU.add))
                for t in range(1, CW):
                    link(dve.scalar_tensor_tensor(out[:, t:SEQ], buf[:, 0:SEQ - t], tap[CW - 1 - t],
                                                  out[:, t:SEQ], ALU.mult, ALU.add))
                dve.wait_ge(s_tail, j + 1)
                dve.tensor_copy(tail[:, j * P:(j + 1) * P], ps[0:CO, 6, 0:P])
                dve.tensor_copy(ext[:, :, 0:CW - 1], ps[:, 7, 0:NB * (CW - 1)].rearrange("p (b r) -> p b r", b=NB))\
                   .then_inc(s_tail_evac, 1)
                dve.wait_ge(s_tail_evac, j + 1)
                link(dve.tensor_copy(ext[:, :, CW - 1:], buf[:, SEQ:TOK].rearrange("p (b t) -> p b t", b=NB)))
                cs = out[:, SEQ:TOK].rearrange("p (b t) -> p b t", b=NB)
                link(dve.tensor_scalar(cs, ext[:, :, 0:NT], tap[0], b, ALU.mult, ALU.add))
                for t in range(1, CW):
                    ins = dve.scalar_tensor_tensor(cs, ext[:, :, t:t + NT], tap[t], cs, ALU.mult, ALU.add)
                    if t < CW - 1:
                        link(ins)
                ins.then_inc(s_conv, 1)

            for kd in range(KD):
                dve.wait_ge(s_xh, kd + 1)
                dve.tensor_tensor(hT_l[:, kd, :], k.hT[:, kd, :], hT_h[:, kd, :].bitcast(F32), ALU.subtract)\
                   .then_inc(s_xl, 1)
            for j in range(12):
                dve.wait_ge(s_used, PER * (j + 1))
                if j < 8:
                    if j >= 2:
                        dve.wait_ge(s_conv, j - 1)
                    dve.tensor_scalar(chunks(pre[j % 2][:]), banks(j), k.cols[:, k.c_b_qk + j:k.c_b_qk + j + 1],
                                      None, ALU.add).then_inc(s_evac, 1)
                    dve.wait_ge(s_evac, j + 1)
                    convolve(j)
                else:
                    if j == 8:
                        dve.wait_ge(s_silu, 8)
                    bcol = k.cols[:, k.c_b_q + j - 8:k.c_b_q + j - 7]
                    dve.tensor_scalar(chunks(k.aq[:, j - 8, :]), banks(j), bcol, QSCALE, ALU.add, ALU.mult)\
                       .then_inc(s_evac, 1)
            dve.wait_ge(s_used, NBK)
            for kd in range(KD - 3):
                dve.tensor_tensor(k.hT[:, kd, :], hT_h[:, kd, :].bitcast(F32), hT_l[:, kd, :].bitcast(F32), ALU.add)


def stage_gates(k):
    nc, ps = k.nc, k.ps
    off = k.RING_OFF

    def row(name, n=TOK):
        nonlocal off
        t = k.at(name, off, [MH, n])
        off += n * 4
        return t

    u, f_m = row("gate_u"), row("gate_F")
    lf = k.at("gate_lf", k.SPARE_OFF, [MH, TOK])
    reset = k.at("gate_reset", k.SPARE_OFF + TOK * 4, [MH, TOK])
    neg_m = k.neg_m
    s_zero, s_turn, s_copy, s_chain = k.sem("gate_zeroed"), k.sem("gate_turned"), k.sem("gate_copied"), k.sem("gate_chain")
    s_abs, s_soft, s_args, s_exp, s_m0 = (k.sem("gate_abs"), k.sem("gate_softplus"), k.sem("gate_args"),
                                          k.sem("gate_exps"), k.sem("m0_loaded"))
    s_cols, s_cols_evac, s_m_out = k.sem("gate_cols"), k.sem("gate_cols_evac"), k.m_stored
    s_const = k.sem("gate_constants")

    def per_sample(t):
        return t[:, SEQ:TOK].rearrange("h (b t) -> h b t", b=NB)

    def per_chunk(t):
        return t[:, 0:SEQ].rearrange("h (c t) -> h c t", c=QT)

    with nc.Block() as block:

        @block.sync
        def _(sp):
            sp.dma_start(k.m_s0[:], k.state_m[0].rearrange("b h -> h b")).then_inc(s_m0, 16)
            sp.wait_ge(s_args, 1)
            sp.dma_start(k.o_m[0][0].rearrange("b h -> h b"), k.m_c[:, QT:QT + 1]).then_inc(s_m_out, 16)
            sp.dma_start(k.o_m[1][0].rearrange("b h -> h b"), k.m_s1[:]).then_inc(s_m_out, 16)
            sp.wait_ge(s_m_out, 32)

        @block.gpsimd
        def _(pool):
            pool.memset(reset[:], 1.0).then_inc(s_const, 1)
            pool.memset(k.select[:], 0.0).then_inc(s_const, 1)
            pool.memset(k.packed[:], 0.0).then_inc(s_const, 1)
            pool.wait_ge(s_const, 3)
            pool.memset(per_chunk(reset)[:, :, 0:1], 0.0)
            pool.memset(per_sample(reset)[:, :, 0:1], 0.0)
            for q in range(2):
                rows = k.select[32 * q:32 * q + MH]
                ins = pool.affine_select(out=rows, in_=rows, compare_op=ALU.not_equal, fill=1.0, base=0,
                                         pattern=[[-1, MH], [0, P]], channel_multiplier=1)
            ins.then_inc(s_const, 1)

        @block.tensor
        def _(pe):
            for which, col in enumerate((R_IG, R_FG)):
                for tt in range(TT):
                    r = P if tt < QT else NS_TOK
                    mm = pe.transpose(ps[0:MH, 3 * which + tt // 4, (tt % 4) * P:(tt % 4) * P + r],
                                      k.rows[0:r, tt, col:col + MH], k.ident[0:r, 0:r])
                mm.then_inc(s_turn, 1)
            pe.wait_ge(s_exp, 5)
            pe.wait_ge(s_args, 3)
            pe.wait_ge(s_const, 4)
            for tt in range(TT):
                r = P if tt < QT else NS_TOK
                pe.transpose(ps[0:r, tt // 4, (tt % 4) * P:(tt % 4 + 1) * P],
                             k.packed[:, tt * P:tt * P + r], k.ident[:])
            for h in range(MH):
                mm = pe.matmul(ps[:, 6, 16 * h:16 * h + 16], k.select[0:MH, h, :], k.decay_row[:],
                               start=True, stop=True)
            mm.then_inc(s_cols, 1)

        @block.scalar
        def _(act):
            act.wait_ge(s_abs, 1)
            act.activation(u[:], u[:], ACT.Exp, scale=-1.0).then_inc(s_soft, 1)
            act.wait_ge(s_soft, 1)
            act.activation(u[:], u[:], ACT.Ln, bias=1.0).then_inc(s_soft, 1)
            act.wait_ge(s_args, 3)
            act.wait_ge(s_const, 4)
            act.activation(k.packed[32:32 + MH, :], lf[:], ACT.Exp).then_inc(s_exp, 1)
            act.activation(k.packed[64:64 + MH, :], f_m[:], ACT.Exp, scale=-1.0).then_inc(s_exp, 1)
            act.activation(k.packed[96:96 + MH, :], reset[:], ACT.Exp).then_inc(s_exp, 1)
            act.activation(k.decay_row[:, 0:QT], k.decay_row[:, 0:QT], ACT.Exp).then_inc(s_exp, 1)
            act.activation(k.decay_row[:, QT:], k.decay_row[:, QT:], ACT.Exp).then_inc(s_exp, 1)

        @block.vector
        def _(dve):
            link = Chain(dve, s_chain)
            dve.wait_ge(s_turn, 2)
            ig, fg = f_m, lf
            for which, dst in enumerate((ig, fg)):
                dve.tensor_copy(dst[:, 0:512], ps[0:MH, 3 * which, :])
                dve.tensor_copy(dst[:, 512:SEQ], ps[0:MH, 3 * which + 1, :])
                ins = dve.tensor_copy(dst[:, SEQ:], ps[0:MH, 3 * which + 2, 0:NS_TOK])
            link(ins)
            dve.scalar_tensor_tensor(u[:], fg[:], -1.0, fg[:], ALU.mult, ALU.max).then_inc(s_abs, 1)
            dve.wait_ge(s_soft, 2)
            link(dve.scalar_tensor_tensor(lf[:], fg[:], 0.0, u[:], ALU.min, ALU.subtract))
            dve.wait_ge(s_const, 4)
            link(dve.tensor_tensor_scan(u[:], reset[:], lf[:], 0.0, ALU.mult, ALU.add))
            link(dve.tensor_tensor(lf[:], ig[:], u[:], ALU.subtract))
            link(dve.tensor_copy(f_m[:], u[:]))
            link(dve.tensor_copy(u[:], lf[:]))
            m_run = neg_m
            link(dve.memset(k.m_c[:, 0:1], NEG))
            for c in range(QT):
                t = slice(c * P, (c + 1) * P)
                link(dve.tensor_tensor_scan(m_run[:, t], u[:, t], u[:, t], k.m_c[:, c:c + 1], ALU.max, ALU.max))
                link(dve.tensor_tensor(k.m_c[:, c + 1:c + 2], f_m[:, t][:, P - 1:P], m_run[:, t][:, P - 1:P], ALU.add))
            dve.wait_ge(s_m0, 16)
            su, sm = per_sample(u), per_sample(m_run)
            for t in range(NT):
                before = k.m_s0[:].unsqueeze(2) if t == 0 else sm[:, :, t - 1:t]
                link(dve.tensor_tensor(sm[:, :, t:t + 1], before, su[:, :, t:t + 1], ALU.max))
            dve.tensor_tensor(k.m_s1[:].unsqueeze(2), per_sample(f_m)[:, :, NT - 1:], sm[:, :, NT - 1:], ALU.add)\
               .then_inc(s_args, 1)
            dve.wait_ge(s_args, 1)
            def both(out, in0, in1, op):
                dve.tensor_tensor(per_chunk(out), in0[0].to_broadcast([MH, QT, P]), in1[0].to_broadcast([MH, QT, P]), op)
                return dve.tensor_tensor(per_sample(out), in0[1].to_broadcast([MH, NB, NT]),
                                         in1[1].to_broadcast([MH, NB, NT]), op)

            m_start = (k.m_c[:, 0:QT].unsqueeze(2), k.m_s0[:].unsqueeze(2))
            m_all = (per_chunk(m_run), sm)
            m_last = (per_chunk(m_run)[:, :, P - 1:P], sm[:, :, NT - 1:])
            both(lf, m_start, m_all, ALU.subtract)
            both(reset, (per_chunk(u), su), m_last, ALU.subtract)
            dve.tensor_tensor(k.decay_row[:, 0:QT].unsqueeze(2), m_start[0], m_last[0], ALU.subtract)
            dve.tensor_tensor(k.decay_row[:, QT:].unsqueeze(2), m_start[1], m_last[1], ALU.subtract)
            dve.tensor_copy(k.packed[0:MH, :], u[:])
            dve.tensor_tensor(f_m[:], f_m[:], m_run[:], ALU.add).then_inc(s_args, 1)
            dve.wait_ge(s_args, 2)
            dve.tensor_scalar(neg_m[:], m_run[:], -1.0, None, ALU.mult).then_inc(s_args, 1)
            dve.wait_ge(s_cols, 1)
            for tt in range(TT):
                r = P if tt < QT else NS_TOK
                src = ps[0:r, tt // 4, (tt % 4) * P:(tt % 4 + 1) * P].rearrange("p (q x) -> p q x", q=4)[:, :, 0:MH]
                dve.tensor_copy(k.gate_cols[0:r, tt, :, :], src)
            dve.tensor_copy(k.decay[:], ps[:, 6, 0:64].rearrange("p (h c) -> p h c", h=MH)).then_inc(s_cols_evac, 1)


def stage_mlstm(k):
    nc, ps = k.nc, k.ps
    V1 = MD + 1
    off = k.SPARE_OFF

    def work(name, shape):
        nonlocal off
        t = k.at(name, off, shape)
        size = 4
        for n in shape[1:]:
            size *= n
        off += (size + 31) // 32 * 32
        return t

    weight = work("mlstm_E", [P, MH, P])
    wt, kws, qi = [work("mlstm_W0", [P, MH, P])], [work("mlstm_Kw0", [P, MH, P])], [work("mlstm_Qi0", [P, MH, P])]
    assert off <= k.HT_OFF
    C_s = k.at("C_samples", k.RING_OFF, [P, NB * MH, V1])
    off = k.WORK_OFF
    for pair_, name in ((wt, "mlstm_W1"), (kws, "mlstm_Kw1"), (qi, "mlstm_Qi1")):
        pair_.append(work(name, [P, MH, P]))
    hn = work("mlstm_hn", [P, MH, P])
    C_p = work("C_prompt", [P, MH, V1])
    q_b = k.qk[:, 0:MH, 0:NB * (NS_TOK + NT)]
    stats, mv = work("ln_stats", [P, MH, 6]), work("ln_mean_var", [P, MH, 2])
    den, r, tmp = work("ln_den", [P, MH]), work("ln_r", [P, MH]), work("ln_tmp", [P, MH])
    n_cols, n_rows = work("n_cols", [P, NB * MH + MH]), work("n_rows", [NB * MH + MH, P])
    n_in = work("n_in", [NB * MH, P])
    block_of, ws_b = work("in_sample", [NS_TOK, NB]), work("ws_by_sample", [NS_TOK, NB, MH])
    assert off <= k.TOP
    n_c, n_n, s_zero = k.sem("C_loaded"), k.sem("n_loaded"), k.sem("mlstm_zeroed")
    s_bcm, s_bc, s_st, s_kt = k.sem("m_broadcast"), k.sem("inter_broadcast"), k.sem("qk_product"), k.sem("keys_turned")
    s_exp, s_mask, s_wt, s_kws, s_qi = (k.sem("E_exps"), k.sem("E_masked"), k.sem("W_ready"), k.sem("Kw_ready"),
                                        k.sem("Qi_ready"))
    s_num, s_dc, s_c, s_var, s_root = (k.sem("num_product"), k.sem("dC_product"), k.sem("C_updated"),
                                       k.sem("var_ready"), k.sem("root_ready"))
    s_hn, s_hnt, s_at, s_out, s_chain = (k.sem("hn_ready"), k.sem("hn_turned"), k.sem("aT_ready"),
                                         k.states_stored, k.sem("mlstm_chain"))
    s_nt, s_nr = k.sem("n_turned"), k.sem("n_rows_ready")
    BCM, BCI, ST, KT, NUM, DC = 0, 1, 2, 3, 4, 6
    S = QT

    def tokens(c):
        return (P if c < S else NS_TOK), slice(c * P, min((c + 1) * P, TOK))

    def heads(bank, n):
        return ps[:, bank, 0:MH * n].rearrange("p (h t) -> p h t", h=MH)

    def pair(bank, h):
        return ps[:, bank + h // 2, (h % 2) * V1:(h % 2 + 1) * V1]

    with nc.Block() as block:

        @block.sync
        def _(sp):
            sp.dma_start(n_in[:], k.state_n[0].rearrange("b h k -> (b h) k")).then_inc(n_n, 16)
            sp.dma_start(C_s[:, :, 0:MD], k.state_C[0].rearrange("b h k v -> k (b h) v")).then_inc(n_c, 16)
            sp.wait_ge(s_c, MH * QT)
            sp.dma_start(k.o_C[0][0, 0].rearrange("h k v -> k h v"), C_p[:, :, 0:MD]).then_inc(s_out, 16)
            sp.wait_ge(s_c, MH * (QT + NB))
            sp.dma_start(k.o_C[1][0].rearrange("b h k v -> k (b h) v"), C_s[:, :, 0:MD]).then_inc(s_out, 16)
            sp.wait_ge(s_nr, 1)
            sp.dma_start(k.o_n[1][0].rearrange("b h k -> (b h) k"), n_rows[0:NB * MH, :]).then_inc(s_out, 16)
            sp.dma_start(k.o_n[0][0, 0], n_rows[NB * MH:, :]).then_inc(s_out, 16)
            sp.wait_ge(s_out, 64)

        @block.gpsimd
        def _(pool):
            pool.memset(C_p[:], 0.0).then_inc(s_zero, 1)
            pool.memset(block_of[:], 1.0).then_inc(s_zero, 1)
            pool.wait_ge(s_zero, 2)
            pool.affine_select(out=block_of[:], in_=block_of[:], compare_op=ALU.is_ge, fill=0.0, base=0,
                               pattern=[[-NT, NB]], channel_multiplier=1).then_inc(s_zero, 1)
            pool.wait_ge(s_zero, 3)
            pool.affine_select(out=block_of[:], in_=block_of[:], compare_op=ALU.is_ge, fill=0.0, base=NT - 1,
                               pattern=[[NT, NB]], channel_multiplier=-1).then_inc(s_zero, 1)
            for c in range(S):
                pool.wait_ge(s_exp, MH * (c + 1))
                if c == 4:
                    pool.wait_ge(s_num, 3)
                    pool.wait_ge(s_qi, 3)
                    pool.memset(q_b, 0.0).then_inc(s_zero, 1)
                pool.affine_select(out=weight[:], in_=weight[:], compare_op=ALU.is_ge, fill=0.0, base=0,
                                   pattern=[[0, MH], [1, P]], channel_multiplier=-1).then_inc(s_mask, 1)
            pool.wait_ge(s_exp, MH * (S + 1))
            e = weight[0:NS_TOK, :, 0:NS_TOK]
            pool.affine_select(out=e, in_=e, compare_op=ALU.is_ge, fill=0.0, base=0,
                               pattern=[[0, MH], [1, NS_TOK]], channel_multiplier=-1).then_inc(s_mask, 1)
            pool.wait_ge(s_mask, S + 1)
            for h in range(MH):
                eh = weight[0:NS_TOK, h, 0:NS_TOK].rearrange("p (b t) -> p b t", b=NB)
                ins = pool.affine_select(out=eh, in_=eh, compare_op=ALU.is_ge, fill=0.0, base=0,
                                         pattern=[[-NT, NB], [0, NT]], channel_multiplier=1)
            ins.then_inc(s_mask, 1)

        @block.tensor
        def _(pe):
            pe.wait_ge(n_n, 16)
            pe.transpose(ps[:, DC, 0:NB * MH], n_in[:], k.ident[0:NB * MH, 0:NB * MH]).then_inc(s_nt, 1)

            def ahead(c):
                n, t = tokens(c)
                if c:
                    pe.wait_ge(s_exp, MH * c)
                for h in range(MH):
                    mm = pe.matmul(heads(BCM, n)[:, h], k.select[0:MH, h, :], k.neg_m[:, t], start=True, stop=True)
                mm.then_inc(s_bcm, 1)
                if c:
                    pe.wait_ge(s_qi, c)
                for h in range(MH):
                    mm = pe.matmul(heads(BCI, n)[:, h], k.select[32:32 + MH, h, :], k.packed[32:32 + MH, t],
                                   start=True, stop=True)
                mm.then_inc(s_bc, 1)
                if c:
                    pe.wait_ge(s_wt, c)
                for h in range(MH):
                    mm = pe.matmul(heads(ST, n)[0:n, h], k.qk[:, MH + h, t], k.qk[:, h, t], start=True, stop=True)
                mm.then_inc(s_st, 1)
                if c:
                    pe.wait_ge(s_kws, c)
                for h in range(MH):
                    mm = pe.transpose(ps[0:n, KT, h * P:(h + 1) * P], k.qk[:, MH + h, t], k.ident[:])
                mm.then_inc(s_kt, 1)

            def turn_out(c, bank):
                n, _ = tokens(c)
                pe.wait_ge(s_hn, c + 1)
                for h in range(MH):
                    mm = pe.transpose(heads(bank, n)[:, h], hn[0:n, h, :], k.ident[0:n, 0:n])
                mm.then_inc(s_hnt, 1)

            ahead(0)
            for c in range(S + 1):
                n, t = tokens(c)
                if c < S:
                    ahead(c + 1)
                if c:
                    pe.wait_ge(s_c, MH * c)
                    turn_out(c - 1, DC + 1)
                pe.wait_ge(s_wt, c + 1)
                pe.wait_ge(s_qi, c + 1)
                if c == 0:
                    pe.wait_ge(s_zero, 1)
                if c == S:
                    pe.wait_ge(n_c, 16)
                    pe.wait_ge(s_nt, 2)
                for h in range(MH):
                    pe.matmul(pair(NUM, h)[0:n], wt[c % 2][0:n, h, 0:n], k.v_aug[0:n, c, h, :], start=True, stop=False)
                    if c < S:
                        mm = pe.matmul(pair(NUM, h), qi[c % 2][:, h, :], C_p[:, h, :], start=False, stop=True)
                    else:
                        for b in range(NB):
                            mm = pe.matmul(pair(NUM, h)[0:n], q_b[:, h, b * NS_TOK:(b + 1) * NS_TOK],
                                           C_s[:, b * MH + h, :], start=False, stop=(b == NB - 1))
                mm.then_inc(s_num, 1)
                if c:
                    pe.wait_ge(s_at, c)
                if c < S:
                    pe.wait_ge(s_kws, c + 1)
                    if c == 0:
                        pe.wait_ge(s_nt, 2)
                    for h in range(MH):
                        mm = pe.matmul(pair(DC, h), kws[c % 2][:, h, :], k.v_aug[:, c, h, :], start=True, stop=True)
                    mm.then_inc(s_dc, 1)
                else:
                    for b in range(NB):
                        pe.wait_ge(s_kws, c + b + 1)
                        pe.wait_ge(s_c, MH * (S + b))
                        for h in range(MH):
                            mm = pe.matmul(pair(DC, h), kws[c % 2][0:n, h, :], k.v_aug[0:n, c, h, :], start=True,
                                           stop=True)
                        mm.then_inc(s_dc, 1)
            turn_out(S, KT)
            pe.wait_ge(s_c, MH * (S + NB))
            pe.wait_ge(s_at, S + 1)
            pe.wait_ge(s_nt, 3)
            pe.transpose(ps[0:NB * MH + MH, KT, 0:P], n_cols[:], k.ident[:]).then_inc(s_nt, 1)

        @block.scalar
        def _(act):
            def exponentials(c):
                n, t = tokens(c)
                act.wait_ge(s_bcm, c + 1)
                if c:
                    act.wait_ge(s_wt, c)
                for h in range(MH):
                    act.activation(weight[0:n, h, 0:n], heads(BCM, n)[0:n, h], ACT.Exp,
                                   bias=k.gate_cols[0:n, c, 0, h:h + 1]).then_inc(s_exp, 1)

            def root(c):
                n, t = tokens(c)
                act.wait_ge(s_var, c + 1)
                act.activation(tmp[0:n], tmp[0:n], ACT.Sqrt).then_inc(s_root, 1)

            exponentials(0)
            exponentials(1)
            for c in range(S + 1):
                root(c)
                if c + 2 <= S:
                    exponentials(c + 2)

        @block.vector
        def _(dve):
            link = Chain(dve, s_chain)
            dve.wait_ge(s_nt, 1)
            dve.tensor_copy(C_s[:, :, MD], ps[:, DC, 0:NB * MH]).then_inc(s_nt, 1)

            def scaled_queries(c):
                n, t = tokens(c)
                dve.wait_ge(s_bc, c + 1)
                if c < S:
                    dve.tensor_tensor(qi[c % 2][:, :, :], k.qk[:, 0:MH, t], heads(BCI, n), ALU.mult).then_inc(s_qi, 1)
                else:
                    dve.wait_ge(s_zero, 5)
                    for h in range(MH):
                        dst = q_b[:, h, :].rearrange("p (b x) -> p b x", b=NB)[:, :, 0:NT]
                        ins = dve.tensor_tensor(dst, k.qk[:, h, t].rearrange("p (b t) -> p b t", b=NB),
                                                heads(BCI, n)[:, h].rearrange("p (b t) -> p b t", b=NB), ALU.mult)
                    ins.then_inc(s_qi, 1)

            def weights(c):
                n, t = tokens(c)
                dve.wait_ge(s_st, c + 1)
                dve.wait_ge(s_mask, c + 1 if c < S else S + 2)
                dve.tensor_tensor(wt[c % 2][0:n, :, 0:n], heads(ST, n)[0:n], weight[0:n, :, 0:n], ALU.mult)\
                   .then_inc(s_wt, 1)
                dve.wait_ge(s_kt, c + 1)
                if c < S:
                    w_s = k.gate_cols[:, c, 3, :].unsqueeze(2).to_broadcast([P, MH, P])
                    dve.tensor_tensor(kws[c % 2][:, :, :], heads(KT, P), w_s, ALU.mult).then_inc(s_kws, 1)

            def sample_states():
                n, c = NS_TOK, S
                for b in range(NB):
                    ins = dve.tensor_scalar(ws_b[:, b, :], k.gate_cols[0:n, c, 3, :], block_of[:, b:b + 1], None,
                                            ALU.mult)
                link(ins)
                for b in range(NB):
                    dve.wait_ge(s_dc, S + b)
                    dve.tensor_tensor(kws[c % 2][0:n], heads(KT, P)[0:n],
                                      ws_b[:, b, :].unsqueeze(2).to_broadcast([n, MH, P]), ALU.mult)\
                       .then_inc(s_kws, 1)
                    if b == 0:
                        dve.wait_ge(s_num, S + 1)
                    dve.wait_ge(s_dc, S + b + 1)
                    for h in range(MH):
                        i = b * MH + h
                        dve.scalar_tensor_tensor(C_s[:, i, :], C_s[:, i, :], k.decay[:, h, QT + b:QT + b + 1],
                                                 pair(DC, h), ALU.mult, ALU.add).then_inc(s_c, 1)

            def layer_norm(c):
                n, t = tokens(c)
                dve.wait_ge(s_num, c + 1)
                for h in range(MH):
                    dve.bn_stats(stats[0:n, h, :], pair(NUM, h)[0:n, 0:MD])
                    ins = dve.tensor_copy(den[0:n, h:h + 1], pair(NUM, h)[0:n, MD:V1])
                link(ins)
                for h in range(MH):
                    dve.bn_aggr(mv[0:n, h, :], stats[0:n, h, :])
                link(dve.scalar_tensor_tensor(r[0:n], den[0:n], -1.0, den[0:n], ALU.mult, ALU.max))
                link(dve.tensor_tensor(den[0:n], r[0:n], k.gate_cols[0:n, c, 2, :], ALU.max))
                link(dve.reciprocal(r[0:n], den[0:n]))
                link(dve.tensor_tensor(tmp[0:n], mv[0:n, :, 1], r[0:n], ALU.mult))
                link(dve.tensor_tensor(tmp[0:n], tmp[0:n], r[0:n], ALU.mult))
                dve.tensor_scalar(tmp[0:n], tmp[0:n], EPS, None, ALU.add).then_inc(s_var, 1)
                dve.wait_ge(s_root, c + 1)
                link(dve.reciprocal(den[0:n], tmp[0:n]))
                link(dve.tensor_tensor(r[0:n], r[0:n], den[0:n], ALU.mult))
                if c:
                    dve.wait_ge(s_hnt, c)
                for h in range(MH):
                    ins = dve.tensor_scalar(hn[0:n, h, :], pair(NUM, h)[0:n, 0:MD], mv[0:n, h, 0:1], r[0:n, h:h + 1],
                                            ALU.subtract, ALU.mult)
                ins.then_inc(s_hn, 1)

            def prompt_state(c):
                dve.wait_ge(s_dc, c + 1)
                for h in range(MH):
                    dve.scalar_tensor_tensor(C_p[:, h, :], C_p[:, h, :], k.decay[:, h, c:c + 1], pair(DC, h),
                                             ALU.mult, ALU.add).then_inc(s_c, 1)

            def gated_output(c, bank):
                n, t = tokens(c)
                dve.wait_ge(s_hnt, c + 1)
                for h in range(MH):
                    ins = dve.scalar_tensor_tensor(k.aT[:, h, t], heads(bank, n)[:, h],
                                                   k.cols[:, k.c_m_norm + h:k.c_m_norm + h + 1], k.aT[:, h, t],
                                                   ALU.mult, ALU.mult)
                ins.then_inc(s_at, 1)

            scaled_queries(0)
            weights(0)
            for c in range(S + 1):
                if c:
                    layer_norm(c - 1)
                    prompt_state(c - 1)
                if c < S:
                    scaled_queries(c + 1)
                if c:
                    gated_output(c - 1, DC + 1)
                if c < S:
                    weights(c + 1)
            sample_states()
            layer_norm(S)
            gated_output(S, KT)
            dve.wait_ge(s_c, MH * (S + NB))
            dve.tensor_copy(n_cols[:, 0:NB * MH], C_s[:, :, MD])
            dve.tensor_copy(n_cols[:, NB * MH:], C_p[:, :, MD]).then_inc(s_nt, 1)
            dve.wait_ge(s_nt, 4)
            dve.tensor_copy(n_rows[:], ps[0:NB * MH + MH, KT, 0:P]).then_inc(s_nr, 1)


def stage_nsa_prompt(k):
    nc, ps = k.nc, k.ps
    NCB = SEQ // STRIDE - 1
    WT = WIN // P + 1
    LW = WT * P
    LC = 120
    off = k.CMP_END
    tables = k.at("bias_tables", off, [P, HG, SEQ + LW + LC])
    off += HG * (SEQ + LW + LC) * 4
    SLEN = SEQ + LW + 64
    job = Compress(k, "prompt", [NB], off, k.TOP, k.SPARE_OFF, (0, 1, 2))
    job_end = off + 6 * STRIDE * GD * 4
    NS = 3
    s_buf = [k.at(f"scores{i}", off + i * SLEN * 4, [P, SLEN]) for i in range(NS)]
    off += NS * SLEN * 4
    NPT = 4
    pt_buf = [k.at(f"probsT{i}", off + i * 2048, [P, 4, P]) for i in range(NPT)]
    off = max(off + NPT * 2048, job_end)
    NQ = 3
    q_pad = [k.at(f"q_beside_zeros{i}", off + i * 512, [P, P]) for i in range(NQ)]
    off += NQ * 512
    dist = k.at("distance", off, [P, SEQ])
    assert off + SEQ * 4 <= k.TOP
    off = k.SPARE_OFF + 5120
    dist_c, dist_w = k.at("distance_cmp", off, [P, LC]), k.at("distance_win", off + 512, [P, LW])
    off += 512 + LW * 4
    top = [k.at(f"row_max{i}", off + 64 * i, [P, 3]) for i in range(2)]
    neg_top = [k.at(f"row_neg_max{i}", off + 64 * i + 32, [P, 3]) for i in range(2)]
    off += 128
    sums = [k.at(f"row_sum{i}", off + 64 * i, [P, 3]) for i in range(2)]
    factor = [k.at(f"row_factor{i}", off + 64 * i + 32, [P, 3]) for i in range(2)]
    off += 128
    valid, in_group = k.at("has_block", off, [P, 1]), k.at("in_group", off + 32, [P, NG])
    off += 64
    assert off <= k.HT_OFF
    units = [(g, qt, i) for g in range(NG) for qt in range(QT) for i in range(HG)]
    NU = len(units)

    def key_tiles(qt):
        first = max(0, qt - WT + 1)
        return ([("slc", kt, kt * P, P) for kt in range(qt + 1)]
                + [("win", kt, SEQ + (kt - first) * P, P) for kt in range(first, qt + 1)]
                + [("cmp", 0, SEQ + LW, NCB)])

    groups = []
    for n, (g, qt, i) in enumerate(units):
        tiles = key_tiles(qt)
        for a in range(0, len(tiles), 4):
            groups.append((n, tiles[a:a + 4], a + 4 >= len(tiles)))
    first_group = [min(x for x, gr in enumerate(groups) if gr[0] == n) for n in range(NU)] + [len(groups)]
    def evacs_before(which, x):
        return (x + 1 - which) // 2

    s_tab, s_gate = k.sem("tables_ready"), k.sem("branch_gates_ready")
    s_a, s_b = k.sem("slc_scores"), k.sem("win_cmp_scores")
    s_ta, s_tb, s_neg = k.sem("slc_biased"), k.sem("win_cmp_biased"), k.sem("neg_max_ready")
    s_exp, s_fac, s_p, s_chain = k.sem("probs_exp"), k.sem("factor_ready"), k.sem("probs_ready"), k.sem("nsa_chain")
    s_turn, s_pv, s_out = k.sem("probs_turned"), k.sem("pv_product"), k.sem("nsa_out_evac")
    s_ev = [k.sem("probsT_evac_act"), k.sem("probsT_evac_dve")]
    s_iota, s_q = k.sem("distances"), k.sem("q_pad_ready")

    s_mask = k.sem("distances_masked")

    with nc.Block() as block:

        @block.sync
        def _(sp):
            for u in range(2):
                src = (k.o_k_cmp, k.o_v_cmp)[u][0][0, 0]
                sp.dma_start(job.x[u][0:job.strides(u), :], src.rearrange("(n j) g d -> n (j g d)", j=STRIDE))\
                  .then_inc(job.s_x[u], 16)
            job.load_weights(sp)

        @block.gpsimd
        def _(pool):
            job.zero(pool)
            io = dict(allow_small_or_imprecise_dtypes=True)
            pool.iota(dist[:], pattern=[[1, SEQ]], base=-(SEQ - P), channel_multiplier=-1, **io).then_inc(s_iota, 1)
            pool.iota(dist_w[:], pattern=[[1, LW]], base=-(LW - P), channel_multiplier=-1, **io).then_inc(s_iota, 1)
            pool.iota(dist_c[:], pattern=[[STRIDE, LC]], base=CBLK - 1 - 56 * STRIDE, channel_multiplier=-1,
                      **io).then_inc(s_iota, 1)
            pool.memset(in_group[:], 1.0)
            pool.tensor_copy(k.kT_last[:], k.kT[:, :, SEQ:TOK])
            pool.memset(valid[:], 1.0).then_inc(s_iota, 1)
            pool.wait_ge(s_iota, 4)
            pool.affine_select(out=dist[:], in_=dist[:], compare_op=ALU.is_ge, fill=NEG, base=SEQ - P,
                               pattern=[[-1, SEQ]], channel_multiplier=1).then_inc(s_mask, 1)
            pool.affine_select(out=dist_c[:], in_=dist_c[:], compare_op=ALU.is_ge, fill=NEG,
                               base=56 * STRIDE - CBLK + 1, pattern=[[-STRIDE, LC]], channel_multiplier=1)\
                .then_inc(s_mask, 1)
            pool.affine_select(out=dist_w[:], in_=dist_w[:], compare_op=ALU.is_ge, fill=NEG, base=WIN,
                               pattern=[[-1, LW]], channel_multiplier=1).then_inc(s_mask, 1)
            pool.wait_ge(s_mask, 3)
            pool.affine_select(out=dist_w[:], in_=dist_w[:], compare_op=ALU.is_ge, fill=NEG, base=0,
                               pattern=[[1, LW]], channel_multiplier=-1).then_inc(s_mask, 1)
            pool.affine_select(out=valid[:], in_=valid[:], compare_op=ALU.is_ge, fill=0.0, base=-(CBLK - 1),
                               pattern=[[0, 1]], channel_multiplier=1).then_inc(s_iota, 1)
            pool.affine_select(out=in_group[:, 0:1], in_=in_group[:, 0:1], compare_op=ALU.is_ge, fill=0.0, base=HD - 1,
                               pattern=[[0, 1]], channel_multiplier=-1).then_inc(s_iota, 1)
            pool.affine_select(out=in_group[:, 1:2], in_=in_group[:, 1:2], compare_op=ALU.is_ge, fill=0.0, base=-HD,
                               pattern=[[0, 1]], channel_multiplier=1).then_inc(s_iota, 1)

            def pad_query(n):
                g, qt, i = units[n]
                if n >= NQ:
                    pool.wait_ge(s_b, n - NQ + 1)
                pool.tensor_scalar(q_pad[n % NQ][:], k.aq[:, i, qt * P:(qt + 1) * P], in_group[:, g:g + 1], None,
                                   ALU.mult).then_inc(s_q, 1)

            job.first_half(pool, 0)
            job.first_half(pool, 1)
            pool.wait_ge(s_iota, 7)
            for n in range(NU):
                pad_query(n)

        @block.tensor
        def _(pe):
            def scores(n):
                g, qt, i = units[n]
                q = q_pad[n % NQ][:]
                pe.wait_ge(s_q, n + 1)
                if n:
                    pe.wait_ge(s_ta, n)
                keys = (qt + 1) * P
                for a in range(0, keys, 512):
                    m = min(512, keys - a)
                    mm = pe.matmul(ps[:, a // 512, 0:m], q, k.kT[:, 0, a:a + m], start=True, stop=True)
                mm.then_inc(s_a, 1)
                if n:
                    pe.wait_ge(s_tb, n)
                first = max(0, qt - WT + 1) * P
                for a in range(0, keys - first, 512):
                    m = min(512, keys - first - a)
                    pe.matmul(ps[:, 2 + a // 512, 0:m], q, k.kT[:, 1, first + a:first + a + m],
                              start=True, stop=True)
                pe.matmul(ps[:, 3, P:P + NCB], q, k.kc_p[:, 0:NCB], start=True, stop=True).then_inc(s_b, 1)

            def turn(x):
                n, tiles, _ = groups[x]
                pe.wait_ge(s_p, n + 1)
                if x >= 2:
                    pe.wait_ge(s_ev[x % 2], evacs_before(x % 2, x))
                for c, (_, _, col, m) in enumerate(tiles):
                    mm = pe.transpose(ps[0:m, 4 + x % 2, c * P:(c + 1) * P], s_buf[n % NS][:, col:col + m], k.ident[:])
                mm.then_inc(s_turn, 1)

            def pv(x):
                n, tiles, last = groups[x]
                g, qt, i = units[n]
                pe.wait_ge(s_ev[x % 2], evacs_before(x % 2, x) + 1)
                if x == first_group[n] and n >= 2:
                    pe.wait_ge(s_out, n - 1)
                for c, (branch, kt, _, m) in enumerate(tiles):
                    cols = slice(g * HD, (g + 1) * HD)
                    if branch == "cmp":
                        v = k.vc_p[0:m, cols]
                    else:
                        r = R_VS if branch == "slc" else R_VW
                        v = k.rows[:, kt, r + g * HD:r + (g + 1) * HD]
                    mm = pe.matmul(ps[cols, 6 + n % 2, 0:P], v, pt_buf[x % NPT][0:m, c, :],
                                   start=(x == first_group[n] and c == 0), stop=(last and c == len(tiles) - 1))
                mm.then_inc(s_pv, 1)

            job.turn(pe, 0)
            job.turn(pe, 1)
            job.map(pe, 0)
            job.map(pe, 1)
            pe.wait_ge(job.s_evac, 2)
            scores(0)
            scores(1)
            for n in range(NU):
                for x in range(first_group[n], first_group[n + 1]):
                    turn(x)
                    if x > first_group[n]:
                        pv(x - 1)
                if n + 2 < NU:
                    scores(n + 2)
                pv(first_group[n + 1] - 1)

        def evacuate(eng, copy, which, x):
            n, tiles, last = groups[x]
            eng.wait_ge(s_turn, x + 1)
            if x >= NPT:
                eng.wait_ge(s_pv, x - NPT + 1)
            full = sum(1 for t in tiles if t[3] == P)
            ins = None
            if full:
                ins = copy(pt_buf[x % NPT][:, 0:full, :].rearrange("p c q -> p (c q)"), ps[:, 4 + x % 2, 0:full * P])
            if full < len(tiles):
                m = tiles[full][3]
                ins = copy(pt_buf[x % NPT][0:m, full, :], ps[0:m, 4 + x % 2, full * P:(full + 1) * P])
            ins.then_inc(s_ev[which], 1)

        @block.scalar
        def _(act):
            def finish(n):
                g, qt, i = units[n]
                rows = slice(g * HD, (g + 1) * HD)
                act.wait_ge(s_pv, first_group[n + 1])
                act.copy(k.bT[rows, i, qt * P:(qt + 1) * P], ps[rows, 6 + n % 2, 0:P]).then_inc(s_out, 1)

            for r, tiles in ((P, slice(0, QT)), (NS_TOK, slice(QT, TT))):
                g_pre = k.rows[0:r, tiles, R_G:R_END].rearrange("p t (h b) -> p t h b", h=NH)
                act.activation(k.gates[0:r, tiles, :, 0:2], g_pre[:, :, :, 1:3], ACT.Sigmoid)
                ins = act.activation(k.gates[0:r, tiles, :, 2:3], g_pre[:, :, :, 0:1], ACT.Sigmoid)
            ins.then_inc(s_gate, 1)

            def exponentials(n):
                g, qt, i = units[n]
                s = s_buf[n % NS]
                act.wait_ge(s_neg, n + 1)
                for br, (a, m) in enumerate(((0, (qt + 1) * P), (SEQ, min(qt + 1, WT) * P), (SEQ + LW, NCB))):
                    ins = act.activation(s[:, a:a + m], s[:, a:a + m], ACT.Exp, bias=neg_top[n % 2][:, br:br + 1],
                                         accum_out=sums[n % 2][:, br:br + 1])
                ins.then_inc(s_exp, 1)

            job.copy_second(act, 0)
            job.copy_second(act, 1)
            job.keep(act, 0)
            job.keep(act, 1)
            exponentials(0)
            for n in range(NU):
                own = [x for x in range(first_group[n], first_group[n + 1]) if x % 2 == 0]
                for x in own[:1]:
                    evacuate(act, act.copy, 0, x)
                if n + 1 < NU:
                    exponentials(n + 1)
                for x in own[1:]:
                    evacuate(act, act.copy, 0, x)
                finish(n)

        @block.vector
        def _(dve):
            link = Chain(dve, s_chain)
            dve.wait_ge(s_mask, 4)
            dve.wait_ge(s_iota, 5)
            for i in range(HG):
                dve.tensor_scalar(tables[:, i, 0:SEQ], dist[:], SLOPES[i], None, ALU.mult)
                dve.tensor_scalar(tables[:, i, SEQ:SEQ + LW], dist_w[:], SLOPES[i], None, ALU.mult)
                dve.tensor_scalar(tables[:, i, SEQ + LW:], dist_c[:], SLOPES[i], None, ALU.mult).then_inc(s_tab, 1)
            job.second_half_and_sums(dve, 0)
            job.second_half_and_sums(dve, 1)
            job.pool_pair(dve, 0)
            job.pool_pair(dve, 1)
            dve.wait_ge(s_tab, HG)
            dve.wait_ge(s_gate, 1)

            def biased(n):
                g, qt, i = units[n]
                s, b = s_buf[n % NS], n % 2
                if n == NU // 2:
                    link(dve.tensor_scalar(tables[:], tables[:], 2.0 ** -HG, None, ALU.mult))
                tab = tables[:, i, :]
                keys = (qt + 1) * P
                win = min(qt + 1, WT) * P
                if n >= NS:
                    dve.wait_ge(s_turn, first_group[n - NS + 1])
                dve.wait_ge(s_a, n + 1)
                two = ps[:, 0:2, :].rearrange("p a n -> p (a n)")
                dve.tensor_tensor_reduce(s[:, 0:keys], two[:, 0:keys], tab[:, SEQ - keys:SEQ], 1.0, 3 * NEG,
                                         ALU.add, ALU.max, top[b][:, 0:1]).then_inc(s_ta, 1)
                dve.wait_ge(s_b, n + 1)
                two = ps[:, 2:4, :].rearrange("p a n -> p (a n)")
                dve.tensor_tensor_reduce(s[:, SEQ:SEQ + win], two[:, 0:win], tab[:, SEQ + LW - win:SEQ + LW], 1.0,
                                         3 * NEG, ALU.add, ALU.max, top[b][:, 1:2])
                dve.tensor_tensor_reduce(s[:, SEQ + LW:SEQ + LW + NCB], ps[:, 3, P:P + NCB],
                                         tab[:, SEQ + LW + 56 - 8 * qt:][:, 0:NCB], 1.0, 3 * NEG, ALU.add, ALU.max,
                                         top[b][:, 2:3]).then_inc(s_tb, 1)
                dve.wait_ge(s_tb, n + 1)
                dve.tensor_scalar(neg_top[b][:], top[b][:], -1.0, None, ALU.mult).then_inc(s_neg, 1)

            def scaled(n):
                g, qt, i = units[n]
                s, b, h = s_buf[n % NS], n % 2, g * HG + i
                keys = (qt + 1) * P
                dve.wait_ge(s_exp, n + 1)
                link(dve.reciprocal(factor[b][:], sums[b][:]))
                ins = dve.tensor_tensor(factor[b][:], factor[b][:], k.gates[:, qt, h, :], ALU.mult)
                if qt == 0:
                    link(ins)
                    ins = dve.tensor_tensor(factor[b][:, 2:3], factor[b][:, 2:3], valid[:], ALU.mult)
                ins.then_inc(s_fac, 1)
                dve.wait_ge(s_fac, n + 1)
                win = min(qt + 1, WT) * P
                dve.tensor_scalar(s[:, 0:keys], s[:, 0:keys], factor[b][:, 0:1], None, ALU.mult)
                dve.tensor_scalar(s[:, SEQ:SEQ + win], s[:, SEQ:SEQ + win], factor[b][:, 1:2], None, ALU.mult)
                dve.tensor_scalar(s[:, SEQ + LW:SEQ + LW + NCB], s[:, SEQ + LW:SEQ + LW + NCB], factor[b][:, 2:3],
                                  None, ALU.mult).then_inc(s_p, 1)

            biased(0)
            scaled(0)
            for n in range(NU):
                if n + 1 < NU:
                    biased(n + 1)
                for x in range(first_group[n], first_group[n + 1]):
                    if x % 2 == 1:
                        evacuate(dve, dve.tensor_copy, 1, x)
                if n + 1 < NU:
                    scaled(n + 1)


def stage_nsa_samples(k):
    nc, ps = k.nc, k.ps
    HALF = NB // 2
    R = NH * NT
    ROW = STRIDE * GD
    NC = NSUB - 1
    SLC, SNEW, WINC, WNEW, CMP = 0, PAST, PAST + NS_TOK, PAST + NS_TOK + WIN, PAST + 2 * NS_TOK + WIN
    WA = WIN // P
    low = k.SPARE_OFF
    rel = k.at("slc_distance", low, [P, PAST])
    assert low + PAST * 4 <= k.HT_OFF
    off = k.KT_OFF
    q_pad = k.at("sample_q_pad", off, [P, NB, R])
    off += NB * R * 4
    new_bias = k.at("new_bias", off, [P, 2, NS_TOK])
    off += 256
    same = k.at("same_token", off, [P, P])
    off += 512
    token_of = k.at("token_of_row", off, [NS_TOK, 2, P])
    off += 1024
    rel_c = k.at("cmp_distance", off, [P, P])
    off += 512
    before = k.at("block_before", off, [P, NBLK, NBLK])
    off += NBLK * NBLK * 4
    assert off <= k.CMP_OFF
    off = k.QK_OFF
    score = k.at("sample_scores", off, [P, CMP + P])
    off += (CMP + P) * 4
    NX = 4
    x = [k.at(f"sample_rows{i}", (off if i < 2 else k.AQ_OFF) + i % 2 * ROW * 4, [P, STRIDE, GD]) for i in range(NX)]
    off += 2 * ROW * 4
    kt = k.at("sample_kT", off, [P, PAST])
    off += PAST * 4
    ktw = k.at("sample_kwT", off, [P, WIN])
    off += WIN * 4
    xw = [k.at(f"window_rows{i}", off + i * 2048, [P, WA, GD]) for i in range(2)]
    off += 4096
    NTILE = STRIDE + WA + 3
    pt_off = off
    pt = k.at("sample_probsT", off, [P, NTILE, P])
    off += NTILE * P * 4
    rel_w = k.at("win_distance", off, [P, WIN])
    off += WIN * 4
    win_mask = k.at("win_mask", off, [P, WA])
    row_gates = k.at("row_gates", off + 32, [P, 2, 3])
    off += 64

    def col(name, n=1, dtype=F32):
        nonlocal off
        t = k.at(name, off, [P, n], dtype)
        off += (n * 4 + 31) // 32 * 32
        return t

    ids = col("row_id", 1, I32)
    ints = [col(f"row_int{i}", 1, I32) for i in range(3)]
    slope, t_of, b4_of, h_of = col("row_slope"), col("row_t"), col("row_b4"), col("row_h")
    head_hot = col("row_head", NH)
    a_iota, tmp = col("a_iota", WA), col("row_tmp", 32)
    tmp2 = col("row_tmp2", 32)
    picked = col("gates_picked", 3 * NH)
    tops, neg_tops, sums, factor = col("s_top", 3), col("s_neg_top", 3), col("s_sum", 3), col("s_factor", 3)
    padded = col("cmp_probs_padded", 4 * (NBLK + 1))
    part, imp, rank = col("block_part", NBLK), col("importance", NBLK), col("block_rank", NBLK)
    drop, o_rows = col("block_drop", NBLK), col("out_rows", GD)
    assert off <= k.TOP
    gt = k.at("block_gt", pt_off, [P, NBLK, NBLK])
    eq = k.at("block_eq", pt_off + (NBLK * NBLK * 4 + 31) // 32 * 32, [P, NBLK, NBLK])
    assert 2 * NBLK * NBLK * 4 + 64 <= NTILE * P * 4

    s_iota, s_setup, s_chain, s_chain_p = k.sem("s_iotas"), k.sem("s_setup"), k.sem("s_chain"), k.sem("s_chain_pool")
    s_x = [k.sem(f"sample_rows_loaded{i}") for i in range(NX)]
    s_xw = [k.sem(f"window_rows_loaded{i}") for i in range(2)]
    s_turn, s_scores, s_cmp_scores = k.sem("s_k_turned"), k.sem("s_scores_done"), k.sem("s_cmp_scores")
    s_ev = [k.sem("s_turn_evac_act"), k.sem("s_turn_evac_dve")]
    s_tables, s_q = k.sem("s_tables_ready"), k.sem("s_queries_ready")
    s_neg, s_exp, s_pb, s_ranked = k.sem("s_neg_ready"), k.sem("s_exps"), k.sem("s_blocks_ready"), k.sem("s_ranked")
    s_p, s_pv, s_out, s_slc_used = k.sem("s_probs_ready"), k.sem("s_pv_product"), k.sem("s_out_evac"), k.sem("s_x_used")
    s_xw_used, s_o, s_ot = k.sem("s_xw_used"), k.sem("s_out_rows"), k.sem("s_out_turned")

    loads = [(h, kv, b) for h in range(2) for kv in range(2) for b in range(HALF)]
    KLOTS = (STRIDE + WA) // 4
    ptiles = ([(SLC + j * P, P) for j in range(STRIDE)] + [(WINC + a * P, P) for a in range(WA)]
              + [(SNEW, NS_TOK), (WNEW, NS_TOK), (CMP, NC)])
    PLOTS = (len(ptiles) + 3) // 4
    IMP = 2 * KLOTS
    LOTS = HALF * KLOTS + 1 + PLOTS

    def evacs(which, x):
        return (x + 1 - which) // 2

    with nc.Block() as block:

        @block.sync
        def _(sp):
            for n, (h, kv, b) in enumerate(loads):
                if n >= 2:
                    h_, kv_, b_ = loads[n - 2]
                    sp.wait_ge(s_xw_used if kv_ else s_scores, HALF * h_ + b_ + 1)
                src = (k.state_k_win, k.state_v_win)[kv][0, HALF * h + b]
                sp.dma_start(xw[n % 2][:].rearrange("p a x -> p (a x)"),
                             src.rearrange("(p a) g d -> p (a g d)", a=WA)).then_inc(s_xw[n % 2], 16)

        @block.gpsimd
        def _(pool):
            link = Chain(pool, s_chain_p)

            def gather(n):
                h, kv, b = loads[n]
                if n >= NX:
                    pool.wait_ge(s_slc_used, n - NX + 1)
                cache = (k.cache_k_slc, k.cache_v_slc)[kv]
                pool.indirect_dma_start(
                    out=x[n % NX][:].rearrange("p j x -> p (j x)"), out_offset=None,
                    in_=cache[0].rearrange("q (s j) g d -> (q s) (j g d)", j=STRIDE),
                    in_offset=bass.IndirectOffsetOnAxis(ap=k.page_idx[:, HALF * h + b:HALF * h + b + 1], axis=0))\
                    .then_inc(s_x[n % NX], 16)

            gather(0)
            gather(1)
            io = dict(allow_small_or_imprecise_dtypes=True)
            pool.iota(ids[:], pattern=[[0, 1]], base=0, channel_multiplier=1).then_inc(s_iota, 1)
            pool.iota(a_iota[:], pattern=[[1, WA]], base=0, channel_multiplier=0, **io).then_inc(s_iota, 1)
            pool.iota(head_hot[:], pattern=[[1, NH]], base=0, channel_multiplier=0, **io).then_inc(s_iota, 1)
            pool.iota(new_bias[:], pattern=[[-4 * HALF, 2], [1, NS_TOK]], base=0, channel_multiplier=0, **io)\
                .then_inc(s_iota, 1)
            pool.memset(q_pad[:], 0.0).then_inc(s_iota, 1)
            pool.memset(padded[:], 0.0).then_inc(s_iota, 1)
            pool.wait_ge(s_q, 1)
            gather(2)
            gather(3)
            pool.iota(rel_c[:], pattern=[[STRIDE, P]], base=CBLK - 1 - PAST, channel_multiplier=0, **io)
            pool.iota(rel_w[:], pattern=[[1, WA], [WA, P]], base=-WIN, channel_multiplier=0, **io)
            pool.iota(rel[:], pattern=[[1, STRIDE], [STRIDE, NSUB]], base=-PAST, channel_multiplier=0, **io)
            pool.memset(same[:], 0.0)
            pool.memset(token_of[:], 0.0)
            link(pool.memset(before[:], 0.0))
            for i in range(HG):
                v = same[:].rearrange("p (b i t) -> p b i t", i=HG, t=NT)
                link(pool.affine_select(out=v, in_=v, compare_op=ALU.not_equal, fill=1.0, base=-NT * i,
                                        pattern=[[-NT * HG, P // (NT * HG)], [0, HG], [-1, NT]], channel_multiplier=1))
            for h in range(2):
                v = token_of[:, h, :].rearrange("p (b h t) -> p b h t", b=HALF, t=NT)
                link(pool.affine_select(out=v, in_=v, compare_op=ALU.not_equal, fill=1.0, base=-NT * HALF * h,
                                        pattern=[[-NT, HALF], [0, NH], [-1, NT]], channel_multiplier=1))
            pool.affine_select(out=before[:], in_=before[:], compare_op=ALU.is_ge, fill=1.0, base=0,
                               pattern=[[-1, NBLK], [1, NBLK]], channel_multiplier=0).then_inc(s_tables, 1)
            for n in range(NX, len(loads)):
                gather(n)

        @block.tensor
        def _(pe):
            lot = [0]

            def turn(tiles):
                x_ = lot[0]
                if x_ >= 2:
                    pe.wait_ge(s_ev[x_ % 2], evacs(x_ % 2, x_))
                for c, (src, rows, m) in enumerate(tiles):
                    mm = pe.transpose(ps[0:m, 6 + x_ % 2, c * P:c * P + rows], src, k.ident[0:rows, 0:rows])
                mm.then_inc(s_turn, 1)
                lot[0] += 1

            def evacuated(x_):
                pe.wait_ge(s_ev[x_ % 2], evacs(x_ % 2, x_) + 1)

            pe.wait_ge(s_setup, 1)
            pe.wait_ge(s_tables, 1)
            for h in range(2):
                for b in range(HALF):
                    bb = HALF * h + b
                    rows = slice(R * b, R * (b + 1))
                    n = 2 * HALF * h + b
                    if b == 0 and h:
                        pe.wait_ge(s_out, h)
                    if b == 0:
                        for q in range(HALF):
                            mm = pe.matmul(ps[R * q:R * (q + 1), 5, 2 * NS_TOK:2 * NS_TOK + NC], q_pad[:, bb + q, :],
                                           k.kc_s[:, bb + q, 0:NC], start=True, stop=True)
                        mm.then_inc(s_cmp_scores, 1)
                        mm = pe.matmul(ps[:, 5, 256:256 + 3 * NH], token_of[:, h, :],
                                       k.gates[0:NS_TOK, QT].rearrange("p h b -> p (h b)"), start=True, stop=True)
                        mm.then_inc(s_cmp_scores, 1)
                    if b == 2:
                        x_ = lot[0]
                        pe.wait_ge(s_ev[x_ % 2], evacs(x_ % 2, x_))
                        pe.wait_ge(s_pb, h + 1)
                        pe.matmul(ps[:, 6 + x_ % 2, 0:NBLK], same[:], part[:], start=True, stop=True).then_inc(s_turn, 1)
                        lot[0] += 1
                    pe.wait_ge(s_x[n % NX], 16 * (n // NX + 1))
                    x0 = lot[0]
                    for j in range(0, STRIDE, 4):
                        turn([(x[n % NX][:, j + c, :], P, P) for c in range(4)])
                    pe.wait_ge(s_xw[n % 2], 16 * (n // 2 + 1))
                    turn([(xw[n % 2][:, a, :], P, P) for a in range(WA)])
                    for c in range(PAST // 512):
                        evacuated(x0 + c)
                        mm = pe.matmul(ps[rows, c, :], q_pad[:, bb, :], kt[:, c * 512:(c + 1) * 512],
                                       start=True, stop=True)
                    mm.then_inc(s_slc_used, 1)
                    evacuated(x0 + KLOTS - 1)
                    pe.matmul(ps[rows, 4, :], q_pad[:, bb, :], ktw[:], start=True, stop=True)
                    for which in range(2):
                        mm = pe.matmul(ps[rows, 5, which * NS_TOK:(which + 1) * NS_TOK], q_pad[:, bb, :],
                                       k.kT_last[:, which, :], start=True, stop=True)
                    mm.then_inc(s_scores, 1)
                pe.wait_ge(s_p, h + 1)
                for a in range(0, len(ptiles), 4):
                    turn([(score[:, c:c + m], P, m) for c, m in ptiles[a:a + 4]])
                evacuated(lot[0] - 2)
                evacuated(lot[0] - 1)
                for b in range(HALF):
                    n = 2 * HALF * h + HALF + b
                    out = ps[R * b:R * (b + 1), 4, 0:GD]
                    cols = slice(R * b, R * (b + 1))
                    pe.wait_ge(s_x[n % NX], 16 * (n // NX + 1))
                    for j in range(STRIDE):
                        mm = pe.matmul(out, pt[:, j, cols], x[n % NX][:, j, :], start=(j == 0), stop=False)
                    mm.then_inc(s_slc_used, 1)
                    pe.wait_ge(s_xw[n % 2], 16 * (n // 2 + 1))
                    for a in range(WA):
                        mm = pe.matmul(out, pt[:, STRIDE + a, cols], xw[n % 2][:, a, :], start=False, stop=False)
                    mm.then_inc(s_xw_used, 1)
                    t0 = STRIDE + WA
                    pe.matmul(out, pt[0:NS_TOK, t0, cols], k.rows[0:NS_TOK, QT, R_VS:R_VS + GD], start=False, stop=False)
                    pe.matmul(out, pt[0:NS_TOK, t0 + 1, cols], k.rows[0:NS_TOK, QT, R_VW:R_VW + GD], start=False,
                              stop=False)
                    mm = pe.matmul(out, pt[0:NC, t0 + 2, cols], k.vc_s[0:NC, HALF * h + b, :], start=False, stop=True)
                mm.then_inc(s_pv, 1)
                pe.wait_ge(s_o, h + 1)
                pe.transpose(ps[:, 4, 0:P], o_rows[:], k.ident[:]).then_inc(s_ot, 1)

        def evacuate(eng, copy, which, h, n):
            x_ = LOTS * h + n
            if x_ % 2 != which:
                return
            eng.wait_ge(s_turn, x_ + 1)
            src = ps[:, 6 + x_ % 2, :]
            if n == IMP:
                if h:
                    eng.wait_ge(s_ranked, h)
                copy(imp[:], src[:, 0:NBLK]).then_inc(s_ev[which], 1)
                return
            n -= n > IMP
            if n < HALF * KLOTS:
                b, c = n // KLOTS, n % KLOTS
                done = HALF * h + b
                if done:
                    eng.wait_ge(s_scores, done)
                dst = kt[:, c * 512:(c + 1) * 512] if c < KLOTS - 1 else ktw[:]
                copy(dst, src).then_inc(s_ev[which], 1)
                return
            a = 4 * (n - HALF * KLOTS)
            if h:
                eng.wait_ge(s_pv, h)
            if a + 4 <= STRIDE + WA:
                copy(pt[:, a:a + 4, :].rearrange("p c q -> p (c q)"), src).then_inc(s_ev[which], 1)
                return
            for c, (_, m) in enumerate(ptiles[a:a + 4]):
                ins = copy(pt[0:m, a + c, :], ps[0:m, 6 + x_ % 2, c * P:(c + 1) * P])
            ins.then_inc(s_ev[which], 1)

        @block.scalar
        def _(act):
            for h in range(2):
                act.wait_ge(s_neg, 2 * h + 1)
                act.activation(score[:, CMP:CMP + NC], score[:, CMP:CMP + NC], ACT.Exp, bias=neg_tops[:, 2:3],
                               accum_out=sums[:, 2:3]).then_inc(s_exp, 1)
                for n in range(HALF * KLOTS + 1):
                    evacuate(act, act.copy, 0, h, n)
                act.wait_ge(s_neg, 2 * h + 2)
                act.activation(score[:, SLC:SNEW + NS_TOK], score[:, SLC:SNEW + NS_TOK], ACT.Exp,
                               bias=neg_tops[:, 0:1], accum_out=sums[:, 0:1])
                act.activation(score[:, WINC:WNEW + NS_TOK], score[:, WINC:WNEW + NS_TOK], ACT.Exp,
                               bias=neg_tops[:, 1:2], accum_out=sums[:, 1:2]).then_inc(s_exp, 1)
                for n in range(HALF * KLOTS + 1, LOTS):
                    evacuate(act, act.copy, 0, h, n)

        @block.vector
        def _(dve):
            link = Chain(dve, s_chain)
            dve.wait_ge(s_iota, 6)
            for g in range(NG):
                rows = slice(g * HD, (g + 1) * HD)
                for i in range(HG):
                    ins = dve.tensor_copy(q_pad[rows, :, (HG * g + i) * NT:(HG * g + i + 1) * NT],
                                          k.aq[rows, i, SEQ:TOK].rearrange("p (b t) -> p b t", b=NB))
            ins.then_inc(s_q, 1)
            link(dve.tensor_single_scalar(ints[0][:], ids[:], 3, ALU.bitwise_and))
            link(dve.tensor_copy(t_of[:], ints[0][:]))
            link(dve.tensor_single_scalar(ints[0][:], ids[:], 5, ALU.arith_shift_right))
            link(dve.tensor_scalar(b4_of[:], ints[0][:], 4.0, None, ALU.mult))
            link(dve.tensor_single_scalar(ints[1][:], ids[:], 2, ALU.arith_shift_right))
            link(dve.tensor_single_scalar(ints[1][:], ints[1][:], 7, ALU.bitwise_and))
            link(dve.tensor_copy(h_of[:], ints[1][:]))
            link(dve.tensor_scalar(ints[2][:], ints[1][:], -1.0, 126.0, ALU.mult, ALU.add))
            link(dve.tensor_single_scalar(slope[:].bitcast(I32), ints[2][:], 23, ALU.logical_shift_left))
            link(dve.tensor_scalar(head_hot[:], head_hot[:], h_of[:], None, ALU.is_equal))
            link(dve.tensor_scalar(win_mask[:], a_iota[:], t_of[:], NEG, ALU.is_lt, ALU.mult))
            for h in range(2):
                v = new_bias[:, h, :]
                link(dve.tensor_scalar(v, v, b4_of[:], None, ALU.subtract))
                link(dve.tensor_scalar(tmp[:], v, 0.0, None, ALU.is_ge))
                link(dve.tensor_scalar(tmp2[:], v, t_of[:], None, ALU.is_le))
                link(dve.tensor_tensor(tmp[:], tmp[:], tmp2[:], ALU.mult))
                link(dve.tensor_scalar(tmp2[:], v, slope[:], None, ALU.mult))
                link(dve.tensor_tensor(tmp2[:], tmp2[:], tmp[:], ALU.mult))
                link(dve.tensor_scalar(tmp[:], tmp[:], -1.0, BIG, ALU.add, ALU.mult))
                ins = dve.tensor_tensor(v, tmp[:], tmp2[:], ALU.add)
                if h == 0:
                    link(ins)
            ins.then_inc(s_setup, 1)
            dve.wait_ge(s_tables, 1)
            for h in range(2):
                dve.wait_ge(s_cmp_scores, 2 * h + 2)
                s_c = score[:, CMP:CMP + NC]
                link(dve.scalar_tensor_tensor(s_c, rel_c[:, 0:NC], slope[:], ps[:, 5, 64:64 + NC], ALU.mult, ALU.add))
                link(dve.tensor_reduce(tops[:, 2:3], s_c, AX.X, ALU.max))
                dve.tensor_scalar(neg_tops[:, 2:3], tops[:, 2:3], -1.0, None, ALU.mult).then_inc(s_neg, 1)
                picked_v = picked[:].rearrange("p (h b) -> p h b", h=NH)
                link(dve.tensor_tensor(picked_v, ps[:, 5, 256:256 + 3 * NH].rearrange("p (h b) -> p h b", h=NH),
                                       head_hot[:].unsqueeze(2).to_broadcast([P, NH, 3]), ALU.mult))
                link(dve.tensor_reduce(row_gates[:, h, :], picked[:].rearrange("p (h b) -> p b h", h=NH), AX.X, ALU.add))
                dve.wait_ge(s_exp, 2 * h + 1)
                link(dve.reciprocal(factor[:, 2:3], sums[:, 2:3]))
                link(dve.tensor_scalar(padded[:, 1:1 + NC], s_c, factor[:, 2:3], None, ALU.mult))
                link(dve.tensor_scalar(s_c, padded[:, 1:1 + NC], row_gates[:, h, 2:3], None, ALU.mult))
                link(dve.tensor_reduce(part[:], padded[:, 0:4 * NBLK].rearrange("p (j x) -> p j x", x=4), AX.X, ALU.add))
                dve.tensor_tensor(part[:].unsqueeze(2), part[:].unsqueeze(2),
                                  padded[:, 4:4 * NBLK + 4].rearrange("p (j x) -> p j x", x=4)[:, :, 0:1], ALU.add)\
                   .then_inc(s_pb, 1)
                for n in range(IMP + 1):
                    evacuate(dve, dve.tensor_copy, 1, h, n)
                x_ = LOTS * h + IMP
                dve.wait_ge(s_ev[x_ % 2], evacs(x_ % 2, x_) + 1)
                link(dve.memset(imp[:, 0:1], BIG))
                link(dve.memset(imp[:, NBLK - 2:NBLK], BIG))
                other = imp[:].unsqueeze(1).to_broadcast([P, NBLK, NBLK])
                own = imp[:].unsqueeze(2).to_broadcast([P, NBLK, NBLK])
                dve.tensor_tensor(gt[:], other, own, ALU.is_gt)
                link(dve.tensor_tensor(eq[:], other, own, ALU.is_equal))
                link(dve.tensor_tensor(eq[:], eq[:], before[:], ALU.mult))
                link(dve.tensor_tensor(gt[:], gt[:], eq[:], ALU.add))
                dve.tensor_reduce(rank[:], gt[:], AX.X, ALU.add).then_inc(s_ranked, 1)
                dve.wait_ge(s_ranked, h + 1)
                link(dve.tensor_scalar(drop[:], rank[:], float(NSEL) - 0.5, NEG, ALU.is_ge, ALU.mult))
                for n in range(IMP + 1, HALF * KLOTS + 1):
                    evacuate(dve, dve.tensor_copy, 1, h, n)
                dve.wait_ge(s_scores, HALF * (h + 1))
                for c in range(PAST // 512):
                    cs = slice(c * 512, (c + 1) * 512)
                    ins = dve.scalar_tensor_tensor(score[:, cs], rel[:, cs], slope[:], ps[:, c, :], ALU.mult, ALU.add)
                dve.tensor_tensor(score[:, SNEW:SNEW + NS_TOK], ps[:, 5, 0:NS_TOK], new_bias[:, h, :], ALU.add)
                dve.scalar_tensor_tensor(score[:, WINC:WNEW], rel_w[:], slope[:], ps[:, 4, :], ALU.mult, ALU.add)
                link(dve.tensor_tensor(score[:, WNEW:WNEW + NS_TOK], ps[:, 5, NS_TOK:2 * NS_TOK], new_bias[:, h, :],
                                       ALU.add))
                by_block = score[:, SLC:SNEW].rearrange("p (j b r) -> p j b r", j=STRIDE, r=SBLK // STRIDE)
                dropped = drop[:, 0:NBLK - 1].unsqueeze(1).unsqueeze(3).to_broadcast(
                    [P, STRIDE, NBLK - 1, SBLK // STRIDE])
                dve.tensor_tensor(by_block, by_block, dropped, ALU.add)
                first = score[:, WINC:WNEW].rearrange("p (a n) -> p a n", a=WA)[:, :, 0]
                link(dve.tensor_tensor(first, first, win_mask[:], ALU.add))
                dve.tensor_reduce(tops[:, 0:1], score[:, SLC:SNEW + NS_TOK], AX.X, ALU.max)
                link(dve.tensor_reduce(tops[:, 1:2], score[:, WINC:WNEW + NS_TOK], AX.X, ALU.max))
                dve.tensor_scalar(neg_tops[:, 0:2], tops[:, 0:2], -1.0, None, ALU.mult).then_inc(s_neg, 1)
                dve.wait_ge(s_exp, 2 * h + 2)
                link(dve.reciprocal(factor[:, 0:2], sums[:, 0:2]))
                link(dve.tensor_tensor(factor[:, 0:2], factor[:, 0:2], row_gates[:, h, 0:2], ALU.mult))
                dve.tensor_scalar(score[:, SLC:SNEW + NS_TOK], score[:, SLC:SNEW + NS_TOK], factor[:, 0:1], None, ALU.mult)
                dve.tensor_scalar(score[:, WINC:WNEW + NS_TOK], score[:, WINC:WNEW + NS_TOK], factor[:, 1:2], None,
                                  ALU.mult).then_inc(s_p, 1)
                for n in range(HALF * KLOTS + 1, LOTS):
                    evacuate(dve, dve.tensor_copy, 1, h, n)
                dve.wait_ge(s_pv, h + 1)
                dve.tensor_copy(o_rows[:], ps[:, 4, 0:GD]).then_inc(s_o, 1)
                dve.wait_ge(s_ot, h + 1)
                for g in range(NG):
                    rows = slice(g * HD, (g + 1) * HD)
                    src = ps[rows, 4, 0:R * HALF].rearrange("p (b g i t) -> p b g i t", b=HALF, g=NG, i=HG)[:, :, g]
                    t0 = SEQ + h * HALF * NT
                    dst = k.bT[rows, :, t0:t0 + HALF * NT].rearrange("p i (b t) -> p b i t", b=HALF)
                    ins = dve.tensor_copy(dst, src)
                ins.then_inc(s_out, 1)


def stage_merge(k):
    nc, ps = k.nc, k.ps
    KB = 4
    NRAW, NSPLIT, LEAD = 5, 3, 2
    act_bytes = HG * TOK * 4
    raw = [k.at(f"merge_raw{i}", k.ROWS_OFF + i * KB * 512, [P, KB, P]) for i in range(NRAW)]
    free = k.ROWS_OFF + NRAW * KB * 512
    b_l, b_h = k.at("bT_l", k.VA_OFF, [P, HG, TOK], F32R), k.at("bT_h", free, [P, HG, TOK], F32R)
    assert free + act_bytes <= k.VA_OFF
    a_l, a_h = k.at("aT_l", k.AT_OFF, [P, MH, TOK], F32R), k.at("aT_h", k.VA_OFF + act_bytes, [P, MH, TOK], F32R)
    assert k.VA_OFF + 2 * act_bytes <= k.AT_OFF
    off = k.QK_OFF
    hT_l, hT_h = k.at("hT_l", k.HT_OFF, [P, KD, TOK], F32R), k.at("hT_h", off, [P, KD, TOK], F32R)
    y_h = k.at("y_h", off, [P, KD, TOK], F32R)
    off += KD * TOK * 4
    y, y_l = k.at("merged_yT", off, [P, KD, TOK]), k.at("y_l", off, [P, KD, TOK], F32R)
    off += KD * TOK * 4
    w_h = [k.at(f"merge_w_h{i}", off + 2 * i * KB * 512, [P, KB, P], F32R) for i in range(NSPLIT)]
    w_l = [k.at(f"merge_w_l{i}", off + (2 * i + 1) * KB * 512, [P, KB, P], F32R) for i in range(NSPLIT)]
    off += 2 * NSPLIT * KB * 512
    assert off <= k.TOP
    off = k.SPARE2_OFF
    sig = [k.at(f"merge_sigmoid{i}", off + i * TOK * 4, [P, NCH, CH]) for i in range(2)]
    tmp = k.at("merge_product", off + 2 * TOK * 4, [P, NCH, CH])
    assert off + 3 * TOK * 4 <= k.HT_OFF
    k.ffn_raw = [k.at(f"ffn_raw{i}", k.ROWS_OFF + i * KD * 512, [P, KD, P]) for i in range(FFN_RAW)]
    k.s_ffn_raw = [k.sem(f"ffn_raw_full{i}") for i in range(FFN_RAW)]
    off = k.ROWS_OFF + FFN_RAW * KD * 512
    x_rows = k.at("x_rows", off, [P, TT, DM])
    off += TT * DM * 4
    ss = k.at("x1_square_sums", off, [P, TOK])
    square = [k.at(f"x1_square{i}", off + (1 + i) * TOK * 4, [P, TOK]) for i in range(2)]
    assert off + 3 * TOK * 4 <= k.QK_OFF
    XG = 4

    blocks = []
    for f in range(KD):
        blocks += [("gate_a", 0, f), ("gate_a", KB, f), ("a", 0, f), ("gate_b", 0, f), ("gate_b", KB, f), ("b", 0, f)]
    NM = len(blocks)
    for f in range(KD):
        blocks += [("o", 0, f), ("o", KB, f)]
    NBK = len(blocks)
    ends = [src in "ab" or kt0 == KB for src, kt0, _ in blocks]
    product = [sum(ends[:n]) for n in range(NBK)]
    n_dma, full_at = [0] * NRAW, []
    for n, (src, _, _) in enumerate(blocks):
        n_dma[n % NRAW] += NG if src == "b" else 1
        full_at.append(16 * n_dma[n % NRAW])

    s_raw = [k.sem(f"merge_raw_full{i}") for i in range(NRAW)]
    s_h, s_l, s_used = k.sem("w_h_ready"), k.sem("w_l_ready"), k.sem("w_block_used")
    s_xh, s_xl = k.sem("operand_h_ready"), k.sem("operand_l_ready")
    s_sig, s_mul, s_y = k.sem("merge_sigmoids"), k.sem("merge_products"), k.sem("y_ready")
    s_x = [k.sem(f"x_cols_loaded{i}") for i in range(XG)]
    s_xt, s_xt_copied, s_x1 = k.sem("x_turned"), k.sem("xT_copied"), k.sem("x1_ready")
    s_sq, s_ss, s_tot, s_rs = k.sem("x1_squared"), k.sem("x1_summed"), k.sem("x1_totals"), k.sem("x1_roots")
    s_ms = k.sem("x1_mean_squares")
    LAST_GATE = NM - 1

    def chunk(c):
        return slice(c * CH, (c + 1) * CH)

    def banks(p):
        return ps[:, 3 * (p % 2):3 * (p % 2) + NCH, 0:CH]

    def flat(t):
        return t[:].rearrange("p c n -> p (c n)")

    with nc.Block() as block:

        @block.sync
        def _(sp):
            w_in = k.w_in[0].rearrange("(k p) n -> p k n", p=P)
            w_a, w_o = (w[0].rearrange("(k p) n -> p k n", p=P) for w in (k.w_a, k.w_o))
            w_b = k.w_b[0].rearrange("(g i d) n -> g d i n", g=NG, i=HG)
            for n, (src, kt, f) in enumerate(blocks):
                if n >= NRAW:
                    sp.wait_ge(s_l, n - NRAW + 1)
                slot, full = raw[n % NRAW], s_raw[n % NRAW]
                cols = slice(f * P, (f + 1) * P)
                if src == "b":
                    for g in range(NG):
                        sp.dma_start(slot[g * HD:(g + 1) * HD], w_b[g, :, :, cols]).then_inc(full, 16)
                elif src == "a":
                    sp.dma_start(slot[:], w_a[:, :, cols]).then_inc(full, 16)
                elif src == "o":
                    sp.dma_start(slot[:], w_o[:, kt:kt + KB, cols]).then_inc(full, 16)
                else:
                    c = C_MRG + (src == "gate_b") * DM + f * P
                    sp.dma_start(slot[:], w_in[:, kt:kt + KB, c:c + P]).then_inc(full, 16)
            sp.wait_ge(s_l, NBK)
            w = k.w_ffn_in[0].rearrange("(k p) n -> p k n", p=P)
            for i in range(FFN_RAW):
                c = (i % 2) * DFF + i // 2 * P
                sp.dma_start(k.ffn_raw[i][:], w[:, :, c:c + P]).then_inc(k.s_ffn_raw[i], 16)

        @block.gpsimd
        def _(pool):
            for f in range(KD):
                pool.wait_ge(s_mul, 2 * (f + 1))
                pool.tensor_tensor(y[:, f, :], y[:, f, :], flat(tmp), ALU.add).then_inc(s_y, 1)
            pool.wait_ge(s_used, NM)
            xp = k.x_prompt[0].rearrange("(t p) d -> p t d", p=P)
            for i in range(XG):
                cols = slice(i * DM // XG, (i + 1) * DM // XG)
                pool.dma_start(x_rows[:, 0:QT, cols], xp[:, :, cols]).then_inc(s_x[i], 16)
                pool.dma_start(x_rows[0:NS_TOK, QT, cols], k.x_sample.rearrange("b t d -> (b t) d")[:, cols])\
                    .then_inc(s_x[i], 16)
            for f in range(1, KD):
                pool.wait_ge(s_sq, f + 1)
                if f > 1:
                    pool.wait_ge(s_ss, f - 1)
                pool.tensor_tensor(ss[:], ss[:], square[f % 2][:], ALU.add).then_inc(s_ss, 1)

        @block.scalar
        def _(act):
            def split(n):
                if n >= NBK:
                    return
                act.wait_ge(s_raw[n % NRAW], full_at[n])
                if n >= NSPLIT:
                    act.wait_ge(s_used, n - NSPLIT + 1)
                act.copy(w_h[n % NSPLIT][:], raw[n % NRAW][:]).then_inc(s_h, 1)

            for n in range(LEAD):
                split(n)
            for src, dst, count in ((k.hT, hT_h, KD), (k.aT, a_h, MH)):
                for kd in range(count):
                    act.copy(dst[:, kd, :], src[:, kd, :]).then_inc(s_xh, 1)
            for n, (src, _, f) in enumerate(blocks[:NM]):
                split(n + LEAD)
                if n == 0:
                    for kd in range(HG):
                        act.copy(b_h[:, kd, :], k.bT[:, kd, :]).then_inc(s_xh, 1)
                if src.startswith("gate") and ends[n]:
                    part = int(src == "gate_b")
                    act.wait_ge(s_used, n + 1)
                    if f:
                        act.wait_ge(s_mul, 2 * f - 1 + part)
                    col = k.c_b_mrg + part * KD + f
                    act.activation(sig[part][:], banks(product[n]), ACT.Sigmoid,
                                   bias=k.cols[:, col:col + 1]).then_inc(s_sig, 1)
            act.wait_ge(s_used, LAST_GATE)
            for kd in range(KD):
                act.wait_ge(s_y, kd + 1)
                act.copy(y_h[:, kd, :], y[:, kd, :]).then_inc(s_xh, 1)

            def square_tile(f):
                act.wait_ge(s_x1, f + 1)
                if f >= 3:
                    act.wait_ge(s_ss, f - 2)
                act.activation(square[f % 2][:] if f else ss[:], k.x1[:, f, :], ACT.Square).then_inc(s_sq, 1)

            for f in range(KD):
                for j, (a, m) in enumerate(TOKEN_CHUNKS):
                    act.wait_ge(s_xt, 3 * f + j + 1)
                    act.copy(k.x1[:, f, a:a + m], ps[:, 6 + (3 * f + j) % 2, 0:m]).then_inc(s_xt_copied, 1)
                split(NM + 2 * f + LEAD)
                if f:
                    square_tile(f - 1)
                split(NM + 2 * f + 1 + LEAD)
            square_tile(KD - 1)
            for c in range(NCH):
                act.wait_ge(s_ms, c + 1)
                act.activation(k.rs[:, chunk(c)], k.rs[:, chunk(c)], ACT.Sqrt).then_inc(s_rs, 1)

        @block.vector
        def _(dve):
            def split(n):
                if n >= NBK:
                    return
                dve.wait_ge(s_h, n + 1)
                dve.tensor_tensor(w_l[n % NSPLIT][:], raw[n % NRAW][:], w_h[n % NSPLIT][:].bitcast(F32), ALU.subtract)\
                   .then_inc(s_l, 1)

            def split_operand(src, h, l, kd, n):
                dve.wait_ge(s_xh, n + 1)
                dve.tensor_tensor(l[:, kd, :], src[:, kd, :], h[:, kd, :].bitcast(F32), ALU.subtract).then_inc(s_xl, 1)

            for n in range(LEAD):
                split(n)
            for kd in range(KD):
                split_operand(k.hT, hT_h, hT_l, kd, kd)
            for kd in range(MH):
                split_operand(k.aT, a_h, a_l, kd, KD + kd)
            for n, (src, _, f) in enumerate(blocks[:NM]):
                split(n + LEAD)
                if n == 0:
                    for kd in range(HG):
                        split_operand(k.bT, b_h, b_l, kd, KD + MH + kd)
                if src in "ab":
                    part = int(src == "b")
                    dve.wait_ge(s_sig, 2 * f + part + 1)
                    dve.wait_ge(s_used, n + 1)
                    if part == 0:
                        dst = y[:, f, :].rearrange("p (c n) -> p c n", c=NCH)
                    else:
                        if f:
                            dve.wait_ge(s_y, f)
                        dst = tmp[:]
                    dve.tensor_tensor(dst, sig[part][:], banks(product[n]), ALU.mult).then_inc(s_mul, 1)
            for kd in range(KD):
                split_operand(y, y_h, y_l, kd, KD + MH + HG + kd)
            for f in range(KD):
                n = NM + 2 * f
                split(n + LEAD)
                split(n + 1 + LEAD)
                dve.wait_ge(s_used, n + 2)
                dve.wait_ge(s_xt_copied, 3 * (f + 1))
                x1 = k.x1[:, f, :].rearrange("p (c n) -> p c n", c=NCH)
                dve.tensor_tensor(x1, x1, banks(product[n]), ALU.add).then_inc(s_x1, 1)
            for c in range(NCH):
                dve.wait_ge(s_tot, c + 1)
                dve.tensor_scalar(k.rs[:, chunk(c)], ps[:, c, 0:CH], 1.0 / DM, EPS, ALU.mult, ALU.add).then_inc(s_ms, 1)
            for c in range(NCH):
                dve.wait_ge(s_rs, c + 1)
                dve.reciprocal(k.rs[:, chunk(c)], k.rs[:, chunk(c)])

        @block.tensor
        def _(pe):
            pieces = [(c, chunk(c)) for c in range(NCH)]
            operand = {"gate_a": (hT_h, hT_l, 0), "gate_b": (hT_h, hT_l, 0), "a": (a_h, a_l, KD),
                       "b": (b_h, b_l, KD + MH), "o": (y_h, y_l, KD + MH + HG)}
            for n, (src, kt0, f) in enumerate(blocks):
                p = product[n]
                if kt0 == 0:
                    if src.startswith("gate") and p:
                        pe.wait_ge(s_sig, 2 * f + int(src == "gate_b"))
                    elif src in "ab" and p > 1:
                        pe.wait_ge(s_mul, 2 * f + int(src == "b"))
                    elif src == "o" and f < 2:
                        pe.wait_ge(s_sig, 2 * KD)
                        pe.wait_ge(s_mul, 2 * KD)
                    elif src == "o":
                        pe.wait_ge(s_x1, f - 1)
                h, l, base = operand[src]
                pe.wait_ge(s_l, n + 1)
                for kt in range(KB):
                    if f == 0:
                        pe.wait_ge(s_xl, base + kt0 + kt + 1)
                    mm = split_product(pe, banks(p), w_h[n % NSPLIT], w_l[n % NSPLIT], kt, h, l, kt0 + kt, pieces,
                                       kt0 + kt == 0, ends[n] and kt == KB - 1)
                mm.then_inc(s_used, 1)
                if src == "o" and kt0 == 0:
                    if f % (KD // XG) == 0:
                        pe.wait_ge(s_x[f // (KD // XG)], 32)
                    for j, (a, m) in enumerate(TOKEN_CHUNKS):
                        if 3 * f + j >= 2:
                            pe.wait_ge(s_xt_copied, 3 * f + j - 1)
                        for t in range(0, m, P):
                            r = min(P, m - t)
                            mm = pe.transpose(ps[:, 6 + (3 * f + j) % 2, t:t + r],
                                              x_rows[0:r, (a + t) // P, f * P:(f + 1) * P], k.ident[0:r, 0:r])
                        mm.then_inc(s_xt, 1)
            pe.wait_ge(s_x1, KD)
            pe.wait_ge(s_ss, KD - 1)
            for c in range(NCH):
                pe.matmul(ps[:, c, 0:CH], k.ones[:], ss[:, chunk(c)], start=True, stop=True).then_inc(s_tot, 1)


def stage_ffn(k):
    nc, ps = k.nc, k.ps
    HT = TOK // 2
    HC = HT // 2
    KB = KD
    NRAW, NSPLIT, LEAD = FFN_RAW, 3, 2
    raw, s_raw = k.ffn_raw, k.s_ffn_raw
    off = k.ROWS_OFF + NRAW * KB * 512
    h2_h, h2_l = (k.at(f"h2_{s}", off + i * KD * HT * 4, [P, KD, HT], F32R) for i, s in enumerate("hl"))
    off += 2 * KD * HT * 4
    act_h, act_l = (k.at(f"act_{s}", off + i * FT * HT * 4, [P, FT, HT], F32R) for i, s in enumerate("hl"))
    off += 2 * FT * HT * 4
    w_h = [k.at(f"ffn_w_h{i}", off + 2 * i * KB * 512, [P, KB, P], F32R) for i in range(NSPLIT)]
    w_l = [k.at(f"ffn_w_l{i}", off + (2 * i + 1) * KB * 512, [P, KB, P], F32R) for i in range(NSPLIT)]
    off += 2 * NSPLIT * KB * 512
    assert off <= k.TOP
    off = k.SPARE2_OFF + TOK * 4
    gu = [k.at(f"ffn_act{i}", off + i * HT * 4, [P, HT]) for i in range(2)]
    off += 2 * HT * 4
    h2 = [k.at(f"h2_tile{i}", off + i * HT * 4, [P, HT]) for i in range(2)]
    off += 2 * HT * 4
    assert off <= k.HT_OFF

    half = []
    for f in range(FT):
        half += [("gate", 0, KD, f), ("up", 0, KD, f)]
    NGU = len(half)
    for f in range(KD):
        half += [("down", kt, min(KB, FT - kt), f) for kt in range(0, FT, KB)]
    NH_ = len(half)
    blocks = [(hf,) + b for hf in range(2) for b in half]
    NBK = len(blocks)
    s_h, s_l, s_used = k.sem("ffn_w_h_ready"), k.sem("ffn_w_l_ready"), k.sem("ffn_block_used")
    s_t2, s_h2h, s_h2, s_h2b = (k.sem("h2_tile_ready"), k.sem("h2_h_ready"), k.sem("h2_ready_first_half"),
                                k.sem("h2_ready_second_half"))
    s_silu, s_mul, s_ah, s_al, s_x2 = (k.sem("silu_done"), k.sem("act_multiplied"), k.sem("act_h_ready"),
                                       k.sem("act_l_ready"), k.sem("x2_ready"))

    def pair(bank):
        return ps[:, bank:bank + 2, 0:HC]

    def two(t):
        return t.rearrange("p (c n) -> p c n", c=2)

    def down_bank(f):
        return 2 * (f % 4)

    with nc.Block() as block:

        @block.sync
        def _(sp):
            w_gu = k.w_ffn_in[0].rearrange("(k p) n -> p k n", p=P)
            w_down = k.w_ffn_out[0].rearrange("(k p) n -> p k n", p=P)
            for n, (hf, src, kt, m, f) in enumerate(blocks):
                if n < NRAW:
                    continue
                sp.wait_ge(s_l, n - NRAW + 1)
                if src == "down":
                    w = w_down[:, kt:kt + m, f * P:(f + 1) * P]
                else:
                    c = (src == "up") * DFF + f * P
                    w = w_gu[:, :, c:c + P]
                sp.dma_start(raw[n % NRAW][:, 0:m, :], w).then_inc(s_raw[n % NRAW], 16)

        @block.gpsimd
        def _(pool):
            for hf in range(2):
                for kd in range(KD if hf else 0):
                    u = KD * hf + kd
                    pool.wait_ge(s_h2h, u + 1)
                    pool.tensor_tensor(h2_l[:, kd, :], h2[u % 2][:], h2_h[:, kd, :].bitcast(F32), ALU.subtract)\
                        .then_inc(s_h2b, 1)
                for f in range(FT):
                    u = FT * hf + f
                    pool.wait_ge(s_ah, u + 1)
                    pool.tensor_tensor(act_l[:, f, :], gu[u % 2][:], act_h[:, f, :].bitcast(F32), ALU.subtract)\
                        .then_inc(s_al, 1)

        @block.scalar
        def _(act):
            def split(n):
                if n >= NBK:
                    return
                m = blocks[n][3]
                act.wait_ge(s_raw[n % NRAW], 16 * (n // NRAW + 1))
                if n >= NSPLIT:
                    act.wait_ge(s_used, n - NSPLIT + 1)
                act.copy(w_h[n % NSPLIT][:, 0:m, :], raw[n % NRAW][:, 0:m, :]).then_inc(s_h, 1)

            def h2_tile(u):
                act.wait_ge(s_t2, u + 1)
                act.copy(h2_h[:, u % KD, :], h2[u % 2][:]).then_inc(s_h2h, 1)

            def act_high(u):
                act.wait_ge(s_mul, u + 1)
                act.copy(act_h[:, u % FT, :], gu[u % 2][:]).then_inc(s_ah, 1)

            for n in range(LEAD):
                split(n)
            for kd in range(KD):
                h2_tile(kd)
            for n, (hf, src, kt, m, f) in enumerate(blocks):
                split(n + LEAD)
                u = FT * hf + f
                if src == "gate":
                    if f:
                        act_high(u - 1)
                    act.wait_ge(s_used, n + 1)
                    if u >= 2:
                        act.wait_ge(s_al, u - 1)
                    act.activation(two(gu[u % 2][:]), pair(4 * (f % 2)), ACT.Silu).then_inc(s_silu, 1)
                elif src == "down" and kt == 0:
                    if f == 0:
                        act_high(FT * hf + FT - 1)
                    if hf == 0:
                        h2_tile(KD + f)

        @block.vector
        def _(dve):
            def split(n):
                if n >= NBK:
                    return
                m = blocks[n][3]
                dve.wait_ge(s_h, n + 1)
                dve.tensor_tensor(w_l[n % NSPLIT][:, 0:m, :], raw[n % NRAW][:, 0:m, :],
                                  w_h[n % NSPLIT][:, 0:m, :].bitcast(F32), ALU.subtract).then_inc(s_l, 1)

            def h2_tile(hf, kd):
                u = KD * hf + kd
                if 2 <= u < KD + 2:
                    dve.wait_ge(s_h2, u - 1)
                elif u >= 2:
                    dve.wait_ge(s_h2b, u - KD - 1)
                tokens = slice(hf * HT, (hf + 1) * HT)
                dve.scalar_tensor_tensor(h2[u % 2][:], k.x1[:, kd, tokens],
                                         k.cols[:, k.c_norm_ffn + kd:k.c_norm_ffn + kd + 1], k.rs[:, tokens],
                                         ALU.mult, ALU.mult).then_inc(s_t2, 1)

            for n in range(LEAD):
                split(n)
            h2_tile(0, 0)
            for kd in range(KD):
                if kd + 1 < KD:
                    h2_tile(0, kd + 1)
                dve.wait_ge(s_h2h, kd + 1)
                dve.tensor_tensor(h2_l[:, kd, :], h2[kd % 2][:], h2_h[:, kd, :].bitcast(F32), ALU.subtract)\
                   .then_inc(s_h2, 1)
            for n, (hf, src, kt, m, f) in enumerate(blocks):
                split(n + LEAD)
                u = FT * hf + f
                if src == "up":
                    dve.wait_ge(s_silu, u + 1)
                    dve.wait_ge(s_used, n + 1)
                    dve.tensor_tensor(two(gu[u % 2][:]), two(gu[u % 2][:]), pair(4 * (f % 2) + 2), ALU.mult)\
                       .then_inc(s_mul, 1)
                elif src == "down":
                    if kt == 0 and hf == 0:
                        dve.wait_ge(s_used, NGU)
                        h2_tile(1, f)
                    if kt + m == FT:
                        dve.wait_ge(s_used, n + 1)
                        x1 = two(k.x1[:, f, hf * HT:(hf + 1) * HT])
                        dve.tensor_tensor(x1, x1, pair(down_bank(f)), ALU.add).then_inc(s_x2, 1)

        @block.tensor
        def _(pe):
            for n, (hf, src, kt0, m, f) in enumerate(blocks):
                u = FT * hf + f
                pe.wait_ge(s_l, n + 1)
                if src == "down":
                    if kt0 == 0:
                        if f < 4:
                            pe.wait_ge(s_mul, FT * (hf + 1) - (1 if f < 2 else 0))
                        else:
                            pe.wait_ge(s_x2, KD * hf + f - 3)
                    if f == 0:
                        pe.wait_ge(s_al, FT * hf + kt0 + m)
                    first_bank = down_bank(f)
                    x_h, x_l = act_h, act_l
                else:
                    if src == "gate" and f >= 2:
                        pe.wait_ge(s_mul, u - 1)
                    elif src == "gate" and hf:
                        pe.wait_ge(s_x2, KD - 2 + 2 * f)
                    first_bank = 4 * (f % 2) + 2 * int(src == "up")
                    x_h, x_l = h2_h, h2_l
                pieces = [(first_bank + c, slice(c * HC, (c + 1) * HC)) for c in range(2)]
                for kt in range(m):
                    if src == "gate" and f == 0:
                        pe.wait_ge(s_h2b if hf else s_h2, kt + 1)
                    last = kt0 + kt == (FT if src == "down" else KD) - 1
                    mm = split_product(pe, ps, w_h[n % NSPLIT], w_l[n % NSPLIT], kt, x_h, x_l, kt0 + kt, pieces,
                                       kt0 + kt == 0, last)
                mm.then_inc(s_used, 1)


def stage_final(k):
    nc, ps = k.nc, k.ps
    NX = TOK // XT
    off = k.ROWS_OFF
    weight = k.at("final_weight", off, [P, DM])
    off += DM * 4
    square = k.at("final_square", off, [P, DM])
    off += DM * 4
    y = [k.at(f"final_rows{i}", off + i * DM * 4, [P, DM]) for i in range(3)]
    off += 3 * DM * 4
    ss = k.at("final_square_sums", off, [P, NX])
    rs = k.at("final_rstd", off + 64, [P, NX])
    s_w, s_turn, s_ss, s_rs, s_y = (k.sem("final_weight_loaded"), k.sem("final_turned"), k.sem("final_ss"),
                                    k.sem("final_rstd_ready"), k.sem("final_ready"))
    s_out = k.y_stored

    with nc.Block() as block:

        @block.sync
        def _(sp):
            sp.dma_start(weight[:], k.norm_final.partition_broadcast(P)).then_inc(s_w, 16)
            n_out = [0] * 3
            for t in range(NX):
                sp.wait_ge(s_y, t + 1)
                a, b = t * XT, (t + 1) * XT
                m = max(0, min(b, SEQ) - a)
                sp.dma_start(k.y_prompt[0, a:a + m], y[t % 3][0:m, :]).then_inc(s_out[t % 3], 16)
                n_out[t % 3] += 16
                if m < XT:
                    sp.dma_start(k.y_sample.rearrange("b t d -> (b t) d"), y[t % 3][m:XT, :]).then_inc(s_out[t % 3], 16)
                    n_out[t % 3] += 16
            for i in range(3):
                sp.wait_ge(s_out[i], n_out[i])

        @block.tensor
        def _(pe):
            for t in range(NX):
                if t >= 3:
                    pe.wait_ge(s_y, t - 2)
                for f in range(KD):
                    mm = pe.transpose(ps[0:XT, 2 * (t % 3) + f // 4, (f % 4) * P:(f % 4 + 1) * P],
                                      k.x1[:, f, t * XT:(t + 1) * XT], k.ident[:])
                mm.then_inc(s_turn, 1)

        @block.scalar
        def _(act):
            def root(t):
                act.wait_ge(s_rs, 3 * t + 1)
                act.activation(rs[0:XT, t:t + 1], rs[0:XT, t:t + 1], ACT.Sqrt).then_inc(s_rs, 1)

            for t in range(NX):
                act.wait_ge(s_turn, t + 1)
                if t:
                    act.wait_ge(s_ss, t)
                rows = ps[0:XT, 2 * (t % 3):2 * (t % 3) + 2, :].rearrange("p a n -> p (a n)")
                act.activation(square[0:XT], rows, ACT.Square, accum_out=ss[0:XT, t:t + 1]).then_inc(s_ss, 1)
                if t:
                    root(t - 1)
            root(NX - 1)

        @block.vector
        def _(dve):
            dve.wait_ge(s_w, 16)
            n_out = 0
            for t in range(NX):
                r = rs[0:XT, t:t + 1]
                dve.wait_ge(s_ss, t + 1)
                dve.tensor_scalar(r, ss[0:XT, t:t + 1], 1.0 / DM, EPS, ALU.mult, ALU.add).then_inc(s_rs, 1)
                dve.wait_ge(s_rs, 3 * t + 2)
                dve.reciprocal(r, r).then_inc(s_rs, 1)
                dve.wait_ge(s_rs, 3 * t + 3)
                if t >= 3:
                    dve.wait_ge(s_out[t % 3], 16 * (t // 3))
                rows = ps[0:XT, 2 * (t % 3):2 * (t % 3) + 2, :].rearrange("p a n -> p (a n)")
                dve.scalar_tensor_tensor(y[t % 3][0:XT], rows, r, weight[0:XT], ALU.mult, ALU.mult).then_inc(s_y, 1)


class Kit:

    BASE = 16512

    def __init__(self, nc, ctx):
        self.nc, self.ctx, self.low, self.stage_sems = nc, ctx, 0, []

    def at(self, name, offset, shape, dtype=F32):
        return self.nc.alloc_sbuf_tensor_at(name, shape, dtype, offset=self.BASE + offset)

    def sb(self, name, shape, dtype=F32):
        t = self.at(name, self.low, shape, dtype)
        size = 4
        for n in shape[1:]:
            size *= n
        self.low += (size + 31) // 32 * 32
        assert self.low <= self.HT_OFF
        return t

    def sem(self, name):
        s = self.nc.alloc_semaphore(name)
        self.stage_sems.append(s)
        return s

    def end_sems(self):
        self.nc.clear_and_free_semaphores(self.stage_sems)
        self.nc.all_engine_barrier()
        self.stage_sems = []

    HT_OFF = 15104
    ROWS_OFF = HT_OFF + KD * TOK * 4
    KT_OFF = ROWS_OFF + TT * R_END * 4
    VA_OFF = KT_OFF + 4 * TOK * 4
    AQ_OFF = VA_OFF + (TT * MH * (MD + 1) * 4 + 31) // 32 * 32
    X_OFF = AQ_OFF
    AT_OFF = AQ_OFF + HG * TOK * 4
    QK_OFF = AT_OFF + MH * TOK * 4
    RING_OFF = QK_OFF + 8 * TOK * 4
    PACK_OFF = RING_OFF + NB * MH * (MD + 1) * 4
    WORK_OFF = PACK_OFF + 2 * TOK * 4
    CMP_OFF = KT_OFF + 2 * TOK * 4
    CMP_END = QK_OFF + (HD + GD) * 4
    TOP = 229376 - 16512 - 32
    OUT_OFF = TOP - TT * O_END * 4


STAGES = [stage_norm_in, stage_token_major, stage_feature_major, stage_gates, stage_mlstm, stage_nsa_prompt,
          stage_nsa_samples, stage_merge, stage_ffn, stage_final]


def build(nc, ins, outs):
    with ExitStack() as ctx:
        k = Kit(nc, ctx)
        (k.x_prompt, k.x_sample, k.cache_k_cmp, k.cache_v_cmp, k.cache_k_slc, k.cache_v_slc, k.state_k_win,
         k.state_v_win, k.state_conv, k.state_C, k.state_n, k.state_m, k.page_table, k.norm_mix, k.w_in, k.b_in,
         k.conv_w, k.conv_b, k.cmp_pos_k, k.cmp_pos_v, k.cmp_proj_k, k.cmp_proj_v, k.m_norm, k.w_a, k.w_b, k.w_o,
         k.norm_ffn, k.w_ffn_in, k.w_ffn_out, k.norm_final) = ins
        k.y_prompt, k.y_sample = outs[0:2]
        (k.o_k_cmp, k.o_v_cmp, k.o_k_slc, k.o_v_slc, k.o_k_win, k.o_v_win, k.o_conv, k.o_C, k.o_n, k.o_m) = [
            tuple(outs[2 + 2 * n:4 + 2 * n]) for n in range(10)]
        k.ps = ctx.enter_context(nc.psum_tensor("banks", [P, 8, 512], F32))
        k.rows_stored, k.windows_stored, k.tail_stored, k.m_stored, k.states_stored = [
            ctx.enter_context(nc.semaphore(f"{name}_stored")) for name in ("rows", "windows", "tail", "m", "states")]
        k.y_stored = [ctx.enter_context(nc.semaphore(f"y_stored{i}")) for i in range(3)]
        place_constants(k)
        k.select = k.sb("select_head", [P, MH, P])
        k.gate_cols = k.sb("gate_cols", [P, TT, 4, MH])
        k.decay, k.decay_row = k.sb("decay", [P, MH, QT + NB]), k.sb("decay_row", [MH, QT + NB])
        k.m_c, k.m_s0, k.m_s1 = k.sb("m_chunks", [MH, QT + 1]), k.sb("m_samples", [MH, NB]), k.sb("m_samples_new", [MH, NB])
        k.gates, k.page_idx = k.sb("branch_gates", [P, TT, NH, 3]), k.sb("page_idx", [P, NB], I32)
        k.SPARE_OFF = k.low
        k.hT = k.at("hT", k.HT_OFF, [P, KD, TOK])
        k.rows = k.at("token_rows", k.ROWS_OFF, [P, TT, R_END])
        k.rows_out = k.at("token_rows_out", k.OUT_OFF, [P, TT, O_END])
        k.kT = k.at("kT_slc_win", k.KT_OFF, [P, 2, TOK])
        k.kc_s = k.at("kcT_samples", k.CMP_OFF, [P, NB, P])
        k.vc_s = k.at("vc_samples", k.CMP_OFF + NB * P * 4, [P, NB, GD])
        k.v_aug = k.at("v_and_ones", k.VA_OFF, [P, TT, MH, MD + 1])
        k.aq = k.at("nsa_qT", k.AQ_OFF, [P, HG, TOK])
        k.aT = k.at("mlstm_outT", k.AT_OFF, [P, MH, TOK])
        k.qk = k.at("mlstm_qkT", k.QK_OFF, [P, 8, TOK])
        k.packed = k.at("gates_packed", k.PACK_OFF, [P, TOK])
        k.neg_m = k.at("neg_m", k.PACK_OFF + TOK * 4, [MH, TOK])
        k.kT_last = k.at("kT_new_rows", k.VA_OFF + HG * TOK * 4, [P, 2, NS_TOK])
        k.bT = k.at("nsa_outT", k.VA_OFF, [P, HG, TOK])
        k.kc_p = k.at("kcT_prompt", k.QK_OFF, [P, HD])
        k.vc_p = k.at("vc_prompt", k.QK_OFF + HD * 4, [P, GD])
        k.x1 = k.at("x1T", k.HT_OFF, [P, KD, TOK])
        k.rs = k.at("x1_rstd", k.SPARE2_OFF, [P, TOK])
        with nc.allow_non_contiguous_dma(reason="small vectors and states"):
            for stage in STAGES:
                stage(k)
                if stage in (stage_mlstm, stage_nsa_samples):
                    k.end_sems()


_INS = ["x_prompt", "x_sample", "cache_k_cmp", "cache_v_cmp", "cache_k_slc", "cache_v_slc", "state_k_win",
        "state_v_win", "state_conv", "state_C", "state_n", "state_m", "page_table", "norm_mix", "w_in", "b_in",
        "conv_w", "conv_b", "cmp_pos_k", "cmp_pos_v", "cmp_proj_k", "cmp_proj_v", "m_norm", "w_a", "w_b", "w_o",
        "norm_ffn", "w_ffn_in", "w_ffn_out", "norm_final"]
_OUTS = [(1, SEQ, DM), (NB, NT, DM)]
for _ in range(4):
    _OUTS += [(1, 1, SEQ, NG, HD), (1, NB, NT, NG, HD)]
for _ in range(2):
    _OUTS += [(1, 1, WIN, NG, HD), (1, NB, WIN, NG, HD)]
_OUTS += [(1, 1, CW - 1, 2 * DA), (1, NB, CW - 1, 2 * DA), (1, 1, MH, MD, MD), (1, NB, MH, MD, MD),
          (1, 1, MH, MD), (1, NB, MH, MD), (1, 1, MH), (1, NB, MH)]


def kernel(**inputs):
    import numpy as _np
    import concourse.bacc as _bacc
    from concourse import mybir as _mybir
    from concourse.bass_utils import run_bass_kernel_spmd as _run

    nc = _bacc.Bacc("TRN2", target_bir_lowering=False, num_devices=1)
    arrays, ins, outs = {}, [], []
    for name in _INS:
        a = _np.ascontiguousarray(inputs[name])
        arrays[f"in_{name}_dram"] = a
        ins.append(nc.dram_tensor(f"in_{name}_dram", a.shape, _mybir.dt.from_np(a.dtype), kind="ExternalInput").ap())
    for i, shape in enumerate(_OUTS):
        outs.append(nc.dram_tensor(f"out_{i}_dram", shape, _mybir.dt.float32, kind="ExternalOutput").ap())
    build(nc, ins, outs)
    r = _run(nc, [arrays], core_ids=[0])
    return tuple(r.results[0][f"out_{i}_dram"] for i in range(len(_OUTS)))
```
